# Optimizing a Trainium2 kernel written in Bass

```python
import jax, jax.numpy as jnp
from jax import lax
import numpy as np
import math
import functools
import jax
import jax.numpy as jnp

D_MODEL = 1024
BATCH = 1
SEQ = 512
DEPTH = 2

HEAD_DIM = 64
A_HEADS = 8
A_KV_HEADS = 2
B_GROUPS = ((128, 1), (512, 4), (2048, 16))
B_HEADS_PER_GROUP = 4
B_HEADS = len(B_GROUPS) * B_HEADS_PER_GROUP
GRID_W = 64
ROPE_THETA = 10000.0
Q_BLOCK = 128
N_EXPERTS = 16
N_GROUPS = 4
EXPERTS_PER_GROUP = N_EXPERTS // N_GROUPS
TOP_K = 2
D_EXPERT = 256
LN_EPS = 1e-5
RMS_EPS = 1e-6
DN_ALPHA = (2.0 * DEPTH) ** 0.25
DN_BETA = (8.0 * DEPTH) ** -0.25

A_Q = A_HEADS * HEAD_DIM
A_KV = A_KV_HEADS * HEAD_DIM
B_W = B_HEADS * HEAD_DIM
B_OUT = B_HEADS_PER_GROUP * HEAD_DIM
N_IN = A_Q + 2 * A_KV + 3 * B_W + 2 * D_MODEL
IN_SPLITS = (A_Q, A_Q + A_KV, A_Q + 2 * A_KV, A_Q + 2 * A_KV + B_W,
             A_Q + 2 * A_KV + 2 * B_W, A_Q + 2 * A_KV + 3 * B_W)


def _layer_norm(x, g=None, b=None):
    xf = x.astype(jnp.float32)
    mu = jnp.mean(xf, -1, keepdims=True)
    var = jnp.mean(jnp.square(xf - mu), -1, keepdims=True)
    y = (xf - mu) * lax.rsqrt(var + LN_EPS)
    if g is not None:
        y = y * g.astype(jnp.float32) + b.astype(jnp.float32)
    return y.astype(x.dtype)

def _rms_norm(x, g):
    xf = x.astype(jnp.float32)
    y = xf * lax.rsqrt(jnp.mean(jnp.square(xf), -1, keepdims=True) + RMS_EPS)
    return (y * g.astype(jnp.float32)).astype(x.dtype)

def _axial_rope_tables(seq):
    rows = seq // GRID_W
    row = jnp.repeat(jnp.arange(rows), GRID_W).astype(jnp.float32)
    col = jnp.tile(jnp.arange(GRID_W), rows).astype(jnp.float32)
    axis_dim = HEAD_DIM // 2
    inv = ROPE_THETA ** (-jnp.arange(0, axis_dim, 2, dtype=jnp.float32) / axis_dim)
    ang = jnp.concatenate([row[:, None] * inv, col[:, None] * inv], -1)
    return jnp.cos(ang), jnp.sin(ang)

def _apply_rope(x, cos, sin):
    xf = x.astype(jnp.float32).reshape(x.shape[:-1] + (HEAD_DIM // 2, 2))
    x0, x1 = xf[..., 0], xf[..., 1]
    c = cos[None, :, None, :]
    s = sin[None, :, None, :]
    out = jnp.stack([x0 * c - x1 * s, x0 * s + x1 * c], -1).reshape(x.shape)
    return out.astype(x.dtype)

def _alibi_slopes(n):
    return jnp.exp2(-8.0 * jnp.arange(1, n + 1, dtype=jnp.float32) / n)

def _global_gqa(q, k, v):
    b, s = q.shape[0], q.shape[1]
    rep = A_HEADS // A_KV_HEADS
    nblk = s // Q_BLOCK
    scale = HEAD_DIM ** -0.5
    qb = q.reshape(b, nblk, Q_BLOCK, A_KV_HEADS, rep, HEAD_DIM).transpose(1, 0, 2, 3, 4, 5)

    def block(qi):
        sc = jnp.einsum('bqgrd,bkgd->bgrqk', qi, k).astype(jnp.float32) * scale
        p = jax.nn.softmax(sc, axis=-1)
        return jnp.einsum('bgrqk,bkgd->bqgrd', p.astype(v.dtype), v)

    o = lax.map(block, qb)
    return o.transpose(1, 0, 2, 3, 4, 5).reshape(b, s, A_Q)

def _dilated_group(q, k, v, window, dilation, slopes):
    b, s, h = q.shape[0], q.shape[1], q.shape[2]
    reach = window // (2 * dilation)
    offs = dilation * jnp.arange(-reach, reach + 1)
    nblk = s // Q_BLOCK
    scale = HEAD_DIM ** -0.5
    qb = q.reshape(b, nblk, Q_BLOCK, h, HEAD_DIM).transpose(1, 0, 2, 3, 4)
    starts = jnp.arange(nblk) * Q_BLOCK
    bias = -slopes[:, None] * jnp.abs(offs).astype(jnp.float32)[None, :]

    def block(args):
        qi, t0 = args
        pos = t0 + jnp.arange(Q_BLOCK)[:, None] + offs[None, :]
        valid = (pos >= 0) & (pos < s)
        idx = jnp.clip(pos, 0, s - 1)
        kg = jnp.take(k, idx, axis=1)
        vg = jnp.take(v, idx, axis=1)
        sc = jnp.einsum('bqhd,bqkhd->bhqk', qi, kg).astype(jnp.float32) * scale + bias[None, :, None, :]
        sc = jnp.where(valid[None, None], sc, -jnp.inf)
        lse = jax.nn.logsumexp(sc, axis=-1)
        p = jnp.exp(sc - lse[..., None])
        o = jnp.einsum('bhqk,bqkhd->bqhd', p.astype(v.dtype), vg)
        return o, lse.transpose(0, 2, 1)

    o, lse = lax.map(block, (qb, starts))
    o = o.transpose(1, 0, 2, 3, 4).reshape(b, s, h, HEAD_DIM)
    lse = lse.transpose(1, 0, 2, 3).reshape(b, s, h)
    return o, lse

def _mixer(h, w_in, qn_g, kn_g, w_pa, w_pb, w_o, cos, sin, slopes):
    b, s, _ = h.shape
    proj = h @ w_in
    qa, ka, va, qd, kd, vd, gates = jnp.split(proj, IN_SPLITS, axis=-1)
    qa = _apply_rope(_rms_norm(qa.reshape(b, s, A_HEADS, HEAD_DIM), qn_g), cos, sin)
    ka = _apply_rope(_rms_norm(ka.reshape(b, s, A_KV_HEADS, HEAD_DIM), kn_g), cos, sin)
    va = va.reshape(b, s, A_KV_HEADS, HEAD_DIM)
    out_a = _global_gqa(qa, ka, va)
    qd = qd.reshape(b, s, B_HEADS, HEAD_DIM)
    kd = kd.reshape(b, s, B_HEADS, HEAD_DIM)
    vd = vd.reshape(b, s, B_HEADS, HEAD_DIM)
    outs, lses = [], []
    for g, (window, dilation) in enumerate(B_GROUPS):
        sl = slice(g * B_HEADS_PER_GROUP, (g + 1) * B_HEADS_PER_GROUP)
        o, l = _dilated_group(qd[:, :, sl], kd[:, :, sl], vd[:, :, sl], window, dilation, slopes[sl])
        outs.append(o)
        lses.append(l)
    wts = jax.nn.softmax(jnp.stack(lses, 0), axis=0)
    out_b = jnp.sum(wts[..., None].astype(h.dtype) * jnp.stack(outs, 0), 0).reshape(b, s, B_OUT)
    g_a, g_b = jnp.split(jax.nn.sigmoid(gates), 2, axis=-1)
    merged = g_a * (out_a @ w_pa) + g_b * (out_b @ w_pb)
    return merged @ w_o

def _moe(h, w_router, router_bias, w_gate, w_up, w_down):
    b, s, d = h.shape
    t = h.reshape(b * s, d)
    scores = jax.nn.sigmoid((t @ w_router).astype(jnp.float32))
    sel = scores + router_bias.astype(jnp.float32)
    grp_score = jnp.sum(lax.top_k(sel.reshape(-1, N_GROUPS, EXPERTS_PER_GROUP), TOP_K)[0], -1)
    best = jnp.argmax(grp_score, axis=-1)
    in_group = (jnp.arange(N_EXPERTS) // EXPERTS_PER_GROUP)[None, :] == best[:, None]
    _, idx = lax.top_k(jnp.where(in_group, sel, -jnp.inf), TOP_K)
    top_s = jnp.take_along_axis(scores, idx, axis=-1)
    gate = top_s / jnp.sum(top_s, -1, keepdims=True)
    combine = jnp.sum(jax.nn.one_hot(idx, N_EXPERTS, dtype=jnp.float32) * gate[..., None], 1)
    hg = jnp.einsum('td,edf->tef', t, w_gate)
    hu = jnp.einsum('td,edf->tef', t, w_up)
    act = jax.nn.silu(hg) * hu * combine[..., None].astype(t.dtype)
    y = jnp.einsum('tef,efd->td', act, w_down)
    return y.reshape(b, s, d)

def first_inputs(seed: int = 0) -> dict:
    key = jax.random.key(seed)
    ks = jax.random.split(key, 24)
    f32 = jnp.float32
    n = lambda k, shape, sc: jax.random.normal(k, shape, f32) * sc
    d = D_MODEL
    return {
        "x": n(ks[0], (BATCH, SEQ, d), 1.0),
        "c": n(ks[1], (BATCH, d), 1.0),
        "w_ada": n(ks[2], (DEPTH, d, 6 * d), 0.5 * d ** -0.5),
        "b_ada": n(ks[3], (DEPTH, 6 * d), 0.02),
        "w_in": n(ks[4], (DEPTH, d, N_IN), d ** -0.5),
        "q_norm_g": 1.0 + n(ks[5], (DEPTH, HEAD_DIM), 0.02),
        "k_norm_g": 1.0 + n(ks[6], (DEPTH, HEAD_DIM), 0.02),
        "w_branch_a": n(ks[7], (DEPTH, A_Q, d), A_Q ** -0.5),
        "w_branch_b": n(ks[8], (DEPTH, B_OUT, d), B_OUT ** -0.5),
        "w_out": n(ks[9], (DEPTH, d, d), DN_BETA * d ** -0.5),
        "ln1_g": 1.0 + n(ks[10], (DEPTH, d), 0.02),
        "ln1_b": n(ks[11], (DEPTH, d), 0.02),
        "w_router": n(ks[12], (d, N_EXPERTS), d ** -0.5),
        "router_bias": n(ks[13], (N_EXPERTS,), 0.01),
        "w_exp_gate": n(ks[14], (DEPTH, N_EXPERTS, d, D_EXPERT), d ** -0.5),
        "w_exp_up": n(ks[15], (DEPTH, N_EXPERTS, d, D_EXPERT), d ** -0.5),
        "w_exp_down": n(ks[16], (DEPTH, N_EXPERTS, D_EXPERT, d), DN_BETA * D_EXPERT ** -0.5),
        "ln2_g": 1.0 + n(ks[17], (DEPTH, d), 0.02),
        "ln2_b": n(ks[18], (DEPTH, d), 0.02),
    }

def first_block(x, c, w_ada, b_ada, w_in, q_norm_g, k_norm_g, w_branch_a, w_branch_b, w_out,
              ln1_g, ln1_b, w_router, router_bias, w_exp_gate, w_exp_up, w_exp_down, ln2_g, ln2_b):
    s = x.shape[1]
    cos, sin = _axial_rope_tables(s)
    slopes = _alibi_slopes(B_HEADS)
    cond = jax.nn.silu(c)
    for l in range(DEPTH):
        mod = cond @ w_ada[l] + b_ada[l]
        sh1, sc1, g1, sh2, sc2, g2 = [m[:, None, :] for m in jnp.split(mod, 6, axis=-1)]
        h = _layer_norm(x) * (1.0 + sc1) + sh1
        mix = _mixer(h, w_in[l], q_norm_g[l], k_norm_g[l], w_branch_a[l], w_branch_b[l],
                     w_out[l], cos, sin, slopes)
        x = _layer_norm(DN_ALPHA * x + g1 * mix, ln1_g[l], ln1_b[l])
        h = _layer_norm(x) * (1.0 + sc2) + sh2
        ffn = _moe(h, w_router, router_bias, w_exp_gate[l], w_exp_up[l], w_exp_down[l])
        x = _layer_norm(DN_ALPHA * x + g2 * ffn, ln2_g[l], ln2_b[l])
    return x


EPS = 1e-6
D_FF = 4 * D_MODEL
N_EVEN = (DEPTH + 1) // 2
N_ODD = DEPTH // 2
CHUNK = 128
BLOCK_Q = 128

REL_BUCKETS = 32
REL_MAX_DIST = 128
N_BIAS_HEADS = 8

SSD_D_INNER = D_MODEL
SSD_HEAD_DIM = 64
SSD_HEADS = SSD_D_INNER // SSD_HEAD_DIM
SSD_GROUPS = 4
SSD_STATE = 128
SSD_CONV = 4
SSD_CONV_CH = SSD_D_INNER + 2 * SSD_GROUPS * SSD_STATE

DIFF_HEADS = N_BIAS_HEADS
DIFF_HEAD_DIM = D_MODEL // (2 * DIFF_HEADS)
DIFF_QK = DIFF_HEADS * 2 * DIFF_HEAD_DIM
DIFF_V = DIFF_HEADS * 2 * DIFF_HEAD_DIM

EVEN_SPLITS = (SSD_D_INNER, SSD_CONV_CH, SSD_HEADS, DIFF_QK, DIFF_QK, DIFF_V)
EVEN_IN = sum(EVEN_SPLITS)
EVEN_MIX = SSD_D_INNER + DIFF_V

RET_HEADS = 4
RET_QK_DIM = 128
RET_V_DIM = 256
ROPE_BASE = 10000.0

SWA_HEADS = N_BIAS_HEADS
SWA_KV_HEADS = 2
SWA_HEAD_DIM = 64
WINDOW = 128

ODD_SPLITS = (RET_HEADS * RET_QK_DIM, RET_HEADS * RET_QK_DIM, RET_HEADS * RET_V_DIM,
              RET_HEADS * RET_V_DIM, SWA_HEADS * SWA_HEAD_DIM,
              SWA_KV_HEADS * SWA_HEAD_DIM, SWA_KV_HEADS * SWA_HEAD_DIM)
ODD_IN = sum(ODD_SPLITS)
ODD_MIX = RET_HEADS * RET_V_DIM + SWA_HEADS * SWA_HEAD_DIM


def rms_norm(x, w=None):
    x32 = x.astype(jnp.float32)
    y = x32 * lax.rsqrt(jnp.mean(x32 * x32, axis=-1, keepdims=True) + EPS)
    if w is not None:
        y = y * w.astype(jnp.float32)
    return y.astype(x.dtype)

def split_cols(a, sizes):
    return jnp.split(a, np.cumsum(sizes)[:-1].tolist(), axis=-1)

def t5_bucket(dist):
    dist = jnp.maximum(dist, 0)
    max_exact = REL_BUCKETS // 2
    logd = jnp.log(jnp.maximum(dist, 1).astype(jnp.float32) / max_exact)
    large = max_exact + (logd / math.log(REL_MAX_DIST / max_exact)
                         * (REL_BUCKETS - max_exact)).astype(jnp.int32)
    large = jnp.minimum(large, REL_BUCKETS - 1)
    return jnp.where(dist < max_exact, dist, large)

def scan_chunk_states(chunk_states, chunk_decay):
    def step(carry, inp):
        st, dec = inp
        return carry * dec + st, carry
    init = jnp.zeros_like(chunk_states[:, 0])
    _, prev = lax.scan(step, init, (jnp.moveaxis(chunk_states, 1, 0), jnp.moveaxis(chunk_decay, 1, 0)))
    return jnp.moveaxis(prev, 0, 1)

def causal_depthwise_conv(x, w, b):
    ch = x.shape[-1]
    out = lax.conv_general_dilated(x, w[:, None, :].astype(x.dtype), window_strides=(1,),
                                   padding=[(SSD_CONV - 1, 0)],
                                   dimension_numbers=("NWC", "WIO", "NWC"),
                                   feature_group_count=ch)
    return out + b.astype(x.dtype)

def ssd_chunked(xh, dt, A, Bg, Cg):
    b, s, h, p = xh.shape
    g, n = Bg.shape[-2:]
    r = h // g
    nc = s // CHUNK
    X = (xh * dt[..., None]).reshape(b, nc, CHUNK, g, r, p)
    Bc = Bg.reshape(b, nc, CHUNK, g, n)
    Cc = Cg.reshape(b, nc, CHUNK, g, n)
    a_cs = jnp.cumsum((dt * A).reshape(b, nc, CHUNK, g, r), axis=2)
    causal = jnp.tril(jnp.ones((CHUNK, CHUNK), dtype=bool))
    seg = a_cs[:, :, :, None] - a_cs[:, :, None, :]
    decay_in = jnp.exp(jnp.where(causal[:, :, None, None], seg, -jnp.inf))
    cb = jnp.einsum("bclgn,bcsgn->bclsg", Cc, Bc)
    y_diag = jnp.einsum("bclsg,bclsgr,bcsgrp->bclgrp", cb, decay_in, X)
    decay_to_end = jnp.exp(a_cs[:, :, -1:] - a_cs)
    chunk_states = jnp.einsum("bcsgn,bcsgr,bcsgrp->bcgrpn", Bc, decay_to_end, X)
    state_prev = scan_chunk_states(chunk_states, jnp.exp(a_cs[:, :, -1])[..., None, None])
    y_off = jnp.einsum("bclgn,bcgrpn,bclgr->bclgrp", Cc, state_prev, jnp.exp(a_cs))
    return (y_diag + y_off).reshape(b, s, h, p)

def ssd_mixer(z, xbc, dt_raw, conv_w, conv_b, dt_bias, A_log, D_skip, norm_w):
    b, s, _ = z.shape
    xbc = jax.nn.silu(causal_depthwise_conv(xbc, conv_w, conv_b))
    xs, Bs, Cs = split_cols(xbc, (SSD_D_INNER, SSD_GROUPS * SSD_STATE, SSD_GROUPS * SSD_STATE))
    xh = xs.astype(jnp.float32).reshape(b, s, SSD_HEADS, SSD_HEAD_DIM)
    dt = jax.nn.softplus(dt_raw.astype(jnp.float32) + dt_bias.astype(jnp.float32))
    A = -jnp.exp(A_log.astype(jnp.float32))
    y = ssd_chunked(xh, dt, A,
                    Bs.astype(jnp.float32).reshape(b, s, SSD_GROUPS, SSD_STATE),
                    Cs.astype(jnp.float32).reshape(b, s, SSD_GROUPS, SSD_STATE))
    y = y + xh * D_skip.astype(jnp.float32)[:, None]
    y = y.reshape(b, s, SSD_D_INNER) * jax.nn.silu(z.astype(jnp.float32))
    return rms_norm(y, norm_w).astype(z.dtype)

def diff_attention(q, k, v, lam, subln_w, rel_bias, layer_idx):
    b, s = q.shape[:2]
    lam_init = 0.8 - 0.6 * math.exp(-0.3 * layer_idx)
    lam32 = lam.astype(jnp.float32)
    lam_full = (jnp.exp(jnp.sum(lam32[0] * lam32[1])) - jnp.exp(jnp.sum(lam32[2] * lam32[3])) + lam_init)
    q32 = q.astype(jnp.float32) * DIFF_HEAD_DIM ** -0.5
    k32 = k.astype(jnp.float32)
    v32 = v.astype(jnp.float32)
    nb = s // BLOCK_Q
    q_blocks = jnp.moveaxis(q32.reshape(b, nb, BLOCK_Q, DIFF_HEADS, 2, DIFF_HEAD_DIM), 1, 0)
    key_pos = jnp.arange(s)

    def one_block(args):
        q_blk, blk = args
        dist = (blk * BLOCK_Q + jnp.arange(BLOCK_Q))[:, None] - key_pos[None, :]
        bias = jnp.transpose(rel_bias[t5_bucket(dist)], (2, 0, 1)).astype(jnp.float32)
        logits = jnp.einsum("bqhmd,bkhmd->bhmqk", q_blk, k32) + bias[None, :, None]
        logits = jnp.where(dist >= 0, logits, -jnp.inf)
        p = jax.nn.softmax(logits, axis=-1)
        attn = p[:, :, 0] - lam_full * p[:, :, 1]
        return jnp.einsum("bhqk,bkhe->bqhe", attn, v32)

    out = lax.map(one_block, (q_blocks, jnp.arange(nb)))
    out = jnp.moveaxis(out, 0, 1).reshape(b, s, DIFF_HEADS, 2 * DIFF_HEAD_DIM)
    out = rms_norm(out, subln_w) * (1.0 - lam_init)
    return out.reshape(b, s, DIFF_V).astype(q.dtype)

def rope(t, pos):
    half = t.shape[-1] // 2
    inv = ROPE_BASE ** (-jnp.arange(half, dtype=jnp.float32) / half)
    ang = pos[:, None] * inv[None]
    cos = jnp.cos(ang)[None, :, None]
    sin = jnp.sin(ang)[None, :, None]
    t1, t2 = t[..., :half], t[..., half:]
    return jnp.concatenate([t1 * cos - t2 * sin, t1 * sin + t2 * cos], axis=-1)

def retention(q, k, v):
    b, s = q.shape[:2]
    nc = s // CHUNK
    pos = jnp.arange(s, dtype=jnp.float32)
    Q = rope(q.astype(jnp.float32), pos).reshape(b, nc, CHUNK, RET_HEADS, RET_QK_DIM)
    K = (rope(k.astype(jnp.float32), pos) * RET_QK_DIM ** -0.5).reshape(b, nc, CHUNK, RET_HEADS, RET_QK_DIM)
    V = v.astype(jnp.float32).reshape(b, nc, CHUNK, RET_HEADS, RET_V_DIM)
    log_gamma = jnp.log(1.0 - 2.0 ** (-5.0 - jnp.arange(RET_HEADS, dtype=jnp.float32)))
    idx = jnp.arange(CHUNK, dtype=jnp.float32)
    rel = idx[:, None] - idx[None, :]
    decay_mat = jnp.where(rel >= 0, jnp.exp(jnp.maximum(rel, 0.0)[None] * log_gamma[:, None, None]), 0.0)
    scores = jnp.einsum("bclhd,bcshd->bchls", Q, K) * decay_mat
    inner = jnp.einsum("bchls,bcshe->bclhe", scores, V)
    zeta = jnp.exp((CHUNK - 1 - idx)[None] * log_gamma[:, None])
    kv = jnp.einsum("bcshd,hs,bcshe->bchde", K, zeta, V)
    chunk_decay = jnp.broadcast_to(jnp.exp(CHUNK * log_gamma)[:, None, None], (b, nc, RET_HEADS, 1, 1))
    state_prev = scan_chunk_states(kv, chunk_decay)
    xi = jnp.exp((idx + 1.0)[None] * log_gamma[:, None])
    cross = jnp.einsum("bclhd,bchde,hl->bclhe", Q, state_prev, xi)
    out = (inner + cross).reshape(b, s, RET_HEADS, RET_V_DIM)
    return rms_norm(out).reshape(b, s, RET_HEADS * RET_V_DIM)

def sliding_window_attention(q, k, v, sinks, rel_bias):
    b, s = q.shape[:2]
    rep = SWA_HEADS // SWA_KV_HEADS
    nb = s // BLOCK_Q
    q32 = q.astype(jnp.float32).reshape(b, nb, BLOCK_Q, SWA_KV_HEADS, rep, SWA_HEAD_DIM) * SWA_HEAD_DIM ** -0.5

    def band(t):
        t = jnp.pad(t.astype(jnp.float32), ((0, 0), (BLOCK_Q, 0), (0, 0), (0, 0)))
        t = t.reshape(b, nb + 1, BLOCK_Q, SWA_KV_HEADS, SWA_HEAD_DIM)
        return jnp.concatenate([t[:, :-1], t[:, 1:]], axis=2)

    kb, vb = band(k), band(v)
    q_off = jnp.arange(BLOCK_Q)
    k_off = jnp.arange(2 * BLOCK_Q) - BLOCK_Q
    dist = q_off[:, None] - k_off[None, :]
    k_pos = (jnp.arange(nb) * BLOCK_Q)[:, None] + k_off[None, :]
    valid = ((dist >= 0) & (dist < WINDOW))[None] & (k_pos >= 0)[:, None, :]
    bias = jnp.transpose(rel_bias[t5_bucket(dist)], (2, 0, 1)).astype(jnp.float32)
    bias = bias.reshape(SWA_KV_HEADS, rep, BLOCK_Q, 2 * BLOCK_Q)
    logits = jnp.einsum("bnqgrd,bnkgd->bngrqk", q32, kb) + bias
    logits = jnp.where(valid[None, :, None, None], logits, -jnp.inf)
    sink = jnp.broadcast_to(sinks.astype(jnp.float32).reshape(1, 1, SWA_KV_HEADS, rep, 1, 1),
                            logits.shape[:-1] + (1,))
    p = jax.nn.softmax(jnp.concatenate([logits, sink], axis=-1), axis=-1)[..., :-1]
    out = jnp.einsum("bngrqk,bnkgd->bnqgrd", p, vb)
    return out.reshape(b, s, SWA_HEADS * SWA_HEAD_DIM).astype(q.dtype)

def even_mixer(h, w_in, conv_w, conv_b, dt_bias, A_log, D_skip, ssd_norm, lam, diff_norm, w_out,
               rel_bias, layer_idx):
    b, s, _ = h.shape
    z, xbc, dt_raw, q, k, v = split_cols(h @ w_in, EVEN_SPLITS)
    y_ssd = ssd_mixer(z, xbc, dt_raw, conv_w, conv_b, dt_bias, A_log, D_skip, ssd_norm)
    y_diff = diff_attention(q.reshape(b, s, DIFF_HEADS, 2, DIFF_HEAD_DIM),
                            k.reshape(b, s, DIFF_HEADS, 2, DIFF_HEAD_DIM),
                            v.reshape(b, s, DIFF_HEADS, 2 * DIFF_HEAD_DIM),
                            lam, diff_norm, rel_bias, layer_idx)
    return jnp.concatenate([y_ssd, y_diff], axis=-1) @ w_out

def odd_mixer(h, w_in, sinks, w_out, rel_bias):
    b, s, _ = h.shape
    rq, rk, rv, rg, sq, sk, sv = split_cols(h @ w_in, ODD_SPLITS)
    y_ret = retention(rq.reshape(b, s, RET_HEADS, RET_QK_DIM),
                      rk.reshape(b, s, RET_HEADS, RET_QK_DIM),
                      rv.reshape(b, s, RET_HEADS, RET_V_DIM))
    y_ret = (y_ret * jax.nn.silu(rg.astype(jnp.float32))).astype(h.dtype)
    y_swa = sliding_window_attention(sq.reshape(b, s, SWA_HEADS, SWA_HEAD_DIM),
                                     sk.reshape(b, s, SWA_KV_HEADS, SWA_HEAD_DIM),
                                     sv.reshape(b, s, SWA_KV_HEADS, SWA_HEAD_DIM),
                                     sinks, rel_bias)
    return jnp.concatenate([y_ret, y_swa], axis=-1) @ w_out

def squared_relu_mlp(h, w1, w2):
    return jnp.square(jax.nn.relu(h @ w1)) @ w2

def sandwich(x, c_act, sublayer, g_pre, g_post, w_mod, b_mod):
    shift, scale, gate = jnp.split(c_act @ w_mod + b_mod, 3, axis=-1)
    h = rms_norm(x, g_pre) * (1 + scale[:, None]) + shift[:, None]
    return x + gate[:, None] * rms_norm(sublayer(h), g_post)

def second_inputs(seed: int = 0) -> dict:
    key = jax.random.key(seed)
    ks = jax.random.split(key, 24)

    def nrm(k, shape, scale):
        return jax.random.normal(k, shape, jnp.float32) * scale

    dt0 = jnp.exp(jax.random.uniform(ks[11], (N_EVEN, SSD_HEADS), jnp.float32,
                                     minval=math.log(1e-3), maxval=math.log(1e-1)))
    return {
        "x": nrm(ks[0], (BATCH, SEQ, D_MODEL), 1.0),
        "c": nrm(ks[1], (BATCH, D_MODEL), 1.0),
        "rel_bias": nrm(ks[2], (REL_BUCKETS, N_BIAS_HEADS), 0.5),
        "norm_gains": 1.0 + nrm(ks[3], (DEPTH, 4, D_MODEL), 0.05),
        "mod_w": nrm(ks[4], (DEPTH, 2, D_MODEL, 3 * D_MODEL), D_MODEL ** -0.5),
        "mod_b": nrm(ks[5], (DEPTH, 2, 3 * D_MODEL), 0.02),
        "mlp_w1": nrm(ks[6], (DEPTH, D_MODEL, D_FF), D_MODEL ** -0.5),
        "mlp_w2": nrm(ks[7], (DEPTH, D_FF, D_MODEL), D_FF ** -0.5),
        "e_w_in": nrm(ks[8], (N_EVEN, D_MODEL, EVEN_IN), D_MODEL ** -0.5),
        "e_conv_w": nrm(ks[9], (N_EVEN, SSD_CONV, SSD_CONV_CH), SSD_CONV ** -0.5),
        "e_conv_b": nrm(ks[10], (N_EVEN, SSD_CONV_CH), 0.02),
        "e_dt_bias": dt0 + jnp.log(-jnp.expm1(-dt0)),
        "e_A_log": jnp.log(jax.random.uniform(ks[12], (N_EVEN, SSD_HEADS), jnp.float32, minval=1.0, maxval=16.0)),
        "e_D": 1.0 + nrm(ks[13], (N_EVEN, SSD_HEADS), 0.05),
        "e_ssd_norm": 1.0 + nrm(ks[14], (N_EVEN, SSD_D_INNER), 0.05),
        "e_lambda": nrm(ks[15], (N_EVEN, 4, DIFF_HEAD_DIM), 0.1),
        "e_diff_norm": 1.0 + nrm(ks[16], (N_EVEN, 2 * DIFF_HEAD_DIM), 0.05),
        "e_w_out": nrm(ks[17], (N_EVEN, EVEN_MIX, D_MODEL), EVEN_MIX ** -0.5),
        "o_w_in": nrm(ks[18], (N_ODD, D_MODEL, ODD_IN), D_MODEL ** -0.5),
        "o_sinks": nrm(ks[19], (N_ODD, SWA_HEADS), 0.5),
        "o_w_out": nrm(ks[20], (N_ODD, ODD_MIX, D_MODEL), ODD_MIX ** -0.5),
    }

def second_block(x, c, rel_bias, norm_gains, mod_w, mod_b, mlp_w1, mlp_w2, e_w_in, e_conv_w, e_conv_b,
              e_dt_bias, e_A_log, e_D, e_ssd_norm, e_lambda, e_diff_norm, e_w_out, o_w_in, o_sinks,
              o_w_out):
    c_act = jax.nn.silu(c)
    for layer in range(DEPTH):
        j = layer // 2
        if layer % 2 == 0:
            mixer = functools.partial(even_mixer, w_in=e_w_in[j], conv_w=e_conv_w[j], conv_b=e_conv_b[j],
                                      dt_bias=e_dt_bias[j], A_log=e_A_log[j], D_skip=e_D[j],
                                      ssd_norm=e_ssd_norm[j], lam=e_lambda[j], diff_norm=e_diff_norm[j],
                                      w_out=e_w_out[j], rel_bias=rel_bias, layer_idx=layer)
        else:
            mixer = functools.partial(odd_mixer, w_in=o_w_in[j], sinks=o_sinks[j], w_out=o_w_out[j],
                                      rel_bias=rel_bias)
        x = sandwich(x, c_act, mixer, norm_gains[layer, 0], norm_gains[layer, 1],
                     mod_w[layer, 0], mod_b[layer, 0])
        mlp = functools.partial(squared_relu_mlp, w1=mlp_w1[layer], w2=mlp_w2[layer])
        x = sandwich(x, c_act, mlp, norm_gains[layer, 2], norm_gains[layer, 3],
                     mod_w[layer, 1], mod_b[layer, 1])
    return x


def setup_inputs(seed=0):
    out = dict(first_inputs(seed))
    for name, value in second_inputs(seed + 1).items():
        if name != "x":
            out[name + "_2"] = value
    return out


def reference(
    x, c, w_ada, b_ada, w_in, q_norm_g, k_norm_g, w_branch_a, w_branch_b, w_out, ln1_g, ln1_b,
    w_router, router_bias, w_exp_gate, w_exp_up, w_exp_down, ln2_g, ln2_b, c_2, rel_bias_2,
    norm_gains_2, mod_w_2, mod_b_2, mlp_w1_2, mlp_w2_2, e_w_in_2, e_conv_w_2, e_conv_b_2,
    e_dt_bias_2, e_A_log_2, e_D_2, e_ssd_norm_2, e_lambda_2, e_diff_norm_2, e_w_out_2, o_w_in_2,
    o_sinks_2, o_w_out_2,
):
    x = first_block(
        x, c, w_ada, b_ada, w_in, q_norm_g, k_norm_g, w_branch_a, w_branch_b, w_out, ln1_g,
        ln1_b, w_router, router_bias, w_exp_gate, w_exp_up, w_exp_down, ln2_g, ln2_b,
    )
    return second_block(
        x, c_2, rel_bias_2, norm_gains_2, mod_w_2, mod_b_2, mlp_w1_2, mlp_w2_2, e_w_in_2,
        e_conv_w_2, e_conv_b_2, e_dt_bias_2, e_A_log_2, e_D_2, e_ssd_norm_2, e_lambda_2,
        e_diff_norm_2, e_w_out_2, o_w_in_2, o_sinks_2, o_w_out_2,
    )


_drawn_inputs = setup_inputs


def setup_inputs(seed=0):
    import zlib

    import numpy as np

    out = dict(_drawn_inputs(seed))
    spreads = {}
    factors = {'b_ada': 3.191,
     'q_norm_g': 8.0,
     'k_norm_g': 21.918,
     'router_bias': 2.669,
     'e_conv_b_2': 5.899,
     'e_D_2': 16.072,
     'o_sinks_2': 8.0}
    for name, (base, spread) in spreads.items():
        noise = np.random.default_rng([zlib.crc32(name.encode()), seed]).standard_normal(out[name].shape)
        drawn = base * np.exp(spread * noise) if base else spread * noise
        out[name] = jnp.asarray(drawn.astype(out[name].dtype))
    for name, factor in factors.items():
        out[name] = (out[name] * factor).astype(out[name].dtype)
    return out
```

```python
import itertools
import math
from contextlib import ExitStack, contextmanager

import numpy as np
import concourse.bass as bass
from concourse import mybir

F32 = mybir.dt.float32
ALU = mybir.AluOpType
ACT = mybir.ActivationFunctionType
AX = mybir.AxisListType.X

P = 128
S = 512
NT = S // P
D = 1024
KD = D // P
DEPTH = 2
HD = 64
A_HEADS, A_KV = 8, 2
B_HEADS = 12
BG = 4
REACH = 64
CLS = 4
N_EXP, EPG, D_EXP = 16, 4, 256
ALPHA = (2.0 * DEPTH) ** 0.25
NEG = -1.0e30
LN_EPS, RMS_EPS = 1e-5, 1e-6
SLOT = 4096
C_GATE, C_QKD, C_VD = 3072, 768, 2304
SSD_HEADS, SSD_GROUPS, SSD_STATE = 16, 4, 128
RET_HEADS, RET_V = 4, 256
BIAS_W = 640


_serial = itertools.count()


def fresh(name):
    return f"{name}_{next(_serial)}"


class Link:

    def __init__(self, eng, sem):
        self.eng, self.sem, self.n, self.base = eng, sem, 0, 0

    def __call__(self, ins):
        self.n += 1
        ins.then_inc(self.sem, 1)
        self.eng.wait_ge(self.sem, self.base + self.n)


@contextmanager
def stage(nc, names):
    nc.reset_free_semaphores(sorted(nc.free_semaphores))
    with ExitStack() as c:
        sems = [c.enter_context(nc.semaphore(fresh(n))) for n in names.split()]
        with nc.Block() as block:
            yield (block, *sems)
        nums = sorted(s.num for s in sems)
        assert nums == list(range(nums[0], nums[-1] + 1))
        nc.multi_engine_barrier(nc.engines, sems_to_clear=range(nums[0], nums[-1] + 1))


def bcast(ap, axis, n):
    u = ap.unsqueeze(axis)
    return u.to_broadcast([n if i == axis else d for i, d in enumerate(u.shape)])


def chain(pe, out, lhs, rhs, ks, first=True, last=True):
    for i, k in enumerate(ks):
        mm = pe.matmul(out, lhs(k), rhs(k), start=first and i == 0, stop=last and i == len(ks) - 1)
    return mm


def constants():
    f = np.float32
    out = {"ident": np.eye(P, dtype=f)}
    tok = np.arange(P)[:, None] * CLS + np.arange(CLS)[None, :]
    inv = (f(10000.0) ** (-np.arange(0, 32, 2, dtype=f) / f(32))).astype(f)
    row, col = (tok // 64).astype(f), (tok % 64).astype(f)
    ang = np.concatenate([row[..., None] * inv, col[..., None] * inv], -1).astype(f)
    out["rope1"] = np.stack([np.cos(ang), np.sin(ang)], 1).astype(f)
    slope = np.exp2(-8.0 * np.arange(1, B_HEADS + 1) / B_HEADS).astype(f)
    p, c = np.arange(P)[:, None], np.arange(256)[None, :]
    dist = np.abs(p - (c - REACH))
    band = np.zeros((P, 3, BG, 256), f)
    for e in range(3):
        ok = (dist <= REACH) & ~((e == 0) & (c < REACH)) & ~((e == 2) & (c >= P + REACH))
        for h in range(BG):
            band[:, e, h] = np.where(ok, -slope[h] * dist.astype(f), f(NEG))
    out["bias_band"] = band
    j = np.arange(P)[None, :]
    d = np.abs(p - j)
    cls = np.zeros((P, 2, BG, P), f)
    for g, ok in enumerate((d <= REACH, d % CLS == 0)):
        for h in range(BG):
            cls[:, g, h] = np.where(ok, -slope[BG * (g + 1) + h] * (CLS * d).astype(f), f(NEG))
    out["bias_class"] = cls
    out["before"] = np.broadcast_to((j[:, :4] < np.arange(4)[:, None]).astype(f), (P, 4, 4)).copy()
    out["causal"] = np.stack([(p <= j).astype(f), np.where(p <= j, f(0), f(NEG))], 1).astype(f)
    dd = 511 - np.arange(BIAS_W)
    n = np.maximum(dd, 0)
    logd = np.log(np.maximum(n, 1).astype(f) / f(16)).astype(f)
    large = 16 + (logd / f(math.log(8.0)) * f(16)).astype(f).astype(np.int32)
    bucket = np.where(n < 16, n, np.minimum(large, 31))
    hot = np.zeros((33, BIAS_W), f)
    hot[np.where(dd >= 0, bucket, 32), np.arange(BIAS_W)] = 1
    out["bucket_hot"] = hot
    pos = np.arange(S, dtype=f)
    inv = (f(10000.0) ** (-np.arange(64, dtype=f) / f(64))).astype(f)
    ang = (pos[:, None] * inv[None]).astype(f).reshape(NT, P, 64).transpose(1, 0, 2)
    out["rope2"] = np.stack([np.cos(ang), np.sin(ang)], 1).astype(f)
    lg = np.log(1.0 - 2.0 ** (-5.0 - np.arange(RET_HEADS, dtype=f))).astype(f)
    kscale = 128.0 ** -0.5
    dec = np.zeros((P, RET_HEADS, P), f)
    for h in range(RET_HEADS):
        dec[:, h] = np.where(j >= p, np.exp(np.maximum(j - p, 0) * lg[h]) * kscale, 0)
    out["ret_decay"] = dec
    xi = np.exp((np.arange(P) + 1.0)[None] * lg[:, None]).astype(f)
    out["ret_xi"] = np.broadcast_to(xi, (P, RET_HEADS, P)).copy()
    out["ret_zeta"] = (np.exp((P - 1 - np.arange(P))[:, None] * lg[None]) * kscale).astype(f)
    out["win_mask"] = np.where(j <= p, f(NEG), f(0)).astype(f)
    return out


RET_STATE_DECAY = [float(math.exp(P * math.log(1.0 - 2.0 ** (-5.0 - h)))) for h in range(RET_HEADS)]


class Core:

    def __init__(self, nc, c, A, K):
        self.nc, self.A, self.K = nc, A, K
        sb = lambda n, s: c.enter_context(nc.sbuf_tensor(fresh(n), s, F32))
        self.x = sb("x_res", [P, NT, D])
        self.hT = sb("hT", [P, KD, S])
        self.ring = sb("ring", [P, 2, SLOT])
        self.ident = sb("ident_sb", [P, P])
        self.mod = sb("mod", [P, 48])
        self.cond = sb("cond", [P, 2, KD])
        self.ps = c.enter_context(nc.psum_tensor("ps", [P, 8, 512], F32))
        self.scratch = nc.dram_tensor("scratch", [4 * S * D], F32, kind="Internal").ap()


def slot_view(k, b, kt, n):
    return k.ring[:, b, 0:kt * n].rearrange("p (k n) -> p k n", k=kt)



def conditions(k):
    nc, A = k.nc, k.A
    with stage(nc, "in_landed cond_done") as (block, in_landed, cond_done), nc.sbuf_tensor(fresh("craw"), [P, 2, KD], F32) as craw:
        @block.sync
        def _(sp):
            sp.dma_start(k.ident[:], k.K["ident"]).then_inc(in_landed, 16)
            for i, name in enumerate(("c", "c_2")):
                sp.dma_start(craw[:, i, :], A[name].rearrange("a (k p) -> (a p) k", p=P), allow_slow_non_contiguous=True).then_inc(in_landed, 16)
            sp.wait_ge(in_landed, 48)

        @block.scalar
        def _(act):
            act.wait_ge(in_landed, 48)
            nc.scalar.activation(k.cond[:], craw[:], ACT.Silu).then_inc(cond_done, 1)
            act.wait_ge(cond_done, 1)


def modulation(k, which, w, b, nslots, out, plus_one):
    nc = k.nc
    ncol = 4 * nslots
    with ExitStack() as c:
        brow = c.enter_context(nc.sbuf_tensor(fresh("brow"), [ncol, P], F32))
        bcol = c.enter_context(nc.sbuf_tensor(fresh("bcol"), [P, ncol], F32))
        block, w0, w1, b_landed, slot_free, cols_done, cols_free, b_done, step = c.enter_context(
            stage(nc, "mod_w0 mod_w1 b_landed slot_free cols_done cols_free b_done step"))
        landed = (w0, w1)

        @block.sync
        def _(sp):
            sp.dma_start(brow[:], b.rearrange("(j p) -> j p", p=P)).then_inc(b_landed, 16)
            with sp.Fori(0, nslots // 2) as t:
                for i in range(2):
                    sp.wait_ge(slot_free, 2 * t + i + 1)
                    sp.dma_start(slot_view(k, i, KD, 512), w[:, :, bass.ds((2 * t + i) * 512, 512)]).then_inc(landed[i], 16)

        @block.tensor
        def _(pe):
            pe.nop().then_inc(slot_free, 2)
            pe.wait_ge(b_landed, 16)
            pe.transpose(k.ps[:, 7, 0:ncol], brow[:], k.ident[0:ncol, 0:ncol]).then_inc(b_done, 1)
            with pe.Fori(0, nslots // 2) as t:
                for i in range(2):
                    pe.wait_ge(landed[i], 16 * t + 16)
                    pe.wait_ge(cols_free, 2 * t + i + 1)
                    wv = slot_view(k, i, KD, 512)
                    for j in range(4):
                        mm = chain(pe, k.ps[:, i, j:j + 1], lambda q: wv[:, q, j * P:(j + 1) * P],
                                   lambda q: k.cond[:, which, q:q + 1], range(KD))
                    mm.then_inc(cols_done, 1)
                    pe.wait_ge(cols_done, 2 * t + i + 1)
                    pe.nop().then_inc(slot_free, 1)

        @block.vector
        def _(dve):
            link = Link(dve, step)
            dve.nop().then_inc(cols_free, 2)
            dve.wait_ge(b_done, 1)
            link(nc.vector.tensor_copy(bcol[:], k.ps[:, 7, 0:ncol]))
            for a, n in plus_one:
                link(nc.vector.tensor_scalar(bcol[:, a:a + n], bcol[:, a:a + n], 1.0, None, ALU.add))
            with dve.Fori(0, nslots // 2) as t:
                for i in range(2):
                    dve.wait_ge(cols_done, 2 * t + i + 1)
                    at = bass.ds((2 * t + i) * 4, 4)
                    nc.vector.tensor_tensor(out[:, at], k.ps[:, i, 0:4], bcol[:, at], ALU.add).then_inc(cols_free, 1)
            dve.wait_ge(cols_free, nslots + 2)


def rows_of(k, cols, rows):
    nc = k.nc
    with stage(nc, "row_done row_out") as (block, row_done, row_out):
        @block.tensor
        def _(pe):
            for n, col in enumerate(cols):
                for j in range(KD):
                    mm = pe.matmul(k.ps[:, 2 * n + j // 4, (j % 4) * P:(j % 4 + 1) * P],
                                   col[:, j:j + 1].to_broadcast([P, P]), k.ident[:], start=True, stop=True)
                mm.then_inc(row_done, 1)

        @block.vector
        def _(dve):
            for n, row in enumerate(rows):
                dve.wait_ge(row_done, n + 1)
                nc.vector.tensor_copy(row[:].rearrange("p (b n) -> p b n", b=2), k.ps[:, 2 * n:2 * n + 2, :]).then_inc(row_out, 1)
            dve.wait_ge(row_out, len(rows))


def norm_to_hT(k, rms, eps, scale, shift, affine=None, store=None, src=None, dst=None):
    nc = k.nc
    src = k.x if src is None else src
    out = k.hT if dst is None else dst
    with ExitStack() as c:
        xn = c.enter_context(nc.sbuf_tensor(fresh("xn"), [P, NT, D], F32))
        st = c.enter_context(nc.sbuf_tensor(fresh("stats"), [P, NT, 2, 6], F32))
        mv = c.enter_context(nc.sbuf_tensor(fresh("mv"), [P, NT, 2], F32))
        tmp = c.enter_context(nc.sbuf_tensor(fresh("tmp"), [P, NT], F32))
        rstd = c.enter_context(nc.sbuf_tensor(fresh("rstd"), [P, NT], F32))
        gb = c.enter_context(nc.sbuf_tensor(fresh("gb"), [P, 2, D], F32)) if affine is not None else None
        block, gb_landed, var_done, root_done, xn_done, t_done, out_act, out_dve, stored, x_done, step = c.enter_context(
            stage(nc, "gb_landed var_done root_done xn_done t_done out_act out_dve stored x_done step"))
        rounds = 1 if affine is None else 2
        if store is not None:
            rounds = 1

        @block.sync
        def _(sp):
            if affine is not None:
                for i in range(2):
                    sp.dma_start(gb[:, i, :], bcast(affine[i], 0, P)).then_inc(gb_landed, 16)
                sp.wait_ge(gb_landed, 32)
            if store is not None:
                for t in range(NT):
                    sp.wait_ge(x_done, t + 1)
                    sp.dma_start(store[t], src[:, t, :]).then_inc(stored, 16)
                sp.wait_ge(stored, 16 * NT)

        @block.vector
        def _(dve):
            link = Link(dve, step)
            for r in range(rounds):
                for t in range(NT):
                    for h in range(2):
                        link(nc.vector.bn_stats(st[:, t, h, :], src[:, t, h * 512:(h + 1) * 512]))
                for t in range(NT):
                    link(nc.vector.bn_aggr(mv[:, t, :], st[:, t, :, :].rearrange("p a b -> p (a b)")))
                var = mv[:, :, 1]
                if rms:
                    link(nc.vector.tensor_tensor(tmp[:], mv[:, :, 0], mv[:, :, 0], ALU.mult))
                    link(nc.vector.tensor_tensor(tmp[:], tmp[:], var, ALU.add))
                    var = tmp[:]
                nc.vector.tensor_scalar(tmp[:], var, eps, None, ALU.add).then_inc(var_done, 1)
                dve.wait_ge(root_done, r + 1)
                link(nc.vector.reciprocal(rstd[:], rstd[:]))
                last = r == rounds - 1 and store is None
                for t in range(NT):
                    dst = xn[:, t, :] if last else src[:, t, :]
                    if rms:
                        ins = nc.vector.tensor_scalar(dst, src[:, t, :], rstd[:, t:t + 1], None, ALU.mult)
                    else:
                        ins = nc.vector.tensor_scalar(dst, src[:, t, :], mv[:, t, 0:1], rstd[:, t:t + 1], ALU.subtract, ALU.mult)
                    if last:
                        ins.then_inc(xn_done, 1)
                        continue
                    link(ins)
                    if t == 0:
                        dve.wait_ge(gb_landed, 32)
                    link(nc.vector.tensor_tensor(dst, dst, gb[:, 0, :], ALU.mult))
                    ins = nc.vector.tensor_tensor(dst, dst, gb[:, 1, :], ALU.add)
                    if store is not None:
                        ins.then_inc(x_done, 1)
                    else:
                        link(ins)
            if store is None:
                for q in range(1, KD, 2):
                    dve.wait_ge(t_done, q + 1)
                    ins = nc.vector.tensor_scalar(out[:, q, :], k.ps[:, q, :], scale[:, q:q + 1],
                                                  shift[:, q:q + 1] if shift is not None else None,
                                                  ALU.mult, ALU.add if shift is not None else ALU.bypass)
                    ins.then_inc(out_dve, 1)
                dve.wait_ge(out_dve, KD // 2)

        @block.scalar
        def _(act):
            for r in range(rounds):
                act.wait_ge(var_done, r + 1)
                nc.scalar.activation(rstd[:], tmp[:], ACT.Sqrt).then_inc(root_done, 1)
            if store is None:
                for q in range(0, KD, 2):
                    act.wait_ge(t_done, q + 1)
                    nc.scalar.activation(out[:, q, :], k.ps[:, q, :], ACT.Identity, scale=scale[:, q:q + 1],
                                         bias=shift[:, q:q + 1] if shift is not None else 0.0).then_inc(out_act, 1)
                act.wait_ge(out_act, KD // 2)

        @block.tensor
        def _(pe):
            if store is None:
                pe.wait_ge(xn_done, NT)
                for q in range(KD):
                    for t in range(NT):
                        mm = pe.transpose(k.ps[:, q, t * P:(t + 1) * P], xn[:, t, q * P:(q + 1) * P], k.ident[:])
                    mm.then_inc(t_done, 1)



def load_x(k):
    nc = k.nc
    with stage(nc, "x_landed spare") as (block, x_landed, _s):
        @block.sync
        def _(sp):
            sp.dma_start(k.x[:], k.A["x"].rearrange("a (i r) d -> (a i) r d", r=CLS)).then_inc(x_landed, 16)
            sp.wait_ge(x_landed, 16)


def in_projection(k, w, T):
    nc = k.nc
    QK0 = C_QKD
    plan = [(0, 512, "qa"), (512, 256, "kva")] + [(QK0 + 512 * i, 512, "qkd") for i in range(3)] + [(C_VD + 256, 512, "vc")]
    n0 = len(plan)
    with ExitStack() as c:
        hn = c.enter_context(nc.sbuf_tensor(fresh("hT_in_order"), [P, KD, S], F32))
        block, w0, w1, slot_free, bank, free_act, free_dve, step, in_order = c.enter_context(
            stage(nc, "w0 w1 slot_free bank free_act free_dve step in_order"))
        landed = (w0, w1)

        @block.gpsimd
        def _(pool):
            for q in range(KD):
                nc.gpsimd.tensor_copy(hn[:, q, :].rearrange("p (i r) -> p i r", r=CLS),
                                      k.hT[:, q, :].rearrange("p (r i) -> p i r", r=CLS)).then_inc(in_order, 1)
            pool.wait_ge(in_order, KD)

        @block.sync
        def _(sp):
            for s, (c0, n, _) in enumerate(plan):
                sp.wait_ge(slot_free, s + 1)
                sp.dma_start(slot_view(k, s % 2, KD, n), w[:, :, c0:c0 + n]).then_inc(landed[s % 2], 16)
            with sp.Fori(0, 2) as t:
                for i in range(2):
                    sp.wait_ge(slot_free, 2 * t + n0 + i + 1)
                    sp.dma_start(slot_view(k, i, KD, 512), w[:, :, bass.ds((2 * t + i) * 512 + C_GATE, 512)]).then_inc(landed[i], 16)
            sp.wait_ge(slot_free, n0 + 5)
            sp.dma_start(slot_view(k, 0, KD, 256), w[:, :, C_VD:C_VD + 256]).then_inc(landed[0], 16)

        @block.tensor
        def _(pe):
            pe.nop().then_inc(slot_free, 2)

            def token_major(b, n):
                wv = slot_view(k, b, KD, n)
                for t in range(NT):
                    chain(pe, k.ps[:, 4 * b + t, 0:n], lambda q: k.hT[:, q, t * P:(t + 1) * P],
                          lambda q: wv[:, q, :], range(KD)).then_inc(bank, 1)

            def feature_major(b):
                wv = slot_view(k, b, KD, 512)
                for m in range(4):
                    chain(pe, k.ps[:, 4 * b + m, :], lambda q: wv[:, q, m * P:(m + 1) * P],
                          lambda q: k.hT[:, q, :], range(KD)).then_inc(bank, 1)

            for s, (c0, n, kind) in enumerate(plan):
                pe.wait_ge(landed[s % 2], 16 * (s // 2) + 16)
                pe.wait_ge(free_act, s + 1)
                pe.wait_ge(free_dve, s + 1)
                if kind == "qkd":
                    feature_major(s % 2)
                else:
                    token_major(s % 2, n)
                pe.wait_ge(bank, 4 * s + 4)
                pe.nop().then_inc(slot_free, 1)
            with pe.Fori(0, 2) as t:
                for i in range(2):
                    pe.wait_ge(landed[i], 16 * t + 16 * (n0 // 2) + 16)
                    pe.wait_ge(free_act, 2 * t + n0 + i + 1)
                    pe.wait_ge(free_dve, 2 * t + n0 + i + 1)
                    feature_major(i)
                    pe.wait_ge(bank, 8 * t + 4 * (n0 + i) + 4)
                    pe.nop().then_inc(slot_free, 1)
            pe.wait_ge(landed[0], 16 * (n0 // 2) + 48)
            pe.wait_ge(free_act, n0 + 5)
            pe.wait_ge(free_dve, n0 + 6)
            pe.wait_ge(free_act, n0 + 6)
            wv = slot_view(k, 0, KD, 256)
            pe.wait_ge(in_order, KD)
            for c in range(5):
                i0, i1 = max(0, P * c - 64), min(S, P * c + 64)
                for q in range(KD):
                    p0 = 64 if c == 0 else 0
                    mm = pe.matmul(k.ps[p0:p0 + i1 - i0, c, 0:256], hn[:, q, i0:i1], wv[:, q, :],
                                   start=q == 0, stop=q == KD - 1)
                mm.then_inc(bank, 1)

        @block.scalar
        def _(act):
            act.nop().then_inc(free_act, 2)

            def out(s, kind, b):
                last = None
                for j in (0, 1):
                    act.wait_ge(bank, 4 * s + j + 1)
                    p = k.ps[:, 4 * b + j, :]
                    if kind == "qa":
                        last = nc.scalar.copy(T["qa"][:, j, :], p)
                    elif kind == "kva":
                        last = nc.scalar.copy(T["kva"][:, j, :], p[:, 0:256])
                    elif kind == "vc":
                        last = nc.scalar.copy(T["vc"][:, j, :], p)
                    elif kind == "qkd":
                        last = qkd_out(nc.scalar, s, j, p)
                last.then_inc(free_act, 1)

            def qkd_out(eng, s, j, p):
                m = 4 * (s - 2) + j
                dst, mul = qkd_dst(T, m)
                if m % 6 < 2:
                    p = p.rearrange("p (r i) -> p i r", r=CLS)
                    dst = dst.rearrange("p (i r) -> p i r", r=CLS)
                return nc.scalar.activation(dst, p, ACT.Copy, scale=mul)

            for s, (c0, n, kind) in enumerate(plan):
                out(s, kind, s % 2)
            with act.Fori(0, 2) as t:
                for i in range(2):
                    for j in range(4):
                        act.wait_ge(bank, 8 * t + 4 * (n0 + i) + j + 1)
                        last = nc.scalar.activation(T["gates"][:, bass.ds(8 * t + 4 * i + j, 1), :].rearrange("p a n -> p (a n)"),
                                                    k.ps[:, 4 * i + j, :], ACT.Sigmoid)
                    last.then_inc(free_act, 1)
            act.wait_ge(free_act, n0 + 6)

        @block.vector
        def _(dve):
            link = Link(dve, step)
            dve.nop().then_inc(free_dve, 2)
            link(nc.vector.memset(T["v0"][0:64, 0, :], 0.0))
            link(nc.vector.memset(T["v0"][64:P, 4, :], 0.0))
            for j in range(4):
                link(nc.vector.memset(T["k0T"][:, j % 2, (0 if j < 2 else S + REACH):(REACH if j < 2 else S + 2 * REACH)], 0.0))
            for s, (c0, n, kind) in enumerate(plan):
                for j in (2, 3):
                    dve.wait_ge(bank, 4 * s + j + 1)
                    p = k.ps[:, 4 * (s % 2) + j, :]
                    if kind == "qa":
                        last = nc.vector.tensor_copy(T["qa"][:, j, :], p)
                    elif kind == "kva":
                        last = nc.vector.tensor_copy(T["kva"][:, j, :], p[:, 0:256])
                    elif kind == "vc":
                        last = nc.vector.tensor_copy(T["vc"][:, j, :], p)
                    else:
                        m = 4 * (s - 2) + j
                        dst, mul = qkd_dst(T, m)
                        if m % 6 < 2:
                            p = p.rearrange("p (r i) -> p i r", r=CLS)
                            dst = dst.rearrange("p (i r) -> p i r", r=CLS)
                        last = nc.vector.tensor_scalar(dst, p, mul, None, ALU.mult)
                last.then_inc(free_dve, 1)
            dve.wait_ge(free_dve, n0 + 2)
            dve.nop().then_inc(free_dve, 4)
            for c in range(5):
                dve.wait_ge(bank, 4 * (n0 + 4) + c + 1)
                a, b = (64, P) if c == 0 else (0, 64 if c == 4 else P)
                link(nc.vector.tensor_copy(T["v0"][a:b, c, :], k.ps[a:b, c, 0:256]))


def qkd_dst(T, m):
    if m < 2:
        return T["q0T"][:, m, :], HD ** -0.5
    if m < 6:
        return T["qcT"][:, m - 2, :], HD ** -0.5
    if m < 8:
        return T["k0T"][:, m - 6, REACH:REACH + S], 1.0
    return T["kcT"][:, m - 8, :], 1.0


def rope_qk(k, gq, gk, T):
    nc = k.nc
    NH = A_HEADS + A_KV
    with ExitStack() as c:
        sb = lambda n, s: c.enter_context(nc.sbuf_tensor(fresh(n), s, F32))
        idle = k.ring[:].rearrange("p b n -> p (b n)")
        qk, sq, ro = (idle[:, i * NT * NH * HD:(i + 1) * NT * NH * HD].rearrange("p (t h d) -> p t h d", t=NT, h=NH) for i in range(3))
        t1 = sb("t1", [P, NT, NH, 32])
        cs = sb("cs", [P, 2, NT, 32])
        g = sb("gqk", [P, 2, HD])
        ms = sb("ms", [P, NT, NH])
        block, in_landed, sq_done, ms_done, root_done, ro_done, t_done, out_a, step = c.enter_context(
            stage(nc, "in_landed sq_done ms_done root_done ro_done t_done out_a step"))

        @block.sync
        def _(sp):
            sp.dma_start(cs[:], k.K["rope1"]).then_inc(in_landed, 16)
            sp.dma_start(g[:, 0, :], bcast(gq, 0, P)).then_inc(in_landed, 16)
            sp.dma_start(g[:, 1, :], bcast(gk, 0, P)).then_inc(in_landed, 16)
            sp.wait_ge(in_landed, 48)

        @block.scalar
        def _(act):
            for t in range(NT):
                nc.scalar.activation(sq[:, t, 0:8, :].rearrange("p h d -> p (h d)"), T["qa"][:, t, :], ACT.Square)
                last = nc.scalar.activation(sq[:, t, 8:10, :].rearrange("p h d -> p (h d)"), T["kva"][:, t, 0:P], ACT.Square)
            last.then_inc(sq_done, 1)
            act.wait_ge(ms_done, 1)
            nc.scalar.activation(ms[:], ms[:], ACT.Sqrt).then_inc(root_done, 1)
            for q in range(3, 6):
                act.wait_ge(t_done, q + 1)
                dst = T["qaT"][:, 3, :] if q == 3 else T["kaT"][:, q - 4, :]
                last = nc.scalar.copy(dst, k.ps[:, q, :])
            last.then_inc(out_a, 1)
            act.wait_ge(out_a, 1)

        @block.vector
        def _(dve):
            link = Link(dve, step)
            dve.wait_ge(sq_done, 1)
            link(nc.vector.tensor_reduce(ms[:].rearrange("p t h -> p (t h)"), sq.rearrange("p t h d -> p (t h) d"), AX, ALU.add))
            nc.vector.tensor_scalar(ms[:], ms[:], 1.0 / HD, RMS_EPS, ALU.mult, ALU.add).then_inc(ms_done, 1)
            dve.wait_ge(root_done, 1)
            link(nc.vector.reciprocal(ms[:], ms[:]))
            dve.wait_ge(in_landed, 48)
            link(nc.vector.tensor_scalar(g[:, 0, :], g[:, 0, :], HD ** -0.5, None, ALU.mult))
            for t in range(NT):
                qv = T["qa"][:, t, :].rearrange("p (h d) -> p h d", d=HD)
                kv = T["kva"][:, t, 0:P].rearrange("p (h d) -> p h d", d=HD)
                link(nc.vector.tensor_tensor(qk[:, t, 0:8, :], qv, bcast(ms[:, t, 0:8], 2, HD), ALU.mult))
                link(nc.vector.tensor_tensor(qk[:, t, 8:10, :], kv, bcast(ms[:, t, 8:10], 2, HD), ALU.mult))
                link(nc.vector.tensor_tensor(qk[:, t, 0:8, :], qk[:, t, 0:8, :], bcast(g[:, 0, :], 1, 8), ALU.mult))
                link(nc.vector.tensor_tensor(qk[:, t, 8:10, :], qk[:, t, 8:10, :], bcast(g[:, 1, :], 1, 2), ALU.mult))
                pr = qk[:, t].rearrange("p h (j e) -> p h j e", e=2)
                po = ro[:, t].rearrange("p h (j e) -> p h j e", e=2)
                cos, sin = (bcast(cs[:, i, t, :], 1, NH) for i in (0, 1))
                link(nc.vector.tensor_tensor(po[:, :, :, 0], pr[:, :, :, 0], cos, ALU.mult))
                link(nc.vector.tensor_tensor(t1[:, t], pr[:, :, :, 1], sin, ALU.mult))
                link(nc.vector.tensor_tensor(po[:, :, :, 0], po[:, :, :, 0], t1[:, t], ALU.subtract))
                link(nc.vector.tensor_tensor(po[:, :, :, 1], pr[:, :, :, 0], sin, ALU.mult))
                link(nc.vector.tensor_tensor(t1[:, t], pr[:, :, :, 1], cos, ALU.mult))
                link(nc.vector.tensor_tensor(po[:, :, :, 1], po[:, :, :, 1], t1[:, t], ALU.add))
                link(nc.vector.tensor_copy(sq[:, t, 0:2, :], bcast(ro[:, t, 8, :], 1, 2)))
                nc.vector.tensor_copy(sq[:, t, 2:4, :], bcast(ro[:, t, 9, :], 1, 2)).then_inc(ro_done, 1)
            for q in range(3):
                dve.wait_ge(t_done, q + 1)
                link(nc.vector.tensor_copy(T["qaT"][:, q, :], k.ps[:, q, :]))

        @block.tensor
        def _(pe):
            pe.wait_ge(ro_done, NT)
            for q in range(6):
                for t in range(NT):
                    src = ro[:, t, 2 * q:2 * q + 2, :] if q < 4 else sq[:, t, 2 * (q - 4):2 * (q - 4) + 2, :]
                    mm = pe.transpose(k.ps[:, q, t * P:(t + 1) * P], src.rearrange("p h d -> p (h d)"), k.ident[:])
                mm.then_inc(t_done, 1)


def attention(k, units, finish=None, name="a"):
    nc = k.nc
    with ExitStack() as c:
        sb = lambda n, s: c.enter_context(nc.sbuf_tensor(fresh(n), s, F32))
        pr = sb("probs", [P, 2, 512])
        sc = sb("biased", [P, 2, 512])
        pT = sb("probsT", [P, 2, 512])
        mx = sb("mx", [P, 4])
        nm = sb("nm", [P, 4])
        ls = sb("ls", [P, 4])
        es = sb("es", [P, 4])
        block, s_ready, max_done, exp_done, t_ready, t_out, o_ready, o_out, step = c.enter_context(
            stage(nc, "s_ready max_done exp_done t_ready t_out o_ready o_out step"))
        N = len(units)
        W = lambda u: units[u]["k"].shape[-1]

        @block.tensor
        def _(pe):
            for i in range(N + 2):
                if i < N:
                    u = units[i]
                    if i >= 2:
                        pe.wait_ge(exp_done, i - 1)
                    pe.matmul(k.ps[:, i % 2, 0:W(i)], u["q"], u["k"], start=True, stop=True).then_inc(s_ready, 1)
                if 1 <= i <= N:
                    v = i - 1
                    pe.wait_ge(exp_done, v + 1)
                    if v >= 2:
                        pe.wait_ge(t_out, v - 1)
                    for j in range(W(v) // P):
                        mm = pe.transpose(k.ps[:, 2 + v % 2, j * P:(j + 1) * P], pr[:, v % 2, j * P:(j + 1) * P], k.ident[:])
                    mm.then_inc(t_ready, 1)
                if i >= 2:
                    v = i - 2
                    pe.wait_ge(t_out, v + 1)
                    if v >= 2:
                        pe.wait_ge(o_out, v - 1)
                    vs = units[v]["v"]
                    chain(pe, k.ps[:, 4 + v % 2, 0:vs[0].shape[-1]], lambda j: pT[:, v % 2, j * P:(j + 1) * P],
                          lambda j: vs[j], range(len(vs))).then_inc(o_ready, 1)

        @block.scalar
        def _(act):
            for i in range(N):
                u = units[i]
                act.wait_ge(max_done, i + 1)
                if i >= 2:
                    act.wait_ge(t_ready, i - 1)
                if i >= 4:
                    act.wait_ge(o_out, i - 3)
                src = k.ps[:, i % 2, 0:W(i)] if u.get("bias") is None else sc[:, i % 2, 0:W(i)]
                l = u["l"] if u.get("l") is not None else ls[:, i % 4:i % 4 + 1]
                if u.get("sink") is not None:
                    nc.scalar.activation(es[:, i % 4:i % 4 + 1], u["sink"], ACT.Exp, bias=nm[:, i % 4:i % 4 + 1])
                nc.scalar.activation(pr[:, i % 2, 0:W(i)], src, ACT.Exp, bias=nm[:, i % 4:i % 4 + 1],
                                     accum_out=l).then_inc(exp_done, 1)

        @block.vector
        def _(dve):
            link = Link(dve, step)
            for i in range(N + 2):
                if i < N:
                    u = units[i]
                    dve.wait_ge(s_ready, i + 1)
                    if i >= 4:
                        dve.wait_ge(exp_done, i - 3)
                    n = nm[:, i % 4:i % 4 + 1]
                    s = k.ps[:, i % 2, 0:W(i)]
                    if u.get("bias") is None:
                        nc.vector.tensor_reduce(n, s, AX, ALU.max, negate=True).then_inc(max_done, 1)
                    else:
                        m = u["m"] if u.get("m") is not None else mx[:, i % 4:i % 4 + 1]
                        if i >= 2:
                            dve.wait_ge(exp_done, i - 1)
                        link(nc.vector.tensor_tensor_reduce(sc[:, i % 2, 0:W(i)], s, u["bias"], 1.0, 2 * NEG, ALU.add, ALU.max, m))
                        if u.get("sink") is not None:
                            link(nc.vector.tensor_tensor(m, m, u["sink"], ALU.max))
                        nc.vector.tensor_scalar(n, m, -1.0, None, ALU.mult).then_inc(max_done, 1)
                if 1 <= i <= N:
                    v = i - 1
                    dve.wait_ge(t_ready, v + 1)
                    if v >= 2:
                        dve.wait_ge(o_ready, v - 1)
                    nc.vector.tensor_copy(pT[:, v % 2, 0:W(v)], k.ps[:, 2 + v % 2, 0:W(v)]).then_inc(t_out, 1)
                if i >= 2:
                    v = i - 2
                    dve.wait_ge(o_ready, v + 1)
                    vs = units[v]["v"]
                    po = k.ps[:, 4 + v % 2, 0:vs[0].shape[-1]]
                    if units[v].get("l") is not None:
                        nc.vector.tensor_copy(units[v]["out"], po).then_inc(o_out, 1)
                    else:
                        l = ls[:, v % 4:v % 4 + 1]
                        if units[v].get("sink") is not None:
                            link(nc.vector.tensor_tensor(l, l, es[:, v % 4:v % 4 + 1], ALU.add))
                        link(nc.vector.reciprocal(l, l))
                        nc.vector.tensor_scalar(units[v]["out"], po, l, None, ALU.mult).then_inc(o_out, 1)
            dve.wait_ge(o_out, N)


def combine_groups(k, T):
    nc = k.nc
    W = BG * (HD + 2)
    nat = k.scratch[0:S * W]
    with ExitStack() as c:
        sb = lambda n, s: c.enter_context(nc.sbuf_tensor(fresh(n), s, F32))
        U0 = sb("U0c", [P, CLS, BG, HD + 2])
        M = sb("Mx", [P, 16])
        f = sb("fg", [P, 3, 16])
        t1 = sb("t1c", [P, 16])
        ob = sb("ob", [P, 16, HD])
        block, moved, f_in, f_done, ob_done, t_done, out_act, step = c.enter_context(
            stage(nc, "moved f_in f_done ob_done t_done out_act step"))
        U = [U0[:].rearrange("p t h d -> p (t h) d"), T["U1"][:].rearrange("p t h d -> p (t h) d"),
             T["U2"][:].rearrange("p t h d -> p (t h) d")]

        @block.sync
        def _(sp):
            sp.dma_start(nat.rearrange("(t p f) -> p t f", p=P, f=W), T["U0"][:].rearrange("p t h d -> p t (h d)")).then_inc(moved, 16)
            sp.wait_ge(moved, 16)
            sp.dma_start(U0[:].rearrange("p t h d -> p (t h d)"), nat.rearrange("(i f) -> i f", i=P)).then_inc(moved, 16)
            sp.wait_ge(moved, 32)

        @block.vector
        def _(dve):
            link = Link(dve, step)
            dve.wait_ge(moved, 32)
            link(nc.vector.tensor_tensor(M[:], U[0][:, :, HD + 1], U[1][:, :, HD + 1], ALU.max))
            link(nc.vector.tensor_tensor(M[:], M[:], U[2][:, :, HD + 1], ALU.max))
            for g in range(3):
                ins = nc.vector.tensor_tensor(f[:, g, :], U[g][:, :, HD + 1], M[:], ALU.subtract)
            ins.then_inc(f_in, 1)
            dve.wait_ge(f_done, 1)
            link(nc.vector.tensor_tensor(M[:], f[:, 0, :], U[0][:, :, HD], ALU.mult))
            for g in (1, 2):
                link(nc.vector.tensor_tensor(t1[:], f[:, g, :], U[g][:, :, HD], ALU.mult))
                link(nc.vector.tensor_tensor(M[:], M[:], t1[:], ALU.add))
            link(nc.vector.reciprocal(M[:], M[:]))
            link(nc.vector.tensor_tensor(f[:], f[:], bcast(M[:], 1, 3), ALU.mult))
            link(nc.vector.tensor_tensor(ob[:], U[0][:, :, 0:HD], bcast(f[:, 0, :], 2, HD), ALU.mult))
            for g in (1, 2):
                link(nc.vector.tensor_tensor(U[g][:, :, 0:HD], U[g][:, :, 0:HD], bcast(f[:, g, :], 2, HD), ALU.mult))
                link(nc.vector.tensor_tensor(ob[:], ob[:], U[g][:, :, 0:HD], ALU.add))
            dve.nop().then_inc(ob_done, 1)
            for q in range(0, 6, 2):
                dve.wait_ge(t_done, q + 1)
                link(nc.vector.tensor_copy(T["oT"][:, q, :], k.ps[:, q, :]))

        @block.scalar
        def _(act):
            act.wait_ge(f_in, 1)
            nc.scalar.activation(f[:], f[:], ACT.Exp).then_inc(f_done, 1)
            for q in range(1, 6, 2):
                act.wait_ge(t_done, q + 1)
                nc.scalar.copy(T["oT"][:, q, :], k.ps[:, q, :]).then_inc(out_act, 1)
            act.wait_ge(out_act, 3)

        @block.tensor
        def _(pe):
            for q in range(4):
                for t in range(NT):
                    mm = pe.transpose(k.ps[:, q, t * P:(t + 1) * P], T["oa"][:, t, q * P:(q + 1) * P], k.ident[:])
                mm.then_inc(t_done, 1)
            pe.wait_ge(ob_done, 1)
            for q in range(2):
                for t in range(NT):
                    src = ob[:, 4 * t + 2 * q:4 * t + 2 * q + 2, :].rearrange("p h d -> p (h d)")
                    mm = pe.transpose(k.ps[:, 4 + q, t * P:(t + 1) * P], src, k.ident[:])
                mm.then_inc(t_done, 1)


def branches(k, wa, wb, wo, T, grow):
    nc = k.nc
    with ExitStack() as c:
        tmp = c.enter_context(nc.sbuf_tensor(fresh("tmp_b"), [P, 2, 2, S], F32))
        block, w0, w1, wo0, wo1, pair, pair_out, m_done, step, merged = c.enter_context(
            stage(nc, "w0 w1 wo0 wo1 pair pair_out m_done step merged"))
        STEP0 = 2 * KD

        @block.sync
        def _(sp):
            sp.dma_start(slot_view(k, 0, 4, D), wa).then_inc(w0, 16)
            sp.dma_start(slot_view(k, 1, 2, D), wb).then_inc(w1, 16)
            for i, s in enumerate((wo0, wo1)):
                sp.wait_ge(pair, KD)
                sp.dma_start(slot_view(k, i, KD, 512), wo[:, :, i * 512:(i + 1) * 512]).then_inc(s, 16)

        @block.tensor
        def _(pe):
            pe.wait_ge(w0, 16)
            pe.wait_ge(w1, 16)
            wav, wbv = slot_view(k, 0, 4, D), slot_view(k, 1, 2, D)
            for m in range(KD):
                if m >= 2:
                    pe.wait_ge(pair_out, m - 1)
                b = 2 * (m % 2)
                chain(pe, k.ps[:, b, :], lambda q: wav[:, q, m * P:(m + 1) * P], lambda q: T["oT"][:, q, :], range(4))
                chain(pe, k.ps[:, b + 1, :], lambda q: wbv[:, q, m * P:(m + 1) * P], lambda q: T["oT"][:, 4 + q, :],
                      range(2)).then_inc(pair, 1)
            pe.wait_ge(merged, KD)
            for n, s in enumerate((wo0, wo1)):
                pe.wait_ge(s, 16)
                wv = slot_view(k, n, KD, 512)
                for t in range(NT):
                    if n == 1:
                        pe.wait_ge(step, STEP0 + 2 * (t + 1))
                    chain(pe, k.ps[:, 4 + t, :], lambda q: k.hT[:, q, t * P:(t + 1) * P], lambda q: wv[:, q, :],
                          range(KD)).then_inc(m_done, 1)

        @block.vector
        def _(dve):
            link = Link(dve, step)
            for m in range(KD):
                dve.wait_ge(pair, m + 1)
                b = 2 * (m % 2)
                link(nc.vector.tensor_tensor(tmp[:, 0, m % 2, :], k.ps[:, b, :], T["gates"][:, m, :], ALU.mult))
                last = nc.vector.tensor_tensor(tmp[:, 1, m % 2, :], k.ps[:, b + 1, :], T["gates"][:, KD + m, :], ALU.mult)
                link(last)
                dve.nop().then_inc(pair_out, 1)
                nc.vector.tensor_tensor(k.hT[:, m, :], tmp[:, 0, m % 2, :], tmp[:, 1, m % 2, :], ALU.add).then_inc(merged, 1)
            for n in range(2):
                for t in range(NT):
                    dve.wait_ge(m_done, NT * n + t + 1)
                    cols = slice(n * 512, (n + 1) * 512)
                    if n == 0 and t == 0:
                        dve.wait_ge(merged, KD)
                    link(nc.vector.tensor_tensor(tmp[:, 0, t % 2, :], k.ps[:, 4 + t, :], grow[:, cols], ALU.mult))
                    link(nc.vector.scalar_tensor_tensor(k.x[:, t, cols], k.x[:, t, cols], ALPHA, tmp[:, 0, t % 2, :], ALU.mult, ALU.add))


def router(k, comb_all):
    nc = k.nc
    G = N_EXP // EPG
    back = k.scratch[0:N_EXP * S].rearrange("(e n) -> e n", e=N_EXP)
    with ExitStack() as c:
        sb = lambda n, s: c.enter_context(nc.sbuf_tensor(fresh(n), s, F32))
        wr = sb("wr", [P, KD, N_EXP])
        rb = sb("rb", [P, N_EXP])
        before = sb("before_sb", [P, 4, 4])
        sc = sb("sc_r", [P, NT, N_EXP])
        sel = sb("sel_r", [P, NT * G, EPG])
        gt = sb("gt_r", [P, NT * G, EPG, EPG])
        eq = sb("eq_r", [P, NT * G, EPG, EPG])
        top = sb("top_r", [P, NT * G, EPG])
        grp = sb("grp_r", [P, NT, G])
        gm = sb("gm_r", [P, NT, G])
        den = sb("den_r", [P, NT])
        cT = sb("cT_r", [N_EXP, S])
        block, in_landed, logit, score, comb, t_done, cT_done, moved, step = c.enter_context(
            stage(nc, "in_landed logit score comb t_done cT_done moved step"))

        @block.sync
        def _(sp):
            sp.dma_start(wr[:], k.A["w_router"].rearrange("(k p) e -> p k e", p=P)).then_inc(in_landed, 16)
            sp.dma_start(rb[:], bcast(k.A["router_bias"], 0, P)).then_inc(in_landed, 16)
            sp.dma_start(before[:], k.K["before"]).then_inc(in_landed, 16)
            sp.wait_ge(cT_done, 1)
            sp.dma_start(back, cT[:]).then_inc(moved, 16)
            sp.wait_ge(moved, 16)
            sp.dma_start(comb_all[:], bcast(back, 0, P)).then_inc(moved, 16)
            sp.wait_ge(moved, 32)

        @block.tensor
        def _(pe):
            pe.wait_ge(in_landed, 48)
            for t in range(NT):
                mm = chain(pe, k.ps[:, 0, t * N_EXP:(t + 1) * N_EXP], lambda q: k.hT[:, q, t * P:(t + 1) * P],
                           lambda q: wr[:, q, :], range(KD))
            mm.then_inc(logit, 1)
            pe.wait_ge(comb, 1)
            for t in range(NT):
                mm = pe.transpose(k.ps[0:N_EXP, 1, t * P:(t + 1) * P], sc[:, t, :], k.ident[:])
            mm.then_inc(t_done, 1)

        @block.scalar
        def _(act):
            act.wait_ge(logit, 1)
            nc.scalar.activation(sc[:], k.ps[:, 0, 0:NT * N_EXP].rearrange("p (t e) -> p t e", t=NT), ACT.Sigmoid).then_inc(score, 1)
            act.wait_ge(t_done, 1)
            nc.scalar.copy(cT[:], k.ps[0:N_EXP, 1, :]).then_inc(cT_done, 1)
            act.wait_ge(cT_done, 1)

        @block.vector
        def _(dve):
            link = Link(dve, step)
            V = nc.vector
            dve.wait_ge(score, 1)
            dve.wait_ge(in_landed, 48)
            link(V.tensor_tensor(sel[:].rearrange("p (t g) e -> p t (g e)", t=NT), sc[:], bcast(rb[:], 1, NT), ALU.add))

            def ranks(v, n, out):
                g, e = gt[:, 0:n], eq[:, 0:n]
                link(V.tensor_tensor(g, bcast(v, 2, 4), bcast(v, 3, 4), ALU.is_gt))
                link(V.tensor_tensor(e, bcast(v, 2, 4), bcast(v, 3, 4), ALU.is_equal))
                link(V.tensor_tensor(e, e, bcast(before[:], 1, n), ALU.mult))
                link(V.tensor_tensor(g, g, e, ALU.add))
                link(V.tensor_reduce(out, g, AX, ALU.add))

            ranks(sel[:], NT * G, top[:])
            link(V.tensor_scalar(top[:], top[:], 1.5, None, ALU.is_lt))
            link(V.tensor_tensor(sel[:], sel[:], top[:], ALU.mult))
            link(V.tensor_reduce(grp[:].rearrange("p t g -> p (t g)"), sel[:], AX, ALU.add))
            ranks(grp[:], NT, gm[:])
            link(V.tensor_scalar(gm[:], gm[:], 0.5, None, ALU.is_lt))
            link(V.tensor_tensor(top[:], top[:], bcast(gm[:].rearrange("p t g -> p (t g)"), 2, EPG), ALU.mult))
            link(V.tensor_tensor(sc[:], sc[:], top[:].rearrange("p (t g) e -> p t (g e)", t=NT), ALU.mult))
            link(V.tensor_reduce(den[:], sc[:], AX, ALU.add))
            link(V.reciprocal(den[:], den[:]))
            V.tensor_tensor(sc[:], sc[:], bcast(den[:], 2, N_EXP), ALU.mult).then_inc(comb, 1)
            dve.wait_ge(comb, 1)


def experts(k, wg, wu, wd, comb_all, grow):
    nc = k.nc
    with ExitStack() as c:
        sb = lambda n, s: c.enter_context(nc.sbuf_tensor(fresh(n), s, F32))
        hid = sb("hid", [P, KD, S])
        sg = sb("sg", [P, 2, 2, S])
        y = sb("y_acc", [P, NT, D])
        block, w0, w1, slot_free, bank, sg_done, free_dve, hid_done, y_out, step = c.enter_context(
            stage(nc, "w0 w1 slot_free bank sg_done free_dve hid_done y_out step"))
        landed = (w0, w1)
        C = N_EXP // 4
        per = [2, 2, 2, 2, 1, 1]
        before = [[sum(per[i] for i in range(j) if i % 2 == j % 2) for j in range(6)], 5]

        @block.sync
        def _(sp):
            with sp.Fori(0, C) as ch:
                for j in range(4):
                    sp.wait_ge(slot_free, 6 * ch + j + 1)
                    v = slot_view(k, j % 2, KD, 512)
                    sp.dma_start(v[:, :, 0:256], wg[:, 4 * ch + j]).then_inc(landed[j % 2], 16)
                    sp.dma_start(v[:, :, 256:512], wu[:, 4 * ch + j]).then_inc(landed[j % 2], 16)
                for n in range(2):
                    sp.wait_ge(slot_free, 6 * ch + 5 + n)
                    sp.dma_start(slot_view(k, n, KD, 512), wd[:, bass.ds(8 * ch, 8), n * 512:(n + 1) * 512]).then_inc(landed[n], 16)

        @block.tensor
        def _(pe):
            pe.nop().then_inc(slot_free, 2)
            with pe.Fori(0, C) as ch:
                for j in range(6):
                    b = j % 2
                    pe.wait_ge(landed[b], 80 * ch + 16 * (before[0][j] + per[j]))
                    pe.wait_ge(free_dve, 6 * ch + j + 1)
                    wv = slot_view(k, b, KD, 512)
                    if j == 4:
                        pe.wait_ge(hid_done, 4 * ch + 5)
                    for m in range(4):
                        if j < 4:
                            mm = chain(pe, k.ps[:, 4 * b + m, :], lambda q: wv[:, q, m * P:(m + 1) * P], lambda q: k.hT[:, q, :], range(KD))
                        else:
                            mm = chain(pe, k.ps[:, 4 * b + m, :], lambda q: hid[:, q, m * P:(m + 1) * P], lambda q: wv[:, q, :], range(KD))
                        mm.then_inc(bank, 1)
                    pe.wait_ge(bank, 24 * ch + 4 * j + 4)
                    pe.nop().then_inc(slot_free, 1)

        @block.scalar
        def _(act):
            with act.Fori(0, C) as ch:
                for j in range(4):
                    act.wait_ge(hid_done, 4 * ch + max(j, 1))
                    for m in range(2):
                        act.wait_ge(bank, 24 * ch + 4 * j + m + 1)
                        nc.scalar.activation(sg[:, j % 2, m, :], k.ps[:, 4 * (j % 2) + m, :], ACT.Silu).then_inc(sg_done, 1)

        @block.vector
        def _(dve):
            link = Link(dve, step)
            link(nc.vector.memset(y[:], 0.0))
            dve.nop().then_inc(free_dve, 2)
            dve.nop().then_inc(hid_done, 1)
            n0 = link.n
            with dve.Fori(0, C) as ch:
                link.n, link.base = n0, ch * (4 * 4 + 8)
                for j in range(4):
                    b = j % 2
                    for m in range(2):
                        dve.wait_ge(bank, 24 * ch + 4 * j + 3 + m)
                        dve.wait_ge(sg_done, 8 * ch + 2 * j + m + 1)
                        w = comb_all[:, bass.ds(4 * ch + j, 1), :].rearrange("p a n -> p (a n)")
                        h = hid[:, 2 * j + m, :]
                        link(nc.vector.tensor_tensor(h, k.ps[:, 4 * b + 2 + m, :], w, ALU.mult))
                        link(nc.vector.tensor_tensor(h, h, sg[:, b, m, :], ALU.mult))
                    dve.nop().then_inc(hid_done, 1)
                    dve.nop().then_inc(free_dve, 1)
                for n in range(2):
                    for t in range(NT):
                        dve.wait_ge(bank, 24 * ch + 16 + 4 * n + t + 1)
                        yv = y[:, t, n * 512:(n + 1) * 512]
                        link(nc.vector.tensor_tensor(yv, yv, k.ps[:, 4 * n + t, :], ALU.add))
                    dve.nop().then_inc(free_dve, 1)
            link.n, link.base = n0 + C * 24, 0
            for t in range(NT):
                link(nc.vector.tensor_tensor(y[:, t, :], y[:, t, :], grow[:], ALU.mult))
                link(nc.vector.scalar_tensor_tensor(k.x[:, t, :], k.x[:, t, :], ALPHA, y[:, t, :], ALU.mult, ALU.add))


def first_layer(k, l, last_store):
    nc, A = k.nc, k.A
    kp = lambda ap: ap.rearrange("l (k p) n -> l p k n", p=P)[l]
    modulation(k, 0, kp(A["w_ada"]), A["b_ada"][l], 12, k.mod, ((8, 8), (32, 8)))
    with ExitStack() as c:
        sb = lambda n, s: c.enter_context(nc.sbuf_tensor(fresh(n), s, F32))
        g1, g2 = sb("g1row", [P, D]), sb("g2row", [P, D])
        rows_of(k, [k.mod[:, 16:24], k.mod[:, 40:48]], [g1, g2])
        norm_to_hT(k, False, LN_EPS, k.mod[:, 8:16], k.mod[:, 0:8])
        with ExitStack() as m:
            sm = lambda n, s: m.enter_context(nc.sbuf_tensor(fresh(n), s, F32))
            T = {"gates": sm("gates", [P, 16, S]), "oT": sm("oT", [P, 6, S])}
            with ExitStack() as q:
                sq = lambda n, s: q.enter_context(nc.sbuf_tensor(fresh(n), s, F32))
                T.update(qa=sq("qa", [P, NT, 512]), kva=sq("kva", [P, NT, 256]), vc=sq("vc", [P, NT, 512]), v0=sq("v0", [P, 5, 256]),
                         q0T=sq("q0T", [P, 2, S]), k0T=sq("k0T", [P, 2, S + 2 * REACH]), qcT=sq("qcT", [P, 4, S]), kcT=sq("kcT", [P, 4, S]))
                in_projection(k, kp(A["w_in"]), T)
                T["oa"] = T["qa"]
                with ExitStack() as r:
                    sr = lambda n, s: r.enter_context(nc.sbuf_tensor(fresh(n), s, F32))
                    T.update(qaT=sr("qaT", [P, 4, S]), kaT=sr("kaT", [P, 2, S]))
                    rope_qk(k, A["q_norm_g"][l], A["k_norm_g"][l], T)
                    units = []
                    for h in range(A_HEADS):
                        p0, g = 64 * (h % 2), h // 4
                        for t in range(NT):
                            units.append(dict(q=T["qaT"][p0:p0 + 64, h // 2, t * P:(t + 1) * P], k=T["kaT"][p0:p0 + 64, g, :],
                                              v=[T["kva"][:, j, 128 + 64 * g:192 + 64 * g] for j in range(NT)],
                                              out=T["oa"][:, t, h * HD:(h + 1) * HD]))
                    attention(k, units)
                with ExitStack() as r:
                    sr = lambda n, s: r.enter_context(nc.sbuf_tensor(fresh(n), s, F32))
                    T.update(U0=sr("U0", [P, NT, BG, HD + 2]), U1=sr("U1", [P, NT, BG, HD + 2]), U2=sr("U2", [P, NT, BG, HD + 2]))
                    band, cls = sr("band", [P, 3, BG, 256]), sr("cls", [P, 2, BG, P])
                    load_constants(k, [(band, "bias_band"), (cls, "bias_class")])
                    units = []
                    for t in range(NT):
                        for h in range(BG):
                            p0, u = 64 * (h % 2), T["U0"][:, t, h, :]
                            units.append(dict(q=T["q0T"][p0:p0 + 64, h // 2, t * P:(t + 1) * P],
                                              k=T["k0T"][p0:p0 + 64, h // 2, t * P:t * P + 256],
                                              bias=band[:, 0 if t == 0 else 2 if t == NT - 1 else 1, h, :],
                                              v=[T["v0"][:, t + j, h * HD:(h + 1) * HD] for j in range(2)],
                                              out=u[:, 0:HD], l=u[:, HD:HD + 1], m=u[:, HD + 1:HD + 2]))
                            for g in range(2):
                                u = T[f"U{g + 1}"][:, t, h, :]
                                i = 2 * g + h // 2
                                units.append(dict(q=T["qcT"][p0:p0 + 64, i, t * P:(t + 1) * P], k=T["kcT"][p0:p0 + 64, i, t * P:(t + 1) * P],
                                                  bias=cls[:, g, h, :], v=[T["vc"][:, t, (4 * g + h) * HD:(4 * g + h + 1) * HD]],
                                                  out=u[:, 0:HD], l=u[:, HD:HD + 1], m=u[:, HD + 1:HD + 2]))
                    attention(k, units)
                    combine_groups(k, T)
            branches(k, A["w_branch_a"].rearrange("l (k p) n -> l p k n", p=P)[l], A["w_branch_b"].rearrange("l (k p) n -> l p k n", p=P)[l],
                     kp(A["w_out"]), T, g1)
        norm_to_hT(k, False, LN_EPS, k.mod[:, 32:40], k.mod[:, 24:32], affine=(A["ln1_g"][l], A["ln1_b"][l]))
        with nc.sbuf_tensor(fresh("comb_all"), [P, N_EXP, S], F32) as comb_all:
            router(k, comb_all)
            ex = lambda ap: ap.rearrange("l e (k p) n -> l p e k n", p=P)[l]
            experts(k, ex(A["w_exp_gate"]), ex(A["w_exp_up"]), A["w_exp_down"].rearrange("l e (f p) n -> l p (e f) n", p=P)[l], comb_all, g2)
    norm_to_hT(k, False, LN_EPS, None, None, affine=(A["ln2_g"][l], A["ln2_b"][l]), store=last_store)


def load_constants(k, pairs):
    nc = k.nc
    with stage(nc, "const_landed spare") as (block, const_landed, _s):
        @block.sync
        def _(sp):
            for dst, name in pairs:
                sp.dma_start(dst[:], k.K[name]).then_inc(const_landed, 16)
            sp.wait_ge(const_landed, 16 * len(pairs))


def first_block(k):
    conditions(k)
    load_x(k)
    mid = k.scratch[2 * S * D:3 * S * D].rearrange("(i r d) -> r i d", r=CLS, d=D)
    with k.nc.Fori(0, DEPTH) as l:
        first_layer(k, l, mid)



def sandwich_columns(k, gains, j):
    nc = k.nc
    with ExitStack() as c:
        raw = c.enter_context(nc.sbuf_tensor(fresh("graw"), [16, P], F32))
        block, landed, t_done, step = c.enter_context(stage(nc, "g_landed t_done step"))

        @block.sync
        def _(sp):
            sp.dma_start(raw[:], gains[j:j + 2].rearrange("g (k p) -> (g k) p", p=P)).then_inc(landed, 16)
            sp.wait_ge(landed, 16)

        @block.tensor
        def _(pe):
            pe.wait_ge(landed, 16)
            pe.transpose(k.ps[:, 0, 0:16], raw[:], k.ident[0:16, 0:16]).then_inc(t_done, 1)

        @block.vector
        def _(dve):
            link = Link(dve, step)
            dve.wait_ge(t_done, 1)
            link(nc.vector.scalar_tensor_tensor(k.mod[:, 8:16], k.mod[:, 8:16], 1.0, k.ps[:, 0, 0:8], ALU.add, ALU.mult))
            link(nc.vector.tensor_tensor(k.mod[:, 16:24], k.mod[:, 16:24], k.ps[:, 0, 8:16], ALU.mult))


def project(k, w, plan):
    nc = k.nc
    N = len(plan)
    with stage(nc, "w0 w1 bank free_act free_dve") as (block, w0, w1, bank, free_act, free_dve):
        landed = (w0, w1)

        @block.sync
        def _(sp):
            for s, (c0, n, *_r) in enumerate(plan):
                if s >= 2:
                    sp.wait_ge(bank, 4 * (s - 1))
                sp.dma_start(slot_view(k, s % 2, KD, n), w[:, :, c0:c0 + n]).then_inc(landed[s % 2], 16)

        @block.tensor
        def _(pe):
            for s, (c0, n, major, _f, _d) in enumerate(plan):
                b = s % 2
                pe.wait_ge(landed[b], 16 * (s // 2) + 16)
                if s >= 2:
                    pe.wait_ge(free_act, s - 1)
                    pe.wait_ge(free_dve, s - 1)
                wv = slot_view(k, b, KD, n)
                for m in range(4):
                    if major == "token":
                        mm = chain(pe, k.ps[:, 4 * b + m, 0:n], lambda q: k.hT[:, q, m * P:(m + 1) * P], lambda q: wv[:, q, :], range(KD))
                    else:
                        mm = chain(pe, k.ps[:, 4 * b + m, :], lambda q: wv[:, q, m * P:(m + 1) * P], lambda q: k.hT[:, q, :], range(KD))
                    mm.then_inc(bank, 1)

        @block.scalar
        def _(act):
            for s, (_c, n, _m, f, dst) in enumerate(plan):
                for j in range(4 if f == "silu" else 2):
                    act.wait_ge(bank, 4 * s + j + 1)
                    src = k.ps[:, 4 * (s % 2) + j, 0:n if _m == "token" else 512]
                    if f == "silu":
                        last = nc.scalar.activation(dst[j], src, ACT.Silu)
                    else:
                        last = nc.scalar.activation(dst[j], src, ACT.Copy, scale=f)
                last.then_inc(free_act, 1)
            act.wait_ge(free_act, N)

        @block.vector
        def _(dve):
            for s, (_c, n, _m, f, dst) in enumerate(plan):
                if f == "silu":
                    if s:
                        dve.wait_ge(free_dve, s)
                    dve.nop().then_inc(free_dve, 1)
                    continue
                for j in (2, 3):
                    dve.wait_ge(bank, 4 * s + j + 1)
                    src = k.ps[:, 4 * (s % 2) + j, 0:n if _m == "token" else 512]
                    last = nc.vector.tensor_scalar(dst[j], src, f, None, ALU.mult)
                last.then_inc(free_dve, 1)
            dve.wait_ge(free_dve, N)


def out_projection(k, w, tiles, y):
    nc = k.nc
    parts = [(n, a, min(a + KD, len(tiles))) for n in range(2) for a in range(0, len(tiles), KD)]
    with stage(nc, "w0 w1 bank read free_dve") as (block, w0, w1, bank, read, free_dve):
        landed = (w0, w1)

        @block.sync
        def _(sp):
            for s, (n, a, e) in enumerate(parts):
                if s >= 2:
                    sp.wait_ge(read, s - 1)
                sp.dma_start(slot_view(k, s % 2, e - a, 512), w[:, a:e, n * 512:(n + 1) * 512]).then_inc(landed[s % 2], 16)

        @block.tensor
        def _(pe):
            for s, (n, a, e) in enumerate(parts):
                pe.wait_ge(landed[s % 2], 16 * (s // 2) + 16)
                wv = slot_view(k, s % 2, e - a, 512)
                for t in range(NT):
                    mm = chain(pe, k.ps[:, 4 * n + t, :], lambda q: tiles[q][:, t * P:(t + 1) * P], lambda q: wv[:, q - a, :],
                               range(a, e), first=a == 0, last=e == len(tiles))
                mm.then_inc(read, 1)

        @block.vector
        def _(dve):
            for n in range(2):
                dve.wait_ge(read, len(parts) // 2 * (n + 1))
                for t in range(NT):
                    nc.vector.tensor_copy(y[:, t, n * 512:(n + 1) * 512], k.ps[:, 4 * n + t, :]).then_inc(free_dve, 1)
            dve.wait_ge(free_dve, 2 * NT)


def mlp(k, w1, w2, y):
    nc = k.nc
    with ExitStack() as c:
        hid = c.enter_context(nc.sbuf_tensor(fresh("hid"), [P, KD, S], F32))
        r = c.enter_context(nc.sbuf_tensor(fresh("relu"), [P, 2, S], F32))
        block, s0, s1, slot_free, bank, relu, free_dve, step = c.enter_context(
            stage(nc, "w0 w1 slot_free bank relu free_dve step"))
        landed = (s0, s1)
        C = 4

        @block.sync
        def _(sp):
            with sp.Fori(0, C) as ch:
                for j in range(4):
                    sp.wait_ge(slot_free, 4 * ch + j + 1)
                    if j < 2:
                        src = w1[:, :, bass.ds(1024 * ch + 512 * j, 512)]
                    else:
                        src = w2[:, bass.ds(8 * ch, 8), (j - 2) * 512:(j - 1) * 512]
                    sp.dma_start(slot_view(k, j % 2, KD, 512), src).then_inc(landed[j % 2], 16)

        @block.tensor
        def _(pe):
            pe.nop().then_inc(slot_free, 2)
            with pe.Fori(0, C) as ch:
                for j in range(4):
                    b = j % 2
                    pe.wait_ge(landed[b], 32 * ch + 16 * (j // 2) + 16)
                    pe.wait_ge(free_dve, 4 * ch + j + 1)
                    wv = slot_view(k, b, KD, 512)
                    if j == 2:
                        pe.wait_ge(free_dve, 4 * ch + 4)
                    for m in range(4):
                        if j < 2:
                            mm = chain(pe, k.ps[:, 4 * b + m, :], lambda q: wv[:, q, m * P:(m + 1) * P], lambda q: k.hT[:, q, :], range(KD))
                        else:
                            mm = chain(pe, k.ps[:, 4 * b + m, :], lambda q: hid[:, q, m * P:(m + 1) * P], lambda q: wv[:, q, :], range(KD))
                        mm.then_inc(bank, 1)
                    pe.wait_ge(bank, 16 * ch + 4 * j + 4)
                    pe.nop().then_inc(slot_free, 1)

        @block.scalar
        def _(act):
            with act.Fori(0, C) as ch:
                for j in range(2):
                    for m in range(4):
                        act.wait_ge(bank, 16 * ch + 4 * j + m + 1)
                        if j or m > 1:
                            act.wait_ge(step, 1 + 16 * ch + 4 * j + m - 1)
                        else:
                            act.wait_ge(step, 1 + 16 * ch)
                        nc.scalar.activation(r[:, m % 2, :], k.ps[:, 4 * j + m, :], ACT.Relu).then_inc(relu, 1)

        @block.vector
        def _(dve):
            link = Link(dve, step)
            link(nc.vector.memset(y[:], 0.0))
            dve.nop().then_inc(free_dve, 2)
            with dve.Fori(0, C) as ch:
                link.n, link.base = 1, 16 * ch
                for j in range(2):
                    for m in range(4):
                        dve.wait_ge(relu, 8 * ch + 4 * j + m + 1)
                        link(nc.vector.tensor_tensor(hid[:, 4 * j + m, :], r[:, m % 2, :], r[:, m % 2, :], ALU.mult))
                    dve.nop().then_inc(free_dve, 1)
                for n in range(2):
                    for t in range(NT):
                        dve.wait_ge(bank, 16 * ch + 8 + 4 * n + t + 1)
                        yv = y[:, t, n * 512:(n + 1) * 512]
                        link(nc.vector.tensor_tensor(yv, yv, k.ps[:, 4 * n + t, :], ALU.add))
                    dve.nop().then_inc(free_dve, 1)


def add_normed(k, y, grow, store=None):
    nc = k.nc
    with ExitStack() as c:
        sb = lambda n, s: c.enter_context(nc.sbuf_tensor(fresh(n), s, F32))
        st, mv, ms = sb("stats_y", [P, NT, 2, 6]), sb("mv_y", [P, NT, 2]), sb("ms_y", [P, NT])
        block, var_done, root_done, x_done, stored, step = c.enter_context(stage(nc, "var_done root_done x_done stored step"))

        @block.sync
        def _(sp):
            if store is not None:
                for t in range(NT):
                    sp.wait_ge(x_done, t + 1)
                    sp.dma_start(store[:, t, :], k.x[:, t, :]).then_inc(stored, 16)
                sp.wait_ge(stored, 16 * NT)

        @block.scalar
        def _(act):
            act.wait_ge(var_done, 1)
            nc.scalar.activation(ms[:], ms[:], ACT.Sqrt).then_inc(root_done, 1)

        @block.vector
        def _(dve):
            link = Link(dve, step)
            for t in range(NT):
                for h in range(2):
                    link(nc.vector.bn_stats(st[:, t, h, :], y[:, t, h * 512:(h + 1) * 512]))
            for t in range(NT):
                link(nc.vector.bn_aggr(mv[:, t, :], st[:, t, :, :].rearrange("p a b -> p (a b)")))
            link(nc.vector.tensor_tensor(ms[:], mv[:, :, 0], mv[:, :, 0], ALU.mult))
            link(nc.vector.tensor_tensor(ms[:], ms[:], mv[:, :, 1], ALU.add))
            nc.vector.tensor_scalar(ms[:], ms[:], RMS_EPS, None, ALU.add).then_inc(var_done, 1)
            dve.wait_ge(root_done, 1)
            link(nc.vector.reciprocal(ms[:], ms[:]))
            for t in range(NT):
                link(nc.vector.scalar_tensor_tensor(y[:, t, :], y[:, t, :], ms[:, t:t + 1], grow[:], ALU.mult, ALU.mult))
                nc.vector.tensor_tensor(k.x[:, t, :], k.x[:, t, :], y[:, t, :], ALU.add).then_inc(x_done, 1)
            dve.wait_ge(x_done, NT)


def relative_bias(k, bias):
    nc = k.nc
    H = 8
    flat = k.scratch[0:H * P * BIAS_W]
    with ExitStack() as c:
        hot = c.enter_context(nc.sbuf_tensor(fresh("hot"), [33, BIAS_W], F32))
        rel = c.enter_context(nc.sbuf_tensor(fresh("rel"), [33, H], F32))
        wide = c.enter_context(nc.sbuf_tensor(fresh("wide"), [P, H, BIAS_W], F32))
        block, in_landed, neg_done, row_done, row_out, moved = c.enter_context(
            stage(nc, "in_landed neg_done row_done row_out moved"))

        @block.sync
        def _(sp):
            sp.dma_start(hot[:], k.K["bucket_hot"]).then_inc(in_landed, 16)
            sp.dma_start(rel[0:32, :], k.A["rel_bias_2"]).then_inc(in_landed, 16)
            sp.wait_ge(row_out, 2 * H)
            sp.dma_start(flat.rearrange("(h p n) -> p h n", p=P, n=BIAS_W), wide[:]).then_inc(moved, 16)
            sp.wait_ge(moved, 16)
            for h in range(H):
                src = flat[h * P * BIAS_W + P - 1:h * P * BIAS_W + P - 1 + P * (BIAS_W - 1)].rearrange("(p n) -> p n", n=BIAS_W - 1)[:, 0:512]
                sp.dma_start(bias[:, h, :], src).then_inc(moved, 16)
            sp.wait_ge(moved, 16 * (H + 1))

        @block.gpsimd
        def _(pool):
            nc.gpsimd.memset(rel[32:33, :], NEG).then_inc(neg_done, 1)

        @block.tensor
        def _(pe):
            pe.wait_ge(in_landed, 32)
            pe.wait_ge(neg_done, 1)
            for h in range(H):
                if h >= 4:
                    pe.wait_ge(row_out, 2 * (h - 3))
                b = 2 * (h % 4)
                pe.matmul(k.ps[:, b, :], rel[:, h:h + 1].to_broadcast([33, P]), hot[:, 0:512], start=True, stop=True)
                pe.matmul(k.ps[:, b + 1, 0:P], rel[:, h:h + 1].to_broadcast([33, P]), hot[:, 512:BIAS_W], start=True, stop=True).then_inc(row_done, 1)

        @block.vector
        def _(dve):
            for h in range(H):
                dve.wait_ge(row_done, h + 1)
                b = 2 * (h % 4)
                nc.vector.tensor_copy(wide[:, h, 0:512], k.ps[:, b, :]).then_inc(row_out, 1)
                nc.vector.tensor_copy(wide[:, h, 512:BIAS_W], k.ps[:, b + 1, 0:P]).then_inc(row_out, 1)
            dve.wait_ge(row_out, 2 * H)


def convolution(k, xbc, T):
    nc = k.nc
    A = k.A
    with ExitStack() as c:
        raw = c.enter_context(nc.sbuf_tensor(fresh("craw"), [80, P], F32))
        w = c.enter_context(nc.sbuf_tensor(fresh("cw"), [P, 80], F32))
        cv = c.enter_context(nc.sbuf_tensor(fresh("cv"), [P, 2, S], F32))
        block, in_landed, wt_done, conv_done, silu_done, t_done, t_out, step = c.enter_context(
            stage(nc, "in_landed wt_done conv_done silu_done t_done t_out step"))

        @block.sync
        def _(sp):
            sp.dma_start(raw[0:64, :], A["e_conv_w_2"].rearrange("e j (q p) -> (e j q) p", p=P)).then_inc(in_landed, 16)
            sp.dma_start(raw[64:80, :], A["e_conv_b_2"].rearrange("e (q p) -> (e q) p", p=P)).then_inc(in_landed, 16)
            sp.wait_ge(in_landed, 32)

        @block.vector
        def _(dve):
            link = Link(dve, step)
            V = nc.vector
            dve.wait_ge(wt_done, 1)
            link(V.tensor_copy(w[:], k.ps[:, 0, 0:80]))
            link(V.memset(xbc[:, :, 0:3], 0.0))
            for q in range(16):
                if q >= 2:
                    dve.wait_ge(silu_done, q - 1)
                o = cv[:, q % 2, :]
                link(V.tensor_scalar(o, xbc[:, q, 0:S], w[:, q:q + 1], w[:, 64 + q:65 + q], ALU.mult, ALU.add))
                for j in (1, 2):
                    link(V.scalar_tensor_tensor(o, xbc[:, q, j:j + S], w[:, 16 * j + q:16 * j + q + 1], o, ALU.mult, ALU.add))
                V.scalar_tensor_tensor(o, xbc[:, q, 3:3 + S], w[:, 48 + q:49 + q], o, ALU.mult, ALU.add).then_inc(conv_done, 1)

        @block.scalar
        def _(act):
            def token_major(q):
                act.wait_ge(t_done, q + 1)
                dst = T["xh"][:, :, q * P:(q + 1) * P] if q < 8 else T["Bt"][:, :, q - 8, :]
                nc.scalar.copy(dst, k.ps[:, 1 + q % 2, :].rearrange("p (t n) -> p t n", t=NT)).then_inc(t_out, 1)

            for q in range(16):
                act.wait_ge(conv_done, q + 1)
                nc.scalar.activation(xbc[:, q, 3:3 + S], cv[:, q % 2, :], ACT.Silu).then_inc(silu_done, 1)
                if 1 <= q < 13:
                    token_major(q - 1)
            act.wait_ge(silu_done, 16)
            act.wait_ge(t_out, 12)

        @block.tensor
        def _(pe):
            pe.wait_ge(in_landed, 32)
            pe.transpose(k.ps[:, 0, 0:80], raw[:], k.ident[0:80, 0:80]).then_inc(wt_done, 1)
            for q in range(12):
                pe.wait_ge(silu_done, q + 1)
                if q >= 2:
                    pe.wait_ge(t_out, q - 1)
                for t in range(NT):
                    mm = pe.transpose(k.ps[:, 1 + q % 2, t * P:(t + 1) * P], xbc[:, q, 3 + t * P:3 + (t + 1) * P], k.ident[:])
                mm.then_inc(t_done, 1)


def ssd(k, xbc, T):
    nc = k.nc
    A = k.A
    H, G, R = SSD_HEADS, SSD_GROUPS, SSD_HEADS // SSD_GROUPS
    with ExitStack() as c:
        sb = lambda n, s: c.enter_context(nc.sbuf_tensor(fresh(n), s, F32))
        par = sb("par", [P, 3, H])
        tri = sb("tri", [P, 2, P])
        ones = sb("ones", [P, P])
        dt = T["dt"]
        e, z, z2, acc = (sb(n, [P, NT, H]) for n in ("e_sp", "z_sp", "z2_sp", "acc_sp"))
        a, nacs, eacs, dte, etot, cs = (sb(n, [P, NT, H]) for n in ("a_ss", "nacs", "eacs", "dte", "etot", "cs_ss"))
        X = sb("Xdt", [P, NT, H, 64])
        Xd = sb("Xdec", [P, 2, R * 64])
        idle = k.ring[:].rearrange("p b n -> p (b n)")
        seg, M = (idle[:, i * 2 * R * P:(i + 1) * 2 * R * P].rearrange("p (b r n) -> p b r n", b=2, r=R) for i in range(2))
        state = sb("state", [P, G, R * 64])
        yt = sb("yt", [P, 2, R * 64])
        (block, in_landed, dt_in, exp1, a_done, sums, sums_out, exp2, front, seg_done, dec_done, m_done, back, y_out,
         xd_done, st_done, step) = c.enter_context(stage(
            nc, "in_landed dt_in exp1 a_done sums sums_out exp2 front seg_done dec_done m_done back y_out xd_done st_done step"))
        units = [(ch, g) for ch in range(NT) for g in range(G)]
        N = len(units)
        BT = lambda ch, g: xbc[:, 8 + g, 3 + ch * P:3 + (ch + 1) * P]
        CT = lambda ch, g: xbc[:, 12 + g, 3 + ch * P:3 + (ch + 1) * P]
        xh = T["xh"][:].rearrange("p t (h d) -> p t h d", d=64)

        @block.sync
        def _(sp):
            for i, n in enumerate(("e_dt_bias_2", "e_A_log_2", "e_D_2")):
                sp.dma_start(par[:, i, :], bcast(A[n][0], 0, P)).then_inc(in_landed, 16)
            sp.dma_start(tri[:], k.K["causal"]).then_inc(in_landed, 16)
            sp.wait_ge(in_landed, 64)

        @block.scalar
        def _(act):
            act.wait_ge(in_landed, 64)
            nc.scalar.activation(par[:, 1, :], par[:, 1, :], ACT.Exp).then_inc(exp1, 1)
            act.wait_ge(dt_in, 1)
            nc.scalar.activation(e[:], e[:], ACT.Exp, scale=-1.0).then_inc(exp1, 1)
            act.wait_ge(sums_out, 1)
            nc.scalar.activation(eacs[:], eacs[:], ACT.Exp)
            nc.scalar.activation(dte[:], dte[:], ACT.Exp)
            nc.scalar.activation(etot[:], etot[:], ACT.Exp).then_inc(exp2, 1)
            for i, (ch, g) in enumerate(units):
                act.wait_ge(seg_done, i + 1)
                for r in range(R):
                    h = g * R + r
                    last = nc.scalar.activation(seg[:, i % 2, r, :], seg[:, i % 2, r, :], ACT.Exp, bias=nacs[:, ch, h:h + 1])
                last.then_inc(dec_done, 1)
            act.wait_ge(dec_done, N)

        @block.tensor
        def _(pe):
            pe.wait_ge(a_done, 1)
            for ch in range(NT):
                pe.matmul(k.ps[:, 0, ch * H:(ch + 1) * H], tri[:, 0, :], a[:, ch, :], start=True, stop=True)
                mm = pe.matmul(k.ps[:, 1, ch * H:(ch + 1) * H], ones[:], a[:, ch, :], start=True, stop=True)
            mm.then_inc(sums, 1)
            pe.wait_ge(sums_out, 1)
            for i in range(N + 1):
                if i < N:
                    ch, g = units[i]
                    if i >= 2:
                        pe.wait_ge(m_done, i - 1)
                    pe.matmul(k.ps[:, i % 2, 0:P], BT(ch, g), CT(ch, g), start=True, stop=True)
                    for r in range(R):
                        h = g * R + r
                        mm = pe.matmul(k.ps[:, 2 + i % 2, r * P:(r + 1) * P], a[:, ch, h:h + 1].to_broadcast([P, P]), tri[:, 0, :],
                                       start=True, stop=True)
                    mm.then_inc(front, 1)
                if i >= 1:
                    v = i - 1
                    ch, g = units[v]
                    pe.wait_ge(m_done, v + 1)
                    pe.wait_ge(xd_done, v + 1)
                    if v >= 2:
                        pe.wait_ge(y_out, v - 1)
                    if v >= G:
                        pe.wait_ge(st_done, v - G + 1)
                    for r in range(R):
                        pe.matmul(k.ps[:, 4 + v % 2, r * 64:(r + 1) * 64], M[:, v % 2, r, :], X[:, ch, g * R + r, :], start=True, stop=True)
                    if ch:
                        pe.matmul(k.ps[:, 4 + v % 2, 256:512], CT(ch, g), state[:, g, :], start=True, stop=True)
                    pe.matmul(k.ps[:, 6 + v % 2, 0:256], T["Bt"][:, ch, g, :], Xd[:, v % 2, :], start=True, stop=True).then_inc(back, 1)

        @block.vector
        def _(dve):
            link = Link(dve, step)
            V = nc.vector
            link(V.memset(ones[:], 1.0))
            dve.wait_ge(in_landed, 64)
            link(V.tensor_tensor(dt[:], dt[:], bcast(par[:, 0, :], 1, NT), ALU.add))
            link(V.scalar_tensor_tensor(e[:], dt[:], -1.0, dt[:], ALU.mult, ALU.max))
            dve.nop().then_inc(dt_in, 1)
            dve.wait_ge(exp1, 2)
            link(V.tensor_scalar(z[:], e[:], 2.0, None, ALU.add))
            link(V.reciprocal(z[:], z[:]))
            link(V.tensor_tensor(z[:], z[:], e[:], ALU.mult))
            link(V.tensor_tensor(z2[:], z[:], z[:], ALU.mult))
            link(V.tensor_scalar(acc[:], z2[:], 1.0 / 19, None, ALU.mult))
            for n in range(8, 0, -1):
                link(V.scalar_tensor_tensor(acc[:], acc[:], 1.0 / (2 * n + 1), z2[:], ALU.add, ALU.mult))
            link(V.scalar_tensor_tensor(acc[:], acc[:], 1.0, z[:], ALU.add, ALU.mult))
            link(V.tensor_scalar(dt[:], dt[:], 0.0, None, ALU.max))
            link(V.scalar_tensor_tensor(dt[:], acc[:], 2.0, dt[:], ALU.mult, ALU.add))
            link(V.tensor_tensor(a[:], dt[:], bcast(par[:, 1, :], 1, NT), ALU.mult))
            V.tensor_scalar(a[:], a[:], -1.0, None, ALU.mult).then_inc(a_done, 1)
            for ch in range(NT):
                link(V.tensor_tensor(X[:, ch], xh[:, ch], bcast(dt[:, ch, :], 2, 64), ALU.mult))
            dve.wait_ge(sums, 1)
            acs, tot = (k.ps[:, b, 0:NT * H].rearrange("p (t h) -> p t h", t=NT) for b in (0, 1))
            link(V.tensor_copy(cs[:], acs))
            link(V.tensor_scalar(nacs[:], cs[:], -1.0, None, ALU.mult))
            link(V.tensor_copy(eacs[:], cs[:]))
            link(V.tensor_copy(etot[:], tot))
            link(V.tensor_tensor(dte[:], etot[:], cs[:], ALU.subtract))
            dve.nop().then_inc(sums_out, 1)
            dve.wait_ge(exp2, 1)
            for i in range(N + 1):
                if i < N:
                    ch, g = units[i]
                    hs = slice(g * R, (g + 1) * R)
                    dve.wait_ge(front, i + 1)
                    V.tensor_tensor(seg[:, i % 2], k.ps[:, 2 + i % 2, :].rearrange("p (r l) -> p r l", r=R), bcast(tri[:, 1, :], 1, R),
                                    ALU.add).then_inc(seg_done, 1)
                    if i >= 2:
                        dve.wait_ge(back, i - 1)
                    V.tensor_tensor(Xd[:, i % 2, :].rearrange("p (r d) -> p r d", r=R), X[:, ch, hs], bcast(dte[:, ch, hs], 2, 64),
                                    ALU.mult).then_inc(xd_done, 1)
                    dve.wait_ge(dec_done, i + 1)
                    V.tensor_tensor(M[:, i % 2], seg[:, i % 2], bcast(k.ps[:, i % 2, 0:P], 1, R), ALU.mult).then_inc(m_done, 1)
                if i >= 1:
                    v = i - 1
                    ch, g = units[v]
                    hs = slice(g * R, (g + 1) * R)
                    dve.wait_ge(back, v + 1)
                    y = yt[:, v % 2, :].rearrange("p (r d) -> p r d", r=R)
                    diag = k.ps[:, 4 + v % 2, 0:256].rearrange("p (r d) -> p r d", r=R)
                    link(V.tensor_tensor(xh[:, ch, hs], xh[:, ch, hs], bcast(par[:, 2, hs], 2, 64), ALU.mult))
                    link(V.tensor_tensor(xh[:, ch, hs], xh[:, ch, hs], diag, ALU.add))
                    if ch:
                        off = k.ps[:, 4 + v % 2, 256:512].rearrange("p (r d) -> p r d", r=R)
                        link(V.tensor_tensor(y, off, bcast(eacs[:, ch, hs], 2, 64), ALU.mult))
                        link(V.tensor_tensor(xh[:, ch, hs], xh[:, ch, hs], y, ALU.add))
                        st = state[:, g, :].rearrange("p (r d) -> p r d", r=R)
                        link(V.tensor_tensor(st, st, bcast(etot[:, ch, hs], 2, 64), ALU.mult))
                        V.tensor_tensor(state[:, g, :], state[:, g, :], k.ps[:, 6 + v % 2, 0:256], ALU.add).then_inc(st_done, 1)
                    else:
                        V.tensor_copy(state[:, g, :], k.ps[:, 6 + v % 2, 0:256]).then_inc(st_done, 1)
                    dve.wait_ge(st_done, v + 1)
                    dve.nop().then_inc(y_out, 1)


def gate_rows(k, y, z):
    nc = k.nc
    with stage(nc, "done_dve done_pool") as (block, done_dve, done_pool):
        @block.vector
        def _(dve):
            for t in (0, 1, 2):
                nc.vector.tensor_tensor(y[:, t, :], y[:, t, :], z[:, t, :], ALU.mult).then_inc(done_dve, 1)
            dve.wait_ge(done_dve, 3)

        @block.gpsimd
        def _(pool):
            nc.gpsimd.tensor_tensor(y[:, 3, :], y[:, 3, :], z[:, 3, :], ALU.mult).then_inc(done_pool, 1)
            pool.wait_ge(done_pool, 1)


def column_of(k, row, n, out, factor=1.0):
    nc = k.nc
    with ExitStack() as c:
        raw = c.enter_context(nc.sbuf_tensor(fresh("rraw"), [max(n, 2), P], F32))
        block, landed, t_done, col_out = c.enter_context(stage(nc, "landed t_done col_out"))

        @block.sync
        def _(sp):
            sp.dma_start(raw[0:n, :], row.rearrange("(k p) -> k p", p=P)).then_inc(landed, 16)
            sp.wait_ge(landed, 16)

        @block.tensor
        def _(pe):
            pe.wait_ge(landed, 16)
            pe.transpose(k.ps[:, 0, 0:n], raw[0:n, :], k.ident[0:n, 0:n]).then_inc(t_done, 1)

        @block.vector
        def _(dve):
            dve.wait_ge(t_done, 1)
            nc.vector.tensor_scalar(out[:, 0:n], k.ps[:, 0, 0:n], factor, None, ALU.mult).then_inc(col_out, 1)
            dve.wait_ge(col_out, 1)


def diff_attention(k, qT, kT, v, bias, lam, lam_init, y):
    nc = k.nc
    with ExitStack() as c:
        sb = lambda n, s: c.enter_context(nc.sbuf_tensor(fresh(n), s, F32))
        lr = sb("lr", [P, 4, 64])
        lp = sb("lp", [P, 64])
        ld = sb("ld", [P, 2])
        nlam = sb("nlam", [P, 1])
        sc = sb("dsc", [P, 2, 2, 512])
        pr = sb("dpr", [P, 2, 2, 512])
        pT = sb("dpT", [P, 2, 512])
        mx, nm, ls = sb("dmx", [P, 2, 2]), sb("dnm", [P, 2, 2]), sb("dls", [P, 2, 2])
        block, in_landed, ld_done, ld_exp, s_ready, max_done, exp_done, p_ready, t_ready, t_out, o_ready, o_out, step = c.enter_context(
            stage(nc, "in_landed ld_done ld_exp s_ready max_done exp_done p_ready t_ready t_out o_ready o_out step"))
        units = [(h, t) for h in range(8) for t in range(NT)]
        N = len(units)
        W = lambda i: P * (units[i][1] + 1)

        @block.sync
        def _(sp):
            sp.dma_start(lr[:], bcast(lam, 0, P)).then_inc(in_landed, 16)
            sp.wait_ge(in_landed, 16)

        @block.tensor
        def _(pe):
            for i in range(N + 2):
                if i < N:
                    h, t = units[i]
                    if i >= 2:
                        pe.wait_ge(max_done, i - 1)
                    for m in range(2):
                        mm = pe.matmul(k.ps[:, 2 * (i % 2) + m, 0:W(i)], qT[64 * m:64 * m + 64, h, t * P:(t + 1) * P],
                                       kT[64 * m:64 * m + 64, h, 0:W(i)], start=True, stop=True)
                    mm.then_inc(s_ready, 1)
                if 1 <= i <= N:
                    u = i - 1
                    pe.wait_ge(p_ready, u + 1)
                    if u >= 2:
                        pe.wait_ge(t_out, u - 1)
                    for j in range(W(u) // P):
                        mm = pe.transpose(k.ps[:, 4 + u % 2, j * P:(j + 1) * P], pr[:, u % 2, 0, j * P:(j + 1) * P], k.ident[:])
                    mm.then_inc(t_ready, 1)
                if i >= 2:
                    u = i - 2
                    h, t = units[u]
                    pe.wait_ge(t_out, u + 1)
                    if u >= 2:
                        pe.wait_ge(o_out, u - 1)
                    chain(pe, k.ps[:, 6 + u % 2, 0:P], lambda j: pT[:, u % 2, j * P:(j + 1) * P],
                          lambda j: v[:, j, h * P:(h + 1) * P], range(t + 1)).then_inc(o_ready, 1)

        @block.scalar
        def _(act):
            act.wait_ge(ld_done, 1)
            nc.scalar.activation(ld[:], ld[:], ACT.Exp).then_inc(ld_exp, 1)
            for i in range(N + 2):
                if i < N:
                    act.wait_ge(max_done, i + 1)
                    if i >= 2:
                        act.wait_ge(t_ready, i - 1)
                    for m in range(2):
                        last = nc.scalar.activation(pr[:, i % 2, m, 0:W(i)], sc[:, i % 2, m, 0:W(i)], ACT.Exp,
                                                    bias=nm[:, i % 2, m:m + 1], accum_out=ls[:, i % 2, m:m + 1])
                    last.then_inc(exp_done, 1)
                if 1 <= i <= N:
                    u = i - 1
                    act.wait_ge(t_ready, u + 1)
                    if u >= 2:
                        act.wait_ge(o_ready, u - 1)
                    nc.scalar.copy(pT[:, u % 2, 0:W(u)], k.ps[:, 4 + u % 2, 0:W(u)]).then_inc(t_out, 1)
                if i >= 2:
                    u = i - 2
                    h, t = units[u]
                    act.wait_ge(o_ready, u + 1)
                    nc.scalar.copy(y[:, t, h * P:(h + 1) * P], k.ps[:, 6 + u % 2, 0:P]).then_inc(o_out, 1)
            act.wait_ge(o_out, N)

        @block.vector
        def _(dve):
            link = Link(dve, step)
            V = nc.vector
            dve.wait_ge(in_landed, 16)
            for m in range(2):
                link(V.tensor_tensor_reduce(lp[:], lr[:, 2 * m, :], lr[:, 2 * m + 1, :], 1.0, 0.0, ALU.mult, ALU.add, ld[:, m:m + 1]))
            dve.nop().then_inc(ld_done, 1)
            dve.wait_ge(ld_exp, 1)
            link(V.tensor_tensor(nlam[:], ld[:, 1:2], ld[:, 0:1], ALU.subtract))
            link(V.tensor_scalar(nlam[:], nlam[:], -lam_init, None, ALU.add))
            for i in range(N + 1):
                if i < N:
                    h, t = units[i]
                    b = bias[:, h, 512 - W(i):512]
                    dve.wait_ge(s_ready, i + 1)
                    if i >= 2:
                        dve.wait_ge(exp_done, i - 1)
                    for m in range(2):
                        link(V.tensor_tensor_reduce(sc[:, i % 2, m, 0:W(i)], k.ps[:, 2 * (i % 2) + m, 0:W(i)], b, 1.0, 2 * NEG,
                                                    ALU.add, ALU.max, mx[:, i % 2, m:m + 1]))
                    V.tensor_scalar(nm[:, i % 2, :], mx[:, i % 2, :], -1.0, None, ALU.mult).then_inc(max_done, 1)
                if i >= 1:
                    u = i - 1
                    dve.wait_ge(exp_done, u + 1)
                    l = ls[:, u % 2, :]
                    link(V.reciprocal(l, l))
                    link(V.tensor_tensor(l[:, 1:2], l[:, 1:2], nlam[:], ALU.mult))
                    p0, p1 = (pr[:, u % 2, m, 0:W(u)] for m in range(2))
                    link(V.tensor_scalar(p0, p0, l[:, 0:1], None, ALU.mult))
                    V.scalar_tensor_tensor(p0, p1, l[:, 1:2], p0, ALU.mult, ALU.add).then_inc(p_ready, 1)
            dve.wait_ge(p_ready, N)


def head_norm_T(k, y, nh, width, mult, scale, out):
    nc = k.nc
    idle = k.ring[:].rearrange("p b n -> p (b n)")[:, 0:NT * D].rearrange("p (t n) -> p t n", t=NT)
    with ExitStack() as c:
        ms = c.enter_context(nc.sbuf_tensor(fresh("ms_h"), [P, NT, nh], F32))
        block, sq_done, ms_done, root_done, y_done, t_done, out_act, step = c.enter_context(
            stage(nc, "sq_done ms_done root_done y_done t_done out_act step"))
        nt = nh * width // P

        @block.scalar
        def _(act):
            for t in range(NT):
                last = nc.scalar.activation(idle[:, t, 0:nh * width], y[:, t, :], ACT.Square)
            last.then_inc(sq_done, 1)
            act.wait_ge(ms_done, 1)
            nc.scalar.activation(ms[:], ms[:], ACT.Sqrt).then_inc(root_done, 1)
            for q in range(nt):
                act.wait_ge(t_done, q + 1)
                if scale is None:
                    last = nc.scalar.copy(out[:, q, :], k.ps[:, q, :])
                else:
                    last = nc.scalar.activation(out[:, q, :], k.ps[:, q, :], ACT.Copy, scale=scale)
            last.then_inc(out_act, 1)
            act.wait_ge(out_act, 1)

        @block.vector
        def _(dve):
            link = Link(dve, step)
            V = nc.vector
            dve.wait_ge(sq_done, 1)
            for t in range(NT):
                link(V.tensor_reduce(ms[:, t, :], idle[:, t, :].rearrange("p (h d) -> p h d", d=width), AX, ALU.add))
            V.tensor_scalar(ms[:], ms[:], 1.0 / width, RMS_EPS, ALU.mult, ALU.add).then_inc(ms_done, 1)
            dve.wait_ge(root_done, 1)
            link(V.reciprocal(ms[:], ms[:]))
            for t in range(NT):
                yv = y[:, t, :].rearrange("p (h d) -> p h d", d=width)
                link(V.tensor_tensor(yv, yv, bcast(ms[:, t, :], 2, width), ALU.mult))
                if mult is not None:
                    link(V.tensor_tensor(y[:, t, :], y[:, t, :], mult[:, t, :], ALU.mult))
            dve.nop().then_inc(y_done, 1)

        @block.tensor
        def _(pe):
            pe.wait_ge(y_done, 1)
            for q in range(nt):
                for t in range(NT):
                    mm = pe.transpose(k.ps[:, q, t * P:(t + 1) * P], y[:, t, q * P:(q + 1) * P], k.ident[:])
                mm.then_inc(t_done, 1)


def transposed(k, src, nt, out):
    nc = k.nc
    with stage(nc, "t_done out_act") as (block, t_done, out_act):
        @block.tensor
        def _(pe):
            for q in range(nt):
                for t in range(NT):
                    mm = pe.transpose(k.ps[:, q, t * P:(t + 1) * P], src(t, q), k.ident[:])
                mm.then_inc(t_done, 1)

        @block.scalar
        def _(act):
            for q in range(nt):
                act.wait_ge(t_done, q + 1)
                nc.scalar.copy(out[:, q, :], k.ps[:, q, :]).then_inc(out_act, 1)
            act.wait_ge(out_act, nt)


def even_mixer(k, bias, y):
    nc, A = k.nc, k.A
    w = A["e_w_in_2"][0].rearrange("(k p) n -> p k n", p=P)
    with ExitStack() as m:
        ysT = m.enter_context(nc.sbuf_tensor(fresh("y_ssdT"), [P, KD, S], F32))
        with ExitStack() as c:
            sb = lambda n, s: c.enter_context(nc.sbuf_tensor(fresh(n), s, F32))
            T = {"xh": y, "dt": sb("dt", [P, NT, SSD_HEADS])}
            z = sb("z", [P, NT, D])
            nw = sb("nw", [P, KD])
            with ExitStack() as d:
                xbc = d.enter_context(nc.sbuf_tensor(fresh("xbcT"), [P, 16, S + 3], F32))
                T["Bt"] = d.enter_context(nc.sbuf_tensor(fresh("B_tok"), [P, NT, SSD_GROUPS, P], F32))
                plan = [(1024 + 512 * s, 512, "feature", 1.0, [xbc[:, 4 * s + j, 3:3 + S] for j in range(4)]) for s in range(4)]
                plan += [(512 * s, 512, "token", "silu", [z[:, t, 512 * s:512 * (s + 1)] for t in range(NT)]) for s in range(2)]
                plan += [(3072, 16, "token", 1.0, [T["dt"][:, t, :] for t in range(NT)])]
                project(k, w, plan)
                convolution(k, xbc, T)
                ssd(k, xbc, T)
            gate_rows(k, y, z)
            column_of(k, A["e_ssd_norm_2"][0], KD, nw)
            norm_to_hT(k, True, RMS_EPS, nw, None, src=y, dst=ysT)
        with ExitStack() as c:
            sb = lambda n, s: c.enter_context(nc.sbuf_tensor(fresh(n), s, F32))
            qT, kT, v = sb("qT", [P, 8, S]), sb("kT", [P, 8, S]), sb("v_tok", [P, NT, D])
            plan = [(3088 + 512 * s, 512, "feature", HD ** -0.5, [qT[:, 4 * s + j, :] for j in range(4)]) for s in range(2)]
            plan += [(4112 + 512 * s, 512, "feature", 1.0, [kT[:, 4 * s + j, :] for j in range(4)]) for s in range(2)]
            plan += [(5136 + 512 * s, 512, "token", 1.0, [v[:, t, 512 * s:512 * (s + 1)] for t in range(NT)]) for s in range(2)]
            project(k, w, plan)
            lam_init = 0.8 - 0.6 * math.exp(-0.3 * 0)
            diff_attention(k, qT, kT, v, bias, A["e_lambda_2"][0], lam_init, y)
            dn = sb("dn", [P, 1])
            column_of(k, A["e_diff_norm_2"][0], 1, dn, 1.0 - lam_init)
            head_norm_T(k, y, 8, P, None, dn[:, 0:1], k.hT)
        tiles = [ysT[:, q, :] for q in range(KD)] + [k.hT[:, q, :] for q in range(KD)]
        out_projection(k, A["e_w_out_2"][0].rearrange("(k p) n -> p k n", p=P), tiles, y)


def retention_inputs(k, T):
    nc = k.nc
    H = RET_HEADS
    idle = k.ring[:].rearrange("p b n -> p (b n)")
    ro = [idle[:, i * 2048:(i + 1) * 2048].rearrange("p (t h e j) -> p t h e j", t=NT, h=H, e=2) for i in range(2)]
    t1 = idle[:, 4096:5120].rearrange("p (t h j) -> p t h j", t=NT, h=H)
    with ExitStack() as c:
        sb = lambda n, s: c.enter_context(nc.sbuf_tensor(fresh(n), s, F32))
        cs = sb("cs2", [P, 2, NT, 64])
        xi = sb("xi", [P, H, P])
        zeta = sb("zeta", [P, H])
        block, in_landed, ro_done, t_done, out_act, x_done, step = c.enter_context(
            stage(nc, "in_landed ro_done t_done out_act x_done step"))

        @block.sync
        def _(sp):
            for dst, n in ((cs, "rope2"), (xi, "ret_xi"), (zeta, "ret_zeta")):
                sp.dma_start(dst[:], k.K[n]).then_inc(in_landed, 16)
            sp.wait_ge(in_landed, 48)

        @block.vector
        def _(dve):
            link = Link(dve, step)
            V = nc.vector
            dve.wait_ge(in_landed, 48)
            for i, n in enumerate(("rq", "rk")):
                for t in range(NT):
                    x = T[n][:, t, :].rearrange("p (h e j) -> p h e j", h=H, e=2)
                    o, cos, sin, tt = ro[i][:, t], bcast(cs[:, 0, t, :], 1, H), bcast(cs[:, 1, t, :], 1, H), t1[:, t]
                    link(V.tensor_tensor(o[:, :, 0, :], x[:, :, 0, :], cos, ALU.mult))
                    link(V.tensor_tensor(tt, x[:, :, 1, :], sin, ALU.mult))
                    link(V.tensor_tensor(o[:, :, 0, :], o[:, :, 0, :], tt, ALU.subtract))
                    link(V.tensor_tensor(o[:, :, 1, :], x[:, :, 0, :], sin, ALU.mult))
                    link(V.tensor_tensor(tt, x[:, :, 1, :], cos, ALU.mult))
                    link(V.tensor_tensor(o[:, :, 1, :], o[:, :, 1, :], tt, ALU.add))
                dve.nop().then_inc(ro_done, 1)
            for h in range(H):
                dve.wait_ge(out_act, h + 1)
                nc.vector.tensor_tensor(T["QxT"][:, h, :].rearrange("p (t l) -> p t l", t=NT), k.ps[:, h, :].rearrange("p (t l) -> p t l", t=NT),
                                        bcast(xi[:, h, :], 1, NT), ALU.mult).then_inc(x_done, 1)
                kz = T["rk"][:].rearrange("p t (h d) -> p t h d", h=H)[:, :, h, :]
                link(V.tensor_scalar(kz, ro[1][:, :, h].rearrange("p t e j -> p t (e j)"), zeta[:, h:h + 1], None, ALU.mult))
            dve.wait_ge(x_done, H)

        @block.scalar
        def _(act):
            for q in range(2 * H):
                act.wait_ge(t_done, q + 1)
                nc.scalar.copy((T["QT"] if q < H else T["KT"])[:, q % H, :], k.ps[:, q, :]).then_inc(out_act, 1)
            act.wait_ge(out_act, 2 * H)

        @block.tensor
        def _(pe):
            for i in range(2):
                pe.wait_ge(ro_done, i + 1)
                for h in range(H):
                    for t in range(NT):
                        mm = pe.transpose(k.ps[:, 4 * i + h, t * P:(t + 1) * P], ro[i][:, t, h].rearrange("p e j -> p (e j)"), k.ident[:])
                    mm.then_inc(t_done, 1)


def retention(k, T, y):
    nc = k.nc
    H = RET_HEADS
    with ExitStack() as c:
        sb = lambda n, s: c.enter_context(nc.sbuf_tensor(fresh(n), s, F32))
        dec = sb("dec", [P, H, P])
        sT = sb("sT", [P, 2, P])
        state = sb("rstate", [P, H, RET_V])
        block, in_landed, front, s_done, back, y_out, st_done, step = c.enter_context(
            stage(nc, "in_landed front s_done back y_out st_done step"))
        units = [(ch, h) for ch in range(NT) for h in range(H)]
        N = len(units)

        @block.sync
        def _(sp):
            sp.dma_start(dec[:], k.K["ret_decay"]).then_inc(in_landed, 16)
            sp.wait_ge(in_landed, 16)

        @block.tensor
        def _(pe):
            for i in range(N + 1):
                if i < N:
                    ch, h = units[i]
                    if i >= 2:
                        pe.wait_ge(s_done, i - 1)
                    at = slice(ch * P, (ch + 1) * P)
                    pe.matmul(k.ps[:, i % 2, 0:P], T["KT"][:, h, at], T["QT"][:, h, at], start=True, stop=True).then_inc(front, 1)
                if i >= 1:
                    v = i - 1
                    ch, h = units[v]
                    at, vv = slice(ch * P, (ch + 1) * P), T["rv"][:, ch, h * RET_V:(h + 1) * RET_V]
                    pe.wait_ge(s_done, v + 1)
                    if v >= 2:
                        pe.wait_ge(y_out, v - 1)
                    if v >= H:
                        pe.wait_ge(st_done, v - H + 1)
                    pe.matmul(k.ps[:, 2 + v % 2, 0:RET_V], sT[:, v % 2, :], vv, start=True, stop=ch == 0)
                    if ch:
                        pe.matmul(k.ps[:, 2 + v % 2, 0:RET_V], T["QxT"][:, h, at], state[:, h, :], start=False, stop=True)
                    pe.matmul(k.ps[:, 4 + v % 2, 0:RET_V], T["rk"][:, ch, h * P:(h + 1) * P], vv, start=True, stop=True).then_inc(back, 1)

        @block.vector
        def _(dve):
            V = nc.vector
            dve.wait_ge(in_landed, 16)
            for i in range(N + 1):
                if i < N:
                    ch, h = units[i]
                    dve.wait_ge(front, i + 1)
                    if i >= 2:
                        dve.wait_ge(back, i - 1)
                    V.tensor_tensor(sT[:, i % 2, :], k.ps[:, i % 2, 0:P], dec[:, h, :], ALU.mult).then_inc(s_done, 1)
                if i >= 1:
                    v = i - 1
                    ch, h = units[v]
                    dve.wait_ge(back, v + 1)
                    new = k.ps[:, 4 + v % 2, 0:RET_V]
                    if ch:
                        dve.wait_ge(st_done, v - H + 1)
                        V.scalar_tensor_tensor(state[:, h, :], state[:, h, :], RET_STATE_DECAY[h], new, ALU.mult, ALU.add).then_inc(st_done, 1)
                    else:
                        V.tensor_copy(state[:, h, :], new).then_inc(st_done, 1)
                    dve.wait_ge(st_done, v + 1)
                    V.tensor_copy(y[:, ch, h * RET_V:(h + 1) * RET_V], k.ps[:, 2 + v % 2, 0:RET_V]).then_inc(y_out, 1)
            dve.wait_ge(y_out, N)


def window_bias(k, bias, sw, sink):
    nc = k.nc
    with ExitStack() as c:
        wm = c.enter_context(nc.sbuf_tensor(fresh("wm"), [P, P], F32))
        block, in_landed, done = c.enter_context(stage(nc, "in_landed done"))

        @block.sync
        def _(sp):
            sp.dma_start(wm[:], k.K["win_mask"]).then_inc(in_landed, 16)
            sp.dma_start(sink[:], bcast(k.A["o_sinks_2"][0], 0, P)).then_inc(in_landed, 16)
            sp.wait_ge(in_landed, 32)

        @block.vector
        def _(dve):
            dve.wait_ge(in_landed, 32)
            nc.vector.tensor_tensor(sw[:, :, 0:P], bias[:, :, 256:384], bcast(wm[:], 1, 8), ALU.add).then_inc(done, 1)
            nc.vector.tensor_copy(sw[:, :, P:256], bias[:, :, 384:512]).then_inc(done, 1)
            dve.wait_ge(done, 2)


def odd_mixer(k, bias, y):
    nc, A = k.nc, k.A
    w = A["o_w_in_2"][0].rearrange("(k p) n -> p k n", p=P)
    with ExitStack() as m:
        sb = lambda n, s: m.enter_context(nc.sbuf_tensor(fresh(n), s, F32))
        sqT, skv, soT = sb("sqT", [P, 4, S]), sb("skv", [P, NT, 256]), sb("soT", [P, 4, S])
        with ExitStack() as c:
            sc = lambda n, s: c.enter_context(nc.sbuf_tensor(fresh(n), s, F32))
            T = {n: sc(n, s) for n, s in (("rq", [P, NT, 512]), ("rk", [P, NT, 512]), ("rv", [P, NT, D]), ("rg", [P, NT, D]))}
            half = lambda t, s: [T[t][:, j, 512 * s:512 * (s + 1)] for j in range(NT)]
            plan = [(0, 512, "token", 1.0, half("rq", 0)), (512, 512, "token", 1.0, half("rk", 0)),
                    (1024, 512, "token", 1.0, half("rv", 0)), (1536, 512, "token", 1.0, half("rv", 1)),
                    (2048, 512, "token", "silu", half("rg", 0)), (2560, 512, "token", "silu", half("rg", 1)),
                    (3072, 512, "feature", HD ** -0.5, [sqT[:, j, :] for j in range(4)]),
                    (3584, 256, "token", 1.0, [skv[:, j, :] for j in range(NT)])]
            project(k, w, plan)
            with ExitStack() as d:
                for n in ("QT", "QxT", "KT"):
                    T[n] = d.enter_context(nc.sbuf_tensor(fresh(n), [P, RET_HEADS, S], F32))
                retention_inputs(k, T)
                retention(k, T, y)
            head_norm_T(k, y, RET_HEADS, RET_V, T["rg"], None, k.hT)
        with ExitStack() as c:
            sc = lambda n, s: c.enter_context(nc.sbuf_tensor(fresh(n), s, F32))
            k2, kT, so, sw, sink = sc("k2", [P, NT, 4, HD]), sc("skT", [P, 2, S]), sc("so", [P, NT, 512]), sc("sw", [P, 8, 256]), sc("sink", [P, 8])
            window_bias(k, bias, sw, sink)
            twice(k, skv, k2)
            transposed(k, lambda t, q: k2[:, t, 2 * q:2 * q + 2, :].rearrange("p h d -> p (h d)"), 2, kT)
            units = []
            for h in range(8):
                p0, g = 64 * (h % 2), h // 4
                for t in range(NT):
                    a = max(0, t - 1)
                    units.append(dict(q=sqT[p0:p0 + 64, h // 2, t * P:(t + 1) * P], k=kT[p0:p0 + 64, g, a * P:(t + 1) * P],
                                      bias=sw[:, h, 0 if t else P:256], sink=sink[:, h:h + 1],
                                      v=[skv[:, j, P + HD * g:P + HD * (g + 1)] for j in range(a, t + 1)],
                                      out=so[:, t, h * HD:(h + 1) * HD]))
            attention(k, units)
            transposed(k, lambda t, q: so[:, t, q * P:(q + 1) * P], 4, soT)
        tiles = [k.hT[:, q, :] for q in range(KD)] + [soT[:, q, :] for q in range(4)]
        out_projection(k, A["o_w_out_2"][0].rearrange("(k p) n -> p k n", p=P), tiles, y)


def twice(k, skv, k2):
    nc = k.nc
    with stage(nc, "done spare") as (block, done, _s):
        @block.vector
        def _(dve):
            for t in range(NT):
                for g in range(2):
                    nc.vector.tensor_copy(k2[:, t, 2 * g:2 * g + 2, :], bcast(skv[:, t, g * HD:(g + 1) * HD], 1, 2)).then_inc(done, 1)
            dve.wait_ge(done, 2 * NT)


def second_block(k, out):
    nc, A = k.nc, k.A
    mid = k.scratch[2 * S * D:3 * S * D]
    with ExitStack() as c:
        sb = lambda n, s: c.enter_context(nc.sbuf_tensor(fresh(n), s, F32))
        bias, grow, y = sb("bias", [P, 8, 512]), sb("grow", [P, D]), sb("y", [P, NT, D])
        with stage(nc, "x_landed spare") as (block, x_landed, _s):
            @block.sync
            def _(sp):
                sp.dma_start(k.x[:], mid.rearrange("(t p d) -> p t d", p=P, d=D)).then_inc(x_landed, 16)
                sp.wait_ge(x_landed, 16)
        relative_bias(k, bias)
        kp = lambda ap: ap.rearrange("(k p) n -> p k n", p=P)
        for layer in range(DEPTH):
            for half in range(2):
                modulation(k, 1, kp(A["mod_w_2"][layer, half]), A["mod_b_2"][layer, half], 6, k.mod, ())
                sandwich_columns(k, A["norm_gains_2"][layer], 2 * half)
                rows_of(k, [k.mod[:, 16:24]], [grow])
                norm_to_hT(k, True, RMS_EPS, k.mod[:, 8:16], k.mod[:, 0:8])
                if half:
                    mlp(k, kp(A["mlp_w1_2"][layer]), kp(A["mlp_w2_2"][layer]), y)
                elif layer % 2 == 0:
                    even_mixer(k, bias, y)
                else:
                    odd_mixer(k, bias, y)
                last = layer == DEPTH - 1 and half == 1
                add_normed(k, y, grow, out[0].rearrange("(t p) d -> p t d", p=P) if last else None)


_INS = ["x", "c", "w_ada", "b_ada", "w_in", "q_norm_g", "k_norm_g", "w_branch_a", "w_branch_b", "w_out", "ln1_g", "ln1_b",
        "w_router", "router_bias", "w_exp_gate", "w_exp_up", "w_exp_down", "ln2_g", "ln2_b", "c_2", "rel_bias_2",
        "norm_gains_2", "mod_w_2", "mod_b_2", "mlp_w1_2", "mlp_w2_2", "e_w_in_2", "e_conv_w_2", "e_conv_b_2",
        "e_dt_bias_2", "e_A_log_2", "e_D_2", "e_ssd_norm_2", "e_lambda_2", "e_diff_norm_2", "e_w_out_2", "o_w_in_2",
        "o_sinks_2", "o_w_out_2"]


def build(nc, A, K, out):
    with ExitStack() as c:
        k = Core(nc, c, A, K)
        first_block(k)
        second_block(k, out)


def kernel(**inputs):
    import numpy as _np
    import concourse.bacc as _bacc
    from concourse import mybir as _mybir
    from concourse.bass_utils import run_bass_kernel_spmd as _run

    nc = _bacc.Bacc("TRN2", target_bir_lowering=False, num_devices=1)
    arrays, args, consts = {}, {}, {}
    for name in _INS:
        a = _np.ascontiguousarray(inputs[name])
        arrays[f"in_{name}_dram"] = a
        args[name] = nc.dram_tensor(f"in_{name}_dram", a.shape, _mybir.dt.from_np(a.dtype), kind="ExternalInput").ap()
    for name, a in constants().items():
        arrays[f"const_{name}_dram"] = a
        consts[name] = nc.dram_tensor(f"const_{name}_dram", a.shape, _mybir.dt.from_np(a.dtype), kind="ExternalInput").ap()
    out = nc.dram_tensor("out_0_dram", (1, S, D), _mybir.dt.float32, kind="ExternalOutput").ap()
    build(nc, args, consts, out)
    r = _run(nc, [arrays], core_ids=[0])
    return r.results[0]["out_0_dram"]
```

```python
import itertools
import math
from contextlib import ExitStack, contextmanager

import numpy as np
import concourse.bass as bass
from concourse import mybir

F32 = mybir.dt.float32
F32R = mybir.dt.float32r
ALU = mybir.AluOpType
ACT = mybir.ActivationFunctionType
AX = mybir.AxisListType.X

P = 128
S = 512
NT = S // P
D = 1024
KD = D // P
DEPTH = 2
HD = 64
A_HEADS, A_KV = 8, 2
B_HEADS = 12
BG = 4
REACH = 64
CLS = 4
N_EXP, EPG, D_EXP = 16, 4, 256
ALPHA = (2.0 * DEPTH) ** 0.25
NEG = -1.0e30
LN_EPS, RMS_EPS = 1e-5, 1e-6
HALF = 2048
C_GATE, C_QKD, C_VD = 3072, 768, 2304
SSD_HEADS, SSD_GROUPS, SSD_STATE = 16, 4, 128
RET_HEADS, RET_V = 4, 256
BIAS_W = 640


_serial = itertools.count()


def fresh(name):
    return f"{name}_{next(_serial)}"


class Link:

    def __init__(self, eng, sem):
        self.eng, self.sem, self.n, self.base = eng, sem, 0, 0

    def __call__(self, ins):
        self.n += 1
        ins.then_inc(self.sem, 1)
        self.eng.wait_ge(self.sem, self.base + self.n)


@contextmanager
def stage(nc, names):
    nc.reset_free_semaphores(sorted(nc.free_semaphores))
    with ExitStack() as c:
        sems = [c.enter_context(nc.semaphore(fresh(n))) for n in names.split()]
        with nc.Block() as block:
            yield (block, *sems)
        nums = sorted(s.num for s in sems)
        assert nums == list(range(nums[0], nums[-1] + 1))
        nc.multi_engine_barrier(nc.engines, sems_to_clear=range(nums[0], nums[-1] + 1))


def bcast(ap, axis, n):
    u = ap.unsqueeze(axis)
    return u.to_broadcast([n if i == axis else d for i, d in enumerate(u.shape)])


def chain(pe, out, lhs, rhs, ks, first=True, last=True):
    for i, k in enumerate(ks):
        mm = pe.matmul(out, lhs(k), rhs(k), start=first and i == 0, stop=last and i == len(ks) - 1)
    return mm


def chain3(pe, out, lhs, rhs, ks, first=True, last=True):
    n = 0
    for k in ks:
        for a, b in ((0, 0), (0, 1), (1, 0)):
            n += 1
            mm = pe.matmul(out, lhs(a, k), rhs(b, k), start=first and n == 1, stop=last and n == 3 * len(ks))
    return mm


class Weights:

    NAMES = "half0_landed half1_landed high_done low_done half_read"

    def __init__(self, k, sems):
        self.k = k
        self.landed, (self.high, self.low, self.read) = sems[0:2], sems[2:5]

    def load(self, sp, u, i, pairs):
        sp.wait_ge(self.low, 2 * u + i + 1)
        for dst, src in pairs:
            sp.dma_start(dst, src).then_inc(self.landed[i], 16)

    def split_high(self, act, u, i, dmas):
        act.wait_ge(self.landed[i], dmas)
        act.wait_ge(self.read, 2 * u + i + 1)
        self.k.nc.scalar.copy(self.k.parts[0][:, i, :], self.k.ring[:, i, :]).then_inc(self.high, 1)

    def start_low(self, pool):
        pool.nop().then_inc(self.low, 2)

    def split_low(self, pool, u, i):
        pool.wait_ge(self.high, 2 * u + i + 1)
        self.k.nc.gpsimd.tensor_tensor(self.k.parts[1][:, i, :], self.k.ring[:, i, :], self.k.parts[0][:, i, :].bitcast(F32),
                                       ALU.subtract).then_inc(self.low, 1)

    def start_read(self, pe):
        pe.nop().then_inc(self.read, 2)

    def high_ready(self, pe, u, i):
        pe.wait_ge(self.high, 2 * u + i + 1)

    def low_ready(self, pe, u, i):
        pe.wait_ge(self.low, 2 * u + i + 3)

    def done(self, eng, u, i):
        eng.wait_ge(self.read, 2 * u + i + 3)

    def raw(self, i, kt, n):
        return self.k.ring[:, i, 0:kt * n].rearrange("p (k n) -> p k n", k=kt)

    def part(self, a, i, kt, n):
        return self.k.parts[a][:, i, 0:kt * n].rearrange("p (k n) -> p k n", k=kt)


def pair_of(nc, c, name, shape, side=None):
    return tuple(c.enter_context(nc.sbuf_tensor(fresh(name + e), shape, F32R, side=side)) for e in ("_hi", "_lo"))


def constants():
    f = np.float32
    out = {"ident": np.eye(P, dtype=f)}
    tok = np.arange(P)[:, None] * CLS + np.arange(CLS)[None, :]
    inv = (f(10000.0) ** (-np.arange(0, 32, 2, dtype=f) / f(32))).astype(f)
    row, col = (tok // 64).astype(f), (tok % 64).astype(f)
    ang = np.concatenate([row[..., None] * inv, col[..., None] * inv], -1).astype(f)
    out["rope1"] = np.stack([np.cos(ang), np.sin(ang)], 1).astype(f)
    slope = np.exp2(-8.0 * np.arange(1, B_HEADS + 1) / B_HEADS).astype(f)
    p, c = np.arange(P)[:, None], np.arange(256)[None, :]
    dist = np.abs(p - (c - REACH))
    band = np.zeros((P, 3, BG, 256), f)
    for e in range(3):
        ok = (dist <= REACH) & ~((e == 0) & (c < REACH)) & ~((e == 2) & (c >= P + REACH))
        for h in range(BG):
            band[:, e, h] = np.where(ok, -slope[h] * dist.astype(f), f(NEG))
    out["bias_band"] = band
    j = np.arange(P)[None, :]
    d = np.abs(p - j)
    cls = np.zeros((P, 2, BG, P), f)
    for g, ok in enumerate((d <= REACH, d % CLS == 0)):
        for h in range(BG):
            cls[:, g, h] = np.where(ok, -slope[BG * (g + 1) + h] * (CLS * d).astype(f), f(NEG))
    out["bias_class"] = cls
    out["before"] = np.broadcast_to((j[:, :4] < np.arange(4)[:, None]).astype(f), (P, 4, 4)).copy()
    out["causal"] = np.stack([(p <= j).astype(f), np.where(p <= j, f(0), f(NEG))], 1).astype(f)
    dd = 511 - np.arange(BIAS_W)
    n = np.maximum(dd, 0)
    logd = np.log(np.maximum(n, 1).astype(f) / f(16)).astype(f)
    large = 16 + (logd / f(math.log(8.0)) * f(16)).astype(f).astype(np.int32)
    bucket = np.where(n < 16, n, np.minimum(large, 31))
    hot = np.zeros((33, BIAS_W), f)
    hot[np.where(dd >= 0, bucket, 32), np.arange(BIAS_W)] = 1
    out["bucket_hot"] = hot
    pos = np.arange(S, dtype=f)
    inv = (f(10000.0) ** (-np.arange(64, dtype=f) / f(64))).astype(f)
    ang = (pos[:, None] * inv[None]).astype(f).reshape(NT, P, 64).transpose(1, 0, 2)
    out["rope2"] = np.stack([np.cos(ang), np.sin(ang)], 1).astype(f)
    lg = np.log(1.0 - 2.0 ** (-5.0 - np.arange(RET_HEADS, dtype=f))).astype(f)
    kscale = 128.0 ** -0.5
    dec = np.zeros((P, RET_HEADS, P), f)
    for h in range(RET_HEADS):
        dec[:, h] = np.where(j >= p, np.exp(np.maximum(j - p, 0) * lg[h]) * kscale, 0)
    out["ret_decay"] = dec
    xi = np.exp((np.arange(P) + 1.0)[None] * lg[:, None]).astype(f)
    out["ret_xi"] = np.broadcast_to(xi, (P, RET_HEADS, P)).copy()
    out["ret_zeta"] = (np.exp((P - 1 - np.arange(P))[:, None] * lg[None]) * kscale).astype(f)
    out["win_mask"] = np.where(j <= p, f(NEG), f(0)).astype(f)
    return out


RET_STATE_DECAY = [float(math.exp(P * math.log(1.0 - 2.0 ** (-5.0 - h)))) for h in range(RET_HEADS)]


class Core:

    def __init__(self, nc, c, A, K):
        self.nc, self.A, self.K = nc, A, K
        sb = lambda n, s: c.enter_context(nc.sbuf_tensor(fresh(n), s, F32))
        self.x = sb("x_res", [P, NT, D])
        self.ring = sb("ring", [P, 2, HALF])
        self.parts = tuple(c.enter_context(nc.sbuf_tensor(n, [P, 2, HALF], F32R)) for n in ("w_hi", "w_lo"))
        self.ident = sb("ident_sb", [P, P])
        self.mod = sb("mod", [P, 48])
        self.cond = sb("cond", [P, 2, KD])
        self.ps = c.enter_context(nc.psum_tensor("ps", [P, 8, 512], F32))
        self.sums = nc.dram_tensor("mod_sums", [5, P, 32 * P], F32, kind="Internal").ap()
        self.scratch = nc.dram_tensor("scratch", [4 * S * D], F32, kind="Internal").ap()


def split_products(pe, W, u, i, outs, weight, other, ks, weight_left, first=True, last=True):
    for part, others in ((0, (0, 1)), (1, (0,))):
        (W.low_ready if part else W.high_ready)(pe, u, i)
        for m, out in enumerate(outs):
            for q in ks:
                for o in others:
                    a, b = weight(part, m, q), other(o, m, q)
                    mm = pe.matmul(out, a if weight_left else b, b if weight_left else a,
                                   start=first and part == 0 and q == ks[0] and o == 0, stop=last and part == 1 and q == ks[-1])
    return mm


def feature_unit(k, pe, W, hT, u, b):
    for i in range(2):
        wv = [W.part(a, i, KD, 256) for a in range(2)]
        split_products(pe, W, u, i, [k.ps[:, 4 * b + 2 * i + m, :] for m in range(2)], lambda a, m, q: wv[a][:, q, m * P:(m + 1) * P],
                       lambda a, m, q: hT[a][:, q, :], range(KD), True).then_inc(W.read, 1)


def token_unit(k, pe, W, hT, u, b, n, kt=KD, before=None):
    for i in range(2):
        if before is not None:
            before(i)
        wv = [W.part(a, i, kt // 2, n) for a in range(2)]
        split_products(pe, W, u, i, [k.ps[:, 4 * b + t, 0:n] for t in range(NT)], lambda a, t, q: wv[a][:, q - kt // 2 * i, :],
                       lambda a, t, q: hT[a][:, q, t * P:(t + 1) * P], range(kt // 2 * i, kt // 2 * (i + 1)), False,
                       first=i == 0, last=i == 1).then_inc(W.read, 1)



def start_up(k, x_source):
    nc, A = k.nc, k.A
    with stage(nc, "in_landed x_landed cond_done zeroed") as (block, in_landed, x_landed, cond_done, zeroed), \
            nc.sbuf_tensor(fresh("craw"), [P, 2, KD], F32) as craw:
        @block.sync
        def _(sp):
            for i, name in enumerate(("c", "c_2")):
                sp.dma_start(craw[:, i, :], A[name].rearrange("a (k p) -> (a p) k", p=P), allow_slow_non_contiguous=True).then_inc(in_landed, 16)
            sp.dma_start(k.ident[:], k.K["ident"]).then_inc(in_landed, 16)
            sp.dma_start(k.x[:], x_source).then_inc(x_landed, 16)
            sp.wait_ge(in_landed, 48)
            sp.wait_ge(x_landed, 16)

        @block.scalar
        def _(act):
            act.wait_ge(in_landed, 48)
            nc.scalar.activation(k.cond[:], craw[:], ACT.Silu).then_inc(cond_done, 1)
            act.wait_ge(cond_done, 1)

        @block.vector
        def _(dve):
            nc.vector.memset(k.ring[:], 0.0).then_inc(zeroed, 1)
            dve.wait_ge(zeroed, 1)


def modulation(k, which, w, b, nslots, out, plus_one):
    nc = k.nc
    ncol = 4 * nslots
    with ExitStack() as c:
        brow = c.enter_context(nc.sbuf_tensor(fresh("brow"), [ncol, P], F32))
        bcol = c.enter_context(nc.sbuf_tensor(fresh("bcol"), [P, ncol], F32))
        slots = c.enter_context(nc.sbuf_tensor(fresh("mod_slots"), [P, 2, KD, 512], F32))
        part = c.enter_context(nc.sbuf_tensor(fresh("mod_part"), [P, 2, 3, 512], F32))
        ones = c.enter_context(nc.sbuf_tensor(fresh("mod_ones"), [P, 1], F32))
        block, w0, w1, b_landed, read_dve, read_act, cols_done, cols_free, b_done, sum_done, act_done, step = c.enter_context(
            stage(nc, "mod_w0 mod_w1 b_landed read_dve read_act cols_done cols_free b_done sum_done act_done step"))
        landed = (w0, w1)

        @block.sync
        def _(sp):
            sp.dma_start(brow[:], b.rearrange("(j p) -> j p", p=P)).then_inc(b_landed, 16)
            with sp.Fori(0, nslots // 2) as t:
                for i in range(2):
                    sp.wait_ge(read_dve, 2 * t + i + 1)
                    sp.wait_ge(read_act, 2 * t + i + 1)
                    sp.dma_start(slots[:, i], w[:, :, bass.ds((2 * t + i) * 512, 512)]).then_inc(landed[i], 16)

        @block.tensor
        def _(pe):
            pe.wait_ge(b_landed, 16)
            pe.transpose(k.ps[:, 7, 0:ncol], brow[:], k.ident[0:ncol, 0:ncol]).then_inc(b_done, 1)
            with pe.Fori(0, nslots // 2) as t:
                for i in range(2):
                    pe.wait_ge(sum_done, 2 * t + i + 1)
                    pe.wait_ge(cols_free, 2 * t + i + 1)
                    for j in range(4):
                        mm = pe.matmul(k.ps[:, i, j:j + 1], part[:, i, 0, j * P:(j + 1) * P], ones[:], start=True, stop=True)
                    mm.then_inc(cols_done, 1)

        @block.scalar
        def _(act):
            act.nop().then_inc(read_act, 2)
            with act.Fori(0, nslots // 2) as t:
                for i in range(2):
                    act.wait_ge(landed[i], 16 * t + 16)
                    act.wait_ge(read_dve, 2 * t + i + 1)
                    for j in range(2):
                        last = nc.scalar.activation(part[:, i, 1 + j, :], slots[:, i, 6 + j, :], ACT.Copy,
                                                    scale=k.cond[:, which, 6 + j:7 + j])
                    last.then_inc(read_act, 1)

        @block.vector
        def _(dve):
            link = Link(dve, step)
            V = nc.vector
            dve.nop().then_inc(cols_free, 2)
            dve.nop().then_inc(cols_done, 2)
            dve.nop().then_inc(read_dve, 2)
            link(V.memset(ones[:], 1.0))
            dve.wait_ge(b_done, 1)
            link(V.tensor_copy(bcol[:], k.ps[:, 7, 0:ncol]))
            for a, n in plus_one:
                link(V.tensor_scalar(bcol[:, a:a + n], bcol[:, a:a + n], 1.0, None, ALU.add))
            n0 = link.n
            with dve.Fori(0, nslots // 2) as t:
                link.n, link.base = n0, 14 * t
                for i in range(2):
                    dve.wait_ge(landed[i], 16 * t + 16)
                    dve.wait_ge(cols_done, 2 * t + i + 1)
                    acc = part[:, i, 0, :]
                    link(V.tensor_scalar(acc, slots[:, i, 0, :], k.cond[:, which, 0:1], None, ALU.mult))
                    for q in range(1, 6):
                        link(V.scalar_tensor_tensor(acc, slots[:, i, q, :], k.cond[:, which, q:q + 1], acc, ALU.mult, ALU.add))
                    dve.wait_ge(read_act, 2 * t + i + 3)
                    link(V.tensor_tensor(acc, acc, part[:, i, 1, :], ALU.add))
                    V.tensor_tensor(acc, acc, part[:, i, 2, :], ALU.add).then_inc(sum_done, 1)
                    dve.wait_ge(sum_done, 2 * t + i + 1)
                    dve.nop().then_inc(read_dve, 1)
                    dve.wait_ge(cols_done, 2 * t + i + 3)
                    at = bass.ds((2 * t + i) * 4, 4)
                    V.tensor_tensor(out[:, at], k.ps[:, i, 0:4], bcol[:, at], ALU.add).then_inc(cols_free, 1)
            dve.wait_ge(cols_free, nslots + 2)


class SideModulation:

    NAMES = "side0_landed side1_landed side0_stored side1_stored side_sum side_step"

    def __init__(self, k, c, sems, which, w, dst):
        self.k, self.which, self.w, self.dst = k, which, w, dst
        self.landed, self.stored, (self.sum, self.step) = sems[0:2], sems[2:4], sems[4:6]
        self.slots = c.enter_context(k.nc.sbuf_tensor(fresh("side_slots"), [P, 2, KD, P], F32))
        self.acc = c.enter_context(k.nc.sbuf_tensor(fresh("side_acc"), [P, 2, P], F32))

    def start(self, dve):
        dve.nop().then_inc(self.sum, 2)
        for i in range(2):
            dve.nop().then_inc(self.stored[i], 16)

    def load(self, sp, s, i):
        sp.wait_ge(self.sum, s + 1)
        sp.dma_start(self.slots[:, i], self.w(s, i)).then_inc(self.landed[i], 16)

    def work(self, dve, s, i, round_):
        V, slot = self.k.nc.vector, self.slots[:, i]
        dve.wait_ge(self.landed[i], 16 * round_ + 16)
        V.tensor_tensor(slot, slot, bcast(self.k.cond[:, self.which, :], 2, P), ALU.mult).then_inc(self.step, 1)
        dve.wait_ge(self.step, s + 1)
        dve.wait_ge(self.stored[i], 16 * round_ + 16)
        V.tensor_reduce(self.acc[:, i, :], slot.rearrange("p k n -> p n k"), AX, ALU.add).then_inc(self.sum, 1)

    def store(self, eng, s, i):
        eng.wait_ge(self.sum, s + 3)
        eng.dma_start(self.dst(s, i), self.acc[:, i, :]).then_inc(self.stored[i], 16)

    def end(self, eng, n):
        for i in range(2):
            eng.wait_ge(self.stored[i], 16 * (n // 2) + 16)


class ModulationTail:

    NAMES = "b_landed sums_landed ones_done b_done sum_done mod_done row_done row_out"

    def __init__(self, k, c, sems, sums, b, n, out, plus_one, gains, rows):
        sb = lambda n_, s: c.enter_context(k.nc.sbuf_tensor(fresh(n_), s, F32))
        self.k, self.sums, self.b, self.n, self.out, self.plus_one, self.gains, self.rows = k, sums, b, n, out, plus_one, gains, rows
        self.b_landed, self.landed, self.ones_done, self.b_done, self.sum_done, self.mod_done, self.row_done, self.row_out = sems
        self.acc, self.raw, self.ones, self.bcol = sb("sums", [P, n, P]), sb("braw", [n + 16, P]), sb("ones_m", [P, 1]), sb("bcol", [P, n + 16])
        self.nr = n + (16 if gains is not None else 0)

    def load(self, sp):
        n = self.n
        sp.dma_start(self.raw[0:n, :], self.b.rearrange("(j p) -> j p", p=P)).then_inc(self.b_landed, 16)
        if self.gains is not None:
            sp.dma_start(self.raw[n:n + 16, :], self.gains.rearrange("g (k p) -> (g k) p", p=P)).then_inc(self.b_landed, 16)
        sp.dma_start(self.acc[:], self.sums).then_inc(self.landed, 16)
        sp.wait_ge(self.landed, 16)

    def add_up(self, pe):
        k, nr = self.k, self.nr
        pe.wait_ge(self.b_landed, 16 if self.gains is None else 32)
        pe.transpose(k.ps[:, 7, 0:nr], self.raw[0:nr, :], k.ident[0:nr, 0:nr]).then_inc(self.b_done, 1)
        pe.wait_ge(self.landed, 16)
        pe.wait_ge(self.ones_done, 1)
        for j in range(self.n):
            mm = pe.matmul(k.ps[:, 6, j:j + 1], self.acc[:, j, :], self.ones[:], start=True, stop=True)
        mm.then_inc(self.sum_done, 1)

    def spread(self, pe):
        k = self.k
        pe.wait_ge(self.mod_done, 1)
        for r, (a, _row) in enumerate(self.rows):
            if r:
                pe.wait_ge(self.row_out, r)
            for j in range(KD):
                mm = pe.matmul(k.ps[:, 6 + j // 4, (j % 4) * P:(j % 4 + 1) * P],
                               self.out[:, a + j:a + j + 1].to_broadcast([P, P]), k.ident[:], start=True, stop=True)
            mm.then_inc(self.row_done, 1)

    def start(self, dve):
        self.k.nc.vector.memset(self.ones[:], 1.0).then_inc(self.ones_done, 1)

    def finish(self, dve, link):
        V, k, n, nr, bcol, out = self.k.nc.vector, self.k, self.n, self.nr, self.bcol, self.out
        dve.wait_ge(self.b_done, 1)
        link(V.tensor_copy(bcol[:, 0:nr], k.ps[:, 7, 0:nr]))
        for a in self.plus_one:
            link(V.tensor_scalar(bcol[:, a:a + KD], bcol[:, a:a + KD], 1.0, None, ALU.add))
        dve.wait_ge(self.sum_done, 1)
        link(V.tensor_tensor(out[:, 0:n], k.ps[:, 6, 0:n], bcol[:, 0:n], ALU.add))
        if self.gains is not None:
            link(V.tensor_tensor(out[:, 8:24], out[:, 8:24], bcol[:, n:n + 16], ALU.mult))
        dve.nop().then_inc(self.mod_done, 1)

    def copy_row(self, dve, r):
        k = self.k
        dve.wait_ge(self.row_done, r + 1)
        k.nc.vector.tensor_copy(self.rows[r][1][:].rearrange("p (b n) -> p b n", b=2), k.ps[:, 6:8, :]).then_inc(self.row_out, 1)


def norm_to_hT(k, out, rms, eps, scale, shift, affine=None, store=None, src=None, mod=None):
    nc = k.nc
    src = k.x if src is None else src
    rounds = 1 if affine is None or store is not None else 2
    with ExitStack() as c:
        sb = lambda n, s: c.enter_context(nc.sbuf_tensor(fresh(n), s, F32))
        xn = k.ring[:].rearrange("p b n -> p (b n)").rearrange("p (t d) -> p t d", t=NT)
        ex, st, mv = sb("exact", [P, 4, S]), sb("stats", [P, NT, 2, 6]), sb("mv", [P, NT, 2])
        tmp, rstd, nb = (sb(n, [P, rounds, NT]) for n in ("var", "rstd", "neg_mean"))
        gb = sb("gb", [P, 2, D]) if affine is not None else None
        names = "gb_landed var_done root_done factors normed t_done high_out exact out_pool stored x_done step"
        block, gb_landed, var_done, root_done, factors, normed, t_done, high_out, exact, out_pool, stored, x_done, step, *sems = c.enter_context(
            stage(nc, names if mod is None else f"{names} {ModulationTail.NAMES}"))
        tail = ModulationTail(k, c, sems, *mod) if mod is not None else None

        @block.sync
        def _(sp):
            if tail is not None:
                tail.load(sp)
            if affine is not None:
                for i in range(2):
                    sp.dma_start(gb[:, i, :], bcast(affine[i], 0, P)).then_inc(gb_landed, 16)
                sp.wait_ge(gb_landed, 32)
            if store is not None:
                for t in range(NT):
                    sp.wait_ge(x_done, t + 1)
                    sp.dma_start(store[t], src[:, t, :]).then_inc(stored, 16)
                sp.wait_ge(stored, 16 * NT)

        @block.vector
        def _(dve):
            link = Link(dve, step)
            V = nc.vector

            def statistics(r, t):
                V.bn_stats(st[:, t, 0, :], src[:, t, 0:512])
                link(V.bn_stats(st[:, t, 1, :], src[:, t, 512:D]))
                link(V.bn_aggr(mv[:, t, :], st[:, t, :, :].rearrange("p a b -> p (a b)")))
                v = tmp[:, r, t:t + 1]
                var = mv[:, t, 1:2]
                if rms:
                    link(V.tensor_tensor(v, mv[:, t, 0:1], mv[:, t, 0:1], ALU.mult))
                    link(V.tensor_tensor(v, v, var, ALU.add))
                    var = v
                V.tensor_scalar(v, var, eps, None, ALU.add).then_inc(var_done, 1)

            def invert(r, t):
                dve.wait_ge(root_done, r * NT + t + 1)
                f = rstd[:, r, t:t + 1]
                if rms:
                    V.reciprocal(f, f).then_inc(factors, 1)
                else:
                    link(V.reciprocal(f, f))
                    V.scalar_tensor_tensor(nb[:, r, t:t + 1], mv[:, t, 0:1], -1.0, f, ALU.mult, ALU.mult).then_inc(factors, 1)

            def affine_rows(t):
                dve.wait_ge(normed, t + 1)
                x = src[:, t, :]
                link(V.tensor_tensor(x, x, gb[:, 0, :], ALU.mult))
                ins = V.tensor_tensor(x, x, gb[:, 1, :], ALU.add)
                if store is not None:
                    ins.then_inc(x_done, 1)
                else:
                    link(ins)

            if tail is not None:
                tail.start(dve)
            for r in range(rounds):
                for t in range(NT):
                    if r == 1:
                        affine_rows(t)
                    statistics(r, t)
                    if t >= 1:
                        invert(r, t - 1)
                invert(r, NT - 1)
                if r == 0 and affine is not None:
                    dve.wait_ge(gb_landed, 32)
            if store is not None:
                for t in range(NT):
                    affine_rows(t)
                return
            if tail is not None:
                tail.finish(dve, link)
                tail.copy_row(dve, 0)
                dve.wait_ge(tail.row_out, 1)
            for q in range(KD):
                dve.wait_ge(high_out, q + 1)
                if q >= 4 and q % 2 == 0:
                    dve.wait_ge(out_pool, q // 2 - 1)
                ins = V.tensor_scalar(ex[:, q % 4, :], k.ps[:, q, :], scale[:, q:q + 1],
                                      shift[:, q:q + 1] if shift is not None else None,
                                      ALU.mult, ALU.add if shift is not None else ALU.bypass)
                if q % 2 == 0:
                    ins.then_inc(exact, 1)
                else:
                    link(ins)
                    link(V.tensor_tensor(out[1][:, q, :], ex[:, q % 4, :], out[0][:, q, :].bitcast(F32), ALU.subtract))

        @block.scalar
        def _(act):
            def normalise(r, t):
                act.wait_ge(factors, r * NT + t + 1)
                dst = xn[:, t, :] if r == rounds - 1 and store is None else src[:, t, :]
                if rms:
                    ins = nc.scalar.activation(dst, src[:, t, :], ACT.Copy, scale=rstd[:, r, t:t + 1])
                else:
                    ins = nc.scalar.activation(dst, src[:, t, :], ACT.Identity, scale=rstd[:, r, t:t + 1], bias=nb[:, r, t:t + 1])
                ins.then_inc(normed, 1)

            for r in range(rounds):
                for t in range(NT):
                    act.wait_ge(var_done, r * NT + t + 1)
                    nc.scalar.activation(rstd[:, r, t:t + 1], tmp[:, r, t:t + 1], ACT.Sqrt).then_inc(root_done, 1)
                    if t >= 1:
                        normalise(r, t - 1)
                normalise(r, NT - 1)
            if tail is not None:
                act.wait_ge(tail.mod_done, 1)
            if store is None:
                for q in range(KD):
                    act.wait_ge(t_done, q + 1)
                    if shift is not None:
                        ins = nc.scalar.activation(out[0][:, q, :], k.ps[:, q, :], ACT.Identity, scale=scale[:, q:q + 1], bias=shift[:, q:q + 1])
                    else:
                        ins = nc.scalar.activation(out[0][:, q, :], k.ps[:, q, :], ACT.Copy, scale=scale[:, q:q + 1])
                    ins.then_inc(high_out, 1)
                act.wait_ge(high_out, KD)

        @block.gpsimd
        def _(pool):
            if store is None:
                for q in range(0, KD, 2):
                    pool.wait_ge(exact, q // 2 + 1)
                    nc.gpsimd.tensor_tensor(out[1][:, q, :], ex[:, q % 4, :], out[0][:, q, :].bitcast(F32), ALU.subtract).then_inc(out_pool, 1)
                pool.wait_ge(out_pool, KD // 2)

        @block.tensor
        def _(pe):
            if store is None:
                def transposes(t, qs):
                    pe.wait_ge(normed, (rounds - 1) * NT + t + 1)
                    for q in qs:
                        mm = pe.transpose(k.ps[:, q, t * P:(t + 1) * P], xn[:, t, q * P:(q + 1) * P], k.ident[:])
                        if t == NT - 1:
                            mm.then_inc(t_done, 1)

                if tail is None:
                    for t in range(NT):
                        transposes(t, range(KD))
                else:
                    for t in range(NT):
                        if t == 2:
                            tail.add_up(pe)
                        if t == 3:
                            tail.spread(pe)
                        transposes(t, range(6))
                    pe.wait_ge(tail.row_out, 1)
                    for t in range(NT):
                        transposes(t, (6, 7))



def in_projection(k, w, hT, T, w_side, side_out):
    nc = k.nc
    plan = [(0, 512, "qa"), (512, 256, "kva")] + [(C_QKD + 512 * i, 512, "qkd") for i in range(3)] + [(C_VD + 256, 512, "vc"), (C_VD, 256, "v0")]
    plan += [(C_GATE + 512 * i, 512, "gate") for i in range(4)]
    with ExitStack() as c:
        v0c = T["v0c"]
        block, *sems, free_act, free_dve, step = c.enter_context(
            stage(nc, f"{Weights.NAMES} {SideModulation.NAMES} free_act free_dve step"))
        W = Weights(k, sems[0:5])
        side = SideModulation(k, c, sems[5:], 0, lambda s, i: w_side[:, :, s * P:(s + 1) * P], lambda s, i: side_out[:, s * P:(s + 1) * P])
        ST = 32
        side_tiles = lambda u: range(3 * u, min(3 * u + 3, ST))

        @block.sync
        def _(sp):
            for u, (c0, n, kind) in enumerate(plan):
                for i in range(2):
                    if kind in ("qkd", "gate"):
                        W.load(sp, u, i, [(W.raw(i, KD, 256), w[:, :, c0 + 256 * i:c0 + 256 * (i + 1)])])
                    else:
                        W.load(sp, u, i, [(W.raw(i, KD // 2, n), w[:, 4 * i:4 * i + 4, c0:c0 + n])])
                for s in side_tiles(u):
                    side.load(sp, s, s % 2)

        @block.tensor
        def _(pe):
            W.start_read(pe)
            for u, (c0, n, kind) in enumerate(plan):
                if u >= 2:
                    pe.wait_ge(free_act, u - 1)
                    pe.wait_ge(free_dve, u - 1)
                if kind in ("qkd", "gate"):
                    feature_unit(k, pe, W, hT, u, u % 2)
                else:
                    token_unit(k, pe, W, hT, u, u % 2, n)

        @block.gpsimd
        def _(pool):
            W.start_low(pool)
            for u in range(len(plan)):
                for i in range(2):
                    W.split_low(pool, u, i)

        @block.scalar
        def _(act):
            for u in range(len(plan) + 1):
                if u < len(plan):
                    for i in range(2):
                        W.split_high(act, u, i, 16 * u + 16)
                    for s in side_tiles(u):
                        side.store(act, s, s % 2)
                if u == 0:
                    continue
                v, kind, b = u - 1, plan[u - 1][2], (u - 1) % 2
                W.done(act, v, 0 if kind == "qkd" else 1)
                for j in range(4 if kind == "gate" else 2):
                    p = k.ps[:, 4 * b + j, :]
                    if kind == "gate":
                        last = nc.scalar.activation(T["gates"][:, 4 * (v - 7) + j, :], p, ACT.Sigmoid)
                    elif kind == "qkd":
                        dst, p, mul = qkd_dst(T, 4 * (v - 2) + j, p)
                        last = nc.scalar.activation(dst, p, ACT.Copy, scale=mul)
                    else:
                        dst = v0c if kind == "v0" else T[kind]
                        last = nc.scalar.copy(dst[:, j, :], p[:, 0:plan[v][1]])
                last.then_inc(free_act, 1)
            act.wait_ge(free_act, len(plan))
            side.end(act, ST)

        @block.vector
        def _(dve):
            link = Link(dve, step)
            for j in range(4):
                link(nc.vector.memset(T["k0T"][:, j % 2, (0 if j < 2 else S + REACH):(REACH if j < 2 else S + 2 * REACH)], 0.0))
            link(nc.vector.memset(T["v0"][0:64, 0, :], 0.0))
            link(nc.vector.memset(T["v0"][64:P, 4, :], 0.0))
            side.start(dve)
            for u, (c0, n, kind) in enumerate(plan):
                for s in side_tiles(u):
                    side.work(dve, s, s % 2, s // 2)
                if kind == "gate":
                    if u:
                        dve.wait_ge(free_dve, u)
                    dve.nop().then_inc(free_dve, 1)
                    continue
                W.done(dve, u, 1)
                for j in (2, 3):
                    p = k.ps[:, 4 * (u % 2) + j, :]
                    if kind == "qkd":
                        dst, p, mul = qkd_dst(T, 4 * (u - 2) + j, p)
                        last = nc.vector.tensor_scalar(dst, p, mul, None, ALU.mult)
                    else:
                        dst = v0c if kind == "v0" else T[kind]
                        last = nc.vector.tensor_copy(dst[:, j, :], p[:, 0:n])
                last.then_inc(free_dve, 1)
            dve.wait_ge(free_dve, len(plan))


def order_v0(k, v0c, v0):
    back = k.scratch[0:S * 256]
    rows = back.rearrange("(t n) -> t n", n=256)
    return [[(back.rearrange("(i f) -> i f", i=P), v0c[:].rearrange("p r n -> p (r n)"))],
            [(v0[:, 1:4, :], rows[64:448].rearrange("(c p) n -> p c n", p=P)), (v0[64:P, 0, :], rows[0:64]), (v0[0:64, 4, :], rows[448:512])]]


def qkd_dst(T, m, p):
    if m < 2:
        dst, mul = T["q0T"][:, m, :], HD ** -0.5
    elif m < 6:
        dst, mul = T["qcT"][:, m - 2, :], HD ** -0.5
    elif m < 8:
        dst, mul = T["k0T"][:, m - 6, REACH:REACH + S], 1.0
    else:
        dst, mul = T["kcT"][:, m - 8, :], 1.0
    if m % 6 < 2:
        p = p.rearrange("p (r i) -> p i r", r=CLS)
        dst = dst.rearrange("p (i r) -> p i r", r=CLS)
    return dst, p, mul


def rope_qk(k, gq, gk, T, mod):
    nc = k.nc
    NH = A_HEADS + A_KV
    with ExitStack() as c:
        sb = lambda n, s: c.enter_context(nc.sbuf_tensor(fresh(n), s, F32))
        idle = k.ring[:].rearrange("p b n -> p (b n)")
        ro = idle[:, 0:NT * NH * HD].rearrange("p (t h d) -> p t h d", t=NT, h=NH)
        qk = idle[:, NT * NH * HD:(NT + 1) * NH * HD].rearrange("p (h d) -> p h d", h=NH)
        k2 = sb("k_twice", [P, NT, 4, HD])
        t1 = sb("t1", [P, NH, 32])
        cs = sb("cs", [P, 2, NT, 32])
        g = sb("gqk", [P, 2, HD])
        ms = sb("ms", [P, NT, NH])
        block, in_landed, sq_done, ms_done, root_done, ro_done, t_done, out_a, step, *sems = c.enter_context(
            stage(nc, f"in_landed sq_done ms_done root_done ro_done t_done out_a step {ModulationTail.NAMES}"))
        tail = ModulationTail(k, c, sems, *mod)

        @block.sync
        def _(sp):
            sp.dma_start(cs[:], k.K["rope1"]).then_inc(in_landed, 16)
            sp.dma_start(g[:, 0, :], bcast(gq, 0, P)).then_inc(in_landed, 16)
            sp.dma_start(g[:, 1, :], bcast(gk, 0, P)).then_inc(in_landed, 16)
            tail.load(sp)
            sp.wait_ge(in_landed, 48)

        @block.scalar
        def _(act):
            for t in range(NT):
                nc.scalar.activation(ro[:, t, 0:8, :].rearrange("p h d -> p (h d)"), T["qa"][:, t, :], ACT.Square)
                last = nc.scalar.activation(ro[:, t, 8:10, :].rearrange("p h d -> p (h d)"), T["kva"][:, t, 0:P], ACT.Square)
            last.then_inc(sq_done, 1)
            act.wait_ge(ms_done, 1)
            nc.scalar.activation(ms[:], ms[:], ACT.Sqrt).then_inc(root_done, 1)
            for q in range(3, 6):
                act.wait_ge(t_done, q + 1)
                dst = T["qaT"][:, 3, :] if q == 3 else T["kaT"][:, q - 4, :]
                last = nc.scalar.copy(dst, k.ps[:, q, :])
            last.then_inc(out_a, 1)
            act.wait_ge(out_a, 1)

        @block.vector
        def _(dve):
            link = Link(dve, step)
            tail.start(dve)
            dve.wait_ge(sq_done, 1)
            link(nc.vector.tensor_reduce(ms[:].rearrange("p t h -> p (t h)"), ro.rearrange("p t h d -> p (t h) d"), AX, ALU.add))
            nc.vector.tensor_scalar(ms[:], ms[:], 1.0 / HD, RMS_EPS, ALU.mult, ALU.add).then_inc(ms_done, 1)
            dve.wait_ge(root_done, 1)
            link(nc.vector.reciprocal(ms[:], ms[:]))
            dve.wait_ge(in_landed, 48)
            link(nc.vector.tensor_scalar(g[:, 0, :], g[:, 0, :], HD ** -0.5, None, ALU.mult))
            for t in range(NT):
                qv = T["qa"][:, t, :].rearrange("p (h d) -> p h d", d=HD)
                kv = T["kva"][:, t, 0:P].rearrange("p (h d) -> p h d", d=HD)
                link(nc.vector.tensor_tensor(qk[:, 0:8, :], qv, bcast(ms[:, t, 0:8], 2, HD), ALU.mult))
                link(nc.vector.tensor_tensor(qk[:, 8:10, :], kv, bcast(ms[:, t, 8:10], 2, HD), ALU.mult))
                link(nc.vector.tensor_tensor(qk[:, 0:8, :], qk[:, 0:8, :], bcast(g[:, 0, :], 1, 8), ALU.mult))
                link(nc.vector.tensor_tensor(qk[:, 8:10, :], qk[:, 8:10, :], bcast(g[:, 1, :], 1, 2), ALU.mult))
                pr = qk.rearrange("p h (j e) -> p h j e", e=2)
                po = ro[:, t].rearrange("p h (j e) -> p h j e", e=2)
                cos, sin = (bcast(cs[:, i, t, :], 1, NH) for i in (0, 1))
                link(nc.vector.tensor_tensor(po[:, :, :, 0], pr[:, :, :, 0], cos, ALU.mult))
                link(nc.vector.tensor_tensor(t1[:], pr[:, :, :, 1], sin, ALU.mult))
                link(nc.vector.tensor_tensor(po[:, :, :, 0], po[:, :, :, 0], t1[:], ALU.subtract))
                link(nc.vector.tensor_tensor(po[:, :, :, 1], pr[:, :, :, 0], sin, ALU.mult))
                link(nc.vector.tensor_tensor(t1[:], pr[:, :, :, 1], cos, ALU.mult))
                link(nc.vector.tensor_tensor(po[:, :, :, 1], po[:, :, :, 1], t1[:], ALU.add))
                link(nc.vector.tensor_copy(k2[:, t, 0:2, :], bcast(ro[:, t, 8, :], 1, 2)))
                nc.vector.tensor_copy(k2[:, t, 2:4, :], bcast(ro[:, t, 9, :], 1, 2)).then_inc(ro_done, 1)
                if t == 0:
                    tail.finish(dve, link)
                elif t < 3:
                    tail.copy_row(dve, t - 1)
            for q in range(3):
                dve.wait_ge(t_done, q + 1)
                link(nc.vector.tensor_copy(T["qaT"][:, q, :], k.ps[:, q, :]))
            dve.wait_ge(tail.row_out, 2)

        @block.tensor
        def _(pe):
            tail.add_up(pe)
            tail.spread(pe)
            pe.wait_ge(ro_done, NT)
            for q in range(6):
                for t in range(NT):
                    src = ro[:, t, 2 * q:2 * q + 2, :] if q < 4 else k2[:, t, 2 * (q - 4):2 * (q - 4) + 2, :]
                    mm = pe.transpose(k.ps[:, q, t * P:(t + 1) * P], src.rearrange("p h d -> p (h d)"), k.ident[:])
                mm.then_inc(t_done, 1)


def attention(k, units, loads=()):
    nc = k.nc
    with ExitStack() as c:
        sb = lambda n, s: c.enter_context(nc.sbuf_tensor(fresh(n), s, F32))
        idle = k.ring[:].rearrange("p b n -> p (b n)").rearrange("p (a i n) -> p a i n", a=4, i=2)
        pr, sc, pT = (idle[:, i] for i in range(3))
        mx = sb("mx", [P, 4])
        nm = sb("nm", [P, 4])
        ls = sb("ls", [P, 4])
        es = sb("es", [P, 4])
        block, s_ready, max_done, exp_done, t_ready, t_out, o_ready, o_out, step, moved = c.enter_context(
            stage(nc, "s_ready max_done exp_done t_ready t_out o_ready o_out step moved"))
        N = len(units)
        W = lambda u: units[u]["k"].shape[-1]

        @block.sync
        def _(sp):
            n = 0
            for pairs in loads:
                for dst, src in pairs:
                    n += 16
                    sp.dma_start(dst, src).then_inc(moved, 16)
                sp.wait_ge(moved, n)

        @block.tensor
        def _(pe):
            for i in range(-1, N + 2):
                if i + 1 < N:
                    n, u = i + 1, units[i + 1]
                    if n >= 2:
                        pe.wait_ge(exp_done, n - 1)
                    pe.matmul(k.ps[:, n % 2, 0:W(n)], u["q"], u["k"], start=True, stop=True).then_inc(s_ready, 1)
                if 1 <= i <= N:
                    v = i - 1
                    pe.wait_ge(exp_done, v + 1)
                    if v >= 2:
                        pe.wait_ge(t_out, v - 1)
                    for j in range(W(v) // P):
                        mm = pe.transpose(k.ps[:, 2 + v % 2, j * P:(j + 1) * P], pr[:, v % 2, j * P:(j + 1) * P], k.ident[:])
                    mm.then_inc(t_ready, 1)
                if i >= 2:
                    v = i - 2
                    pe.wait_ge(t_out, v + 1)
                    if v >= 2:
                        pe.wait_ge(o_out, v - 1)
                    vs = units[v]["v"]
                    chain(pe, k.ps[:, 4 + v % 2, 0:vs[0].shape[-1]], lambda j: pT[:, v % 2, j * P:(j + 1) * P],
                          lambda j: vs[j], range(len(vs))).then_inc(o_ready, 1)

        @block.scalar
        def _(act):
            for i in range(N):
                u = units[i]
                act.wait_ge(max_done, i + 1)
                if i >= 2:
                    act.wait_ge(t_ready, i - 1)
                if i >= 4:
                    act.wait_ge(o_out, i - 3)
                src = k.ps[:, i % 2, 0:W(i)] if u.get("bias") is None else sc[:, i % 2, 0:W(i)]
                l = u["l"] if u.get("l") is not None else ls[:, i % 4:i % 4 + 1]
                if u.get("sink") is not None:
                    nc.scalar.activation(es[:, i % 4:i % 4 + 1], u["sink"], ACT.Exp, bias=nm[:, i % 4:i % 4 + 1])
                nc.scalar.activation(pr[:, i % 2, 0:W(i)], src, ACT.Exp, bias=nm[:, i % 4:i % 4 + 1],
                                     accum_out=l).then_inc(exp_done, 1)

        @block.vector
        def _(dve):
            link = Link(dve, step)
            for i in range(N + 2):
                if i < N:
                    u = units[i]
                    dve.wait_ge(s_ready, i + 1)
                    if i >= 4:
                        dve.wait_ge(exp_done, i - 3)
                    n = nm[:, i % 4:i % 4 + 1]
                    s = k.ps[:, i % 2, 0:W(i)]
                    if u.get("bias") is None:
                        nc.vector.tensor_reduce(n, s, AX, ALU.max, negate=True).then_inc(max_done, 1)
                    else:
                        m = u["m"] if u.get("m") is not None else mx[:, i % 4:i % 4 + 1]
                        if i >= 2:
                            dve.wait_ge(exp_done, i - 1)
                        link(nc.vector.tensor_tensor_reduce(sc[:, i % 2, 0:W(i)], s, u["bias"], 1.0, 2 * NEG, ALU.add, ALU.max, m))
                        if u.get("sink") is not None:
                            link(nc.vector.tensor_tensor(m, m, u["sink"], ALU.max))
                        nc.vector.tensor_scalar(n, m, -1.0, None, ALU.mult).then_inc(max_done, 1)
                if 1 <= i <= N:
                    v = i - 1
                    dve.wait_ge(t_ready, v + 1)
                    if v >= 2:
                        dve.wait_ge(o_ready, v - 1)
                    nc.vector.tensor_copy(pT[:, v % 2, 0:W(v)], k.ps[:, 2 + v % 2, 0:W(v)]).then_inc(t_out, 1)
                if i >= 2:
                    v = i - 2
                    dve.wait_ge(o_ready, v + 1)
                    vs = units[v]["v"]
                    po = k.ps[:, 4 + v % 2, 0:vs[0].shape[-1]]
                    if units[v].get("l") is not None:
                        nc.vector.tensor_copy(units[v]["out"], po).then_inc(o_out, 1)
                    else:
                        l = ls[:, v % 4:v % 4 + 1]
                        if units[v].get("sink") is not None:
                            link(nc.vector.tensor_tensor(l, l, es[:, v % 4:v % 4 + 1], ALU.add))
                        link(nc.vector.reciprocal(l, l))
                        nc.vector.tensor_scalar(units[v]["out"], po, l, None, ALU.mult).then_inc(o_out, 1)
            dve.wait_ge(o_out, N)


def combine_groups(k, T):
    nc = k.nc
    W = BG * (HD + 2)
    nat = k.scratch[0:S * W]
    with ExitStack() as c:
        sb = lambda n, s: c.enter_context(nc.sbuf_tensor(fresh(n), s, F32))
        U0 = sb("U0c", [P, CLS, BG, HD + 2])
        M = sb("Mx", [P, 16])
        f = sb("fg", [P, 3, 16])
        t1 = sb("t1c", [P, 16])
        ob = sb("ob", [P, 16, HD])
        block, moved, f_in, f_done, ob_done, t_done, out_act, step = c.enter_context(
            stage(nc, "moved f_in f_done ob_done t_done out_act step"))
        U = [U0[:].rearrange("p t h d -> p (t h) d"), T["U1"][:].rearrange("p t h d -> p (t h) d"),
             T["U2"][:].rearrange("p t h d -> p (t h) d")]

        @block.sync
        def _(sp):
            sp.dma_start(nat.rearrange("(t p f) -> p t f", p=P, f=W), T["U0"][:].rearrange("p t h d -> p t (h d)")).then_inc(moved, 16)
            sp.wait_ge(moved, 16)
            sp.dma_start(U0[:].rearrange("p t h d -> p (t h d)"), nat.rearrange("(i f) -> i f", i=P)).then_inc(moved, 16)
            sp.wait_ge(moved, 32)

        @block.vector
        def _(dve):
            link = Link(dve, step)
            dve.wait_ge(moved, 32)
            link(nc.vector.tensor_tensor(M[:], U[0][:, :, HD + 1], U[1][:, :, HD + 1], ALU.max))
            link(nc.vector.tensor_tensor(M[:], M[:], U[2][:, :, HD + 1], ALU.max))
            for g in range(3):
                ins = nc.vector.tensor_tensor(f[:, g, :], U[g][:, :, HD + 1], M[:], ALU.subtract)
            ins.then_inc(f_in, 1)
            dve.wait_ge(f_done, 1)
            link(nc.vector.tensor_tensor(M[:], f[:, 0, :], U[0][:, :, HD], ALU.mult))
            for g in (1, 2):
                link(nc.vector.tensor_tensor(t1[:], f[:, g, :], U[g][:, :, HD], ALU.mult))
                link(nc.vector.tensor_tensor(M[:], M[:], t1[:], ALU.add))
            link(nc.vector.reciprocal(M[:], M[:]))
            link(nc.vector.tensor_tensor(f[:], f[:], bcast(M[:], 1, 3), ALU.mult))
            link(nc.vector.tensor_tensor(ob[:], U[0][:, :, 0:HD], bcast(f[:, 0, :], 2, HD), ALU.mult))
            for g in (1, 2):
                link(nc.vector.tensor_tensor(U[g][:, :, 0:HD], U[g][:, :, 0:HD], bcast(f[:, g, :], 2, HD), ALU.mult))
                link(nc.vector.tensor_tensor(ob[:], ob[:], U[g][:, :, 0:HD], ALU.add))
            dve.nop().then_inc(ob_done, 1)
            for q in range(6):
                dve.wait_ge(out_act, q + 1)
                link(nc.vector.tensor_tensor(T["oT"][1][:, q, :], k.ps[:, q, :], T["oT"][0][:, q, :].bitcast(F32), ALU.subtract))

        @block.scalar
        def _(act):
            act.wait_ge(f_in, 1)
            nc.scalar.activation(f[:], f[:], ACT.Exp).then_inc(f_done, 1)
            for q in range(6):
                act.wait_ge(t_done, q + 1)
                nc.scalar.copy(T["oT"][0][:, q, :], k.ps[:, q, :]).then_inc(out_act, 1)
            act.wait_ge(out_act, 6)

        @block.tensor
        def _(pe):
            for q in range(4):
                for t in range(NT):
                    mm = pe.transpose(k.ps[:, q, t * P:(t + 1) * P], T["oa"][:, t, q * P:(q + 1) * P], k.ident[:])
                mm.then_inc(t_done, 1)
            pe.wait_ge(ob_done, 1)
            for q in range(2):
                for t in range(NT):
                    src = ob[:, 4 * t + 2 * q:4 * t + 2 * q + 2, :].rearrange("p h d -> p (h d)")
                    mm = pe.transpose(k.ps[:, 4 + q, t * P:(t + 1) * P], src, k.ident[:])
                mm.then_inc(t_done, 1)


def branches(k, wa, wb, wo, T, grow):
    nc = k.nc
    with ExitStack() as c:
        tmp = c.enter_context(nc.sbuf_tensor(fresh("tmp_b"), [P, 2, 2, S], F32))
        mT = pair_of(nc, c, "merged", [P, KD, S])
        block, *sems, pair_out, merged, res_out, step = c.enter_context(stage(nc, Weights.NAMES + " pair_out merged res_out step"))
        W = Weights(k, sems)
        cols = lambda h: slice(256 * h, 256 * (h + 1))

        def both(v, i):
            r = v[:, i, 0:1536].rearrange("p (k n) -> p k n", k=6)
            return r[:, 0:4, :], r[:, 4:6, :]

        @block.sync
        def _(sp):
            for h in range(4):
                ra, rb = both(k.ring, h % 2)
                W.load(sp, h // 2, h % 2, [(ra, wa[:, :, cols(h)]), (rb, wb[:, :, cols(h)])])
            for n in range(2):
                for i in range(2):
                    W.load(sp, 2 + n, i, [(W.raw(i, 4, 512), wo[:, 4 * i:4 * i + 4, n * 512:(n + 1) * 512])])

        @block.scalar
        def _(act):
            for u in range(4):
                for i in range(2):
                    W.split_high(act, u, i, 32 * (u + 1) if u < 2 else 64 + 16 * (u - 1))

        @block.gpsimd
        def _(pool):
            W.start_low(pool)
            for u in range(4):
                for i in range(2):
                    W.split_low(pool, u, i)

        @block.tensor
        def _(pe):
            W.start_read(pe)
            for h in range(4):
                if h >= 2:
                    pe.wait_ge(pair_out, 2 * (h - 1))
                pa, pb = zip(*(both(k.parts[a], h % 2) for a in range(2)))
                o = T["oT"]
                for x, (p, ks) in enumerate(((pa, range(4)), (pb, range(2)))):
                    mm = split_products(pe, W, h // 2, h % 2, [k.ps[:, 4 * (h % 2) + 2 * m + x, :] for m in range(2)],
                                        lambda a, m, q: p[a][:, q, m * P:(m + 1) * P], lambda a, m, q: o[a][:, 4 * x + q, :], ks, True)
                mm.then_inc(W.read, 1)
            pe.wait_ge(merged, KD)
            for n in range(2):
                token_unit(k, pe, W, mT, 2 + n, n, 512)

        @block.vector
        def _(dve):
            link = Link(dve, step)
            V = nc.vector
            for m in range(KD):
                W.done(dve, m // 4, m // 2 % 2)
                b = 4 * (m // 2 % 2) + 2 * (m % 2)
                t1, t2 = tmp[:, 0, m % 2, :], tmp[:, 1, m % 2, :]
                link(V.tensor_tensor(t1, k.ps[:, b, :], T["gates"][:, m, :], ALU.mult))
                link(V.tensor_tensor(t2, k.ps[:, b + 1, :], T["gates"][:, KD + m, :], ALU.mult))
                dve.nop().then_inc(pair_out, 1)
                link(V.tensor_tensor(t1, t1, t2, ALU.add))
                link(V.tensor_copy(mT[0][:, m, :], t1))
                V.tensor_tensor(mT[1][:, m, :], t1, mT[0][:, m, :].bitcast(F32), ALU.subtract).then_inc(merged, 1)
            dve.wait_ge(merged, KD)
            for n in range(2):
                W.done(dve, 2 + n, 1)
                for t in range(NT):
                    c2 = slice(n * 512, (n + 1) * 512)
                    link(V.tensor_tensor(tmp[:, 0, t % 2, :], k.ps[:, 4 * n + t, :], grow[:, c2], ALU.mult))
                    link(V.scalar_tensor_tensor(k.x[:, t, c2], k.x[:, t, c2], ALPHA, tmp[:, 0, t % 2, :], ALU.mult, ALU.add))


def router(k, hT, cT):
    nc = k.nc
    G = N_EXP // EPG
    with ExitStack() as c:
        sb = lambda n, s: c.enter_context(nc.sbuf_tensor(fresh(n), s, F32))
        wr = sb("wr", [P, KD, N_EXP])
        wp = pair_of(nc, c, "wr", [P, KD, N_EXP])
        rb = sb("rb", [P, N_EXP])
        before = sb("before_sb", [P, 4, 4])
        sc = sb("sc_r", [P, NT, N_EXP])
        sel = sb("sel_r", [P, NT * G, EPG])
        gt = sb("gt_r", [P, NT * G, EPG, EPG])
        eq = sb("eq_r", [P, NT * G, EPG, EPG])
        top = sb("top_r", [P, NT * G, EPG])
        grp = sb("grp_r", [P, NT, G])
        gm = sb("gm_r", [P, NT, G])
        den = sb("den_r", [P, NT])
        block, in_landed, w_split, logit, score, comb, t_done, cT_done, step = c.enter_context(
            stage(nc, "in_landed w_split logit score comb t_done cT_done step"))

        @block.sync
        def _(sp):
            sp.dma_start(wr[:], k.A["w_router"].rearrange("(k p) e -> p k e", p=P)).then_inc(in_landed, 16)
            sp.dma_start(rb[:], bcast(k.A["router_bias"], 0, P)).then_inc(in_landed, 16)
            sp.dma_start(before[:], k.K["before"]).then_inc(in_landed, 16)
            sp.wait_ge(in_landed, 48)

        @block.tensor
        def _(pe):
            pe.wait_ge(w_split, 1)
            for t in range(NT):
                mm = chain3(pe, k.ps[:, 0, t * N_EXP:(t + 1) * N_EXP], lambda a, q: hT[a][:, q, t * P:(t + 1) * P],
                            lambda a, q: wp[a][:, q, :], range(KD))
            mm.then_inc(logit, 1)
            pe.wait_ge(comb, 1)
            for t in range(NT):
                mm = pe.transpose(k.ps[0:N_EXP, 1, t * P:(t + 1) * P], sc[:, t, :], k.ident[:])
            mm.then_inc(t_done, 1)

        @block.scalar
        def _(act):
            act.wait_ge(logit, 1)
            nc.scalar.activation(sc[:], k.ps[:, 0, 0:NT * N_EXP].rearrange("p (t e) -> p t e", t=NT), ACT.Sigmoid).then_inc(score, 1)
            act.wait_ge(t_done, 1)
            nc.scalar.copy(cT[:], k.ps[0:N_EXP, 1, :]).then_inc(cT_done, 1)
            act.wait_ge(cT_done, 1)

        @block.vector
        def _(dve):
            link = Link(dve, step)
            V = nc.vector
            dve.wait_ge(in_landed, 48)
            link(V.tensor_copy(wp[0][:], wr[:]))
            V.tensor_tensor(wp[1][:], wr[:], wp[0][:].bitcast(F32), ALU.subtract).then_inc(w_split, 1)
            dve.wait_ge(score, 1)
            link(V.tensor_tensor(sel[:].rearrange("p (t g) e -> p t (g e)", t=NT), sc[:], bcast(rb[:], 1, NT), ALU.add))

            def ranks(v, n, out):
                g, e = gt[:, 0:n], eq[:, 0:n]
                link(V.tensor_tensor(g, bcast(v, 2, 4), bcast(v, 3, 4), ALU.is_gt))
                link(V.tensor_tensor(e, bcast(v, 2, 4), bcast(v, 3, 4), ALU.is_equal))
                link(V.tensor_tensor(e, e, bcast(before[:], 1, n), ALU.mult))
                link(V.tensor_tensor(g, g, e, ALU.add))
                link(V.tensor_reduce(out, g, AX, ALU.add))

            ranks(sel[:], NT * G, top[:])
            link(V.tensor_scalar(top[:], top[:], 1.5, None, ALU.is_lt))
            link(V.tensor_tensor(sel[:], sel[:], top[:], ALU.mult))
            link(V.tensor_reduce(grp[:].rearrange("p t g -> p (t g)"), sel[:], AX, ALU.add))
            ranks(grp[:], NT, gm[:])
            link(V.tensor_scalar(gm[:], gm[:], 0.5, None, ALU.is_lt))
            link(V.tensor_tensor(top[:], top[:], bcast(gm[:].rearrange("p t g -> p (t g)"), 2, EPG), ALU.mult))
            link(V.tensor_tensor(sc[:], sc[:], top[:].rearrange("p (t g) e -> p t (g e)", t=NT), ALU.mult))
            link(V.tensor_reduce(den[:], sc[:], AX, ALU.add))
            link(V.reciprocal(den[:], den[:]))
            V.tensor_tensor(sc[:], sc[:], bcast(den[:], 2, N_EXP), ALU.mult).then_inc(comb, 1)
            dve.wait_ge(comb, 1)


def experts(k, hT, wg, wu, wd, cT, grow, w_side, side_out):
    nc = k.nc
    with ExitStack() as c:
        sb = lambda n, s: c.enter_context(nc.sbuf_tensor(fresh(n), s, F32))
        hid = pair_of(nc, c, "hid", [P, KD, S])
        sg = sb("sg", [P, 2, S])
        ex = sb("hid_exact", [P, 2, S])
        y = sb("y_acc", [P, NT, D])
        comb_all = sb("comb_all", [P, N_EXP, S])
        back = k.scratch[0:N_EXP * S].rearrange("(e n) -> e n", e=N_EXP)
        block, *sems, sg_done, free_dve, hid_done, step, comb_moved = c.enter_context(
            stage(nc, f"{Weights.NAMES} {SideModulation.NAMES} sg_done free_dve hid_done step comb_moved"))
        W = Weights(k, sems[0:5])
        side = SideModulation(k, c, sems[5:], 1, lambda s, i: w_side[i][:, :, bass.ds(64 * (s - i), P)],
                              lambda s, i: side_out[i][:, bass.ds(64 * (s - i), P)])
        C = N_EXP // 4

        @block.sync
        def _(sp):
            with sp.Fori(0, C) as ch:
                for j in range(4):
                    for i in range(2):
                        v = W.raw(i, KD, 256)
                        at = slice(i * P, (i + 1) * P)
                        W.load(sp, 6 * ch + j, i, [(v[:, :, 0:P], wg[:, 4 * ch + j, :, at]), (v[:, :, P:256], wu[:, 4 * ch + j, :, at])])
                    for i in range(2):
                        side.load(sp, 12 * ch + 2 * j + i, i)
                for n in range(2):
                    for i in range(2):
                        v = W.raw(i, 4, 512)
                        W.load(sp, 6 * ch + 4 + n, i, [(v[:, 2 * e:2 * e + 2, :], wd[:, bass.ds(8 * ch + 4 * i + 2 * e, 2), n * 512:(n + 1) * 512])
                                                       for e in range(2)])
                    for i in range(2):
                        side.load(sp, 12 * ch + 8 + 2 * n + i, i)

        @block.gpsimd
        def _(pool):
            W.start_low(pool)
            with pool.Fori(0, C) as ch:
                for j in range(6):
                    for i in range(2):
                        W.split_low(pool, 6 * ch + j, i)

        @block.tensor
        def _(pe):
            W.start_read(pe)
            with pe.Fori(0, C) as ch:
                for j in range(6):
                    pe.wait_ge(free_dve, 6 * ch + j + 1)
                    if j < 4:
                        feature_unit(k, pe, W, hT, 6 * ch + j, j % 2)
                    else:
                        token_unit(k, pe, W, hid, 6 * ch + j, j % 2, 512,
                                   before=(lambda i: pe.wait_ge(hid_done, 8 * ch + 4 * i + 4)) if j == 4 else None)

        @block.scalar
        def _(act):
            act.dma_start(back, cT[:]).then_inc(comb_moved, 16)
            act.wait_ge(comb_moved, 16)
            act.dma_start(comb_all[:], bcast(back, 0, P)).then_inc(comb_moved, 16)
            with act.Fori(0, C) as ch:
                for j in range(6):
                    for i in range(2):
                        W.split_high(act, 6 * ch + j, i, 192 * ch + 32 * j + 32)
                    if 1 <= j < 5:
                        for i in range(2):
                            W.done(act, 6 * ch + j - 1, i)
                            act.wait_ge(step, 1 + 32 * ch + max(0, 6 * (j - 2) + 3 * i + 2))
                            nc.scalar.activation(sg[:, i, :], k.ps[:, 4 * ((j - 1) % 2) + 2 * i, :], ACT.Silu).then_inc(sg_done, 1)
                    for i in range(2):
                        side.store(act, 12 * ch + 2 * j + i, i)
            side.end(act, 48)

        @block.vector
        def _(dve):
            link = Link(dve, step)
            V = nc.vector
            link(V.memset(y[:], 0.0))
            dve.nop().then_inc(free_dve, 2)
            side.start(dve)
            dve.wait_ge(comb_moved, 32)
            with dve.Fori(0, C) as ch:
                link.n, link.base = 1, 32 * ch
                for j in range(4):
                    for i in range(2):
                        side.work(dve, 12 * ch + 2 * j + i, i, 6 * ch + j)
                    w = comb_all[:, bass.ds(4 * ch + j, 1), :].rearrange("p a n -> p (a n)")
                    for i in range(2):
                        dve.wait_ge(sg_done, 8 * ch + 2 * j + i + 1)
                        h, e = 2 * j + i, ex[:, i, :]
                        link(V.tensor_tensor(e, k.ps[:, 4 * (j % 2) + 2 * i + 1, :], w, ALU.mult))
                        link(V.tensor_tensor(e, e, sg[:, i, :], ALU.mult))
                        link(V.tensor_copy(hid[0][:, h, :], e))
                        V.tensor_tensor(hid[1][:, h, :], e, hid[0][:, h, :].bitcast(F32), ALU.subtract).then_inc(hid_done, 1)
                    dve.nop().then_inc(free_dve, 1)
                for n in range(2):
                    for i in range(2):
                        side.work(dve, 12 * ch + 8 + 2 * n + i, i, 6 * ch + 4 + n)
                    W.done(dve, 6 * ch + 4 + n, 1)
                    for t in range(NT):
                        yv = y[:, t, n * 512:(n + 1) * 512]
                        link(V.tensor_tensor(yv, yv, k.ps[:, 4 * n + t, :], ALU.add))
                    dve.nop().then_inc(free_dve, 1)
            link.n, link.base = 1 + C * 32, 0
            for t in range(NT):
                link(V.tensor_tensor(y[:, t, :], y[:, t, :], grow[:], ALU.mult))
                link(V.scalar_tensor_tensor(k.x[:, t, :], k.x[:, t, :], ALPHA, y[:, t, :], ALU.mult, ALU.add))


def first_layer(k, l, last_store):
    nc, A = k.nc, k.A
    kp = lambda ap: ap.rearrange("l (k p) n -> l p k n", p=P)[l]
    modulation(k, 0, kp(A["w_ada"]), A["b_ada"][l][0:2 * D], 4, k.mod, ((8, 8),))
    with ExitStack() as c:
        sb = lambda n, s: c.enter_context(nc.sbuf_tensor(fresh(n), s, F32))
        g1, g2 = sb("g1row", [P, D]), sb("g2row", [P, D])
        with ExitStack() as m:
            sm = lambda n, s: m.enter_context(nc.sbuf_tensor(fresh(n), s, F32))
            T = {"gates": sm("gates", [P, 16, S])}
            with ExitStack() as q:
                sq = lambda n, s: q.enter_context(nc.sbuf_tensor(fresh(n), s, F32))
                T.update(qa=sq("qa", [P, NT, 512]), kva=sq("kva", [P, NT, 256]), vc=sq("vc", [P, NT, 512]), v0=sq("v0", [P, 5, 256]),
                         q0T=sq("q0T", [P, 2, S]), k0T=sq("k0T", [P, 2, S + 2 * REACH]), qcT=sq("qcT", [P, 4, S]), kcT=sq("kcT", [P, 4, S]))
                T["v0c"] = sq("v0c", [P, CLS, 256])
                with ExitStack() as h:
                    hT = pair_of(nc, h, "hT", [P, KD, S])
                    norm_to_hT(k, hT, False, LN_EPS, k.mod[:, 8:16], k.mod[:, 0:8])
                    sums = k.sums[4]
                    in_projection(k, kp(A["w_in"]), hT, T, kp(A["w_ada"])[:, :, 2 * D:6 * D], sums)
                T["oa"] = T["qa"]
                T.update(U0=sq("U0", [P, NT, BG, HD + 2]), U1=sq("U1", [P, NT, BG, HD + 2]), U2=sq("U2", [P, NT, BG, HD + 2]))
                with ExitStack() as b:
                    with ExitStack() as r:
                        sr = lambda n, s: r.enter_context(nc.sbuf_tensor(fresh(n), s, F32, side="right"))
                        T.update(qaT=sr("qaT", [P, 4, S]), kaT=sr("kaT", [P, 2, S]))
                        rope_qk(k, A["q_norm_g"][l], A["k_norm_g"][l], T,
                                (sums, A["b_ada"][l][2 * D:6 * D], 32, k.mod[:, 16:48], (16,), None, [(0, g1), (24, g2)]))
                        band, cls = (b.enter_context(nc.sbuf_tensor(fresh(n), s, F32)) for n, s in (("band", [P, 3, BG, 256]), ("cls", [P, 2, BG, P])))
                        attention(k, global_units(T), loads=[[(band[:], k.K["bias_band"]), (cls[:], k.K["bias_class"])]] + order_v0(k, T["v0c"], T["v0"]))
                    attention(k, dilated_units(T, band, cls))
                T["oT"] = pair_of(nc, m, "oT", [P, 6, S], side="right")
                combine_groups(k, T)
            branches(k, kp(A["w_branch_a"]), kp(A["w_branch_b"]), kp(A["w_out"]), T, g1)
        with ExitStack() as m:
            hT = pair_of(nc, m, "hT", [P, KD, S])
            norm_to_hT(k, hT, False, LN_EPS, k.mod[:, 32:40], k.mod[:, 24:32], affine=(A["ln1_g"][l], A["ln1_b"][l]))
            cT = m.enter_context(nc.sbuf_tensor(fresh("cT"), [N_EXP, S], F32))
            router(k, hT, cT)
            ex = lambda ap: ap.rearrange("l e (k p) n -> l p e k n", p=P)[l]
            experts(k, hT, ex(A["w_exp_gate"]), ex(A["w_exp_up"]), A["w_exp_down"].rearrange("l e (f p) n -> l p (e f) n", p=P)[l], cT, g2,
                    [A["mod_w_2"][:, i].rearrange("l (k p) n -> l p k n", p=P)[l] for i in range(2)],
                    [k.sums[0:4].rearrange("(l i) p n -> l i p n", i=2)[:, i][l][:, 0:24 * P] for i in range(2)])
    norm_to_hT(k, None, False, LN_EPS, None, None, affine=(A["ln2_g"][l], A["ln2_b"][l]), store=last_store)


def global_units(T):
    units = []
    for h in range(A_HEADS):
        p0, g = 64 * (h % 2), h // 4
        for t in range(NT):
            units.append(dict(q=T["qaT"][p0:p0 + 64, h // 2, t * P:(t + 1) * P], k=T["kaT"][p0:p0 + 64, g, :],
                              v=[T["kva"][:, j, 128 + 64 * g:192 + 64 * g] for j in range(NT)],
                              out=T["oa"][:, t, h * HD:(h + 1) * HD]))
    return units


def dilated_units(T, band, cls):
    units = []
    for t in range(NT):
        for h in range(BG):
            p0, u = 64 * (h % 2), T["U0"][:, t, h, :]
            units.append(dict(q=T["q0T"][p0:p0 + 64, h // 2, t * P:(t + 1) * P],
                              k=T["k0T"][p0:p0 + 64, h // 2, t * P:t * P + 256],
                              bias=band[:, 0 if t == 0 else 2 if t == NT - 1 else 1, h, :],
                              v=[T["v0"][:, t + j, h * HD:(h + 1) * HD] for j in range(2)],
                              out=u[:, 0:HD], l=u[:, HD:HD + 1], m=u[:, HD + 1:HD + 2]))
            for g in range(2):
                u = T[f"U{g + 1}"][:, t, h, :]
                i = 2 * g + h // 2
                units.append(dict(q=T["qcT"][p0:p0 + 64, i, t * P:(t + 1) * P], k=T["kcT"][p0:p0 + 64, i, t * P:(t + 1) * P],
                                  bias=cls[:, g, h, :], v=[T["vc"][:, t, (4 * g + h) * HD:(4 * g + h + 1) * HD]],
                                  out=u[:, 0:HD], l=u[:, HD:HD + 1], m=u[:, HD + 1:HD + 2]))
    return units


def first_block(k):
    start_up(k, k.A["x"].rearrange("a (i r) d -> (a i) r d", r=CLS))
    mid = k.scratch[2 * S * D:3 * S * D].rearrange("(i r d) -> r i d", r=CLS, d=D)
    with k.nc.Fori(0, DEPTH) as l:
        first_layer(k, l, mid)



def project(k, w, hT, plan, loads=()):
    nc = k.nc
    N = len(plan)
    with stage(nc, Weights.NAMES + " free_act free_dve moved") as (block, *sems, free_act, free_dve, moved):
        W = Weights(k, sems)

        @block.sync
        def _(sp):
            for u, (c0, n, major, *_r) in enumerate(plan):
                for i in range(2):
                    if major == "feature":
                        W.load(sp, u, i, [(W.raw(i, KD, 256), w[:, :, c0 + 256 * i:c0 + 256 * (i + 1)])])
                    else:
                        W.load(sp, u, i, [(W.raw(i, KD // 2, n), w[:, 4 * i:4 * i + 4, c0:c0 + n])])
                if u == 1:
                    for dst, src in loads:
                        sp.dma_start(dst, src).then_inc(moved, 16)
            if loads:
                sp.wait_ge(moved, 16 * len(loads))

        @block.gpsimd
        def _(pool):
            W.start_low(pool)
            for u in range(N):
                for i in range(2):
                    W.split_low(pool, u, i)

        @block.tensor
        def _(pe):
            W.start_read(pe)
            for u, (c0, n, major, *_r) in enumerate(plan):
                if u >= 2:
                    pe.wait_ge(free_act, u - 1)
                    pe.wait_ge(free_dve, u - 1)
                if major == "feature":
                    feature_unit(k, pe, W, hT, u, u % 2)
                else:
                    token_unit(k, pe, W, hT, u, u % 2, n)

        @block.scalar
        def _(act):
            for u in range(N + 1):
                if u < N:
                    for i in range(2):
                        W.split_high(act, u, i, 16 * u + 16)
                if u >= 1:
                    _c, n, major, f, dst = plan[u - 1]
                    W.done(act, u - 1, 1)
                    for j in range(4 if f == "silu" else 2):
                        src = k.ps[:, 4 * ((u - 1) % 2) + j, 0:n if major == "token" else S]
                        if f == "silu":
                            last = nc.scalar.activation(dst[j], src, ACT.Silu)
                        else:
                            last = nc.scalar.activation(dst[j], src, ACT.Copy, scale=f)
                    last.then_inc(free_act, 1)
            act.wait_ge(free_act, N)

        @block.vector
        def _(dve):
            for u, (_c, n, major, f, dst) in enumerate(plan):
                if f == "silu":
                    if u:
                        dve.wait_ge(free_dve, u)
                    dve.nop().then_inc(free_dve, 1)
                    continue
                W.done(dve, u, 1)
                for j in (2, 3):
                    src = k.ps[:, 4 * (u % 2) + j, 0:n if major == "token" else S]
                    last = nc.vector.tensor_scalar(dst[j], src, f, None, ALU.mult)
                last.then_inc(free_dve, 1)
            dve.wait_ge(free_dve, N)


def out_projection(k, w, src, kt, y, first):
    nc = k.nc
    with stage(nc, Weights.NAMES + " y_done spare") as (block, *sems, y_done, _s):
        W = Weights(k, sems)
        half = kt // 2

        @block.sync
        def _(sp):
            for n in range(2):
                for i in range(2):
                    W.load(sp, n, i, [(W.raw(i, half, 512), w[:, half * i:half * (i + 1), n * 512:(n + 1) * 512])])

        @block.scalar
        def _(act):
            for n in range(2):
                for i in range(2):
                    W.split_high(act, n, i, 16 * n + 16)
            act.wait_ge(W.high, 4)

        @block.gpsimd
        def _(pool):
            W.start_low(pool)
            for n in range(2):
                for i in range(2):
                    W.split_low(pool, n, i)
            pool.wait_ge(W.low, 6)

        @block.tensor
        def _(pe):
            W.start_read(pe)
            for n in range(2):
                token_unit(k, pe, W, src, n, n, 512, kt=kt)

        @block.vector
        def _(dve):
            for n in range(2):
                W.done(dve, n, 1)
                for t in range(NT):
                    yv, p = y[:, t, n * 512:(n + 1) * 512], k.ps[:, 4 * n + t, :]
                    if first:
                        nc.vector.tensor_copy(yv, p).then_inc(y_done, 1)
                    else:
                        nc.vector.tensor_tensor(yv, yv, p, ALU.add).then_inc(y_done, 1)
            dve.wait_ge(y_done, 2 * NT)


def mlp(k, w1, w2, hT, y):
    nc = k.nc
    with ExitStack() as c:
        hid = pair_of(nc, c, "hid", [P, KD, S])
        ex = c.enter_context(nc.sbuf_tensor(fresh("hid_exact"), [P, 4, S], F32))
        block, *sems, free_dve, hid_done, step = c.enter_context(stage(nc, Weights.NAMES + " free_dve hid_done step"))
        W = Weights(k, sems)
        C = 4

        @block.sync
        def _(sp):
            with sp.Fori(0, C) as ch:
                for j in range(4):
                    for i in range(2):
                        if j < 2:
                            W.load(sp, 4 * ch + j, i, [(W.raw(i, KD, 256), w1[:, :, bass.ds(1024 * ch + 512 * j + 256 * i, 256)])])
                        else:
                            W.load(sp, 4 * ch + j, i, [(W.raw(i, 4, 512), w2[:, bass.ds(8 * ch + 4 * i, 4), (j - 2) * 512:(j - 1) * 512])])

        @block.scalar
        def _(act):
            with act.Fori(0, C) as ch:
                for j in range(4):
                    for i in range(2):
                        W.split_high(act, 4 * ch + j, i, 64 * ch + 16 * j + 16)

        @block.gpsimd
        def _(pool):
            W.start_low(pool)
            with pool.Fori(0, C) as ch:
                for j in range(4):
                    for i in range(2):
                        W.split_low(pool, 4 * ch + j, i)

        @block.tensor
        def _(pe):
            W.start_read(pe)
            with pe.Fori(0, C) as ch:
                for j in range(4):
                    pe.wait_ge(free_dve, 4 * ch + j + 1)
                    if j < 2:
                        feature_unit(k, pe, W, hT, 4 * ch + j, j % 2)
                    else:
                        token_unit(k, pe, W, hid, 4 * ch + j, j % 2, 512,
                                   before=(lambda i: pe.wait_ge(hid_done, 8 * ch + 4 * i + 4)) if j == 2 else None)

        @block.vector
        def _(dve):
            link = Link(dve, step)
            V = nc.vector
            link(V.memset(y[:], 0.0))
            dve.nop().then_inc(free_dve, 2)
            with dve.Fori(0, C) as ch:
                link.n, link.base = 1, 32 * ch
                for j in range(2):
                    for m in range(4):
                        W.done(dve, 4 * ch + j, m // 2)
                        q, e = 4 * j + m, ex[:, m, :]
                        link(V.tensor_scalar(e, k.ps[:, 4 * j + m, :], 0.0, None, ALU.max))
                        if m == 3:
                            dve.nop().then_inc(free_dve, 1)
                        link(V.tensor_tensor(e, e, e, ALU.mult))
                        link(V.tensor_copy(hid[0][:, q, :], e))
                        V.tensor_tensor(hid[1][:, q, :], e, hid[0][:, q, :].bitcast(F32), ALU.subtract).then_inc(hid_done, 1)
                    dve.wait_ge(hid_done, 8 * ch + 4 * j + 4)
                for n in range(2):
                    W.done(dve, 4 * ch + 2 + n, 1)
                    for t in range(NT):
                        yv = y[:, t, n * 512:(n + 1) * 512]
                        link(V.tensor_tensor(yv, yv, k.ps[:, 4 * n + t, :], ALU.add))
                    dve.nop().then_inc(free_dve, 1)


def add_normed(k, y, grow, store=None):
    nc = k.nc
    with ExitStack() as c:
        sb = lambda n, s: c.enter_context(nc.sbuf_tensor(fresh(n), s, F32))
        st, mv, ms = sb("stats_y", [P, NT, 2, 6]), sb("mv_y", [P, NT, 2]), sb("ms_y", [P, NT])
        block, var_done, root_done, x_done, stored, step = c.enter_context(stage(nc, "var_done root_done x_done stored step"))

        @block.sync
        def _(sp):
            if store is not None:
                for t in range(NT):
                    sp.wait_ge(x_done, t + 1)
                    sp.dma_start(store[:, t, :], k.x[:, t, :]).then_inc(stored, 16)
                sp.wait_ge(stored, 16 * NT)

        @block.scalar
        def _(act):
            act.wait_ge(var_done, 1)
            nc.scalar.activation(ms[:], ms[:], ACT.Sqrt).then_inc(root_done, 1)

        @block.vector
        def _(dve):
            link = Link(dve, step)
            for t in range(NT):
                for h in range(2):
                    link(nc.vector.bn_stats(st[:, t, h, :], y[:, t, h * 512:(h + 1) * 512]))
            for t in range(NT):
                link(nc.vector.bn_aggr(mv[:, t, :], st[:, t, :, :].rearrange("p a b -> p (a b)")))
            link(nc.vector.tensor_tensor(ms[:], mv[:, :, 0], mv[:, :, 0], ALU.mult))
            link(nc.vector.tensor_tensor(ms[:], ms[:], mv[:, :, 1], ALU.add))
            nc.vector.tensor_scalar(ms[:], ms[:], RMS_EPS, None, ALU.add).then_inc(var_done, 1)
            dve.wait_ge(root_done, 1)
            link(nc.vector.reciprocal(ms[:], ms[:]))
            for t in range(NT):
                link(nc.vector.scalar_tensor_tensor(y[:, t, :], y[:, t, :], ms[:, t:t + 1], grow[:], ALU.mult, ALU.mult))
                nc.vector.tensor_tensor(k.x[:, t, :], k.x[:, t, :], y[:, t, :], ALU.add).then_inc(x_done, 1)
            dve.wait_ge(x_done, NT)


def relative_bias(k, x_source):
    nc = k.nc
    H = 8
    flat = k.scratch[0:H * P * BIAS_W]
    with ExitStack() as c:
        hot = c.enter_context(nc.sbuf_tensor(fresh("hot"), [33, BIAS_W], F32))
        rel = c.enter_context(nc.sbuf_tensor(fresh("rel"), [33, H], F32))
        wide = c.enter_context(nc.sbuf_tensor(fresh("wide"), [P, H, BIAS_W], F32))
        block, in_landed, neg_done, row_done, row_out, moved, x_landed = c.enter_context(
            stage(nc, "in_landed neg_done row_done row_out moved x_landed"))

        @block.sync
        def _(sp):
            sp.dma_start(hot[:], k.K["bucket_hot"]).then_inc(in_landed, 16)
            sp.dma_start(rel[0:32, :], k.A["rel_bias_2"]).then_inc(in_landed, 16)
            sp.dma_start(k.x[:], x_source).then_inc(x_landed, 16)
            sp.wait_ge(row_out, 2 * H)
            sp.dma_start(flat.rearrange("(h p n) -> p h n", p=P, n=BIAS_W), wide[:]).then_inc(moved, 16)
            sp.wait_ge(moved, 16)
            sp.wait_ge(x_landed, 16)

        @block.gpsimd
        def _(pool):
            nc.gpsimd.memset(rel[32:33, :], NEG).then_inc(neg_done, 1)

        @block.tensor
        def _(pe):
            pe.wait_ge(in_landed, 32)
            pe.wait_ge(neg_done, 1)
            for h in range(H):
                if h >= 4:
                    pe.wait_ge(row_out, 2 * (h - 3))
                b = 2 * (h % 4)
                pe.matmul(k.ps[:, b, :], rel[:, h:h + 1].to_broadcast([33, P]), hot[:, 0:512], start=True, stop=True)
                pe.matmul(k.ps[:, b + 1, 0:P], rel[:, h:h + 1].to_broadcast([33, P]), hot[:, 512:BIAS_W], start=True, stop=True).then_inc(row_done, 1)

        @block.vector
        def _(dve):
            for h in range(H):
                dve.wait_ge(row_done, h + 1)
                b = 2 * (h % 4)
                nc.vector.tensor_copy(wide[:, h, 0:512], k.ps[:, b, :]).then_inc(row_out, 1)
                nc.vector.tensor_copy(wide[:, h, 512:BIAS_W], k.ps[:, b + 1, 0:P]).then_inc(row_out, 1)
            dve.wait_ge(row_out, 2 * H)


def bias_loads(k, bias, a):
    out = []
    for h in range(8):
        at = h * P * BIAS_W + P - 1
        out.append((bias[:, h, :], k.scratch[at:at + P * (BIAS_W - 1)].rearrange("(p n) -> p n", n=BIAS_W - 1)[:, a:512]))
    return out


def convolution(k, xbc, T):
    nc = k.nc
    A = k.A
    with ExitStack() as c:
        raw = c.enter_context(nc.sbuf_tensor(fresh("craw"), [80, P], F32))
        w = c.enter_context(nc.sbuf_tensor(fresh("cw"), [P, 80], F32))
        cv = c.enter_context(nc.sbuf_tensor(fresh("cv"), [P, 2, S], F32))
        block, in_landed, wt_done, conv_done, silu_done, t_done, t_out, step = c.enter_context(
            stage(nc, "in_landed wt_done conv_done silu_done t_done t_out step"))

        @block.sync
        def _(sp):
            sp.dma_start(raw[0:64, :], A["e_conv_w_2"].rearrange("e j (q p) -> (e j q) p", p=P)).then_inc(in_landed, 16)
            sp.dma_start(raw[64:80, :], A["e_conv_b_2"].rearrange("e (q p) -> (e q) p", p=P)).then_inc(in_landed, 16)
            sp.wait_ge(in_landed, 32)

        @block.vector
        def _(dve):
            link = Link(dve, step)
            V = nc.vector
            dve.wait_ge(wt_done, 1)
            link(V.tensor_copy(w[:], k.ps[:, 0, 0:80]))
            link(V.memset(xbc[:, :, 0:3], 0.0))
            for q in range(16):
                if q >= 2:
                    dve.wait_ge(silu_done, q - 1)
                o = cv[:, q % 2, :]
                link(V.tensor_scalar(o, xbc[:, q, 0:S], w[:, q:q + 1], w[:, 64 + q:65 + q], ALU.mult, ALU.add))
                for j in (1, 2):
                    link(V.scalar_tensor_tensor(o, xbc[:, q, j:j + S], w[:, 16 * j + q:16 * j + q + 1], o, ALU.mult, ALU.add))
                V.scalar_tensor_tensor(o, xbc[:, q, 3:3 + S], w[:, 48 + q:49 + q], o, ALU.mult, ALU.add).then_inc(conv_done, 1)

        @block.scalar
        def _(act):
            def token_major(q):
                act.wait_ge(t_done, q + 1)
                dst = T["xh"][:, :, q * P:(q + 1) * P] if q < 8 else T["Bt"][:, :, q - 8, :]
                nc.scalar.copy(dst, k.ps[:, 1 + q % 2, :].rearrange("p (t n) -> p t n", t=NT)).then_inc(t_out, 1)

            for q in range(16):
                act.wait_ge(conv_done, q + 1)
                nc.scalar.activation(xbc[:, q, 3:3 + S], cv[:, q % 2, :], ACT.Silu).then_inc(silu_done, 1)
                if 1 <= q < 13:
                    token_major(q - 1)
            act.wait_ge(silu_done, 16)
            act.wait_ge(t_out, 12)

        @block.tensor
        def _(pe):
            pe.wait_ge(in_landed, 32)
            pe.transpose(k.ps[:, 0, 0:80], raw[:], k.ident[0:80, 0:80]).then_inc(wt_done, 1)
            for q in range(12):
                pe.wait_ge(silu_done, q + 1)
                if q >= 2:
                    pe.wait_ge(t_out, q - 1)
                for t in range(NT):
                    mm = pe.transpose(k.ps[:, 1 + q % 2, t * P:(t + 1) * P], xbc[:, q, 3 + t * P:3 + (t + 1) * P], k.ident[:])
                mm.then_inc(t_done, 1)


def ssd(k, xbc, T):
    nc = k.nc
    A = k.A
    H, G, R = SSD_HEADS, SSD_GROUPS, SSD_HEADS // SSD_GROUPS
    with ExitStack() as c:
        sb = lambda n, s: c.enter_context(nc.sbuf_tensor(fresh(n), s, F32))
        par = sb("par", [P, 3, H])
        tri = sb("tri", [P, 2, P])
        ones = sb("ones", [P, P])
        dt = T["dt"]
        e, z, z2, acc = (sb(n, [P, NT, H]) for n in ("e_sp", "z_sp", "z2_sp", "acc_sp"))
        a, nacs, eacs, dte, etot, cs = (sb(n, [P, NT, H]) for n in ("a_ss", "nacs", "eacs", "dte", "etot", "cs_ss"))
        X = sb("Xdt", [P, NT, H, 64])
        Xd = sb("Xdec", [P, 2, R * 64])
        idle = k.ring[:].rearrange("p b n -> p (b n)")
        seg, M = (idle[:, i * 2 * R * P:(i + 1) * 2 * R * P].rearrange("p (b r n) -> p b r n", b=2, r=R) for i in range(2))
        state = sb("state", [P, G, R * 64])
        yt = sb("yt", [P, 2, R * 64])
        (block, in_landed, dt_in, exp1, a_done, sums, sums_out, exp2, front, seg_done, dec_done, m_done, back, y_out,
         xd_done, st_done, step) = c.enter_context(stage(
            nc, "in_landed dt_in exp1 a_done sums sums_out exp2 front seg_done dec_done m_done back y_out xd_done st_done step"))
        units = [(ch, g) for ch in range(NT) for g in range(G)]
        N = len(units)
        BT = lambda ch, g: xbc[:, 8 + g, 3 + ch * P:3 + (ch + 1) * P]
        CT = lambda ch, g: xbc[:, 12 + g, 3 + ch * P:3 + (ch + 1) * P]
        xh = T["xh"][:].rearrange("p t (h d) -> p t h d", d=64)

        @block.sync
        def _(sp):
            for i, n in enumerate(("e_dt_bias_2", "e_A_log_2", "e_D_2")):
                sp.dma_start(par[:, i, :], bcast(A[n][0], 0, P)).then_inc(in_landed, 16)
            sp.dma_start(tri[:], k.K["causal"]).then_inc(in_landed, 16)
            sp.wait_ge(in_landed, 64)

        @block.scalar
        def _(act):
            act.wait_ge(in_landed, 64)
            nc.scalar.activation(par[:, 1, :], par[:, 1, :], ACT.Exp).then_inc(exp1, 1)
            act.wait_ge(dt_in, 1)
            nc.scalar.activation(e[:], e[:], ACT.Exp, scale=-1.0).then_inc(exp1, 1)
            act.wait_ge(sums_out, 1)
            nc.scalar.activation(eacs[:], eacs[:], ACT.Exp)
            nc.scalar.activation(dte[:], dte[:], ACT.Exp)
            nc.scalar.activation(etot[:], etot[:], ACT.Exp).then_inc(exp2, 1)
            for i, (ch, g) in enumerate(units):
                act.wait_ge(seg_done, i + 1)
                for r in range(R):
                    h = g * R + r
                    last = nc.scalar.activation(seg[:, i % 2, r, :], seg[:, i % 2, r, :], ACT.Exp, bias=nacs[:, ch, h:h + 1])
                last.then_inc(dec_done, 1)
            act.wait_ge(dec_done, N)

        @block.tensor
        def _(pe):
            pe.wait_ge(a_done, 1)
            for ch in range(NT):
                pe.matmul(k.ps[:, 0, ch * H:(ch + 1) * H], tri[:, 0, :], a[:, ch, :], start=True, stop=True)
                mm = pe.matmul(k.ps[:, 1, ch * H:(ch + 1) * H], ones[:], a[:, ch, :], start=True, stop=True)
            mm.then_inc(sums, 1)
            pe.wait_ge(sums_out, 1)
            for v in range(-1, N):
                if v + 1 < N:
                    i = v + 1
                    ch, g = units[i]
                    if i >= 2:
                        pe.wait_ge(m_done, i - 1)
                    pe.matmul(k.ps[:, i % 2, 0:P], BT(ch, g), CT(ch, g), start=True, stop=True)
                    for r in range(R):
                        h = g * R + r
                        mm = pe.matmul(k.ps[:, 2 + i % 2, r * P:(r + 1) * P], a[:, ch, h:h + 1].to_broadcast([P, P]), tri[:, 0, :],
                                       start=True, stop=True)
                    mm.then_inc(front, 1)
                if v >= 0:
                    ch, g = units[v]
                    pe.wait_ge(m_done, v + 1)
                    pe.wait_ge(xd_done, v + 1)
                    if v >= 2:
                        pe.wait_ge(y_out, v - 1)
                    if v >= G:
                        pe.wait_ge(st_done, v - G + 1)
                    for r in range(R):
                        pe.matmul(k.ps[:, 4 + v % 2, r * 64:(r + 1) * 64], M[:, v % 2, r, :], X[:, ch, g * R + r, :], start=True, stop=True)
                    if ch:
                        pe.matmul(k.ps[:, 4 + v % 2, 256:512], CT(ch, g), state[:, g, :], start=True, stop=True)
                    pe.matmul(k.ps[:, 6 + v % 2, 0:256], T["Bt"][:, ch, g, :], Xd[:, v % 2, :], start=True, stop=True).then_inc(back, 1)

        @block.vector
        def _(dve):
            link = Link(dve, step)
            V = nc.vector
            link(V.memset(ones[:], 1.0))
            dve.wait_ge(in_landed, 64)
            link(V.tensor_tensor(dt[:], dt[:], bcast(par[:, 0, :], 1, NT), ALU.add))
            link(V.scalar_tensor_tensor(e[:], dt[:], -1.0, dt[:], ALU.mult, ALU.max))
            dve.nop().then_inc(dt_in, 1)
            dve.wait_ge(exp1, 2)
            link(V.tensor_scalar(z[:], e[:], 2.0, None, ALU.add))
            link(V.reciprocal(z[:], z[:]))
            link(V.tensor_tensor(z[:], z[:], e[:], ALU.mult))
            link(V.tensor_tensor(z2[:], z[:], z[:], ALU.mult))
            link(V.tensor_scalar(acc[:], z2[:], 1.0 / 19, None, ALU.mult))
            for n in range(8, 0, -1):
                link(V.scalar_tensor_tensor(acc[:], acc[:], 1.0 / (2 * n + 1), z2[:], ALU.add, ALU.mult))
            link(V.scalar_tensor_tensor(acc[:], acc[:], 1.0, z[:], ALU.add, ALU.mult))
            link(V.tensor_scalar(dt[:], dt[:], 0.0, None, ALU.max))
            link(V.scalar_tensor_tensor(dt[:], acc[:], 2.0, dt[:], ALU.mult, ALU.add))
            link(V.tensor_tensor(a[:], dt[:], bcast(par[:, 1, :], 1, NT), ALU.mult))
            V.tensor_scalar(a[:], a[:], -1.0, None, ALU.mult).then_inc(a_done, 1)
            for ch in range(NT):
                link(V.tensor_tensor(X[:, ch], xh[:, ch], bcast(dt[:, ch, :], 2, 64), ALU.mult))
            dve.wait_ge(sums, 1)
            acs, tot = (k.ps[:, b, 0:NT * H].rearrange("p (t h) -> p t h", t=NT) for b in (0, 1))
            link(V.tensor_copy(cs[:], acs))
            link(V.tensor_scalar(nacs[:], cs[:], -1.0, None, ALU.mult))
            link(V.tensor_copy(eacs[:], cs[:]))
            link(V.tensor_copy(etot[:], tot))
            link(V.tensor_tensor(dte[:], etot[:], cs[:], ALU.subtract))
            dve.nop().then_inc(sums_out, 1)
            dve.wait_ge(exp2, 1)
            for j in range(-1, N + 1):
                if j + 1 < N:
                    i = j + 1
                    ch, g = units[i]
                    hs = slice(g * R, (g + 1) * R)
                    dve.wait_ge(front, i + 1)
                    if i >= 2:
                        dve.wait_ge(m_done, i - 1)
                    V.tensor_tensor(seg[:, i % 2], k.ps[:, 2 + i % 2, :].rearrange("p (r l) -> p r l", r=R), bcast(tri[:, 1, :], 1, R),
                                    ALU.add).then_inc(seg_done, 1)
                    if i >= 2:
                        dve.wait_ge(back, i - 1)
                    V.tensor_tensor(Xd[:, i % 2, :].rearrange("p (r d) -> p r d", r=R), X[:, ch, hs], bcast(dte[:, ch, hs], 2, 64),
                                    ALU.mult).then_inc(xd_done, 1)
                if 0 <= j < N:
                    dve.wait_ge(dec_done, j + 1)
                    if j >= 2:
                        dve.wait_ge(back, j - 1)
                    V.tensor_tensor(M[:, j % 2], seg[:, j % 2], bcast(k.ps[:, j % 2, 0:P], 1, R), ALU.mult).then_inc(m_done, 1)
                if j >= 1:
                    v = j - 1
                    ch, g = units[v]
                    hs = slice(g * R, (g + 1) * R)
                    dve.wait_ge(back, v + 1)
                    y = yt[:, v % 2, :].rearrange("p (r d) -> p r d", r=R)
                    diag = k.ps[:, 4 + v % 2, 0:256].rearrange("p (r d) -> p r d", r=R)
                    link(V.tensor_tensor(xh[:, ch, hs], xh[:, ch, hs], bcast(par[:, 2, hs], 2, 64), ALU.mult))
                    link(V.tensor_tensor(xh[:, ch, hs], xh[:, ch, hs], diag, ALU.add))
                    if ch:
                        off = k.ps[:, 4 + v % 2, 256:512].rearrange("p (r d) -> p r d", r=R)
                        link(V.tensor_tensor(y, off, bcast(eacs[:, ch, hs], 2, 64), ALU.mult))
                        link(V.tensor_tensor(xh[:, ch, hs], xh[:, ch, hs], y, ALU.add))
                        st = state[:, g, :].rearrange("p (r d) -> p r d", r=R)
                        link(V.tensor_tensor(st, st, bcast(etot[:, ch, hs], 2, 64), ALU.mult))
                        V.tensor_tensor(state[:, g, :], state[:, g, :], k.ps[:, 6 + v % 2, 0:256], ALU.add).then_inc(st_done, 1)
                    else:
                        V.tensor_copy(state[:, g, :], k.ps[:, 6 + v % 2, 0:256]).then_inc(st_done, 1)
                    dve.wait_ge(st_done, v + 1)
                    dve.nop().then_inc(y_out, 1)


def gate_rows(k, y, z):
    nc = k.nc
    with stage(nc, "done_dve done_pool") as (block, done_dve, done_pool):
        @block.vector
        def _(dve):
            for t in (0, 1, 2):
                nc.vector.tensor_tensor(y[:, t, :], y[:, t, :], z[:, t, :], ALU.mult).then_inc(done_dve, 1)
            dve.wait_ge(done_dve, 3)

        @block.gpsimd
        def _(pool):
            nc.gpsimd.tensor_tensor(y[:, 3, :], y[:, 3, :], z[:, 3, :], ALU.mult).then_inc(done_pool, 1)
            pool.wait_ge(done_pool, 1)


def column_of(k, row, n, out, factor=1.0):
    nc = k.nc
    with ExitStack() as c:
        raw = c.enter_context(nc.sbuf_tensor(fresh("rraw"), [max(n, 2), P], F32))
        block, landed, t_done, col_out = c.enter_context(stage(nc, "landed t_done col_out"))

        @block.sync
        def _(sp):
            sp.dma_start(raw[0:n, :], row.rearrange("(k p) -> k p", p=P)).then_inc(landed, 16)
            sp.wait_ge(landed, 16)

        @block.tensor
        def _(pe):
            pe.wait_ge(landed, 16)
            pe.transpose(k.ps[:, 0, 0:n], raw[0:n, :], k.ident[0:n, 0:n]).then_inc(t_done, 1)

        @block.vector
        def _(dve):
            dve.wait_ge(t_done, 1)
            nc.vector.tensor_scalar(out[:, 0:n], k.ps[:, 0, 0:n], factor, None, ALU.mult).then_inc(col_out, 1)
            dve.wait_ge(col_out, 1)


def diff_attention(k, qT, kT, v, bias, lam, lam_init, y):
    nc = k.nc
    with ExitStack() as c:
        sb = lambda n, s: c.enter_context(nc.sbuf_tensor(fresh(n), s, F32))
        lr = sb("lr", [P, 4, 64])
        lp = sb("lp", [P, 64])
        ld = sb("ld", [P, 2])
        nlam = sb("nlam", [P, 1])
        idle = k.ring[:].rearrange("p b (m n) -> p b m n", m=4)
        sc, pr = idle[:, :, 0:2, :], idle[:, :, 2:4, :]
        pT = sb("dpT", [P, 2, 512])
        mx, nm, ls = sb("dmx", [P, 2, 2]), sb("dnm", [P, 2, 2]), sb("dls", [P, 2, 2])
        block, in_landed, ld_done, ld_exp, s_ready, max_done, exp_done, p_ready, t_ready, t_out, o_ready, o_out, step = c.enter_context(
            stage(nc, "in_landed ld_done ld_exp s_ready max_done exp_done p_ready t_ready t_out o_ready o_out step"))
        units = [(h, t) for h in range(8) for t in range(NT)]
        N = len(units)
        W = lambda i: P * (units[i][1] + 1)

        @block.sync
        def _(sp):
            sp.dma_start(lr[:], bcast(lam, 0, P)).then_inc(in_landed, 16)
            sp.wait_ge(in_landed, 16)

        @block.tensor
        def _(pe):
            for i in range(-1, N + 2):
                if i + 1 < N:
                    n = i + 1
                    h, t = units[n]
                    if n >= 2:
                        pe.wait_ge(max_done, n - 1)
                    for m in range(2):
                        mm = pe.matmul(k.ps[:, 2 * (n % 2) + m, 0:W(n)], qT[64 * m:64 * m + 64, h, t * P:(t + 1) * P],
                                       kT[64 * m:64 * m + 64, h, 0:W(n)], start=True, stop=True)
                    mm.then_inc(s_ready, 1)
                if 1 <= i <= N:
                    u = i - 1
                    pe.wait_ge(p_ready, u + 1)
                    if u >= 2:
                        pe.wait_ge(t_out, u - 1)
                    for j in range(W(u) // P):
                        mm = pe.transpose(k.ps[:, 4 + u % 2, j * P:(j + 1) * P], pr[:, u % 2, 0, j * P:(j + 1) * P], k.ident[:])
                    mm.then_inc(t_ready, 1)
                if i >= 2:
                    u = i - 2
                    h, t = units[u]
                    pe.wait_ge(t_out, u + 1)
                    if u >= 2:
                        pe.wait_ge(o_out, u - 1)
                    chain(pe, k.ps[:, 6 + u % 2, 0:P], lambda j: pT[:, u % 2, j * P:(j + 1) * P],
                          lambda j: v[:, j, h * P:(h + 1) * P], range(t + 1)).then_inc(o_ready, 1)

        @block.scalar
        def _(act):
            act.wait_ge(ld_done, 1)
            nc.scalar.activation(ld[:], ld[:], ACT.Exp).then_inc(ld_exp, 1)
            for i in range(N + 2):
                if i < N:
                    act.wait_ge(max_done, i + 1)
                    if i >= 2:
                        act.wait_ge(t_ready, i - 1)
                    for m in range(2):
                        last = nc.scalar.activation(pr[:, i % 2, m, 0:W(i)], sc[:, i % 2, m, 0:W(i)], ACT.Exp,
                                                    bias=nm[:, i % 2, m:m + 1], accum_out=ls[:, i % 2, m:m + 1])
                    last.then_inc(exp_done, 1)
                if 1 <= i <= N:
                    u = i - 1
                    act.wait_ge(t_ready, u + 1)
                    if u >= 2:
                        act.wait_ge(o_ready, u - 1)
                    nc.scalar.copy(pT[:, u % 2, 0:W(u)], k.ps[:, 4 + u % 2, 0:W(u)]).then_inc(t_out, 1)
                if i >= 2:
                    u = i - 2
                    h, t = units[u]
                    act.wait_ge(o_ready, u + 1)
                    nc.scalar.copy(y[:, t, h * P:(h + 1) * P], k.ps[:, 6 + u % 2, 0:P]).then_inc(o_out, 1)
            act.wait_ge(o_out, N)

        @block.vector
        def _(dve):
            link = Link(dve, step)
            V = nc.vector
            dve.wait_ge(in_landed, 16)
            for m in range(2):
                link(V.tensor_tensor_reduce(lp[:], lr[:, 2 * m, :], lr[:, 2 * m + 1, :], 1.0, 0.0, ALU.mult, ALU.add, ld[:, m:m + 1]))
            dve.nop().then_inc(ld_done, 1)
            dve.wait_ge(ld_exp, 1)
            link(V.tensor_tensor(nlam[:], ld[:, 1:2], ld[:, 0:1], ALU.subtract))
            link(V.tensor_scalar(nlam[:], nlam[:], -lam_init, None, ALU.add))
            for i in range(N + 1):
                if i < N:
                    h, t = units[i]
                    b = bias[:, h, 512 - W(i):512]
                    dve.wait_ge(s_ready, i + 1)
                    if i >= 2:
                        dve.wait_ge(exp_done, i - 1)
                    for m in range(2):
                        link(V.tensor_tensor_reduce(sc[:, i % 2, m, 0:W(i)], k.ps[:, 2 * (i % 2) + m, 0:W(i)], b, 1.0, 2 * NEG,
                                                    ALU.add, ALU.max, mx[:, i % 2, m:m + 1]))
                    V.tensor_scalar(nm[:, i % 2, :], mx[:, i % 2, :], -1.0, None, ALU.mult).then_inc(max_done, 1)
                if i >= 1:
                    u = i - 1
                    dve.wait_ge(exp_done, u + 1)
                    l = ls[:, u % 2, :]
                    link(V.reciprocal(l, l))
                    link(V.tensor_tensor(l[:, 1:2], l[:, 1:2], nlam[:], ALU.mult))
                    p0, p1 = (pr[:, u % 2, m, 0:W(u)] for m in range(2))
                    link(V.tensor_scalar(p0, p0, l[:, 0:1], None, ALU.mult))
                    V.scalar_tensor_tensor(p0, p1, l[:, 1:2], p0, ALU.mult, ALU.add).then_inc(p_ready, 1)
            dve.wait_ge(p_ready, N)


def head_norm_T(k, y, nh, width, mult, scale, out):
    nc = k.nc
    idle = k.ring[:].rearrange("p b n -> p (b n)")[:, 0:NT * D].rearrange("p (t n) -> p t n", t=NT)
    with ExitStack() as c:
        ms = c.enter_context(nc.sbuf_tensor(fresh("ms_h"), [P, NT, nh], F32))
        block, sq_done, ms_done, root_done, y_done, t_done, out_act, step = c.enter_context(
            stage(nc, "sq_done ms_done root_done y_done t_done out_act step"))
        nt = nh * width // P

        @block.scalar
        def _(act):
            for t in range(NT):
                last = nc.scalar.activation(idle[:, t, 0:nh * width], y[:, t, :], ACT.Square)
            last.then_inc(sq_done, 1)
            act.wait_ge(ms_done, 1)
            nc.scalar.activation(ms[:], ms[:], ACT.Sqrt).then_inc(root_done, 1)
            for q in range(nt):
                act.wait_ge(t_done, q + 1)
                if scale is None:
                    nc.scalar.copy(out[0][:, q, :], k.ps[:, q, :]).then_inc(out_act, 1)
                else:
                    nc.scalar.activation(out[0][:, q, :], k.ps[:, q, :], ACT.Copy, scale=scale).then_inc(out_act, 1)
            act.wait_ge(out_act, nt)

        @block.vector
        def _(dve):
            link = Link(dve, step)
            V = nc.vector
            dve.wait_ge(sq_done, 1)
            for t in range(NT):
                link(V.tensor_reduce(ms[:, t, :], idle[:, t, :].rearrange("p (h d) -> p h d", d=width), AX, ALU.add))
            V.tensor_scalar(ms[:], ms[:], 1.0 / width, RMS_EPS, ALU.mult, ALU.add).then_inc(ms_done, 1)
            dve.wait_ge(root_done, 1)
            link(V.reciprocal(ms[:], ms[:]))
            for t in range(NT):
                yv = y[:, t, :].rearrange("p (h d) -> p h d", d=width)
                link(V.tensor_tensor(yv, yv, bcast(ms[:, t, :], 2, width), ALU.mult))
                if mult is not None:
                    link(V.tensor_tensor(y[:, t, :], y[:, t, :], mult[:, t, :], ALU.mult))
            dve.nop().then_inc(y_done, 1)
            for q in range(nt):
                dve.wait_ge(out_act, q + 1)
                low, high = out[1][:, q, :], out[0][:, q, :].bitcast(F32)
                if scale is None:
                    link(V.tensor_tensor(low, k.ps[:, q, :], high, ALU.subtract))
                else:
                    link(V.scalar_tensor_tensor(low, k.ps[:, q, :], scale, high, ALU.mult, ALU.subtract))

        @block.tensor
        def _(pe):
            pe.wait_ge(y_done, 1)
            for q in range(nt):
                for t in range(NT):
                    mm = pe.transpose(k.ps[:, q, t * P:(t + 1) * P], y[:, t, q * P:(q + 1) * P], k.ident[:])
                mm.then_inc(t_done, 1)


def transposed(k, src, nt, out, low=None):
    nc = k.nc
    with stage(nc, "t_done out_act out_dve") as (block, t_done, out_act, out_dve):
        @block.tensor
        def _(pe):
            for q in range(nt):
                for t in range(NT):
                    mm = pe.transpose(k.ps[:, q, t * P:(t + 1) * P], src(t, q), k.ident[:])
                mm.then_inc(t_done, 1)

        @block.scalar
        def _(act):
            for q in range(nt):
                act.wait_ge(t_done, q + 1)
                nc.scalar.copy(out[:, q, :], k.ps[:, q, :]).then_inc(out_act, 1)
            act.wait_ge(out_act, nt)

        @block.vector
        def _(dve):
            if low is not None:
                for q in range(nt):
                    dve.wait_ge(out_act, q + 1)
                    nc.vector.tensor_tensor(low[:, q, :], k.ps[:, q, :], out[:, q, :].bitcast(F32), ALU.subtract).then_inc(out_dve, 1)
                dve.wait_ge(out_dve, nt)


def even_mixer(k, h, hT, y):
    nc, A = k.nc, k.A
    w = A["e_w_in_2"][0].rearrange("(k p) n -> p k n", p=P)
    wo = A["e_w_out_2"][0].rearrange("(k p) n -> p k n", p=P)
    with ExitStack() as m:
        yd = m.enter_context(nc.sbuf_tensor(fresh("y_diff"), [P, NT, D], F32))
        dn = m.enter_context(nc.sbuf_tensor(fresh("dn"), [P, 1], F32))
        lam_init = 0.8 - 0.6 * math.exp(-0.3 * 0)
        with ExitStack() as c:
            sb = lambda n, s: c.enter_context(nc.sbuf_tensor(fresh(n), s, F32))
            qT, kT, v = sb("qT", [P, 8, S]), sb("kT", [P, 8, S]), sb("v_tok", [P, NT, D])
            plan = [(3088 + 512 * s, 512, "feature", HD ** -0.5, [qT[:, 4 * s + j, :] for j in range(4)]) for s in range(2)]
            plan += [(4112 + 512 * s, 512, "feature", 1.0, [kT[:, 4 * s + j, :] for j in range(4)]) for s in range(2)]
            plan += [(5136 + 512 * s, 512, "token", 1.0, [v[:, t, 512 * s:512 * (s + 1)] for t in range(NT)]) for s in range(2)]
            bias = sb("bias", [P, 8, 512])
            project(k, w, hT, plan, loads=bias_loads(k, bias, 0))
            diff_attention(k, qT, kT, v, bias, A["e_lambda_2"][0], lam_init, yd)
        column_of(k, A["e_diff_norm_2"][0], 1, dn, 1.0 - lam_init)
        ydT = pair_of(nc, m, "y_diffT", [P, KD, S])
        head_norm_T(k, yd, 8, P, None, dn[:, 0:1], ydT)
        out_projection(k, wo[:, KD:2 * KD, :], ydT, KD, y, True)
    with ExitStack() as c:
        sb = lambda n, s: c.enter_context(nc.sbuf_tensor(fresh(n), s, F32))
        T = {"xh": sb("xh", [P, NT, D]), "dt": sb("dt", [P, NT, SSD_HEADS])}
        z = sb("z", [P, NT, D])
        nw = sb("nw", [P, KD])
        with ExitStack() as d:
            xbc = d.enter_context(nc.sbuf_tensor(fresh("xbcT"), [P, 16, S + 3], F32))
            T["Bt"] = d.enter_context(nc.sbuf_tensor(fresh("B_tok"), [P, NT, SSD_GROUPS, P], F32))
            plan = [(1024 + 512 * s, 512, "feature", 1.0, [xbc[:, 4 * s + j, 3:3 + S] for j in range(4)]) for s in range(4)]
            plan += [(512 * s, 512, "token", "silu", [z[:, t, 512 * s:512 * (s + 1)] for t in range(NT)]) for s in range(2)]
            plan += [(3072, 16, "token", 1.0, [T["dt"][:, t, :] for t in range(NT)])]
            project(k, w, hT, plan)
            h.close()
            convolution(k, xbc, T)
            ssd(k, xbc, T)
        gate_rows(k, T["xh"], z)
        column_of(k, A["e_ssd_norm_2"][0], KD, nw)
        ysT = pair_of(nc, c, "y_ssdT", [P, KD, S])
        norm_to_hT(k, ysT, True, RMS_EPS, nw, None, src=T["xh"])
        out_projection(k, wo[:, 0:KD, :], ysT, KD, y, False)


def retention_inputs(k, T):
    nc = k.nc
    H = RET_HEADS
    idle = k.ring[:].rearrange("p b n -> p (b n)")
    ro = [idle[:, i * 2048:(i + 1) * 2048].rearrange("p (t h e j) -> p t h e j", t=NT, h=H, e=2) for i in range(2)]
    with ExitStack() as c:
        sb = lambda n, s: c.enter_context(nc.sbuf_tensor(fresh(n), s, F32))
        t1 = sb("t1r", [P, NT, H, 64])
        cs = sb("cs2", [P, 2, NT, 64])
        xi = sb("xi", [P, H, P])
        zeta = sb("zeta", [P, H])
        block, in_landed, ro_done, t_done, out_act, x_done, step = c.enter_context(
            stage(nc, "in_landed ro_done t_done out_act x_done step"))

        @block.sync
        def _(sp):
            for dst, n in ((cs, "rope2"), (xi, "ret_xi"), (zeta, "ret_zeta")):
                sp.dma_start(dst[:], k.K[n]).then_inc(in_landed, 16)
            sp.wait_ge(in_landed, 48)

        @block.vector
        def _(dve):
            link = Link(dve, step)
            V = nc.vector
            dve.wait_ge(in_landed, 48)
            for i, n in enumerate(("rq", "rk")):
                for t in range(NT):
                    x = T[n][:, t, :].rearrange("p (h e j) -> p h e j", h=H, e=2)
                    o, cos, sin, tt = ro[i][:, t], bcast(cs[:, 0, t, :], 1, H), bcast(cs[:, 1, t, :], 1, H), t1[:, t]
                    link(V.tensor_tensor(o[:, :, 0, :], x[:, :, 0, :], cos, ALU.mult))
                    link(V.tensor_tensor(tt, x[:, :, 1, :], sin, ALU.mult))
                    link(V.tensor_tensor(o[:, :, 0, :], o[:, :, 0, :], tt, ALU.subtract))
                    link(V.tensor_tensor(o[:, :, 1, :], x[:, :, 0, :], sin, ALU.mult))
                    link(V.tensor_tensor(tt, x[:, :, 1, :], cos, ALU.mult))
                    link(V.tensor_tensor(o[:, :, 1, :], o[:, :, 1, :], tt, ALU.add))
                dve.nop().then_inc(ro_done, 1)
            for h in range(H):
                dve.wait_ge(out_act, h + 1)
                nc.vector.tensor_tensor(T["QxT"][:, h, :].rearrange("p (t l) -> p t l", t=NT), k.ps[:, h, :].rearrange("p (t l) -> p t l", t=NT),
                                        bcast(xi[:, h, :], 1, NT), ALU.mult).then_inc(x_done, 1)
                kz = T["rk"][:].rearrange("p t (h d) -> p t h d", h=H)[:, :, h, :]
                link(V.tensor_scalar(kz, ro[1][:, :, h].rearrange("p t e j -> p t (e j)"), zeta[:, h:h + 1], None, ALU.mult))
            dve.wait_ge(x_done, H)

        @block.scalar
        def _(act):
            for q in range(2 * H):
                act.wait_ge(t_done, q + 1)
                nc.scalar.copy((T["QT"] if q < H else T["KT"])[:, q % H, :], k.ps[:, q, :]).then_inc(out_act, 1)
            act.wait_ge(out_act, 2 * H)

        @block.tensor
        def _(pe):
            for i in range(2):
                pe.wait_ge(ro_done, i + 1)
                for h in range(H):
                    for t in range(NT):
                        mm = pe.transpose(k.ps[:, 4 * i + h, t * P:(t + 1) * P], ro[i][:, t, h].rearrange("p e j -> p (e j)"), k.ident[:])
                    mm.then_inc(t_done, 1)


def retention(k, T, y):
    nc = k.nc
    H = RET_HEADS
    with ExitStack() as c:
        sb = lambda n, s: c.enter_context(nc.sbuf_tensor(fresh(n), s, F32))
        dec = sb("dec", [P, H, P])
        sT = sb("sT", [P, 2, P])
        state = sb("rstate", [P, H, RET_V])
        block, in_landed, front, s_done, back, y_out, st_done, step = c.enter_context(
            stage(nc, "in_landed front s_done back y_out st_done step"))
        units = [(ch, h) for ch in range(NT) for h in range(H)]
        N = len(units)

        @block.sync
        def _(sp):
            sp.dma_start(dec[:], k.K["ret_decay"]).then_inc(in_landed, 16)
            sp.wait_ge(in_landed, 16)

        @block.tensor
        def _(pe):
            for i in range(N + 1):
                if i < N:
                    ch, h = units[i]
                    if i >= 2:
                        pe.wait_ge(s_done, i - 1)
                    at = slice(ch * P, (ch + 1) * P)
                    pe.matmul(k.ps[:, i % 2, 0:P], T["KT"][:, h, at], T["QT"][:, h, at], start=True, stop=True).then_inc(front, 1)
                if i >= 1:
                    v = i - 1
                    ch, h = units[v]
                    at, vv = slice(ch * P, (ch + 1) * P), T["rv"][:, ch, h * RET_V:(h + 1) * RET_V]
                    pe.wait_ge(s_done, v + 1)
                    if v >= 2:
                        pe.wait_ge(y_out, v - 1)
                    if v >= H:
                        pe.wait_ge(st_done, v - H + 1)
                    pe.matmul(k.ps[:, 2 + v % 2, 0:RET_V], sT[:, v % 2, :], vv, start=True, stop=ch == 0)
                    if ch:
                        pe.matmul(k.ps[:, 2 + v % 2, 0:RET_V], T["QxT"][:, h, at], state[:, h, :], start=False, stop=True)
                    pe.matmul(k.ps[:, 4 + v % 2, 0:RET_V], T["rk"][:, ch, h * P:(h + 1) * P], vv, start=True, stop=True).then_inc(back, 1)

        @block.vector
        def _(dve):
            V = nc.vector
            dve.wait_ge(in_landed, 16)
            for i in range(N + 1):
                if i < N:
                    ch, h = units[i]
                    dve.wait_ge(front, i + 1)
                    if i >= 2:
                        dve.wait_ge(back, i - 1)
                    V.tensor_tensor(sT[:, i % 2, :], k.ps[:, i % 2, 0:P], dec[:, h, :], ALU.mult).then_inc(s_done, 1)
                if i >= 1:
                    v = i - 1
                    ch, h = units[v]
                    dve.wait_ge(back, v + 1)
                    new = k.ps[:, 4 + v % 2, 0:RET_V]
                    if ch:
                        dve.wait_ge(st_done, v - H + 1)
                        V.scalar_tensor_tensor(state[:, h, :], state[:, h, :], RET_STATE_DECAY[h], new, ALU.mult, ALU.add).then_inc(st_done, 1)
                    else:
                        V.tensor_copy(state[:, h, :], new).then_inc(st_done, 1)
                    dve.wait_ge(st_done, v + 1)
                    V.tensor_copy(y[:, ch, h * RET_V:(h + 1) * RET_V], k.ps[:, 2 + v % 2, 0:RET_V]).then_inc(y_out, 1)
            dve.wait_ge(y_out, N)


def window_bias(k, sw, sink):
    nc = k.nc
    with ExitStack() as c:
        wm = c.enter_context(nc.sbuf_tensor(fresh("wm"), [P, P], F32))
        block, in_landed, done = c.enter_context(stage(nc, "in_landed done"))

        @block.sync
        def _(sp):
            sp.dma_start(wm[:], k.K["win_mask"]).then_inc(in_landed, 16)
            sp.dma_start(sink[:], bcast(k.A["o_sinks_2"][0], 0, P)).then_inc(in_landed, 16)
            sp.wait_ge(in_landed, 32)

        @block.vector
        def _(dve):
            dve.wait_ge(in_landed, 32)
            nc.vector.tensor_tensor(sw[:, :, 0:P], sw[:, :, 0:P], bcast(wm[:], 1, 8), ALU.add).then_inc(done, 1)
            dve.wait_ge(done, 1)


def odd_mixer(k, h, hT, y):
    nc, A = k.nc, k.A
    w = A["o_w_in_2"][0].rearrange("(k p) n -> p k n", p=P)
    wo = A["o_w_out_2"][0].rearrange("(k p) n -> p k n", p=P)
    with ExitStack() as m:
        sb = lambda n, s: m.enter_context(nc.sbuf_tensor(fresh(n), s, F32))
        sqT, skv, sw = sb("sqT", [P, 4, S]), sb("skv", [P, NT, 256]), sb("sw", [P, 8, 256])
        with ExitStack() as c:
            sc = lambda n, s: c.enter_context(nc.sbuf_tensor(fresh(n), s, F32))
            T = {n: sc(n, s) for n, s in (("rq", [P, NT, 512]), ("rk", [P, NT, 512]), ("rv", [P, NT, D]), ("rg", [P, NT, D]))}
            half = lambda t, s: [T[t][:, j, 512 * s:512 * (s + 1)] for j in range(NT)]
            plan = [(0, 512, "token", 1.0, half("rq", 0)), (512, 512, "token", 1.0, half("rk", 0)),
                    (1024, 512, "token", 1.0, half("rv", 0)), (1536, 512, "token", 1.0, half("rv", 1)),
                    (2048, 512, "token", "silu", half("rg", 0)), (2560, 512, "token", "silu", half("rg", 1)),
                    (3072, 512, "feature", HD ** -0.5, [sqT[:, j, :] for j in range(4)]),
                    (3584, 256, "token", 1.0, [skv[:, j, :] for j in range(NT)])]
            project(k, w, hT, plan, loads=bias_loads(k, sw, 256))
            h.close()
            yr = sc("y_ret", [P, NT, D])
            with ExitStack() as d:
                for n in ("QT", "QxT", "KT"):
                    T[n] = d.enter_context(nc.sbuf_tensor(fresh(n), [P, RET_HEADS, S], F32))
                retention_inputs(k, T)
                retention(k, T, yr)
            yrT = pair_of(nc, c, "y_retT", [P, KD, S])
            head_norm_T(k, yr, RET_HEADS, RET_V, T["rg"], None, yrT)
            out_projection(k, wo[:, 0:KD, :], yrT, KD, y, True)
        with ExitStack() as c:
            sc = lambda n, s: c.enter_context(nc.sbuf_tensor(fresh(n), s, F32))
            k2, kT, so, sink = sc("k2", [P, NT, 4, HD]), sc("skT", [P, 2, S]), sc("so", [P, NT, 512]), sc("sink", [P, 8])
            soT = pair_of(nc, c, "soT", [P, 4, S])
            window_bias(k, sw, sink)
            twice(k, skv, k2)
            transposed(k, lambda t, q: k2[:, t, 2 * q:2 * q + 2, :].rearrange("p h d -> p (h d)"), 2, kT)
            units = []
            for h in range(8):
                p0, g = 64 * (h % 2), h // 4
                for t in range(NT):
                    a = max(0, t - 1)
                    units.append(dict(q=sqT[p0:p0 + 64, h // 2, t * P:(t + 1) * P], k=kT[p0:p0 + 64, g, a * P:(t + 1) * P],
                                      bias=sw[:, h, 0 if t else P:256], sink=sink[:, h:h + 1],
                                      v=[skv[:, j, P + HD * g:P + HD * (g + 1)] for j in range(a, t + 1)],
                                      out=so[:, t, h * HD:(h + 1) * HD]))
            attention(k, units)
            transposed(k, lambda t, q: so[:, t, q * P:(q + 1) * P], 4, soT[0], soT[1])
            out_projection(k, wo[:, KD:KD + 4, :], soT, 4, y, False)


def twice(k, skv, k2):
    nc = k.nc
    with stage(nc, "done spare") as (block, done, _s):
        @block.vector
        def _(dve):
            for t in range(NT):
                for g in range(2):
                    nc.vector.tensor_copy(k2[:, t, 2 * g:2 * g + 2, :], bcast(skv[:, t, g * HD:(g + 1) * HD], 1, 2)).then_inc(done, 1)
            dve.wait_ge(done, 2 * NT)


def second_block(k, out):
    nc, A = k.nc, k.A
    mid = k.scratch[2 * S * D:3 * S * D]
    with ExitStack() as c:
        sb = lambda n, s: c.enter_context(nc.sbuf_tensor(fresh(n), s, F32))
        grow, y = sb("grow", [P, D]), sb("y", [P, NT, D])
        relative_bias(k, mid.rearrange("(t p d) -> p t d", p=P, d=D))
        kp = lambda ap: ap.rearrange("(k p) n -> p k n", p=P)
        for layer in range(DEPTH):
            for half in range(2):
                mod = (k.sums[2 * layer + half][:, 0:24 * P], A["mod_b_2"][layer, half], 24, k.mod, (8,),
                       A["norm_gains_2"][layer, 2 * half:2 * half + 2], [(16, grow)])
                with ExitStack() as h:
                    hT = pair_of(nc, h, "hT", [P, KD, S], side="right")
                    norm_to_hT(k, hT, True, RMS_EPS, k.mod[:, 8:16], k.mod[:, 0:8], mod=mod)
                    if half:
                        mlp(k, kp(A["mlp_w1_2"][layer]), kp(A["mlp_w2_2"][layer]), hT, y)
                    elif layer % 2 == 0:
                        even_mixer(k, h, hT, y)
                    else:
                        odd_mixer(k, h, hT, y)
                last = layer == DEPTH - 1 and half == 1
                add_normed(k, y, grow, out[0].rearrange("(t p) d -> p t d", p=P) if last else None)


_INS = ["x", "c", "w_ada", "b_ada", "w_in", "q_norm_g", "k_norm_g", "w_branch_a", "w_branch_b", "w_out", "ln1_g", "ln1_b",
        "w_router", "router_bias", "w_exp_gate", "w_exp_up", "w_exp_down", "ln2_g", "ln2_b", "c_2", "rel_bias_2",
        "norm_gains_2", "mod_w_2", "mod_b_2", "mlp_w1_2", "mlp_w2_2", "e_w_in_2", "e_conv_w_2", "e_conv_b_2",
        "e_dt_bias_2", "e_A_log_2", "e_D_2", "e_ssd_norm_2", "e_lambda_2", "e_diff_norm_2", "e_w_out_2", "o_w_in_2",
        "o_sinks_2", "o_w_out_2"]


def build(nc, A, K, out):
    with ExitStack() as c:
        k = Core(nc, c, A, K)
        first_block(k)
        second_block(k, out)


def kernel(**inputs):
    import numpy as _np
    import concourse.bacc as _bacc
    from concourse import mybir as _mybir
    from concourse.bass_utils import run_bass_kernel_spmd as _run

    nc = _bacc.Bacc("TRN2", target_bir_lowering=False, num_devices=1)
    arrays, args, consts = {}, {}, {}
    for name in _INS:
        a = _np.ascontiguousarray(inputs[name])
        arrays[f"in_{name}_dram"] = a
        args[name] = nc.dram_tensor(f"in_{name}_dram", a.shape, _mybir.dt.from_np(a.dtype), kind="ExternalInput").ap()
    for name, a in constants().items():
        arrays[f"const_{name}_dram"] = a
        consts[name] = nc.dram_tensor(f"const_{name}_dram", a.shape, _mybir.dt.from_np(a.dtype), kind="ExternalInput").ap()
    out = nc.dram_tensor("out_0_dram", (1, S, D), _mybir.dt.float32, kind="ExternalOutput").ap()
    build(nc, args, consts, out)
    r = _run(nc, [arrays], core_ids=[0])
    return r.results[0]["out_0_dram"]
```

```python
import itertools
import math
from contextlib import ExitStack, contextmanager

import numpy as np
import concourse.bass as bass
from concourse import mybir

F32 = mybir.dt.float32
F32R = mybir.dt.float32r
ALU = mybir.AluOpType
ACT = mybir.ActivationFunctionType
AX = mybir.AxisListType.X

P = 128
S = 512
NT = S // P
D = 1024
KD = D // P
DEPTH = 2
HD = 64
A_HEADS, A_KV = 8, 2
B_HEADS = 12
BG = 4
REACH = 64
CLS = 4
N_EXP, EPG, D_EXP = 16, 4, 256
ALPHA = (2.0 * DEPTH) ** 0.25
NEG = -1.0e30
LN_EPS, RMS_EPS = 1e-5, 1e-6
HALF = 2048
C_GATE, C_QKD, C_VD = 3072, 768, 2304
SSD_HEADS, SSD_GROUPS, SSD_STATE = 16, 4, 128
RET_HEADS, RET_V = 4, 256
BIAS_W = 640


_serial = itertools.count()


def fresh(name):
    return f"{name}_{next(_serial)}"


class Link:

    def __init__(self, eng, sem):
        self.eng, self.sem, self.n, self.base = eng, sem, 0, 0

    def __call__(self, ins):
        self.n += 1
        ins.then_inc(self.sem, 1)
        self.eng.wait_ge(self.sem, self.base + self.n)


@contextmanager
def stage(nc, names):
    nc.reset_free_semaphores(sorted(nc.free_semaphores))
    with ExitStack() as c:
        sems = [c.enter_context(nc.semaphore(fresh(n))) for n in names.split()]
        with nc.Block() as block:
            yield (block, *sems)
        nums = sorted(s.num for s in sems)
        assert nums == list(range(nums[0], nums[-1] + 1))
        nc.multi_engine_barrier(nc.engines, sems_to_clear=range(nums[0], nums[-1] + 1))


def bcast(ap, axis, n):
    u = ap.unsqueeze(axis)
    return u.to_broadcast([n if i == axis else d for i, d in enumerate(u.shape)])


def chain(pe, out, lhs, rhs, ks, first=True, last=True):
    for i, k in enumerate(ks):
        mm = pe.matmul(out, lhs(k), rhs(k), start=first and i == 0, stop=last and i == len(ks) - 1)
    return mm


def chain3(pe, out, lhs, rhs, ks, first=True, last=True):
    n = 0
    for k in ks:
        for a, b in ((0, 0), (0, 1), (1, 0)):
            n += 1
            mm = pe.matmul(out, lhs(a, k), rhs(b, k), start=first and n == 1, stop=last and n == 3 * len(ks))
    return mm


def warm_up(k, pe, bank, n=12):
    for _ in range(n):
        pe.matmul(k.ps[:, bank, 0:P], k.ident[:], k.ident[:], start=True, stop=True)


class Weights:

    NAMES = "half0_landed half1_landed high_done low_done half_read"

    def __init__(self, k, sems):
        self.k = k
        self.landed, (self.high, self.low, self.read) = sems[0:2], sems[2:5]

    def load(self, sp, u, i, pairs):
        sp.wait_ge(self.low, 2 * u + i + 1)
        for dst, src in pairs:
            sp.dma_start(dst, src).then_inc(self.landed[i], 16)

    def split_high(self, act, u, i, dmas, words=HALF):
        act.wait_ge(self.landed[i], dmas)
        act.wait_ge(self.read, 2 * u + i + 1)
        self.k.nc.scalar.copy(self.k.parts[0][:, i, 0:words], self.k.ring[:, i, 0:words]).then_inc(self.high, 1)

    def start_low(self, pool):
        pool.nop().then_inc(self.low, 2)

    def split_low(self, pool, u, i, words=HALF):
        pool.wait_ge(self.high, 2 * u + i + 1)
        self.k.nc.gpsimd.tensor_tensor(self.k.parts[1][:, i, 0:words], self.k.ring[:, i, 0:words],
                                       self.k.parts[0][:, i, 0:words].bitcast(F32), ALU.subtract).then_inc(self.low, 1)

    def start_read(self, pe):
        pe.nop().then_inc(self.read, 2)
        warm_up(self.k, pe, 0, 16)

    def high_ready(self, pe, u, i):
        pe.wait_ge(self.high, 2 * u + i + 1)

    def low_ready(self, pe, u, i):
        pe.wait_ge(self.low, 2 * u + i + 3)

    def done(self, eng, u, i):
        eng.wait_ge(self.read, 2 * u + i + 3)

    def raw(self, i, kt, n):
        return self.k.ring[:, i, 0:kt * n].rearrange("p (k n) -> p k n", k=kt)

    def part(self, a, i, kt, n):
        return self.k.parts[a][:, i, 0:kt * n].rearrange("p (k n) -> p k n", k=kt)


def pair_of(nc, c, name, shape, side=None):
    return tuple(c.enter_context(nc.sbuf_tensor(fresh(name + e), shape, F32R, side=side)) for e in ("_hi", "_lo"))


def constants():
    f = np.float32
    out = {"ident": np.eye(P, dtype=f)}
    tok = np.arange(P)[:, None] * CLS + np.arange(CLS)[None, :]
    inv = (f(10000.0) ** (-np.arange(0, 32, 2, dtype=f) / f(32))).astype(f)
    row, col = (tok // 64).astype(f), (tok % 64).astype(f)
    ang = np.concatenate([row[..., None] * inv, col[..., None] * inv], -1).astype(f)
    out["rope1"] = np.stack([np.cos(ang), np.sin(ang)], 1).astype(f)
    slope = np.exp2(-8.0 * np.arange(1, B_HEADS + 1) / B_HEADS).astype(f)
    p, c = np.arange(P)[:, None], np.arange(256)[None, :]
    dist = np.abs(p - (c - REACH))
    band = np.zeros((P, 3, BG, 256), f)
    for e in range(3):
        ok = (dist <= REACH) & ~((e == 0) & (c < REACH)) & ~((e == 2) & (c >= P + REACH))
        for h in range(BG):
            band[:, e, h] = np.where(ok, -slope[h] * dist.astype(f), f(NEG))
    out["bias_band"] = band
    j = np.arange(P)[None, :]
    d = np.abs(p - j)
    cls = np.zeros((P, 2, BG, P), f)
    for g, ok in enumerate((d <= REACH, d % CLS == 0)):
        for h in range(BG):
            cls[:, g, h] = np.where(ok, -slope[BG * (g + 1) + h] * (CLS * d).astype(f), f(NEG))
    out["bias_class"] = cls
    out["before"] = np.broadcast_to((j[:, :4] < np.arange(4)[:, None]).astype(f), (P, 4, 4)).copy()
    out["causal"] = np.stack([(p <= j).astype(f), np.where(p <= j, f(0), f(NEG))], 1).astype(f)
    dd = 511 - np.arange(BIAS_W)
    n = np.maximum(dd, 0)
    logd = np.log(np.maximum(n, 1).astype(f) / f(16)).astype(f)
    large = 16 + (logd / f(math.log(8.0)) * f(16)).astype(f).astype(np.int32)
    bucket = np.where(n < 16, n, np.minimum(large, 31))
    hot = np.zeros((33, BIAS_W), f)
    hot[np.where(dd >= 0, bucket, 32), np.arange(BIAS_W)] = 1
    out["bucket_hot"] = hot
    pos = np.arange(S, dtype=f)
    inv = (f(10000.0) ** (-np.arange(64, dtype=f) / f(64))).astype(f)
    ang = (pos[:, None] * inv[None]).astype(f).reshape(NT, P, 64).transpose(1, 0, 2)
    out["rope2"] = np.stack([np.cos(ang), np.sin(ang)], 1).astype(f)
    lg = np.log(1.0 - 2.0 ** (-5.0 - np.arange(RET_HEADS, dtype=f))).astype(f)
    kscale = 128.0 ** -0.5
    dec = np.zeros((P, RET_HEADS, P), f)
    for h in range(RET_HEADS):
        dec[:, h] = np.where(j >= p, np.exp(np.maximum(j - p, 0) * lg[h]) * kscale, 0)
    out["ret_decay"] = dec
    xi = np.exp((np.arange(P) + 1.0)[None] * lg[:, None]).astype(f)
    out["ret_xi"] = np.broadcast_to(xi, (P, RET_HEADS, P)).copy()
    out["ret_zeta"] = (np.exp((P - 1 - np.arange(P))[:, None] * lg[None]) * kscale).astype(f)
    out["win_mask"] = np.where(j <= p, f(NEG), f(0)).astype(f)
    return out


RET_STATE_DECAY = [float(math.exp(P * math.log(1.0 - 2.0 ** (-5.0 - h)))) for h in range(RET_HEADS)]


class Core:

    def __init__(self, nc, c, A, K):
        self.nc, self.A, self.K = nc, A, K
        sb = lambda n, s: c.enter_context(nc.sbuf_tensor(fresh(n), s, F32))
        self.x = sb("x_res", [P, NT, D])
        self.ring = sb("ring", [P, 2, HALF])
        self.parts = tuple(c.enter_context(nc.sbuf_tensor(n, [P, 2, HALF], F32R)) for n in ("w_hi", "w_lo"))
        self.ident = sb("ident_sb", [P, P])
        self.mod = sb("mod", [P, 48])
        self.cond = sb("cond", [P, 2, KD])
        self.ps = c.enter_context(nc.psum_tensor("ps", [P, 8, 512], F32))
        self.sums = nc.dram_tensor("mod_sums", [6, P, 32 * P], F32, kind="Internal").ap()
        self.scratch = nc.dram_tensor("scratch", [4 * S * D], F32, kind="Internal").ap()


def split_products(pe, W, u, i, outs, weight, other, ks, weight_left, first=True, last=True):
    for part, others in ((0, (0, 1)), (1, (0,))):
        (W.low_ready if part else W.high_ready)(pe, u, i)
        for m, out in enumerate(outs):
            for q in ks:
                for o in others:
                    a, b = weight(part, m, q), other(o, m, q)
                    mm = pe.matmul(out, a if weight_left else b, b if weight_left else a,
                                   start=first and part == 0 and q == ks[0] and o == 0, stop=last and part == 1 and q == ks[-1])
    return mm


def feature_unit(k, pe, W, hT, u, b):
    for i in range(2):
        wv = [W.part(a, i, KD, 256) for a in range(2)]
        split_products(pe, W, u, i, [k.ps[:, 4 * b + 2 * i + m, :] for m in range(2)], lambda a, m, q: wv[a][:, q, m * P:(m + 1) * P],
                       lambda a, m, q: hT[a][:, q, :], range(KD), True).then_inc(W.read, 1)


def token_unit(k, pe, W, hT, u, b, n, kt=KD, before=None):
    for i in range(2):
        if before is not None:
            before(i)
        wv = [W.part(a, i, kt // 2, n) for a in range(2)]
        split_products(pe, W, u, i, [k.ps[:, 4 * b + t, 0:n] for t in range(NT)], lambda a, t, q: wv[a][:, q - kt // 2 * i, :],
                       lambda a, t, q: hT[a][:, q, t * P:(t + 1) * P], range(kt // 2 * i, kt // 2 * (i + 1)), False,
                       first=i == 0, last=i == 1).then_inc(W.read, 1)



def start_up(k, x_source, w, sums):
    nc, A = k.nc, k.A
    with ExitStack() as c:
        craw = c.enter_context(nc.sbuf_tensor(fresh("craw"), [P, 2, KD], F32))
        slots = c.enter_context(nc.sbuf_tensor(fresh("first_slots"), [P, 4, KD, 512], F32))
        acc = c.enter_context(nc.sbuf_tensor(fresh("first_acc"), [P, 4, 512], F32))
        block, in_landed, x_landed, *landed, cond_done, acc_done, stored, step = c.enter_context(
            stage(nc, "in_landed x_landed w0 w1 w2 w3 cond_done acc_done stored step"))

        @block.sync
        def _(sp):
            for i, name in enumerate(("c", "c_2")):
                sp.dma_start(craw[:, i, :], A[name].rearrange("a (k p) -> (a p) k", p=P), allow_slow_non_contiguous=True).then_inc(in_landed, 16)
            for i in range(4):
                sp.dma_start(slots[:, i], w[:, :, 512 * i:512 * (i + 1)]).then_inc(landed[i], 16)
            sp.dma_start(k.ident[:], k.K["ident"]).then_inc(x_landed, 16)
            sp.dma_start(k.x[:], x_source).then_inc(x_landed, 16)
            for i in range(4):
                sp.wait_ge(acc_done, i + 1)
                sp.dma_start(sums[:, 512 * i:512 * (i + 1)], acc[:, i, :]).then_inc(stored, 16)
            sp.wait_ge(stored, 64)
            sp.wait_ge(x_landed, 32)

        @block.scalar
        def _(act):
            act.wait_ge(in_landed, 32)
            nc.scalar.activation(k.cond[:], craw[:], ACT.Silu).then_inc(cond_done, 1)

        @block.vector
        def _(dve):
            link = Link(dve, step)
            V = nc.vector
            dve.wait_ge(cond_done, 1)
            for i in range(4):
                dve.wait_ge(landed[i], 16)
                a = acc[:, i, :]
                link(V.tensor_scalar(a, slots[:, i, 0, :], k.cond[:, 0, 0:1], None, ALU.mult))
                for q in range(1, KD):
                    ins = V.scalar_tensor_tensor(a, slots[:, i, q, :], k.cond[:, 0, q:q + 1], a, ALU.mult, ALU.add)
                    if q < KD - 1:
                        link(ins)
                ins.then_inc(acc_done, 1)


class SideModulation:

    NAMES = "side0_landed side1_landed side0_stored side1_stored side_sum side_step"

    def __init__(self, k, c, sems, which, w, dst):
        self.k, self.which, self.w, self.dst = k, which, w, dst
        self.landed, self.stored, (self.sum, self.step) = sems[0:2], sems[2:4], sems[4:6]
        self.slots = c.enter_context(k.nc.sbuf_tensor(fresh("side_slots"), [P, 2, KD, P], F32))
        self.acc = c.enter_context(k.nc.sbuf_tensor(fresh("side_acc"), [P, 2, P], F32))

    def start(self, dve):
        dve.nop().then_inc(self.sum, 2)
        for i in range(2):
            dve.nop().then_inc(self.stored[i], 16)

    def load(self, sp, s, i):
        sp.wait_ge(self.sum, s + 1)
        sp.dma_start(self.slots[:, i], self.w(s, i)).then_inc(self.landed[i], 16)

    def work(self, dve, s, i, round_):
        V, slot = self.k.nc.vector, self.slots[:, i]
        dve.wait_ge(self.landed[i], 16 * round_ + 16)
        V.tensor_tensor(slot, slot, bcast(self.k.cond[:, self.which, :], 2, P), ALU.mult).then_inc(self.step, 1)
        dve.wait_ge(self.step, s + 1)
        dve.wait_ge(self.stored[i], 16 * round_ + 16)
        V.tensor_reduce(self.acc[:, i, :], slot.rearrange("p k n -> p n k"), AX, ALU.add).then_inc(self.sum, 1)

    def store(self, eng, s, i):
        eng.wait_ge(self.sum, s + 3)
        eng.dma_start(self.dst(s, i), self.acc[:, i, :]).then_inc(self.stored[i], 16)

    def end(self, eng, n):
        for i in range(2):
            eng.wait_ge(self.stored[i], 16 * (n // 2) + 16)


class ModulationTail:

    NAMES = "b_landed sums_landed ones_done b_done sum_done mod_done"

    def __init__(self, k, c, sems, sums, b, n, out, plus_one, gains):
        sb = lambda n_, s: c.enter_context(k.nc.sbuf_tensor(fresh(n_), s, F32))
        self.k, self.sums, self.b, self.n, self.out, self.plus_one, self.gains = k, sums, b, n, out, plus_one, gains
        self.b_landed, self.landed, self.ones_done, self.b_done, self.sum_done, self.mod_done = sems
        self.acc, self.raw, self.ones, self.bcol = sb("sums", [P, n, P]), sb("braw", [n + 16, P]), sb("ones_m", [P, 1]), sb("bcol", [P, n + 16])
        self.nr = n + (16 if gains is not None else 0)

    def load(self, sp):
        n = self.n
        sp.dma_start(self.acc[:], self.sums).then_inc(self.landed, 16)
        sp.dma_start(self.raw[0:n, :], self.b.rearrange("(j p) -> j p", p=P)).then_inc(self.b_landed, 16)
        if self.gains is not None:
            sp.dma_start(self.raw[n:n + 16, :], self.gains.rearrange("g (k p) -> (g k) p", p=P)).then_inc(self.b_landed, 16)
        sp.wait_ge(self.landed, 16)

    def add_up(self, pe):
        k, nr = self.k, self.nr
        pe.wait_ge(self.b_landed, 16 if self.gains is None else 32)
        pe.transpose(k.ps[:, 7, 0:nr], self.raw[0:nr, :], k.ident[0:nr, 0:nr]).then_inc(self.b_done, 1)
        pe.wait_ge(self.landed, 16)
        pe.wait_ge(self.ones_done, 1)
        for j in range(self.n):
            mm = pe.matmul(k.ps[:, 6, j:j + 1], self.acc[:, j, :], self.ones[:], start=True, stop=True)
        mm.then_inc(self.sum_done, 1)

    def start(self, dve):
        self.k.nc.vector.memset(self.ones[:], 1.0).then_inc(self.ones_done, 1)

    def finish(self, dve, link):
        V, k, n, nr, bcol, out = self.k.nc.vector, self.k, self.n, self.nr, self.bcol, self.out
        dve.wait_ge(self.b_done, 1)
        link(V.tensor_copy(bcol[:, 0:nr], k.ps[:, 7, 0:nr]))
        for a in self.plus_one:
            link(V.tensor_scalar(bcol[:, a:a + KD], bcol[:, a:a + KD], 1.0, None, ALU.add))
        dve.wait_ge(self.sum_done, 1)
        link(V.tensor_tensor(out[:, 0:n], k.ps[:, 6, 0:n], bcol[:, 0:n], ALU.add))
        if self.gains is not None:
            link(V.tensor_tensor(out[:, 8:24], out[:, 8:24], bcol[:, n:n + 16], ALU.mult))
        dve.nop().then_inc(self.mod_done, 1)


def norm_to_hT(k, out, rms, eps, scale, shift, affine=None, store=None, src=None, mod=None):
    nc = k.nc
    src = k.x if src is None else src
    rounds = 1 if affine is None or store is not None else 2
    with ExitStack() as c:
        sb = lambda n, s: c.enter_context(nc.sbuf_tensor(fresh(n), s, F32))
        xn = k.ring[:].rearrange("p b n -> p (b n)").rearrange("p (t d) -> p t d", t=NT)
        ex, st, mv = sb("exact", [P, 4, S]), sb("stats", [P, NT, 2, 6]), sb("mv", [P, NT, 2])
        tmp, rstd, nb = (sb(n, [P, rounds, NT]) for n in ("var", "rstd", "neg_mean"))
        gb = sb("gb", [P, 2, D]) if affine is not None else None
        names = "gb_landed var_done root_done factors normed t_done high_out exact out_pool stored x_done step"
        block, gb_landed, var_done, root_done, factors, normed, t_done, high_out, exact, out_pool, stored, x_done, step, *sems = c.enter_context(
            stage(nc, names if mod is None else f"{names} {ModulationTail.NAMES}"))
        tail = ModulationTail(k, c, sems, *mod) if mod is not None else None

        @block.sync
        def _(sp):
            if tail is not None:
                tail.load(sp)
            if affine is not None:
                for i in range(2):
                    sp.dma_start(gb[:, i, :], bcast(affine[i], 0, P)).then_inc(gb_landed, 16)
                sp.wait_ge(gb_landed, 32)
            if store is not None:
                for t in range(NT):
                    sp.wait_ge(x_done, t + 1)
                    sp.dma_start(store[t], src[:, t, :]).then_inc(stored, 16)
                sp.wait_ge(stored, 16 * NT)

        @block.vector
        def _(dve):
            link = Link(dve, step)
            V = nc.vector

            def statistics(r, t):
                V.bn_stats(st[:, t, 0, :], src[:, t, 0:512])
                link(V.bn_stats(st[:, t, 1, :], src[:, t, 512:D]))
                link(V.bn_aggr(mv[:, t, :], st[:, t, :, :].rearrange("p a b -> p (a b)")))
                v = tmp[:, r, t:t + 1]
                var = mv[:, t, 1:2]
                if rms:
                    link(V.tensor_tensor(v, mv[:, t, 0:1], mv[:, t, 0:1], ALU.mult))
                    link(V.tensor_tensor(v, v, var, ALU.add))
                    var = v
                V.tensor_scalar(v, var, eps, None, ALU.add).then_inc(var_done, 1)

            def invert(r, t):
                dve.wait_ge(root_done, r * NT + t + 1)
                f = rstd[:, r, t:t + 1]
                if rms:
                    V.reciprocal(f, f).then_inc(factors, 1)
                else:
                    link(V.reciprocal(f, f))
                    V.scalar_tensor_tensor(nb[:, r, t:t + 1], mv[:, t, 0:1], -1.0, f, ALU.mult, ALU.mult).then_inc(factors, 1)

            def affine_rows(t):
                dve.wait_ge(normed, t + 1)
                x = src[:, t, :]
                link(V.tensor_tensor(x, x, gb[:, 0, :], ALU.mult))
                ins = V.tensor_tensor(x, x, gb[:, 1, :], ALU.add)
                if store is not None:
                    ins.then_inc(x_done, 1)
                else:
                    link(ins)

            if tail is not None:
                tail.start(dve)
            for r in range(rounds):
                for t in range(NT):
                    if r == 1:
                        affine_rows(t)
                    statistics(r, t)
                    if t >= 1:
                        invert(r, t - 1)
                invert(r, NT - 1)
                if r == 0 and affine is not None:
                    dve.wait_ge(gb_landed, 32)
            if store is not None:
                for t in range(NT):
                    affine_rows(t)
                return
            if tail is not None:
                tail.finish(dve, link)
            for q in range(KD):
                dve.wait_ge(high_out, q + 1)
                if q >= 4 and q % 2 == 0:
                    dve.wait_ge(out_pool, q // 2 - 1)
                ins = V.tensor_scalar(ex[:, q % 4, :], k.ps[:, q, :], scale[:, q:q + 1],
                                      shift[:, q:q + 1] if shift is not None else None,
                                      ALU.mult, ALU.add if shift is not None else ALU.bypass)
                if q % 2 == 0:
                    ins.then_inc(exact, 1)
                else:
                    link(ins)
                    link(V.tensor_tensor(out[1][:, q, :], ex[:, q % 4, :], out[0][:, q, :].bitcast(F32), ALU.subtract))

        @block.scalar
        def _(act):
            def normalise(r, t):
                act.wait_ge(factors, r * NT + t + 1)
                dst = xn[:, t, :] if r == rounds - 1 and store is None else src[:, t, :]
                if rms:
                    ins = nc.scalar.activation(dst, src[:, t, :], ACT.Copy, scale=rstd[:, r, t:t + 1])
                else:
                    ins = nc.scalar.activation(dst, src[:, t, :], ACT.Identity, scale=rstd[:, r, t:t + 1], bias=nb[:, r, t:t + 1])
                ins.then_inc(normed, 1)

            for r in range(rounds):
                for t in range(NT):
                    act.wait_ge(var_done, r * NT + t + 1)
                    nc.scalar.activation(rstd[:, r, t:t + 1], tmp[:, r, t:t + 1], ACT.Sqrt).then_inc(root_done, 1)
                    if t >= 1:
                        normalise(r, t - 1)
                normalise(r, NT - 1)
            if tail is not None:
                act.wait_ge(tail.mod_done, 1)
            if store is None:
                for q in range(KD):
                    act.wait_ge(t_done, q + 1)
                    if shift is not None:
                        ins = nc.scalar.activation(out[0][:, q, :], k.ps[:, q, :], ACT.Identity, scale=scale[:, q:q + 1], bias=shift[:, q:q + 1])
                    else:
                        ins = nc.scalar.activation(out[0][:, q, :], k.ps[:, q, :], ACT.Copy, scale=scale[:, q:q + 1])
                    ins.then_inc(high_out, 1)
                act.wait_ge(high_out, KD)

        @block.gpsimd
        def _(pool):
            if store is None:
                for q in range(0, KD, 2):
                    pool.wait_ge(exact, q // 2 + 1)
                    nc.gpsimd.tensor_tensor(out[1][:, q, :], ex[:, q % 4, :], out[0][:, q, :].bitcast(F32), ALU.subtract).then_inc(out_pool, 1)
                pool.wait_ge(out_pool, KD // 2)

        @block.tensor
        def _(pe):
            if store is None:
                def transposes(t, qs):
                    pe.wait_ge(normed, (rounds - 1) * NT + t + 1)
                    for q in qs:
                        mm = pe.transpose(k.ps[:, q, t * P:(t + 1) * P], xn[:, t, q * P:(q + 1) * P], k.ident[:])
                        if t == NT - 1:
                            mm.then_inc(t_done, 1)

                if tail is None:
                    for t in range(NT):
                        transposes(t, range(KD))
                else:
                    for t in range(NT):
                        if t == 2:
                            tail.add_up(pe)
                        transposes(t, range(6))
                    pe.wait_ge(tail.mod_done, 1)
                    for t in range(NT):
                        transposes(t, (6, 7))



def in_projection(k, w, hT, T, w_side, side_out):
    nc = k.nc
    plan = [(0, 512, "qa"), (512, 512, "kva v0")] + [(C_QKD + 512 * i, 512, "qkd") for i in range(3)] + [(C_VD + 256, 512, "vc")]
    plan += [(C_GATE + 512 * i, 512, "gate") for i in range(4)]
    with ExitStack() as c:
        v0c = T["v0c"]
        block, *sems, free_act, free_dve, step = c.enter_context(
            stage(nc, f"{Weights.NAMES} {SideModulation.NAMES} free_act free_dve step"))
        W = Weights(k, sems[0:5])
        side = SideModulation(k, c, sems[5:], 0, lambda s, i: w_side(s), lambda s, i: side_out(s))
        ST = 6 * KD
        side_tiles = lambda u: range(ST * u // len(plan), ST * (u + 1) // len(plan))

        @block.sync
        def _(sp):
            for u, (c0, n, kind) in enumerate(plan):
                for i in range(2):
                    if kind in ("qkd", "gate"):
                        W.load(sp, u, i, [(W.raw(i, KD, 256), w[:, :, c0 + 256 * i:c0 + 256 * (i + 1)])])
                    elif kind == "kva v0":
                        v, ks = W.raw(i, KD // 2, n), slice(4 * i, 4 * i + 4)
                        W.load(sp, u, i, [(v[:, :, 0:256], w[:, ks, c0:c0 + 256]), (v[:, :, 256:512], w[:, ks, C_VD:C_VD + 256])])
                    else:
                        W.load(sp, u, i, [(W.raw(i, KD // 2, n), w[:, 4 * i:4 * i + 4, c0:c0 + n])])
                for s in side_tiles(u):
                    side.load(sp, s, s % 2)

        @block.tensor
        def _(pe):
            W.start_read(pe)
            for u, (c0, n, kind) in enumerate(plan):
                if u >= 2:
                    pe.wait_ge(free_act, u - 1)
                    pe.wait_ge(free_dve, u - 1)
                if kind in ("qkd", "gate"):
                    feature_unit(k, pe, W, hT, u, u % 2)
                else:
                    token_unit(k, pe, W, hT, u, u % 2, n)

        @block.gpsimd
        def _(pool):
            W.start_low(pool)
            for u in range(len(plan)):
                for i in range(2):
                    W.split_low(pool, u, i)

        @block.scalar
        def _(act):
            for u in range(len(plan) + 1):
                if u < len(plan):
                    for i in range(2):
                        W.split_high(act, u, i, 16 * u + (32 if u else 16))
                v, kind, b = u - 1, plan[u - 1][2], (u - 1) % 2
                if u == 0:
                    for s in side_tiles(u):
                        side.store(act, s, s % 2)
                    continue
                W.done(act, v, 0 if kind == "qkd" else 1)
                for j in range(4 if kind == "gate" else 2):
                    p = k.ps[:, 4 * b + j, :]
                    if kind == "gate":
                        last = nc.scalar.activation(T["gates"][:, 4 * (v - 6) + j, :], p, ACT.Sigmoid)
                    elif kind == "qkd":
                        dst, p, mul = qkd_dst(T, 4 * (v - 2) + j, p)
                        last = nc.scalar.activation(dst, p, ACT.Copy, scale=mul)
                    elif kind == "kva v0":
                        nc.scalar.copy(T["kva"][:, j, :], p[:, 0:256])
                        last = nc.scalar.copy(v0c[:, j, :], p[:, 256:512])
                    else:
                        last = nc.scalar.copy(T[kind][:, j, :], p)
                last.then_inc(free_act, 1)
                for s in side_tiles(u) if u < len(plan) else ():
                    side.store(act, s, s % 2)
            act.wait_ge(free_act, len(plan))
            side.end(act, ST)

        @block.vector
        def _(dve):
            link = Link(dve, step)
            for j in range(4):
                link(nc.vector.memset(T["k0T"][:, j % 2, (0 if j < 2 else S + REACH):(REACH if j < 2 else S + 2 * REACH)], 0.0))
            link(nc.vector.memset(T["v0"][0:64, 0, :], 0.0))
            link(nc.vector.memset(T["v0"][64:P, 4, :], 0.0))
            side.start(dve)
            for u, (c0, n, kind) in enumerate(plan):
                for s in side_tiles(u):
                    side.work(dve, s, s % 2, s // 2)
                if kind == "gate":
                    if u:
                        dve.wait_ge(free_dve, u)
                    dve.nop().then_inc(free_dve, 1)
                    continue
                W.done(dve, u, 1)
                for j in (2, 3):
                    p = k.ps[:, 4 * (u % 2) + j, :]
                    if kind == "qkd":
                        dst, p, mul = qkd_dst(T, 4 * (u - 2) + j, p)
                        last = nc.vector.tensor_scalar(dst, p, mul, None, ALU.mult)
                    elif kind == "kva v0":
                        nc.vector.tensor_copy(T["kva"][:, j, :], p[:, 0:256])
                        last = nc.vector.tensor_copy(v0c[:, j, :], p[:, 256:512])
                    else:
                        last = nc.vector.tensor_copy(T[kind][:, j, :], p)
                last.then_inc(free_dve, 1)
            dve.wait_ge(free_dve, len(plan))


def order_v0(k, v0c, v0):
    back = k.scratch[0:S * 256]
    rows = back.rearrange("(t n) -> t n", n=256)
    return [[(back.rearrange("(i f) -> i f", i=P), v0c[:].rearrange("p r n -> p (r n)"))],
            [(v0[:, 1:4, :], rows[64:448].rearrange("(c p) n -> p c n", p=P)), (v0[64:P, 0, :], rows[0:64]), (v0[0:64, 4, :], rows[448:512])]]


def qkd_dst(T, m, p):
    if m < 2:
        dst, mul = T["q0T"][:, m, :], HD ** -0.5
    elif m < 6:
        dst, mul = T["qcT"][:, m - 2, :], HD ** -0.5
    elif m < 8:
        dst, mul = T["k0T"][:, m - 6, REACH:REACH + S], 1.0
    else:
        dst, mul = T["kcT"][:, m - 8, :], 1.0
    if m % 6 < 2:
        p = p.rearrange("p (r i) -> p i r", r=CLS)
        dst = dst.rearrange("p (i r) -> p i r", r=CLS)
    return dst, p, mul


def rope_qk(k, gq, gk, T, mod):
    nc = k.nc
    NH = A_HEADS + A_KV
    with ExitStack() as c:
        sb = lambda n, s: c.enter_context(nc.sbuf_tensor(fresh(n), s, F32))
        idle = k.ring[:].rearrange("p b n -> p (b n)")
        ro = idle[:, 0:NT * NH * HD].rearrange("p (t h d) -> p t h d", t=NT, h=NH)
        qk = idle[:, NT * NH * HD:(NT + 1) * NH * HD].rearrange("p (h d) -> p h d", h=NH)
        k2 = sb("k_twice", [P, NT, 4, HD])
        t1 = sb("t1", [P, NH, 32])
        cs = sb("cs", [P, 2, NT, 32])
        g = sb("gqk", [P, 2, HD])
        ms = sb("ms", [P, NT, NH])
        block, in_landed, sq_done, ms_done, root_done, ro_done, t_done, out_a, step, *sems = c.enter_context(
            stage(nc, f"in_landed sq_done ms_done root_done ro_done t_done out_a step {ModulationTail.NAMES}"))
        tail = ModulationTail(k, c, sems, *mod)

        @block.sync
        def _(sp):
            sp.dma_start(cs[:], k.K["rope1"]).then_inc(in_landed, 16)
            sp.dma_start(g[:, 0, :], bcast(gq, 0, P)).then_inc(in_landed, 16)
            sp.dma_start(g[:, 1, :], bcast(gk, 0, P)).then_inc(in_landed, 16)
            tail.load(sp)
            sp.wait_ge(in_landed, 48)

        @block.scalar
        def _(act):
            for t in range(NT):
                nc.scalar.activation(ro[:, t, 0:8, :].rearrange("p h d -> p (h d)"), T["qa"][:, t, :], ACT.Square)
                last = nc.scalar.activation(ro[:, t, 8:10, :].rearrange("p h d -> p (h d)"), T["kva"][:, t, 0:P], ACT.Square)
            last.then_inc(sq_done, 1)
            act.wait_ge(ms_done, 1)
            nc.scalar.activation(ms[:], ms[:], ACT.Sqrt).then_inc(root_done, 1)
            for q in range(3, 6):
                act.wait_ge(t_done, q + 1)
                dst = T["qaT"][:, 3, :] if q == 3 else T["kaT"][:, q - 4, :]
                last = nc.scalar.copy(dst, k.ps[:, q, :])
            last.then_inc(out_a, 1)
            act.wait_ge(out_a, 1)

        @block.vector
        def _(dve):
            link = Link(dve, step)
            tail.start(dve)
            dve.wait_ge(sq_done, 1)
            link(nc.vector.tensor_reduce(ms[:].rearrange("p t h -> p (t h)"), ro.rearrange("p t h d -> p (t h) d"), AX, ALU.add))
            nc.vector.tensor_scalar(ms[:], ms[:], 1.0 / HD, RMS_EPS, ALU.mult, ALU.add).then_inc(ms_done, 1)
            dve.wait_ge(root_done, 1)
            link(nc.vector.reciprocal(ms[:], ms[:]))
            dve.wait_ge(in_landed, 48)
            link(nc.vector.tensor_scalar(g[:, 0, :], g[:, 0, :], HD ** -0.5, None, ALU.mult))
            for t in range(NT):
                qv = T["qa"][:, t, :].rearrange("p (h d) -> p h d", d=HD)
                kv = T["kva"][:, t, 0:P].rearrange("p (h d) -> p h d", d=HD)
                link(nc.vector.tensor_tensor(qk[:, 0:8, :], qv, bcast(ms[:, t, 0:8], 2, HD), ALU.mult))
                link(nc.vector.tensor_tensor(qk[:, 8:10, :], kv, bcast(ms[:, t, 8:10], 2, HD), ALU.mult))
                link(nc.vector.tensor_tensor(qk[:, 0:8, :], qk[:, 0:8, :], bcast(g[:, 0, :], 1, 8), ALU.mult))
                link(nc.vector.tensor_tensor(qk[:, 8:10, :], qk[:, 8:10, :], bcast(g[:, 1, :], 1, 2), ALU.mult))
                pr = qk.rearrange("p h (j e) -> p h j e", e=2)
                po = ro[:, t].rearrange("p h (j e) -> p h j e", e=2)
                cos, sin = (bcast(cs[:, i, t, :], 1, NH) for i in (0, 1))
                link(nc.vector.tensor_tensor(po[:, :, :, 0], pr[:, :, :, 0], cos, ALU.mult))
                link(nc.vector.tensor_tensor(t1[:], pr[:, :, :, 1], sin, ALU.mult))
                link(nc.vector.tensor_tensor(po[:, :, :, 0], po[:, :, :, 0], t1[:], ALU.subtract))
                link(nc.vector.tensor_tensor(po[:, :, :, 1], pr[:, :, :, 0], sin, ALU.mult))
                link(nc.vector.tensor_tensor(t1[:], pr[:, :, :, 1], cos, ALU.mult))
                link(nc.vector.tensor_tensor(po[:, :, :, 1], po[:, :, :, 1], t1[:], ALU.add))
                link(nc.vector.tensor_copy(k2[:, t, 0:2, :], bcast(ro[:, t, 8, :], 1, 2)))
                nc.vector.tensor_copy(k2[:, t, 2:4, :], bcast(ro[:, t, 9, :], 1, 2)).then_inc(ro_done, 1)
                if t == 2:
                    tail.finish(dve, link)
            for q in range(3):
                dve.wait_ge(t_done, q + 1)
                link(nc.vector.tensor_copy(T["qaT"][:, q, :], k.ps[:, q, :]))
            dve.wait_ge(tail.mod_done, 1)

        @block.tensor
        def _(pe):
            tail.add_up(pe)
            for t in range(NT):
                pe.wait_ge(ro_done, t + 1)
                for q in range(6):
                    src = ro[:, t, 2 * q:2 * q + 2, :] if q < 4 else k2[:, t, 2 * (q - 4):2 * (q - 4) + 2, :]
                    mm = pe.transpose(k.ps[:, q, t * P:(t + 1) * P], src.rearrange("p h d -> p (h d)"), k.ident[:])
                    if t == NT - 1:
                        mm.then_inc(t_done, 1)


def attention(k, units, loads=()):
    nc = k.nc
    with ExitStack() as c:
        sb = lambda n, s: c.enter_context(nc.sbuf_tensor(fresh(n), s, F32))
        idle = k.ring[:].rearrange("p b n -> p (b n)").rearrange("p (a n) -> p a n", a=8)
        pr, sc, pT = idle[:, 0:4], idle[:, 4:6], idle[:, 6:8]
        bank = (0, 1, 6, 7)
        mx = sb("mx", [P, 4])
        nm = sb("nm", [P, 4])
        ls = sb("ls", [P, 4])
        es = sb("es", [P, 4])
        block, s_ready, max_done, exp_done, t_ready, t_out, o_ready, o_out, step, moved = c.enter_context(
            stage(nc, "s_ready max_done exp_done t_ready t_out o_ready o_out step moved"))
        N = len(units)
        W = lambda u: units[u]["k"].shape[-1]

        @block.sync
        def _(sp):
            n = 0
            for pairs in loads:
                for dst, src in pairs:
                    n += 16
                    sp.dma_start(dst, src).then_inc(moved, 16)
                sp.wait_ge(moved, n)

        @block.tensor
        def _(pe):
            warm_up(k, pe, 4)
            for i in range(-2, N + 2):
                if i + 2 < N:
                    n, u = i + 2, units[i + 2]
                    if n >= 4:
                        pe.wait_ge(exp_done, n - 3)
                    pe.matmul(k.ps[:, bank[n % 4], 0:W(n)], u["q"], u["k"], start=True, stop=True).then_inc(s_ready, 1)
                if 1 <= i <= N:
                    v = i - 1
                    pe.wait_ge(exp_done, v + 1)
                    if v >= 2:
                        pe.wait_ge(t_out, v - 1)
                    for j in range(W(v) // P):
                        mm = pe.transpose(k.ps[:, 2 + v % 2, j * P:(j + 1) * P], pr[:, v % 4, j * P:(j + 1) * P], k.ident[:])
                    mm.then_inc(t_ready, 1)
                if i >= 2:
                    v = i - 2
                    pe.wait_ge(t_out, v + 1)
                    if v >= 2:
                        pe.wait_ge(o_out, v - 1)
                    vs = units[v]["v"]
                    chain(pe, k.ps[:, 4 + v % 2, 0:vs[0].shape[-1]], lambda j: pT[:, v % 2, j * P:(j + 1) * P],
                          lambda j: vs[j], range(len(vs))).then_inc(o_ready, 1)

        @block.scalar
        def _(act):
            for i in range(N):
                u = units[i]
                act.wait_ge(max_done, i + 1)
                if i >= 4:
                    act.wait_ge(t_ready, i - 3)
                    act.wait_ge(o_out, i - 3)
                src = k.ps[:, bank[i % 4], 0:W(i)] if u.get("bias") is None else sc[:, i % 2, 0:W(i)]
                l = u["l"] if u.get("l") is not None else ls[:, i % 4:i % 4 + 1]
                if u.get("sink") is not None:
                    nc.scalar.activation(es[:, i % 4:i % 4 + 1], u["sink"], ACT.Exp, bias=nm[:, i % 4:i % 4 + 1])
                nc.scalar.activation(pr[:, i % 4, 0:W(i)], src, ACT.Exp, bias=nm[:, i % 4:i % 4 + 1],
                                     accum_out=l).then_inc(exp_done, 1)

        @block.vector
        def _(dve):
            link = Link(dve, step)
            for ahead in range(N + 3):
                i = ahead
                if i < N:
                    u = units[i]
                    dve.wait_ge(s_ready, i + 1)
                    if i >= 4:
                        dve.wait_ge(exp_done, i - 3)
                    n = nm[:, i % 4:i % 4 + 1]
                    s = k.ps[:, bank[i % 4], 0:W(i)]
                    if u.get("bias") is None:
                        nc.vector.tensor_reduce(n, s, AX, ALU.max, negate=True).then_inc(max_done, 1)
                    else:
                        m = u["m"] if u.get("m") is not None else mx[:, i % 4:i % 4 + 1]
                        if i >= 2:
                            dve.wait_ge(exp_done, i - 1)
                        link(nc.vector.tensor_tensor_reduce(sc[:, i % 2, 0:W(i)], s, u["bias"], 1.0, 2 * NEG, ALU.add, ALU.max, m))
                        if u.get("sink") is not None:
                            link(nc.vector.tensor_tensor(m, m, u["sink"], ALU.max))
                        nc.vector.tensor_scalar(n, m, -1.0, None, ALU.mult).then_inc(max_done, 1)
                i = ahead - 1
                if 1 <= i <= N:
                    v = i - 1
                    dve.wait_ge(t_ready, v + 1)
                    if v >= 2:
                        dve.wait_ge(o_ready, v - 1)
                    nc.vector.tensor_copy(pT[:, v % 2, 0:W(v)], k.ps[:, 2 + v % 2, 0:W(v)]).then_inc(t_out, 1)
                if i >= 2:
                    v = i - 2
                    dve.wait_ge(o_ready, v + 1)
                    vs = units[v]["v"]
                    po = k.ps[:, 4 + v % 2, 0:vs[0].shape[-1]]
                    if units[v].get("l") is not None:
                        nc.vector.tensor_copy(units[v]["out"], po).then_inc(o_out, 1)
                    else:
                        l = ls[:, v % 4:v % 4 + 1]
                        if units[v].get("sink") is not None:
                            link(nc.vector.tensor_tensor(l, l, es[:, v % 4:v % 4 + 1], ALU.add))
                        link(nc.vector.reciprocal(l, l))
                        nc.vector.tensor_scalar(units[v]["out"], po, l, None, ALU.mult).then_inc(o_out, 1)
            dve.wait_ge(o_out, N)


def combine_groups(k, T, rows):
    nc = k.nc
    W = BG * (HD + 2)
    nat = k.scratch[0:S * W]
    with ExitStack() as c:
        sb = lambda n, s: c.enter_context(nc.sbuf_tensor(fresh(n), s, F32))
        U0 = sb("U0c", [P, CLS, BG, HD + 2])
        M = sb("Mx", [P, 16])
        f = sb("fg", [P, 3, 16])
        t1 = sb("t1c", [P, 16])
        ob = sb("ob", [P, 16, HD])
        block, moved, f_in, f_done, ob_done, t_done, out_act, step, row_done, row_out = c.enter_context(
            stage(nc, "moved f_in f_done ob_done t_done out_act step row_done row_out"))
        U = [U0[:].rearrange("p t h d -> p (t h) d"), T["U1"][:].rearrange("p t h d -> p (t h) d"),
             T["U2"][:].rearrange("p t h d -> p (t h) d")]

        @block.sync
        def _(sp):
            sp.dma_start(nat.rearrange("(t p f) -> p t f", p=P, f=W), T["U0"][:].rearrange("p t h d -> p t (h d)")).then_inc(moved, 16)
            sp.wait_ge(moved, 16)
            sp.dma_start(U0[:].rearrange("p t h d -> p (t h d)"), nat.rearrange("(i f) -> i f", i=P)).then_inc(moved, 16)
            sp.wait_ge(moved, 32)

        @block.vector
        def _(dve):
            link = Link(dve, step)
            for r, (_cols, row) in enumerate(rows):
                dve.wait_ge(row_done, r + 1)
                nc.vector.tensor_copy(row[:].rearrange("p (b n) -> p b n", b=2), k.ps[:, 6:8, :]).then_inc(row_out, 1)
            dve.wait_ge(moved, 32)
            link(nc.vector.tensor_tensor(M[:], U[0][:, :, HD + 1], U[1][:, :, HD + 1], ALU.max))
            link(nc.vector.tensor_tensor(M[:], M[:], U[2][:, :, HD + 1], ALU.max))
            for g in range(3):
                ins = nc.vector.tensor_tensor(f[:, g, :], U[g][:, :, HD + 1], M[:], ALU.subtract)
            ins.then_inc(f_in, 1)
            dve.wait_ge(f_done, 1)
            link(nc.vector.tensor_tensor(M[:], f[:, 0, :], U[0][:, :, HD], ALU.mult))
            for g in (1, 2):
                link(nc.vector.tensor_tensor(t1[:], f[:, g, :], U[g][:, :, HD], ALU.mult))
                link(nc.vector.tensor_tensor(M[:], M[:], t1[:], ALU.add))
            link(nc.vector.reciprocal(M[:], M[:]))
            link(nc.vector.tensor_tensor(f[:], f[:], bcast(M[:], 1, 3), ALU.mult))
            link(nc.vector.tensor_tensor(ob[:], U[0][:, :, 0:HD], bcast(f[:, 0, :], 2, HD), ALU.mult))
            for g in (1, 2):
                link(nc.vector.tensor_tensor(U[g][:, :, 0:HD], U[g][:, :, 0:HD], bcast(f[:, g, :], 2, HD), ALU.mult))
                link(nc.vector.tensor_tensor(ob[:], ob[:], U[g][:, :, 0:HD], ALU.add))
            dve.nop().then_inc(ob_done, 1)
            for q in range(6):
                dve.wait_ge(out_act, q + 1)
                link(nc.vector.tensor_tensor(T["oT"][1][:, q, :], k.ps[:, q, :], T["oT"][0][:, q, :].bitcast(F32), ALU.subtract))

        @block.scalar
        def _(act):
            act.wait_ge(f_in, 1)
            nc.scalar.activation(f[:], f[:], ACT.Exp).then_inc(f_done, 1)
            for q in range(6):
                act.wait_ge(t_done, q + 1)
                nc.scalar.copy(T["oT"][0][:, q, :], k.ps[:, q, :]).then_inc(out_act, 1)
            act.wait_ge(out_act, 6)

        @block.tensor
        def _(pe):
            for r, (cols, _row) in enumerate(rows):
                if r:
                    pe.wait_ge(row_out, r)
                for j in range(KD):
                    mm = pe.matmul(k.ps[:, 6 + j // 4, (j % 4) * P:(j % 4 + 1) * P], cols[:, j:j + 1].to_broadcast([P, P]), k.ident[:],
                                   start=True, stop=True)
                mm.then_inc(row_done, 1)
            for q in range(4):
                for t in range(NT):
                    mm = pe.transpose(k.ps[:, q, t * P:(t + 1) * P], T["oa"][:, t, q * P:(q + 1) * P], k.ident[:])
                mm.then_inc(t_done, 1)
            pe.wait_ge(ob_done, 1)
            for q in range(2):
                for t in range(NT):
                    src = ob[:, 4 * t + 2 * q:4 * t + 2 * q + 2, :].rearrange("p h d -> p (h d)")
                    mm = pe.transpose(k.ps[:, 4 + q, t * P:(t + 1) * P], src, k.ident[:])
                mm.then_inc(t_done, 1)


def branches(k, wa, wb, wo, T, grow):
    nc = k.nc
    with ExitStack() as c:
        tmp = c.enter_context(nc.sbuf_tensor(fresh("tmp_b"), [P, 2, 2, S], F32))
        mT = pair_of(nc, c, "merged", [P, KD, S])
        block, *sems, pair_out, merged, res_out, step = c.enter_context(stage(nc, Weights.NAMES + " pair_out merged res_out step"))
        W = Weights(k, sems)
        cols = lambda h: slice(256 * h, 256 * (h + 1))

        def both(v, i):
            r = v[:, i, 0:1536].rearrange("p (k n) -> p k n", k=6)
            return r[:, 0:4, :], r[:, 4:6, :]

        @block.sync
        def _(sp):
            for h in range(4):
                ra, rb = both(k.ring, h % 2)
                W.load(sp, h // 2, h % 2, [(ra, wa[:, :, cols(h)]), (rb, wb[:, :, cols(h)])])
            for n in range(2):
                for i in range(2):
                    W.load(sp, 2 + n, i, [(W.raw(i, 4, 512), wo[:, 4 * i:4 * i + 4, n * 512:(n + 1) * 512])])

        @block.scalar
        def _(act):
            for u in range(4):
                for i in range(2):
                    W.split_high(act, u, i, 32 * (u + 1) if u < 2 else 64 + 16 * (u - 1), 1536 if u < 2 else HALF)

        @block.gpsimd
        def _(pool):
            W.start_low(pool)
            for u in range(4):
                for i in range(2):
                    W.split_low(pool, u, i, 1536 if u < 2 else HALF)

        @block.tensor
        def _(pe):
            W.start_read(pe)
            for h in range(4):
                if h >= 2:
                    pe.wait_ge(pair_out, 2 * (h - 1))
                pa, pb = zip(*(both(k.parts[a], h % 2) for a in range(2)))
                o = T["oT"]
                for x, (p, ks) in enumerate(((pa, range(4)), (pb, range(2)))):
                    mm = split_products(pe, W, h // 2, h % 2, [k.ps[:, 4 * (h % 2) + 2 * m + x, :] for m in range(2)],
                                        lambda a, m, q: p[a][:, q, m * P:(m + 1) * P], lambda a, m, q: o[a][:, 4 * x + q, :], ks, True)
                mm.then_inc(W.read, 1)
            pe.wait_ge(merged, KD)
            for n in range(2):
                token_unit(k, pe, W, mT, 2 + n, n, 512)

        @block.vector
        def _(dve):
            link = Link(dve, step)
            V = nc.vector
            for m in range(KD):
                W.done(dve, m // 4, m // 2 % 2)
                b = 4 * (m // 2 % 2) + 2 * (m % 2)
                t1, t2 = tmp[:, 0, m % 2, :], tmp[:, 1, m % 2, :]
                link(V.tensor_tensor(t1, k.ps[:, b, :], T["gates"][:, m, :], ALU.mult))
                link(V.tensor_tensor(t2, k.ps[:, b + 1, :], T["gates"][:, KD + m, :], ALU.mult))
                dve.nop().then_inc(pair_out, 1)
                link(V.tensor_tensor(t1, t1, t2, ALU.add))
                link(V.tensor_copy(mT[0][:, m, :], t1))
                V.tensor_tensor(mT[1][:, m, :], t1, mT[0][:, m, :].bitcast(F32), ALU.subtract).then_inc(merged, 1)
            dve.wait_ge(merged, KD)
            for n in range(2):
                W.done(dve, 2 + n, 1)
                for t in range(NT):
                    c2 = slice(n * 512, (n + 1) * 512)
                    link(V.tensor_tensor(tmp[:, 0, t % 2, :], k.ps[:, 4 * n + t, :], grow[:, c2], ALU.mult))
                    link(V.scalar_tensor_tensor(k.x[:, t, c2], k.x[:, t, c2], ALPHA, tmp[:, 0, t % 2, :], ALU.mult, ALU.add))


def router(k, hT, cT):
    nc = k.nc
    G = N_EXP // EPG
    with ExitStack() as c:
        sb = lambda n, s: c.enter_context(nc.sbuf_tensor(fresh(n), s, F32))
        wr = sb("wr", [P, KD, N_EXP])
        wp = pair_of(nc, c, "wr", [P, KD, N_EXP])
        rb = sb("rb", [P, N_EXP])
        before = sb("before_sb", [P, 4, 4])
        sc = sb("sc_r", [P, NT, N_EXP])
        sel = sb("sel_r", [P, NT * G, EPG])
        gt = sb("gt_r", [P, NT * G, EPG, EPG])
        eq = sb("eq_r", [P, NT * G, EPG, EPG])
        top = sb("top_r", [P, NT * G, EPG])
        grp = sb("grp_r", [P, NT, G])
        gm = sb("gm_r", [P, NT, G])
        den = sb("den_r", [P, NT])
        block, in_landed, w_split, logit, score, score_t, comb, t_done, cT_done, step = c.enter_context(
            stage(nc, "in_landed w_split logit score score_t comb t_done cT_done step"))

        @block.sync
        def _(sp):
            sp.dma_start(wr[:], k.A["w_router"].rearrange("(k p) e -> p k e", p=P)).then_inc(in_landed, 16)
            sp.dma_start(rb[:], bcast(k.A["router_bias"], 0, P)).then_inc(in_landed, 16)
            sp.dma_start(before[:], k.K["before"]).then_inc(in_landed, 16)
            sp.wait_ge(in_landed, 48)

        @block.tensor
        def _(pe):
            pe.wait_ge(w_split, 1)
            chain3(pe, k.ps[0:N_EXP, 0, :], lambda a, q: wp[a][:, q, :], lambda a, q: hT[a][:, q, :], range(KD)).then_inc(logit, 1)
            pe.wait_ge(score, 1)
            for t in range(NT):
                mm = pe.transpose(k.ps[:, 2, t * N_EXP:(t + 1) * N_EXP], cT[:, t * P:(t + 1) * P], k.ident[0:N_EXP, 0:N_EXP])
            mm.then_inc(score_t, 1)
            pe.wait_ge(comb, 1)
            for t in range(NT):
                mm = pe.transpose(k.ps[0:N_EXP, 1, t * P:(t + 1) * P], sc[:, t, :], k.ident[:])
            mm.then_inc(t_done, 1)

        @block.scalar
        def _(act):
            act.wait_ge(logit, 1)
            nc.scalar.activation(cT[:], k.ps[0:N_EXP, 0, :], ACT.Sigmoid).then_inc(score, 1)
            act.wait_ge(t_done, 1)
            nc.scalar.copy(cT[:], k.ps[0:N_EXP, 1, :]).then_inc(cT_done, 1)
            act.wait_ge(cT_done, 1)

        @block.vector
        def _(dve):
            link = Link(dve, step)
            V = nc.vector
            dve.wait_ge(in_landed, 48)
            link(V.tensor_copy(wp[0][:], wr[:]))
            V.tensor_tensor(wp[1][:], wr[:], wp[0][:].bitcast(F32), ALU.subtract).then_inc(w_split, 1)
            dve.wait_ge(score_t, 1)
            link(V.tensor_copy(sc[:], k.ps[:, 2, 0:NT * N_EXP].rearrange("p (t e) -> p t e", t=NT)))
            link(V.tensor_tensor(sel[:].rearrange("p (t g) e -> p t (g e)", t=NT), sc[:], bcast(rb[:], 1, NT), ALU.add))

            def ranks(v, n, out):
                g, e = gt[:, 0:n], eq[:, 0:n]
                link(V.tensor_tensor(g, bcast(v, 2, 4), bcast(v, 3, 4), ALU.is_gt))
                link(V.tensor_tensor(e, bcast(v, 2, 4), bcast(v, 3, 4), ALU.is_equal))
                link(V.tensor_tensor(e, e, bcast(before[:], 1, n), ALU.mult))
                link(V.tensor_tensor(g, g, e, ALU.add))
                link(V.tensor_reduce(out, g, AX, ALU.add))

            ranks(sel[:], NT * G, top[:])
            link(V.tensor_scalar(top[:], top[:], 1.5, None, ALU.is_lt))
            link(V.tensor_tensor(sel[:], sel[:], top[:], ALU.mult))
            link(V.tensor_reduce(grp[:].rearrange("p t g -> p (t g)"), sel[:], AX, ALU.add))
            ranks(grp[:], NT, gm[:])
            link(V.tensor_scalar(gm[:], gm[:], 0.5, None, ALU.is_lt))
            link(V.tensor_tensor(top[:], top[:], bcast(gm[:].rearrange("p t g -> p (t g)"), 2, EPG), ALU.mult))
            link(V.tensor_tensor(sc[:], sc[:], top[:].rearrange("p (t g) e -> p t (g e)", t=NT), ALU.mult))
            link(V.tensor_reduce(den[:], sc[:], AX, ALU.add))
            link(V.reciprocal(den[:], den[:]))
            V.tensor_tensor(sc[:], sc[:], bcast(den[:], 2, N_EXP), ALU.mult).then_inc(comb, 1)
            dve.wait_ge(comb, 1)


def experts(k, hT, wg, wu, wd, cT, grow, w_side, side_out):
    nc = k.nc
    with ExitStack() as c:
        sb = lambda n, s: c.enter_context(nc.sbuf_tensor(fresh(n), s, F32))
        hid = pair_of(nc, c, "hid", [P, KD, S])
        sg = sb("sg", [P, 2, S])
        ex = sb("hid_exact", [P, 2, S])
        y = sb("y_acc", [P, NT, D])
        comb_all = sb("comb_all", [P, N_EXP, S])
        back = k.scratch[0:N_EXP * S].rearrange("(e n) -> e n", e=N_EXP)
        block, *sems, sg_done, free_dve, hid_done, step, comb_moved = c.enter_context(
            stage(nc, f"{Weights.NAMES} {SideModulation.NAMES} sg_done free_dve hid_done step comb_moved"))
        W = Weights(k, sems[0:5])
        side = SideModulation(k, c, sems[5:], 1, lambda s, i: w_side[i][:, :, bass.ds(64 * (s - i), P)],
                              lambda s, i: side_out[i][:, bass.ds(64 * (s - i), P)])
        C = N_EXP // 4

        @block.sync
        def _(sp):
            with sp.Fori(0, C) as ch:
                for j in range(4):
                    for i in range(2):
                        v = W.raw(i, KD, 256)
                        at = slice(i * P, (i + 1) * P)
                        W.load(sp, 6 * ch + j, i, [(v[:, :, 0:P], wg[:, 4 * ch + j, :, at]), (v[:, :, P:256], wu[:, 4 * ch + j, :, at])])
                    for i in range(2):
                        side.load(sp, 12 * ch + 2 * j + i, i)
                for n in range(2):
                    for i in range(2):
                        v = W.raw(i, 4, 512)
                        W.load(sp, 6 * ch + 4 + n, i, [(v[:, 2 * e:2 * e + 2, :], wd[:, bass.ds(8 * ch + 4 * i + 2 * e, 2), n * 512:(n + 1) * 512])
                                                       for e in range(2)])
                    for i in range(2):
                        side.load(sp, 12 * ch + 8 + 2 * n + i, i)

        @block.gpsimd
        def _(pool):
            W.start_low(pool)
            with pool.Fori(0, C) as ch:
                for j in range(6):
                    for i in range(2):
                        W.split_low(pool, 6 * ch + j, i)

        @block.tensor
        def _(pe):
            W.start_read(pe)
            with pe.Fori(0, C) as ch:
                for j in range(6):
                    pe.wait_ge(free_dve, 6 * ch + j + 1)
                    if j < 4:
                        feature_unit(k, pe, W, hT, 6 * ch + j, j % 2)
                    else:
                        token_unit(k, pe, W, hid, 6 * ch + j, j % 2, 512,
                                   before=(lambda i: pe.wait_ge(hid_done, 8 * ch + 4 * i + 4)) if j == 4 else None)

        @block.scalar
        def _(act):
            act.dma_start(back, cT[:]).then_inc(comb_moved, 16)
            act.wait_ge(comb_moved, 16)
            act.dma_start(comb_all[:], bcast(back, 0, P)).then_inc(comb_moved, 16)
            with act.Fori(0, C) as ch:
                for j in range(6):
                    for i in range(2):
                        W.split_high(act, 6 * ch + j, i, 192 * ch + 32 * j + 32)
                    if 1 <= j < 5:
                        for i in range(2):
                            W.done(act, 6 * ch + j - 1, i)
                            act.wait_ge(step, 1 + 32 * ch + max(0, 6 * (j - 2) + 3 * i + 2))
                            nc.scalar.activation(sg[:, i, :], k.ps[:, 4 * ((j - 1) % 2) + 2 * i, :], ACT.Silu).then_inc(sg_done, 1)
                    for i in range(2):
                        side.store(act, 12 * ch + 2 * j + i, i)
            side.end(act, 48)

        @block.vector
        def _(dve):
            link = Link(dve, step)
            V = nc.vector
            link(V.memset(y[:], 0.0))
            dve.nop().then_inc(free_dve, 2)
            side.start(dve)
            dve.wait_ge(comb_moved, 32)
            with dve.Fori(0, C) as ch:
                link.n, link.base = 1, 32 * ch
                for j in range(4):
                    for i in range(2):
                        side.work(dve, 12 * ch + 2 * j + i, i, 6 * ch + j)
                    w = comb_all[:, bass.ds(4 * ch + j, 1), :].rearrange("p a n -> p (a n)")
                    for i in range(2):
                        dve.wait_ge(sg_done, 8 * ch + 2 * j + i + 1)
                        h, e = 2 * j + i, ex[:, i, :]
                        link(V.tensor_tensor(e, k.ps[:, 4 * (j % 2) + 2 * i + 1, :], w, ALU.mult))
                        link(V.tensor_tensor(e, e, sg[:, i, :], ALU.mult))
                        link(V.tensor_copy(hid[0][:, h, :], e))
                        V.tensor_tensor(hid[1][:, h, :], e, hid[0][:, h, :].bitcast(F32), ALU.subtract).then_inc(hid_done, 1)
                    dve.nop().then_inc(free_dve, 1)
                for n in range(2):
                    for i in range(2):
                        side.work(dve, 12 * ch + 8 + 2 * n + i, i, 6 * ch + 4 + n)
                    W.done(dve, 6 * ch + 4 + n, 1)
                    for t in range(NT):
                        yv = y[:, t, n * 512:(n + 1) * 512]
                        link(V.tensor_tensor(yv, yv, k.ps[:, 4 * n + t, :], ALU.add))
                    dve.nop().then_inc(free_dve, 1)
            link.n, link.base = 1 + C * 32, 0
            for t in range(NT):
                link(V.tensor_tensor(y[:, t, :], y[:, t, :], grow[:], ALU.mult))
                link(V.scalar_tensor_tensor(k.x[:, t, :], k.x[:, t, :], ALPHA, y[:, t, :], ALU.mult, ALU.add))


def first_layer(k, l, last_store):
    nc, A = k.nc, k.A
    kp = lambda ap: ap.rearrange("l (k p) n -> l p k n", p=P)[l]
    sums, next_sums = k.sums[4], k.sums[5]
    with ExitStack() as c:
        sb = lambda n, s: c.enter_context(nc.sbuf_tensor(fresh(n), s, F32))
        g1, g2 = sb("g1row", [P, D]), sb("g2row", [P, D])
        with ExitStack() as m:
            sm = lambda n, s: m.enter_context(nc.sbuf_tensor(fresh(n), s, F32))
            T = {"gates": sm("gates", [P, 16, S])}
            with ExitStack() as q:
                sq = lambda n, s: q.enter_context(nc.sbuf_tensor(fresh(n), s, F32))
                T.update(qa=sq("qa", [P, NT, 512]), kva=sq("kva", [P, NT, 256]), vc=sq("vc", [P, NT, 512]), v0=sq("v0", [P, 5, 256]),
                         q0T=sq("q0T", [P, 2, S]), k0T=sq("k0T", [P, 2, S + 2 * REACH]), qcT=sq("qcT", [P, 4, S]), kcT=sq("kcT", [P, 4, S]))
                T["v0c"] = sq("v0c", [P, CLS, 256])
                with ExitStack() as h:
                    hT = pair_of(nc, h, "hT", [P, KD, S])
                    norm_to_hT(k, hT, False, LN_EPS, k.mod[:, 8:16], k.mod[:, 0:8],
                               mod=(next_sums[:, 0:2 * D], A["b_ada"][l][0:2 * D], 16, k.mod, (8,), None))
                    ada = [kp(A["w_ada"]), A["w_ada"][DEPTH - 1].rearrange("(k p) n -> p k n", p=P)]
                    in_projection(k, kp(A["w_in"]), hT, T,
                                  lambda s: ada[0][:, :, 2 * D + s * P:2 * D + (s + 1) * P] if s < 32 else ada[1][:, :, (s - 32) * P:(s - 31) * P],
                                  lambda s: sums[:, s * P:(s + 1) * P] if s < 32 else next_sums[:, (s - 32) * P:(s - 31) * P])
                T["oa"] = T["qa"]
                T.update(U0=sq("U0", [P, NT, BG, HD + 2]), U1=sq("U1", [P, NT, BG, HD + 2]), U2=sq("U2", [P, NT, BG, HD + 2]))
                with ExitStack() as b:
                    with ExitStack() as r:
                        sr = lambda n, s: r.enter_context(nc.sbuf_tensor(fresh(n), s, F32, side="right"))
                        T.update(qaT=sr("qaT", [P, 4, S]), kaT=sr("kaT", [P, 2, S]))
                        rope_qk(k, A["q_norm_g"][l], A["k_norm_g"][l], T,
                                (sums, A["b_ada"][l][2 * D:6 * D], 32, k.mod[:, 16:48], (16,), None))
                        band, cls = (b.enter_context(nc.sbuf_tensor(fresh(n), s, F32)) for n, s in (("band", [P, 3, BG, 256]), ("cls", [P, 2, BG, P])))
                        attention(k, global_units(T), loads=[[(band[:], k.K["bias_band"]), (cls[:], k.K["bias_class"])]] + order_v0(k, T["v0c"], T["v0"]))
                    attention(k, dilated_units(T, band, cls))
                T["oT"] = pair_of(nc, m, "oT", [P, 6, S], side="right")
                combine_groups(k, T, [(k.mod[:, 16:24], g1), (k.mod[:, 40:48], g2)])
            branches(k, kp(A["w_branch_a"]), kp(A["w_branch_b"]), kp(A["w_out"]), T, g1)
        with ExitStack() as m:
            hT = pair_of(nc, m, "hT", [P, KD, S])
            norm_to_hT(k, hT, False, LN_EPS, k.mod[:, 32:40], k.mod[:, 24:32], affine=(A["ln1_g"][l], A["ln1_b"][l]))
            cT = m.enter_context(nc.sbuf_tensor(fresh("cT"), [N_EXP, S], F32))
            router(k, hT, cT)
            ex = lambda ap: ap.rearrange("l e (k p) n -> l p e k n", p=P)[l]
            experts(k, hT, ex(A["w_exp_gate"]), ex(A["w_exp_up"]), A["w_exp_down"].rearrange("l e (f p) n -> l p (e f) n", p=P)[l], cT, g2,
                    [A["mod_w_2"][:, i].rearrange("l (k p) n -> l p k n", p=P)[l] for i in range(2)],
                    [k.sums[0:4].rearrange("(l i) p n -> l i p n", i=2)[:, i][l][:, 0:24 * P] for i in range(2)])
    norm_to_hT(k, None, False, LN_EPS, None, None, affine=(A["ln2_g"][l], A["ln2_b"][l]), store=last_store)


def global_units(T):
    units = []
    for h in range(A_HEADS):
        p0, g = 64 * (h % 2), h // 4
        for t in range(NT):
            units.append(dict(q=T["qaT"][p0:p0 + 64, h // 2, t * P:(t + 1) * P], k=T["kaT"][p0:p0 + 64, g, :],
                              v=[T["kva"][:, j, 128 + 64 * g:192 + 64 * g] for j in range(NT)],
                              out=T["oa"][:, t, h * HD:(h + 1) * HD]))
    return units


def dilated_units(T, band, cls):
    units = []
    for t in range(NT):
        for h in range(BG):
            p0, u = 64 * (h % 2), T["U0"][:, t, h, :]
            units.append(dict(q=T["q0T"][p0:p0 + 64, h // 2, t * P:(t + 1) * P],
                              k=T["k0T"][p0:p0 + 64, h // 2, t * P:t * P + 256],
                              bias=band[:, 0 if t == 0 else 2 if t == NT - 1 else 1, h, :],
                              v=[T["v0"][:, t + j, h * HD:(h + 1) * HD] for j in range(2)],
                              out=u[:, 0:HD], l=u[:, HD:HD + 1], m=u[:, HD + 1:HD + 2]))
            for g in range(2):
                u = T[f"U{g + 1}"][:, t, h, :]
                i = 2 * g + h // 2
                units.append(dict(q=T["qcT"][p0:p0 + 64, i, t * P:(t + 1) * P], k=T["kcT"][p0:p0 + 64, i, t * P:(t + 1) * P],
                                  bias=cls[:, g, h, :], v=[T["vc"][:, t, (4 * g + h) * HD:(4 * g + h + 1) * HD]],
                                  out=u[:, 0:HD], l=u[:, HD:HD + 1], m=u[:, HD + 1:HD + 2]))
    return units


def first_block(k):
    start_up(k, k.A["x"].rearrange("a (i r) d -> (a i) r d", r=CLS), k.A["w_ada"][0].rearrange("(k p) n -> p k n", p=P), k.sums[5])
    mid = k.scratch[2 * S * D:3 * S * D].rearrange("(i r d) -> r i d", r=CLS, d=D)
    with k.nc.Fori(0, DEPTH) as l:
        first_layer(k, l, mid)



def project(k, w, hT, plan, loads=()):
    nc = k.nc
    N = len(plan)
    with stage(nc, Weights.NAMES + " free_act free_dve moved") as (block, *sems, free_act, free_dve, moved):
        W = Weights(k, sems)

        @block.sync
        def _(sp):
            for u, (c0, n, major, *_r) in enumerate(plan):
                for i in range(2):
                    if major == "feature":
                        W.load(sp, u, i, [(W.raw(i, KD, 256), w[:, :, c0 + 256 * i:c0 + 256 * (i + 1)])])
                    else:
                        W.load(sp, u, i, [(W.raw(i, KD // 2, n), w[:, 4 * i:4 * i + 4, c0:c0 + n])])
                if u == 1:
                    for dst, src in loads:
                        sp.dma_start(dst, src).then_inc(moved, 16)
            if loads:
                sp.wait_ge(moved, 16 * len(loads))

        @block.gpsimd
        def _(pool):
            W.start_low(pool)
            for u in range(N):
                for i in range(2):
                    W.split_low(pool, u, i, KD // 2 * plan[u][1])

        @block.tensor
        def _(pe):
            W.start_read(pe)
            for u, (c0, n, major, *_r) in enumerate(plan):
                if u >= 2:
                    pe.wait_ge(free_act, u - 1)
                    pe.wait_ge(free_dve, u - 1)
                if major == "feature":
                    feature_unit(k, pe, W, hT, u, u % 2)
                elif major == "few":
                    for i in range(2):
                        wv = [W.part(a, i, KD // 2, n) for a in range(2)]
                        split_products(pe, W, u, i, [k.ps[0:n, 4 * (u % 2), :]], lambda a, m, q: wv[a][:, q - 4 * i, :],
                                       lambda a, m, q: hT[a][:, q, :], range(4 * i, 4 * i + 4), True, first=i == 0, last=i == 1).then_inc(W.read, 1)
                else:
                    token_unit(k, pe, W, hT, u, u % 2, n)

        @block.scalar
        def _(act):
            for u in range(N + 1):
                if u < N:
                    for i in range(2):
                        W.split_high(act, u, i, 16 * u + 16, KD // 2 * plan[u][1])
                if u >= 1:
                    _c, n, major, f, dst = plan[u - 1]
                    W.done(act, u - 1, 1)
                    for j in range(4 if f == "silu" else 1 if major == "few" else 2):
                        src = k.ps[0:n if major == "few" else P, 4 * ((u - 1) % 2) + j, 0:n if major == "token" else S]
                        if f == "silu":
                            last = nc.scalar.activation(dst[j], src, ACT.Silu)
                        else:
                            last = nc.scalar.activation(dst[j], src, ACT.Copy, scale=f)
                    last.then_inc(free_act, 1)
            act.wait_ge(free_act, N)

        @block.vector
        def _(dve):
            for u, (_c, n, major, f, dst) in enumerate(plan):
                if f == "silu" or major == "few":
                    if u:
                        dve.wait_ge(free_dve, u)
                    dve.nop().then_inc(free_dve, 1)
                    continue
                W.done(dve, u, 1)
                for j in (2, 3):
                    src = k.ps[:, 4 * (u % 2) + j, 0:n if major == "token" else S]
                    last = nc.vector.tensor_scalar(dst[j], src, f, None, ALU.mult)
                last.then_inc(free_dve, 1)
            dve.wait_ge(free_dve, N)


def out_projection(k, w, src, kt, y, first):
    nc = k.nc
    with stage(nc, Weights.NAMES + " y_done spare") as (block, *sems, y_done, _s):
        W = Weights(k, sems)
        half = kt // 2

        @block.sync
        def _(sp):
            for n in range(2):
                for i in range(2):
                    W.load(sp, n, i, [(W.raw(i, half, 512), w[:, half * i:half * (i + 1), n * 512:(n + 1) * 512])])

        @block.scalar
        def _(act):
            for n in range(2):
                for i in range(2):
                    W.split_high(act, n, i, 16 * n + 16, 512 * half)
            act.wait_ge(W.high, 4)

        @block.gpsimd
        def _(pool):
            W.start_low(pool)
            for n in range(2):
                for i in range(2):
                    W.split_low(pool, n, i, 512 * half)
            pool.wait_ge(W.low, 6)

        @block.tensor
        def _(pe):
            W.start_read(pe)
            for n in range(2):
                token_unit(k, pe, W, src, n, n, 512, kt=kt)

        @block.vector
        def _(dve):
            for n in range(2):
                W.done(dve, n, 1)
                for t in range(NT):
                    yv, p = y[:, t, n * 512:(n + 1) * 512], k.ps[:, 4 * n + t, :]
                    if first:
                        nc.vector.tensor_copy(yv, p).then_inc(y_done, 1)
                    else:
                        nc.vector.tensor_tensor(yv, yv, p, ALU.add).then_inc(y_done, 1)
            dve.wait_ge(y_done, 2 * NT)


def mlp(k, w1, w2, hT, y):
    nc = k.nc
    with ExitStack() as c:
        hid = pair_of(nc, c, "hid", [P, KD, S])
        ex = c.enter_context(nc.sbuf_tensor(fresh("hid_exact"), [P, 4, S], F32))
        block, *sems, free_dve, hid_done, step = c.enter_context(stage(nc, Weights.NAMES + " free_dve hid_done step"))
        W = Weights(k, sems)
        C = 4

        @block.sync
        def _(sp):
            with sp.Fori(0, C) as ch:
                for j in range(4):
                    for i in range(2):
                        if j < 2:
                            W.load(sp, 4 * ch + j, i, [(W.raw(i, KD, 256), w1[:, :, bass.ds(1024 * ch + 512 * j + 256 * i, 256)])])
                        else:
                            W.load(sp, 4 * ch + j, i, [(W.raw(i, 4, 512), w2[:, bass.ds(8 * ch + 4 * i, 4), (j - 2) * 512:(j - 1) * 512])])

        @block.scalar
        def _(act):
            with act.Fori(0, C) as ch:
                for j in range(4):
                    for i in range(2):
                        W.split_high(act, 4 * ch + j, i, 64 * ch + 16 * j + 16)

        @block.gpsimd
        def _(pool):
            W.start_low(pool)
            with pool.Fori(0, C) as ch:
                for j in range(4):
                    for i in range(2):
                        W.split_low(pool, 4 * ch + j, i)

        @block.tensor
        def _(pe):
            W.start_read(pe)
            with pe.Fori(0, C) as ch:
                for j in range(4):
                    pe.wait_ge(free_dve, 4 * ch + j + 1)
                    if j < 2:
                        feature_unit(k, pe, W, hT, 4 * ch + j, j % 2)
                    else:
                        token_unit(k, pe, W, hid, 4 * ch + j, j % 2, 512,
                                   before=(lambda i: pe.wait_ge(hid_done, 8 * ch + 4 * i + 4)) if j == 2 else None)

        @block.vector
        def _(dve):
            link = Link(dve, step)
            V = nc.vector
            link(V.memset(y[:], 0.0))
            dve.nop().then_inc(free_dve, 2)
            with dve.Fori(0, C) as ch:
                link.n, link.base = 1, 32 * ch
                for j in range(2):
                    for m in range(4):
                        W.done(dve, 4 * ch + j, m // 2)
                        q, e = 4 * j + m, ex[:, m, :]
                        link(V.tensor_scalar(e, k.ps[:, 4 * j + m, :], 0.0, None, ALU.max))
                        if m == 3:
                            dve.nop().then_inc(free_dve, 1)
                        link(V.tensor_tensor(e, e, e, ALU.mult))
                        link(V.tensor_copy(hid[0][:, q, :], e))
                        V.tensor_tensor(hid[1][:, q, :], e, hid[0][:, q, :].bitcast(F32), ALU.subtract).then_inc(hid_done, 1)
                    dve.wait_ge(hid_done, 8 * ch + 4 * j + 4)
                for n in range(2):
                    W.done(dve, 4 * ch + 2 + n, 1)
                    for t in range(NT):
                        yv = y[:, t, n * 512:(n + 1) * 512]
                        link(V.tensor_tensor(yv, yv, k.ps[:, 4 * n + t, :], ALU.add))
                    dve.nop().then_inc(free_dve, 1)


def add_normed(k, y, gate, mod, store=None):
    nc = k.nc
    with ExitStack() as c:
        sb = lambda n, s: c.enter_context(nc.sbuf_tensor(fresh(n), s, F32))
        st, mv, ms = sb("stats_y", [P, NT, 2, 6]), sb("mv_y", [P, NT, 2]), sb("ms_y", [P, NT])
        block, row_done, var_done, root_done, x_done, stored, step, *sems = c.enter_context(
            stage(nc, "row_done var_done root_done x_done stored step" + (f" {ModulationTail.NAMES}" if mod is not None else "")))
        tail = ModulationTail(k, c, sems, *mod) if mod is not None else None
        grow = k.ps[:, 0:2, :].rearrange("p b n -> p (b n)")

        @block.tensor
        def _(pe):
            for j in range(KD):
                mm = pe.matmul(k.ps[:, j // 4, (j % 4) * P:(j % 4 + 1) * P], gate[:, j:j + 1].to_broadcast([P, P]), k.ident[:],
                               start=True, stop=True)
            mm.then_inc(row_done, 1)
            if tail is not None:
                tail.add_up(pe)

        @block.sync
        def _(sp):
            if tail is not None:
                tail.load(sp)
            if store is not None:
                for t in range(NT):
                    sp.wait_ge(x_done, t + 1)
                    sp.dma_start(store[:, t, :], k.x[:, t, :]).then_inc(stored, 16)
                sp.wait_ge(stored, 16 * NT)

        @block.scalar
        def _(act):
            act.wait_ge(var_done, 1)
            nc.scalar.activation(ms[:], ms[:], ACT.Sqrt).then_inc(root_done, 1)

        @block.vector
        def _(dve):
            link = Link(dve, step)
            if tail is not None:
                tail.start(dve)
            for t in range(NT):
                for h in range(2):
                    link(nc.vector.bn_stats(st[:, t, h, :], y[:, t, h * 512:(h + 1) * 512]))
            for t in range(NT):
                link(nc.vector.bn_aggr(mv[:, t, :], st[:, t, :, :].rearrange("p a b -> p (a b)")))
            link(nc.vector.tensor_tensor(ms[:], mv[:, :, 0], mv[:, :, 0], ALU.mult))
            link(nc.vector.tensor_tensor(ms[:], ms[:], mv[:, :, 1], ALU.add))
            nc.vector.tensor_scalar(ms[:], ms[:], RMS_EPS, None, ALU.add).then_inc(var_done, 1)
            dve.wait_ge(root_done, 1)
            link(nc.vector.reciprocal(ms[:], ms[:]))
            for t in range(NT):
                if t == 0:
                    dve.wait_ge(row_done, 1)
                link(nc.vector.scalar_tensor_tensor(y[:, t, :], y[:, t, :], ms[:, t:t + 1], grow, ALU.mult, ALU.mult))
                nc.vector.tensor_tensor(k.x[:, t, :], k.x[:, t, :], y[:, t, :], ALU.add).then_inc(x_done, 1)
            if tail is not None:
                tail.finish(dve, link)
            dve.wait_ge(x_done, NT)


def relative_bias(k, mod, x_source):
    nc = k.nc
    H = 8
    flat = k.scratch[0:H * P * BIAS_W]
    small = k.scratch[H * P * BIAS_W:H * (P + 1) * BIAS_W]
    with ExitStack() as c:
        hot = c.enter_context(nc.sbuf_tensor(fresh("hot"), [33, BIAS_W], F32))
        rel = c.enter_context(nc.sbuf_tensor(fresh("rel"), [33, H], F32))
        row = c.enter_context(nc.sbuf_tensor(fresh("bias_row"), [H, BIAS_W], F32))
        block, in_landed, neg_done, row_done, row_out, moved, x_landed, step, *sems = c.enter_context(
            stage(nc, f"in_landed neg_done row_done row_out moved x_landed step {ModulationTail.NAMES}"))
        tail = ModulationTail(k, c, sems, *mod)

        @block.sync
        def _(sp):
            sp.dma_start(hot[:], k.K["bucket_hot"]).then_inc(in_landed, 16)
            sp.dma_start(rel[0:32, :], k.A["rel_bias_2"]).then_inc(in_landed, 16)
            sp.wait_ge(row_out, 1)
            sp.dma_start(small.rearrange("(h n) -> h n", h=H), row[:]).then_inc(moved, 16)
            sp.wait_ge(moved, 16)
            sp.dma_start(flat.rearrange("(h p n) -> h p n", p=P, n=BIAS_W), bcast(small.rearrange("(h n) -> h n", h=H), 1, P)).then_inc(moved, 16)
            sp.wait_ge(moved, 32)

        @block.scalar
        def _(act):
            act.dma_start(k.x[:], x_source).then_inc(x_landed, 16)
            tail.load(act)
            act.wait_ge(x_landed, 16)

        @block.gpsimd
        def _(pool):
            nc.gpsimd.memset(rel[32:33, :], NEG).then_inc(neg_done, 1)

        @block.tensor
        def _(pe):
            pe.wait_ge(in_landed, 32)
            pe.wait_ge(neg_done, 1)
            pe.matmul(k.ps[0:H, 0, :], rel[:], hot[:, 0:512], start=True, stop=True)
            pe.matmul(k.ps[0:H, 1, 0:P], rel[:], hot[:, 512:BIAS_W], start=True, stop=True).then_inc(row_done, 1)
            tail.add_up(pe)

        @block.vector
        def _(dve):
            tail.start(dve)
            link = Link(dve, step)
            dve.wait_ge(row_done, 1)
            link(nc.vector.tensor_copy(row[:, 0:512], k.ps[0:H, 0, :]))
            nc.vector.tensor_copy(row[:, 512:BIAS_W], k.ps[0:H, 1, 0:P]).then_inc(row_out, 1)
            tail.finish(dve, link)


def bias_loads(k, bias, a):
    out = []
    for h in range(8):
        at = h * P * BIAS_W + P - 1
        out.append((bias[:, h, :], k.scratch[at:at + P * (BIAS_W - 1)].rearrange("(p n) -> p n", n=BIAS_W - 1)[:, a:512]))
    return out


def convolution(k, xbc, T):
    nc = k.nc
    A = k.A
    with ExitStack() as c:
        raw = c.enter_context(nc.sbuf_tensor(fresh("craw"), [80, P], F32))
        w = c.enter_context(nc.sbuf_tensor(fresh("cw"), [P, 80], F32))
        cv = c.enter_context(nc.sbuf_tensor(fresh("cv"), [P, 3, S], F32))
        block, in_landed, wt_done, w_out, dt_t, dt_out, first_tap, conv_done, silu_done, t_done, t_out, step = c.enter_context(
            stage(nc, "in_landed wt_done w_out dt_t dt_out first_tap conv_done silu_done t_done t_out step"))

        @block.sync
        def _(sp):
            sp.dma_start(raw[0:64, :], A["e_conv_w_2"].rearrange("e j (q p) -> (e j q) p", p=P)).then_inc(in_landed, 16)
            sp.dma_start(raw[64:80, :], A["e_conv_b_2"].rearrange("e (q p) -> (e q) p", p=P)).then_inc(in_landed, 16)
            sp.wait_ge(in_landed, 32)

        @block.vector
        def _(dve):
            link = Link(dve, step)
            V = nc.vector
            dve.wait_ge(wt_done, 1)
            link(V.tensor_copy(w[:], k.ps[:, 0, 0:80]))
            V.memset(xbc[:, :, 0:3], 0.0).then_inc(w_out, 1)
            dve.wait_ge(w_out, 1)
            for q in range(16):
                dve.wait_ge(first_tap, q + 1)
                o = cv[:, q % 3, :]
                for j in (1, 2):
                    link(V.scalar_tensor_tensor(o, xbc[:, q, j:j + S], w[:, 16 * j + q:16 * j + q + 1], o, ALU.mult, ALU.add))
                V.scalar_tensor_tensor(o, xbc[:, q, 3:3 + S], w[:, 48 + q:49 + q], o, ALU.mult, ALU.add).then_inc(conv_done, 1)

        @block.scalar
        def _(act):
            def token_major(q):
                act.wait_ge(t_done, q + 1)
                dst = T["xh"][:, :, q * P:(q + 1) * P] if q < 8 else T["Bt"][:, :, q - 8, :]
                nc.scalar.copy(dst, k.ps[:, 1 + q % 2, :].rearrange("p (t n) -> p t n", t=NT)).then_inc(t_out, 1)

            def tap(q):
                if q >= 3:
                    act.wait_ge(silu_done, q - 2)
                nc.scalar.activation(cv[:, q % 3, :], xbc[:, q, 0:S], ACT.Identity, scale=w[:, q:q + 1], bias=w[:, 64 + q:65 + q]).then_inc(first_tap, 1)

            act.wait_ge(dt_t, 1)
            nc.scalar.copy(T["dt"][:], k.ps[:, 3, 0:NT * SSD_HEADS].rearrange("p (t h) -> p t h", t=NT)).then_inc(dt_out, 1)
            act.wait_ge(w_out, 1)
            tap(0)
            tap(1)
            for q in range(16):
                if q + 2 < 16:
                    tap(q + 2)
                act.wait_ge(conv_done, q + 1)
                nc.scalar.activation(xbc[:, q, 3:3 + S], cv[:, q % 3, :], ACT.Silu).then_inc(silu_done, 1)
                if 1 <= q < 13:
                    token_major(q - 1)
            act.wait_ge(dt_out, 1)
            act.wait_ge(silu_done, 16)
            act.wait_ge(t_out, 12)

        @block.tensor
        def _(pe):
            for t in range(NT):
                mm = pe.transpose(k.ps[:, 3, t * SSD_HEADS:(t + 1) * SSD_HEADS], T["dtT"][:, t * P:(t + 1) * P], k.ident[0:SSD_HEADS, 0:SSD_HEADS])
            mm.then_inc(dt_t, 1)
            pe.wait_ge(in_landed, 32)
            pe.transpose(k.ps[:, 0, 0:80], raw[:], k.ident[0:80, 0:80]).then_inc(wt_done, 1)
            for q in range(12):
                pe.wait_ge(silu_done, q + 1)
                if q >= 2:
                    pe.wait_ge(t_out, q - 1)
                for t in range(NT):
                    mm = pe.transpose(k.ps[:, 1 + q % 2, t * P:(t + 1) * P], xbc[:, q, 3 + t * P:3 + (t + 1) * P], k.ident[:])
                mm.then_inc(t_done, 1)


def ssd(k, xbc, T):
    nc = k.nc
    A = k.A
    H, G, R = SSD_HEADS, SSD_GROUPS, SSD_HEADS // SSD_GROUPS
    with ExitStack() as c:
        sb = lambda n, s: c.enter_context(nc.sbuf_tensor(fresh(n), s, F32))
        par = sb("par", [P, 3, H])
        tri = sb("tri", [P, 2, P])
        ones = sb("ones", [P, P])
        dt = T["dt"]
        e, z, z2, acc = (sb(n, [P, NT, H]) for n in ("e_sp", "z_sp", "z2_sp", "acc_sp"))
        a, nacs, eacs, dte, etot, cs = (sb(n, [P, NT, H]) for n in ("a_ss", "nacs", "eacs", "dte", "etot", "cs_ss"))
        X = sb("Xdt", [P, NT, H, 64])
        Xd = sb("Xdec", [P, 2, R * 64])
        idle = k.ring[:].rearrange("p b n -> p (b n)")
        seg, M = (idle[:, i * 2 * R * P:(i + 1) * 2 * R * P].rearrange("p (b r n) -> p b r n", b=2, r=R) for i in range(2))
        state = sb("state", [P, G, R * 64])
        yt = sb("yt", [P, 2, R * 64])
        (block, in_landed, dt_in, exp1, a_done, sums, sums_out, exp2, front, seg_done, dec_done, m_done, back, y_out,
         xd_done, st_done, x_used, skip_done, step) = c.enter_context(stage(
            nc, "in_landed dt_in exp1 a_done sums sums_out exp2 front seg_done dec_done m_done back y_out xd_done st_done x_used skip_done step"))
        units = [(ch, g) for ch in range(NT) for g in range(G)]
        N = len(units)
        BT = lambda ch, g: xbc[:, 8 + g, 3 + ch * P:3 + (ch + 1) * P]
        CT = lambda ch, g: xbc[:, 12 + g, 3 + ch * P:3 + (ch + 1) * P]
        xh = T["xh"][:].rearrange("p t (h d) -> p t h d", d=64)

        @block.sync
        def _(sp):
            for i, n in enumerate(("e_dt_bias_2", "e_A_log_2", "e_D_2")):
                sp.dma_start(par[:, i, :], bcast(A[n][0], 0, P)).then_inc(in_landed, 16)
            sp.dma_start(tri[:], k.K["causal"]).then_inc(in_landed, 16)
            sp.wait_ge(in_landed, 64)

        @block.gpsimd
        def _(pool):
            pool.wait_ge(in_landed, 64)
            for ch in range(NT):
                pool.wait_ge(x_used, ch + 1)
                nc.gpsimd.tensor_tensor(xh[:, ch], xh[:, ch], bcast(par[:, 2, :], 2, 64), ALU.mult).then_inc(skip_done, 1)
            pool.wait_ge(skip_done, NT)

        @block.scalar
        def _(act):
            act.wait_ge(in_landed, 64)
            nc.scalar.activation(par[:, 1, :], par[:, 1, :], ACT.Exp).then_inc(exp1, 1)
            act.wait_ge(dt_in, 1)
            nc.scalar.activation(e[:], e[:], ACT.Exp, scale=-1.0).then_inc(exp1, 1)
            act.wait_ge(sums_out, 1)
            nc.scalar.activation(eacs[:], eacs[:], ACT.Exp)
            nc.scalar.activation(dte[:], dte[:], ACT.Exp)
            nc.scalar.activation(etot[:], etot[:], ACT.Exp).then_inc(exp2, 1)
            for i, (ch, g) in enumerate(units):
                act.wait_ge(seg_done, i + 1)
                for r in range(R):
                    h = g * R + r
                    last = nc.scalar.activation(seg[:, i % 2, r, :], seg[:, i % 2, r, :], ACT.Exp, bias=nacs[:, ch, h:h + 1])
                last.then_inc(dec_done, 1)
            act.wait_ge(dec_done, N)

        @block.tensor
        def _(pe):
            pe.wait_ge(a_done, 1)
            for ch in range(NT):
                pe.matmul(k.ps[:, 0, ch * H:(ch + 1) * H], tri[:, 0, :], a[:, ch, :], start=True, stop=True)
                mm = pe.matmul(k.ps[:, 1, ch * H:(ch + 1) * H], ones[:], a[:, ch, :], start=True, stop=True)
            mm.then_inc(sums, 1)
            pe.wait_ge(sums_out, 1)
            warm_up(k, pe, 7, 26)
            for v in range(-1, N):
                if v + 1 < N:
                    i = v + 1
                    ch, g = units[i]
                    if i >= 2:
                        pe.wait_ge(m_done, i - 1)
                    pe.matmul(k.ps[:, i % 2, 0:P], BT(ch, g), CT(ch, g), start=True, stop=True)
                    for r in range(R):
                        h = g * R + r
                        mm = pe.matmul(k.ps[:, 2 + i % 2, r * P:(r + 1) * P], a[:, ch, h:h + 1].to_broadcast([P, P]), tri[:, 0, :],
                                       start=True, stop=True)
                    mm.then_inc(front, 1)
                if v >= 0:
                    ch, g = units[v]
                    pe.wait_ge(m_done, v + 1)
                    pe.wait_ge(xd_done, v + 1)
                    if v >= 2:
                        pe.wait_ge(y_out, v - 1)
                    if v >= G:
                        pe.wait_ge(st_done, v - G + 1)
                    for r in range(R):
                        pe.matmul(k.ps[:, 4 + v % 2, r * 64:(r + 1) * 64], M[:, v % 2, r, :], X[:, ch, g * R + r, :], start=True, stop=True)
                    if ch:
                        pe.matmul(k.ps[:, 4 + v % 2, 256:512], CT(ch, g), state[:, g, :], start=True, stop=True)
                    pe.matmul(k.ps[:, 6 + v % 2, 0:256], T["Bt"][:, ch, g, :], Xd[:, v % 2, :], start=True, stop=True).then_inc(back, 1)

        @block.vector
        def _(dve):
            link = Link(dve, step)
            V = nc.vector
            link(V.memset(ones[:], 1.0))
            dve.wait_ge(in_landed, 64)
            link(V.tensor_tensor(dt[:], dt[:], bcast(par[:, 0, :], 1, NT), ALU.add))
            link(V.scalar_tensor_tensor(e[:], dt[:], -1.0, dt[:], ALU.mult, ALU.max))
            dve.nop().then_inc(dt_in, 1)
            dve.wait_ge(exp1, 2)
            link(V.tensor_scalar(z[:], e[:], 2.0, None, ALU.add))
            link(V.reciprocal(z[:], z[:]))
            link(V.tensor_tensor(z[:], z[:], e[:], ALU.mult))
            link(V.tensor_tensor(z2[:], z[:], z[:], ALU.mult))
            link(V.tensor_scalar(acc[:], z2[:], 1.0 / 19, None, ALU.mult))
            for n in range(8, 0, -1):
                link(V.scalar_tensor_tensor(acc[:], acc[:], 1.0 / (2 * n + 1), z2[:], ALU.add, ALU.mult))
            link(V.scalar_tensor_tensor(acc[:], acc[:], 1.0, z[:], ALU.add, ALU.mult))
            link(V.tensor_scalar(dt[:], dt[:], 0.0, None, ALU.max))
            link(V.scalar_tensor_tensor(dt[:], acc[:], 2.0, dt[:], ALU.mult, ALU.add))
            link(V.tensor_tensor(a[:], dt[:], bcast(par[:, 1, :], 1, NT), ALU.mult))
            V.tensor_scalar(a[:], a[:], -1.0, None, ALU.mult).then_inc(a_done, 1)
            for ch in range(NT):
                V.tensor_tensor(X[:, ch], xh[:, ch], bcast(dt[:, ch, :], 2, 64), ALU.mult).then_inc(x_used, 1)
            dve.wait_ge(x_used, NT)
            dve.wait_ge(sums, 1)
            acs, tot = (k.ps[:, b, 0:NT * H].rearrange("p (t h) -> p t h", t=NT) for b in (0, 1))
            link(V.tensor_copy(cs[:], acs))
            link(V.tensor_scalar(nacs[:], cs[:], -1.0, None, ALU.mult))
            link(V.tensor_copy(eacs[:], cs[:]))
            link(V.tensor_copy(etot[:], tot))
            link(V.tensor_tensor(dte[:], etot[:], cs[:], ALU.subtract))
            dve.nop().then_inc(sums_out, 1)
            dve.wait_ge(exp2, 1)
            for j in range(-1, N + 1):
                if j + 1 < N:
                    i = j + 1
                    ch, g = units[i]
                    hs = slice(g * R, (g + 1) * R)
                    dve.wait_ge(front, i + 1)
                    if i >= 2:
                        dve.wait_ge(m_done, i - 1)
                    V.tensor_tensor(seg[:, i % 2], k.ps[:, 2 + i % 2, :].rearrange("p (r l) -> p r l", r=R), bcast(tri[:, 1, :], 1, R),
                                    ALU.add).then_inc(seg_done, 1)
                if 0 <= j < N:
                    dve.wait_ge(dec_done, j + 1)
                    if j >= 2:
                        dve.wait_ge(back, j - 1)
                    V.tensor_tensor(M[:, j % 2], seg[:, j % 2], bcast(k.ps[:, j % 2, 0:P], 1, R), ALU.mult).then_inc(m_done, 1)
                if j + 1 < N:
                    if i >= 2:
                        dve.wait_ge(back, i - 1)
                    V.tensor_tensor(Xd[:, i % 2, :].rearrange("p (r d) -> p r d", r=R), X[:, ch, hs], bcast(dte[:, ch, hs], 2, 64),
                                    ALU.mult).then_inc(xd_done, 1)
                if j >= 1:
                    v = j - 1
                    ch, g = units[v]
                    hs = slice(g * R, (g + 1) * R)
                    dve.wait_ge(back, v + 1)
                    dve.wait_ge(skip_done, ch + 1)
                    y = yt[:, v % 2, :].rearrange("p (r d) -> p r d", r=R)
                    diag = k.ps[:, 4 + v % 2, 0:256].rearrange("p (r d) -> p r d", r=R)
                    link(V.tensor_tensor(xh[:, ch, hs], xh[:, ch, hs], diag, ALU.add))
                    if ch:
                        off = k.ps[:, 4 + v % 2, 256:512].rearrange("p (r d) -> p r d", r=R)
                        link(V.tensor_tensor(y, off, bcast(eacs[:, ch, hs], 2, 64), ALU.mult))
                        link(V.tensor_tensor(xh[:, ch, hs], xh[:, ch, hs], y, ALU.add))
                        st = state[:, g, :].rearrange("p (r d) -> p r d", r=R)
                        link(V.tensor_tensor(st, st, bcast(etot[:, ch, hs], 2, 64), ALU.mult))
                        V.tensor_tensor(state[:, g, :], state[:, g, :], k.ps[:, 6 + v % 2, 0:256], ALU.add).then_inc(st_done, 1)
                    else:
                        V.tensor_copy(state[:, g, :], k.ps[:, 6 + v % 2, 0:256]).then_inc(st_done, 1)
                    dve.wait_ge(st_done, v + 1)
                    dve.nop().then_inc(y_out, 1)


def gate_rows(k, y, z):
    nc = k.nc
    with stage(nc, "done_dve done_pool") as (block, done_dve, done_pool):
        @block.vector
        def _(dve):
            for t in (0, 1, 2):
                nc.vector.tensor_tensor(y[:, t, :], y[:, t, :], z[:, t, :], ALU.mult).then_inc(done_dve, 1)
            dve.wait_ge(done_dve, 3)

        @block.gpsimd
        def _(pool):
            nc.gpsimd.tensor_tensor(y[:, 3, :], y[:, 3, :], z[:, 3, :], ALU.mult).then_inc(done_pool, 1)
            pool.wait_ge(done_pool, 1)


def column_of(k, row, n, out, factor=1.0):
    nc = k.nc
    with ExitStack() as c:
        raw = c.enter_context(nc.sbuf_tensor(fresh("rraw"), [max(n, 2), P], F32))
        block, landed, t_done, col_out = c.enter_context(stage(nc, "landed t_done col_out"))

        @block.sync
        def _(sp):
            sp.dma_start(raw[0:n, :], row.rearrange("(k p) -> k p", p=P)).then_inc(landed, 16)
            sp.wait_ge(landed, 16)

        @block.tensor
        def _(pe):
            pe.wait_ge(landed, 16)
            pe.transpose(k.ps[:, 0, 0:n], raw[0:n, :], k.ident[0:n, 0:n]).then_inc(t_done, 1)

        @block.vector
        def _(dve):
            dve.wait_ge(t_done, 1)
            nc.vector.tensor_scalar(out[:, 0:n], k.ps[:, 0, 0:n], factor, None, ALU.mult).then_inc(col_out, 1)
            dve.wait_ge(col_out, 1)


def diff_attention(k, qT, kT, v, bias, lam, lam_init, y):
    nc = k.nc
    with ExitStack() as c:
        sb = lambda n, s: c.enter_context(nc.sbuf_tensor(fresh(n), s, F32))
        lr = sb("lr", [P, 4, 64])
        lp = sb("lp", [P, 64])
        ld = sb("ld", [P, 2])
        nlam = sb("nlam", [P, 1])
        idle = k.ring[:].rearrange("p b (m n) -> p b m n", m=4)
        sc, pr = idle[:, :, 0:2, :], idle[:, :, 2:4, :]
        pT = sb("dpT", [P, 2, 512])
        mx, nm, ls = sb("dmx", [P, 2, 2]), sb("dnm", [P, 2, 2]), sb("dls", [P, 2, 2])
        block, in_landed, ld_done, ld_exp, s_ready, max_done, exp_done, p_ready, t_ready, t_out, o_ready, o_out, step = c.enter_context(
            stage(nc, "in_landed ld_done ld_exp s_ready max_done exp_done p_ready t_ready t_out o_ready o_out step"))
        units = [(h, t) for h in range(8) for t in range(NT)]
        N = len(units)
        W = lambda i: P * (units[i][1] + 1)

        @block.sync
        def _(sp):
            sp.dma_start(lr[:], bcast(lam, 0, P)).then_inc(in_landed, 16)
            sp.wait_ge(in_landed, 16)

        @block.tensor
        def _(pe):
            warm_up(k, pe, 7)
            for i in range(-1, N + 2):
                if i + 1 < N:
                    n = i + 1
                    h, t = units[n]
                    if n >= 2:
                        pe.wait_ge(max_done, n - 1)
                    for m in range(2):
                        mm = pe.matmul(k.ps[:, 2 * (n % 2) + m, 0:W(n)], qT[64 * m:64 * m + 64, h, t * P:(t + 1) * P],
                                       kT[64 * m:64 * m + 64, h, 0:W(n)], start=True, stop=True)
                    mm.then_inc(s_ready, 1)
                if 1 <= i <= N:
                    u = i - 1
                    pe.wait_ge(p_ready, u + 1)
                    if u >= 2:
                        pe.wait_ge(t_out, u - 1)
                    for j in range(W(u) // P):
                        mm = pe.transpose(k.ps[:, 4 + u % 2, j * P:(j + 1) * P], pr[:, u % 2, 0, j * P:(j + 1) * P], k.ident[:])
                    mm.then_inc(t_ready, 1)
                if i >= 2:
                    u = i - 2
                    h, t = units[u]
                    pe.wait_ge(t_out, u + 1)
                    if u >= 2:
                        pe.wait_ge(o_out, u - 1)
                    chain(pe, k.ps[:, 6 + u % 2, 0:P], lambda j: pT[:, u % 2, j * P:(j + 1) * P],
                          lambda j: v[:, j, h * P:(h + 1) * P], range(t + 1)).then_inc(o_ready, 1)

        @block.scalar
        def _(act):
            act.wait_ge(ld_done, 1)
            nc.scalar.activation(ld[:], ld[:], ACT.Exp).then_inc(ld_exp, 1)
            for i in range(N + 2):
                if i < N:
                    act.wait_ge(max_done, i + 1)
                    if i >= 2:
                        act.wait_ge(t_ready, i - 1)
                    for m in range(2):
                        last = nc.scalar.activation(pr[:, i % 2, m, 0:W(i)], sc[:, i % 2, m, 0:W(i)], ACT.Exp,
                                                    bias=nm[:, i % 2, m:m + 1], accum_out=ls[:, i % 2, m:m + 1])
                    last.then_inc(exp_done, 1)
                if 1 <= i <= N:
                    u = i - 1
                    act.wait_ge(t_ready, u + 1)
                    if u >= 2:
                        act.wait_ge(o_ready, u - 1)
                    nc.scalar.copy(pT[:, u % 2, 0:W(u)], k.ps[:, 4 + u % 2, 0:W(u)]).then_inc(t_out, 1)
                if i >= 2:
                    u = i - 2
                    h, t = units[u]
                    act.wait_ge(o_ready, u + 1)
                    nc.scalar.copy(y[:, t, h * P:(h + 1) * P], k.ps[:, 6 + u % 2, 0:P]).then_inc(o_out, 1)
            act.wait_ge(o_out, N)

        @block.vector
        def _(dve):
            link = Link(dve, step)
            V = nc.vector
            dve.wait_ge(in_landed, 16)
            for m in range(2):
                link(V.tensor_tensor_reduce(lp[:], lr[:, 2 * m, :], lr[:, 2 * m + 1, :], 1.0, 0.0, ALU.mult, ALU.add, ld[:, m:m + 1]))
            dve.nop().then_inc(ld_done, 1)
            dve.wait_ge(ld_exp, 1)
            link(V.tensor_tensor(nlam[:], ld[:, 1:2], ld[:, 0:1], ALU.subtract))
            link(V.tensor_scalar(nlam[:], nlam[:], -lam_init, None, ALU.add))
            for i in range(N + 1):
                if i < N:
                    h, t = units[i]
                    b = bias[:, h, 512 - W(i):512]
                    dve.wait_ge(s_ready, i + 1)
                    if i >= 2:
                        dve.wait_ge(exp_done, i - 1)
                    for m in range(2):
                        link(V.tensor_tensor_reduce(sc[:, i % 2, m, 0:W(i)], k.ps[:, 2 * (i % 2) + m, 0:W(i)], b, 1.0, 2 * NEG,
                                                    ALU.add, ALU.max, mx[:, i % 2, m:m + 1]))
                    V.tensor_scalar(nm[:, i % 2, :], mx[:, i % 2, :], -1.0, None, ALU.mult).then_inc(max_done, 1)
                if i >= 1:
                    u = i - 1
                    dve.wait_ge(exp_done, u + 1)
                    l = ls[:, u % 2, :]
                    link(V.reciprocal(l, l))
                    link(V.tensor_tensor(l[:, 1:2], l[:, 1:2], nlam[:], ALU.mult))
                    p0, p1 = (pr[:, u % 2, m, 0:W(u)] for m in range(2))
                    link(V.tensor_scalar(p0, p0, l[:, 0:1], None, ALU.mult))
                    V.scalar_tensor_tensor(p0, p1, l[:, 1:2], p0, ALU.mult, ALU.add).then_inc(p_ready, 1)
            dve.wait_ge(p_ready, N)


def head_norm_T(k, y, nh, width, mult, scale, out):
    nc = k.nc
    idle = k.ring[:].rearrange("p b n -> p (b n)")[:, 0:NT * D].rearrange("p (t n) -> p t n", t=NT)
    with ExitStack() as c:
        ms = c.enter_context(nc.sbuf_tensor(fresh("ms_h"), [P, NT, nh], F32))
        block, sq_done, ms_done, root_done, y_done, t_done, out_act, step = c.enter_context(
            stage(nc, "sq_done ms_done root_done y_done t_done out_act step"))
        nt = nh * width // P

        @block.scalar
        def _(act):
            for t in range(NT):
                nc.scalar.activation(idle[:, t, 0:nh * width], y[:, t, :], ACT.Square).then_inc(sq_done, 1)
            act.wait_ge(ms_done, 1)
            nc.scalar.activation(ms[:], ms[:], ACT.Sqrt).then_inc(root_done, 1)
            for q in range(nt):
                act.wait_ge(t_done, q + 1)
                if scale is None:
                    nc.scalar.copy(out[0][:, q, :], k.ps[:, q, :]).then_inc(out_act, 1)
                else:
                    nc.scalar.activation(out[0][:, q, :], k.ps[:, q, :], ACT.Copy, scale=scale).then_inc(out_act, 1)
            act.wait_ge(out_act, nt)

        @block.vector
        def _(dve):
            link = Link(dve, step)
            V = nc.vector
            for t in range(NT):
                dve.wait_ge(sq_done, t + 1)
                link(V.tensor_reduce(ms[:, t, :], idle[:, t, :].rearrange("p (h d) -> p h d", d=width), AX, ALU.add))
            V.tensor_scalar(ms[:], ms[:], 1.0 / width, RMS_EPS, ALU.mult, ALU.add).then_inc(ms_done, 1)
            dve.wait_ge(root_done, 1)
            link(V.reciprocal(ms[:], ms[:]))
            for t in range(NT):
                yv = y[:, t, :].rearrange("p (h d) -> p h d", d=width)
                link(V.tensor_tensor(yv, yv, bcast(ms[:, t, :], 2, width), ALU.mult))
                if mult is not None:
                    link(V.tensor_tensor(y[:, t, :], y[:, t, :], mult[:, t, :], ALU.mult))
                dve.nop().then_inc(y_done, 1)
            for q in range(nt):
                dve.wait_ge(out_act, q + 1)
                low, high = out[1][:, q, :], out[0][:, q, :].bitcast(F32)
                if scale is None:
                    link(V.tensor_tensor(low, k.ps[:, q, :], high, ALU.subtract))
                else:
                    link(V.scalar_tensor_tensor(low, k.ps[:, q, :], scale, high, ALU.mult, ALU.subtract))

        @block.tensor
        def _(pe):
            for t in range(NT):
                pe.wait_ge(y_done, t + 1)
                for q in range(nt):
                    mm = pe.transpose(k.ps[:, q, t * P:(t + 1) * P], y[:, t, q * P:(q + 1) * P], k.ident[:])
                    if t == NT - 1:
                        mm.then_inc(t_done, 1)


def transposed(k, src, nt, out, low=None):
    nc = k.nc
    with stage(nc, "t_done out_act out_dve") as (block, t_done, out_act, out_dve):
        @block.tensor
        def _(pe):
            for q in range(nt):
                for t in range(NT):
                    mm = pe.transpose(k.ps[:, q, t * P:(t + 1) * P], src(t, q), k.ident[:])
                mm.then_inc(t_done, 1)

        @block.scalar
        def _(act):
            for q in range(nt):
                act.wait_ge(t_done, q + 1)
                nc.scalar.copy(out[:, q, :], k.ps[:, q, :]).then_inc(out_act, 1)
            act.wait_ge(out_act, nt)

        @block.vector
        def _(dve):
            if low is not None:
                for q in range(nt):
                    dve.wait_ge(out_act, q + 1)
                    nc.vector.tensor_tensor(low[:, q, :], k.ps[:, q, :], out[:, q, :].bitcast(F32), ALU.subtract).then_inc(out_dve, 1)
                dve.wait_ge(out_dve, nt)


def even_mixer(k, h, hT, y):
    nc, A = k.nc, k.A
    w = A["e_w_in_2"][0].rearrange("(k p) n -> p k n", p=P)
    wo = A["e_w_out_2"][0].rearrange("(k p) n -> p k n", p=P)
    with ExitStack() as m:
        yd = m.enter_context(nc.sbuf_tensor(fresh("y_diff"), [P, NT, D], F32))
        dn = m.enter_context(nc.sbuf_tensor(fresh("dn"), [P, 1], F32))
        lam_init = 0.8 - 0.6 * math.exp(-0.3 * 0)
        with ExitStack() as c:
            sb = lambda n, s: c.enter_context(nc.sbuf_tensor(fresh(n), s, F32))
            qT, kT, v = sb("qT", [P, 8, S]), sb("kT", [P, 8, S]), sb("v_tok", [P, NT, D])
            plan = [(3088 + 512 * s, 512, "feature", HD ** -0.5, [qT[:, 4 * s + j, :] for j in range(4)]) for s in range(2)]
            plan += [(4112 + 512 * s, 512, "feature", 1.0, [kT[:, 4 * s + j, :] for j in range(4)]) for s in range(2)]
            plan += [(5136 + 512 * s, 512, "token", 1.0, [v[:, t, 512 * s:512 * (s + 1)] for t in range(NT)]) for s in range(2)]
            bias = sb("bias", [P, 8, 512])
            project(k, w, hT, plan, loads=bias_loads(k, bias, 0))
            diff_attention(k, qT, kT, v, bias, A["e_lambda_2"][0], lam_init, yd)
        column_of(k, A["e_diff_norm_2"][0], 1, dn, 1.0 - lam_init)
        ydT = pair_of(nc, m, "y_diffT", [P, KD, S])
        head_norm_T(k, yd, 8, P, None, dn[:, 0:1], ydT)
        out_projection(k, wo[:, KD:2 * KD, :], ydT, KD, y, True)
    with ExitStack() as c:
        sb = lambda n, s: c.enter_context(nc.sbuf_tensor(fresh(n), s, F32))
        T = {"xh": sb("xh", [P, NT, D]), "dt": sb("dt", [P, NT, SSD_HEADS])}
        z = sb("z", [P, NT, D])
        nw = sb("nw", [P, KD])
        with ExitStack() as d:
            xbc = d.enter_context(nc.sbuf_tensor(fresh("xbcT"), [P, 16, S + 3], F32))
            T["dtT"] = d.enter_context(nc.sbuf_tensor(fresh("dtT"), [SSD_HEADS, S], F32))
            T["Bt"] = d.enter_context(nc.sbuf_tensor(fresh("B_tok"), [P, NT, SSD_GROUPS, P], F32))
            plan = [(1024 + 512 * s, 512, "feature", 1.0, [xbc[:, 4 * s + j, 3:3 + S] for j in range(4)]) for s in range(4)]
            plan += [(512 * s, 512, "token", "silu", [z[:, t, 512 * s:512 * (s + 1)] for t in range(NT)]) for s in range(2)]
            plan += [(3072, SSD_HEADS, "few", 1.0, [T["dtT"][:]])]
            project(k, w, hT, plan)
            h.close()
            convolution(k, xbc, T)
            ssd(k, xbc, T)
        gate_rows(k, T["xh"], z)
        column_of(k, A["e_ssd_norm_2"][0], KD, nw)
        ysT = pair_of(nc, c, "y_ssdT", [P, KD, S])
        norm_to_hT(k, ysT, True, RMS_EPS, nw, None, src=T["xh"])
        out_projection(k, wo[:, 0:KD, :], ysT, KD, y, False)


def retention_inputs(k, T):
    nc = k.nc
    H = RET_HEADS
    idle = k.ring[:].rearrange("p b n -> p (b n)")
    ro = [idle[:, i * 2048:(i + 1) * 2048].rearrange("p (t h e j) -> p t h e j", t=NT, h=H, e=2) for i in range(2)]
    with ExitStack() as c:
        sb = lambda n, s: c.enter_context(nc.sbuf_tensor(fresh(n), s, F32))
        t1 = sb("t1r", [P, NT, H, 64])
        cs = sb("cs2", [P, 2, NT, 64])
        xi = sb("xi", [P, H, P])
        zeta = sb("zeta", [P, H])
        block, in_landed, ro_done, t_done, out_act, x_done, step = c.enter_context(
            stage(nc, "in_landed ro_done t_done out_act x_done step"))

        @block.sync
        def _(sp):
            for dst, n in ((cs, "rope2"), (xi, "ret_xi"), (zeta, "ret_zeta")):
                sp.dma_start(dst[:], k.K[n]).then_inc(in_landed, 16)
            sp.wait_ge(in_landed, 48)

        @block.vector
        def _(dve):
            link = Link(dve, step)
            V = nc.vector
            dve.wait_ge(in_landed, 48)
            for i, n in enumerate(("rq", "rk")):
                for t in range(NT):
                    x = T[n][:, t, :].rearrange("p (h e j) -> p h e j", h=H, e=2)
                    o, cos, sin, tt = ro[i][:, t], bcast(cs[:, 0, t, :], 1, H), bcast(cs[:, 1, t, :], 1, H), t1[:, t]
                    link(V.tensor_tensor(o[:, :, 0, :], x[:, :, 0, :], cos, ALU.mult))
                    link(V.tensor_tensor(tt, x[:, :, 1, :], sin, ALU.mult))
                    link(V.tensor_tensor(o[:, :, 0, :], o[:, :, 0, :], tt, ALU.subtract))
                    link(V.tensor_tensor(o[:, :, 1, :], x[:, :, 0, :], sin, ALU.mult))
                    link(V.tensor_tensor(tt, x[:, :, 1, :], cos, ALU.mult))
                    link(V.tensor_tensor(o[:, :, 1, :], o[:, :, 1, :], tt, ALU.add))
                    dve.nop().then_inc(ro_done, 1)
            for h in range(H):
                dve.wait_ge(out_act, h + 1)
                nc.vector.tensor_tensor(T["QxT"][:, h, :].rearrange("p (t l) -> p t l", t=NT), k.ps[:, h, :].rearrange("p (t l) -> p t l", t=NT),
                                        bcast(xi[:, h, :], 1, NT), ALU.mult).then_inc(x_done, 1)
                kz = T["rk"][:].rearrange("p t (h d) -> p t h d", h=H)[:, :, h, :]
                link(V.tensor_scalar(kz, ro[1][:, :, h].rearrange("p t e j -> p t (e j)"), zeta[:, h:h + 1], None, ALU.mult))
            dve.wait_ge(x_done, H)

        @block.scalar
        def _(act):
            for q in range(2 * H):
                act.wait_ge(t_done, q + 1)
                nc.scalar.copy((T["QT"] if q < H else T["KT"])[:, q % H, :], k.ps[:, q, :]).then_inc(out_act, 1)
            act.wait_ge(out_act, 2 * H)

        @block.tensor
        def _(pe):
            for i in range(2):
                for t in range(NT):
                    pe.wait_ge(ro_done, NT * i + t + 1)
                    for h in range(H):
                        mm = pe.transpose(k.ps[:, 4 * i + h, t * P:(t + 1) * P], ro[i][:, t, h].rearrange("p e j -> p (e j)"), k.ident[:])
                        if t == NT - 1:
                            mm.then_inc(t_done, 1)


def retention(k, T, y):
    nc = k.nc
    H = RET_HEADS
    with ExitStack() as c:
        sb = lambda n, s: c.enter_context(nc.sbuf_tensor(fresh(n), s, F32))
        dec = sb("dec", [P, H, P])
        sT = sb("sT", [P, 2, P])
        state = sb("rstate", [P, H, RET_V])
        block, in_landed, front, s_done, back, y_out, st_done, step = c.enter_context(
            stage(nc, "in_landed front s_done back y_out st_done step"))
        units = [(ch, h) for ch in range(NT) for h in range(H)]
        N = len(units)

        @block.sync
        def _(sp):
            sp.dma_start(dec[:], k.K["ret_decay"]).then_inc(in_landed, 16)
            sp.wait_ge(in_landed, 16)

        @block.tensor
        def _(pe):
            warm_up(k, pe, 6)
            for i in range(N + 1):
                if i < N:
                    ch, h = units[i]
                    if i >= 2:
                        pe.wait_ge(s_done, i - 1)
                    at = slice(ch * P, (ch + 1) * P)
                    pe.matmul(k.ps[:, i % 2, 0:P], T["KT"][:, h, at], T["QT"][:, h, at], start=True, stop=True).then_inc(front, 1)
                if i >= 1:
                    v = i - 1
                    ch, h = units[v]
                    at, vv = slice(ch * P, (ch + 1) * P), T["rv"][:, ch, h * RET_V:(h + 1) * RET_V]
                    pe.wait_ge(s_done, v + 1)
                    if v >= 2:
                        pe.wait_ge(y_out, v - 1)
                    if v >= H:
                        pe.wait_ge(st_done, v - H + 1)
                    pe.matmul(k.ps[:, 2 + v % 2, 0:RET_V], sT[:, v % 2, :], vv, start=True, stop=ch == 0)
                    if ch:
                        pe.matmul(k.ps[:, 2 + v % 2, 0:RET_V], T["QxT"][:, h, at], state[:, h, :], start=False, stop=True)
                    pe.matmul(k.ps[:, 4 + v % 2, 0:RET_V], T["rk"][:, ch, h * P:(h + 1) * P], vv, start=True, stop=True).then_inc(back, 1)

        @block.vector
        def _(dve):
            V = nc.vector
            dve.wait_ge(in_landed, 16)
            for i in range(N + 1):
                if i < N:
                    ch, h = units[i]
                    dve.wait_ge(front, i + 1)
                    if i >= 2:
                        dve.wait_ge(back, i - 1)
                    V.tensor_tensor(sT[:, i % 2, :], k.ps[:, i % 2, 0:P], dec[:, h, :], ALU.mult).then_inc(s_done, 1)
                if i >= 1:
                    v = i - 1
                    ch, h = units[v]
                    dve.wait_ge(back, v + 1)
                    new = k.ps[:, 4 + v % 2, 0:RET_V]
                    if ch:
                        dve.wait_ge(st_done, v - H + 1)
                        V.scalar_tensor_tensor(state[:, h, :], state[:, h, :], RET_STATE_DECAY[h], new, ALU.mult, ALU.add).then_inc(st_done, 1)
                    else:
                        V.tensor_copy(state[:, h, :], new).then_inc(st_done, 1)
                    dve.wait_ge(st_done, v + 1)
                    V.tensor_copy(y[:, ch, h * RET_V:(h + 1) * RET_V], k.ps[:, 2 + v % 2, 0:RET_V]).then_inc(y_out, 1)
            dve.wait_ge(y_out, N)


def window_bias(k, sw, sink):
    nc = k.nc
    with ExitStack() as c:
        wm = c.enter_context(nc.sbuf_tensor(fresh("wm"), [P, P], F32))
        block, in_landed, done = c.enter_context(stage(nc, "in_landed done"))

        @block.sync
        def _(sp):
            sp.dma_start(wm[:], k.K["win_mask"]).then_inc(in_landed, 16)
            sp.dma_start(sink[:], bcast(k.A["o_sinks_2"][0], 0, P)).then_inc(in_landed, 16)
            sp.wait_ge(in_landed, 32)

        @block.vector
        def _(dve):
            dve.wait_ge(in_landed, 32)
            nc.vector.tensor_tensor(sw[:, :, 0:P], sw[:, :, 0:P], bcast(wm[:], 1, 8), ALU.add).then_inc(done, 1)
            dve.wait_ge(done, 1)


def odd_mixer(k, h, hT, y):
    nc, A = k.nc, k.A
    w = A["o_w_in_2"][0].rearrange("(k p) n -> p k n", p=P)
    wo = A["o_w_out_2"][0].rearrange("(k p) n -> p k n", p=P)
    with ExitStack() as m:
        sb = lambda n, s: m.enter_context(nc.sbuf_tensor(fresh(n), s, F32))
        sqT, skv, sw = sb("sqT", [P, 4, S]), sb("skv", [P, NT, 256]), sb("sw", [P, 8, 256])
        with ExitStack() as c:
            sc = lambda n, s: c.enter_context(nc.sbuf_tensor(fresh(n), s, F32))
            T = {n: sc(n, s) for n, s in (("rq", [P, NT, 512]), ("rk", [P, NT, 512]), ("rv", [P, NT, D]), ("rg", [P, NT, D]))}
            half = lambda t, s: [T[t][:, j, 512 * s:512 * (s + 1)] for j in range(NT)]
            plan = [(0, 512, "token", 1.0, half("rq", 0)), (512, 512, "token", 1.0, half("rk", 0)),
                    (1024, 512, "token", 1.0, half("rv", 0)), (1536, 512, "token", 1.0, half("rv", 1)),
                    (2048, 512, "token", "silu", half("rg", 0)), (2560, 512, "token", "silu", half("rg", 1)),
                    (3072, 512, "feature", HD ** -0.5, [sqT[:, j, :] for j in range(4)]),
                    (3584, 256, "token", 1.0, [skv[:, j, :] for j in range(NT)])]
            project(k, w, hT, plan, loads=bias_loads(k, sw, 256))
            h.close()
            yr = sc("y_ret", [P, NT, D])
            with ExitStack() as d:
                for n in ("QT", "QxT", "KT"):
                    T[n] = d.enter_context(nc.sbuf_tensor(fresh(n), [P, RET_HEADS, S], F32))
                retention_inputs(k, T)
                retention(k, T, yr)
            yrT = pair_of(nc, c, "y_retT", [P, KD, S])
            head_norm_T(k, yr, RET_HEADS, RET_V, T["rg"], None, yrT)
            out_projection(k, wo[:, 0:KD, :], yrT, KD, y, True)
        with ExitStack() as c:
            sc = lambda n, s: c.enter_context(nc.sbuf_tensor(fresh(n), s, F32))
            k2, kT, so, sink = sc("k2", [P, NT, 4, HD]), sc("skT", [P, 2, S]), sc("so", [P, NT, 512]), sc("sink", [P, 8])
            soT = pair_of(nc, c, "soT", [P, 4, S])
            window_bias(k, sw, sink)
            twice(k, skv, k2)
            transposed(k, lambda t, q: k2[:, t, 2 * q:2 * q + 2, :].rearrange("p h d -> p (h d)"), 2, kT)
            units = []
            for h in range(8):
                p0, g = 64 * (h % 2), h // 4
                for t in range(NT):
                    a = max(0, t - 1)
                    units.append(dict(q=sqT[p0:p0 + 64, h // 2, t * P:(t + 1) * P], k=kT[p0:p0 + 64, g, a * P:(t + 1) * P],
                                      bias=sw[:, h, 0 if t else P:256], sink=sink[:, h:h + 1],
                                      v=[skv[:, j, P + HD * g:P + HD * (g + 1)] for j in range(a, t + 1)],
                                      out=so[:, t, h * HD:(h + 1) * HD]))
            attention(k, units)
            transposed(k, lambda t, q: so[:, t, q * P:(q + 1) * P], 4, soT[0], soT[1])
            out_projection(k, wo[:, KD:KD + 4, :], soT, 4, y, False)


def twice(k, skv, k2):
    nc = k.nc
    with stage(nc, "done spare") as (block, done, _s):
        @block.vector
        def _(dve):
            for t in range(NT):
                for g in range(2):
                    nc.vector.tensor_copy(k2[:, t, 2 * g:2 * g + 2, :], bcast(skv[:, t, g * HD:(g + 1) * HD], 1, 2)).then_inc(done, 1)
            dve.wait_ge(done, 2 * NT)


def second_block(k, out):
    nc, A = k.nc, k.A
    mid = k.scratch[2 * S * D:3 * S * D]
    with ExitStack() as c:
        sb = lambda n, s: c.enter_context(nc.sbuf_tensor(fresh(n), s, F32))
        y = sb("y", [P, NT, D])
        def modulation(n):
            if n == 2 * DEPTH:
                return None
            layer, half = divmod(n, 2)
            return (k.sums[n][:, 0:24 * P], A["mod_b_2"][layer, half], 24, k.mod, (8,), A["norm_gains_2"][layer, 2 * half:2 * half + 2])

        relative_bias(k, modulation(0), mid.rearrange("(t p d) -> p t d", p=P, d=D))
        kp = lambda ap: ap.rearrange("(k p) n -> p k n", p=P)
        for layer in range(DEPTH):
            for half in range(2):
                with ExitStack() as h:
                    hT = pair_of(nc, h, "hT", [P, KD, S], side="right")
                    norm_to_hT(k, hT, True, RMS_EPS, k.mod[:, 8:16], k.mod[:, 0:8])
                    if half:
                        mlp(k, kp(A["mlp_w1_2"][layer]), kp(A["mlp_w2_2"][layer]), hT, y)
                    elif layer % 2 == 0:
                        even_mixer(k, h, hT, y)
                    else:
                        odd_mixer(k, h, hT, y)
                last = layer == DEPTH - 1 and half == 1
                add_normed(k, y, k.mod[:, 16:24], modulation(2 * layer + half + 1), out[0].rearrange("(t p) d -> p t d", p=P) if last else None)


_INS = ["x", "c", "w_ada", "b_ada", "w_in", "q_norm_g", "k_norm_g", "w_branch_a", "w_branch_b", "w_out", "ln1_g", "ln1_b",
        "w_router", "router_bias", "w_exp_gate", "w_exp_up", "w_exp_down", "ln2_g", "ln2_b", "c_2", "rel_bias_2",
        "norm_gains_2", "mod_w_2", "mod_b_2", "mlp_w1_2", "mlp_w2_2", "e_w_in_2", "e_conv_w_2", "e_conv_b_2",
        "e_dt_bias_2", "e_A_log_2", "e_D_2", "e_ssd_norm_2", "e_lambda_2", "e_diff_norm_2", "e_w_out_2", "o_w_in_2",
        "o_sinks_2", "o_w_out_2"]


def build(nc, A, K, out):
    with ExitStack() as c:
        k = Core(nc, c, A, K)
        first_block(k)
        second_block(k, out)


def kernel(**inputs):
    import numpy as _np
    import concourse.bacc as _bacc
    from concourse import mybir as _mybir
    from concourse.bass_utils import run_bass_kernel_spmd as _run

    nc = _bacc.Bacc("TRN2", target_bir_lowering=False, num_devices=1)
    arrays, args, consts = {}, {}, {}
    for name in _INS:
        a = _np.ascontiguousarray(inputs[name])
        arrays[f"in_{name}_dram"] = a
        args[name] = nc.dram_tensor(f"in_{name}_dram", a.shape, _mybir.dt.from_np(a.dtype), kind="ExternalInput").ap()
    for name, a in constants().items():
        arrays[f"const_{name}_dram"] = a
        consts[name] = nc.dram_tensor(f"const_{name}_dram", a.shape, _mybir.dt.from_np(a.dtype), kind="ExternalInput").ap()
    out = nc.dram_tensor("out_0_dram", (1, S, D), _mybir.dt.float32, kind="ExternalOutput").ap()
    build(nc, args, consts, out)
    r = _run(nc, [arrays], core_ids=[0])
    return r.results[0]["out_0_dram"]
```
